# Optimizing a Trainium2 kernel written in Bass

```python
import math
import jax, jax.numpy as jnp
from jax import lax
import numpy as np

D_MODEL = 2048
BATCH = 1
SEQ = 256
DEPTH = 1

GRID_W = 64
CTX_LEN = 256
EPS = 1e-6
RWKV_HEADS = 16
RWKV_HEAD = 64
RWKV_DIM = RWKV_HEADS * RWKV_HEAD
DECAY_LORA = 96
AAA_LORA = 96
GATE_LORA = 256
N_DIR = 2
DECAY_SCALE = math.exp(-0.5)
LNX_EPS = 64e-5
MLA_HEADS = 16
Q_LORA = 512
KV_LORA = 512
QK_NOPE = 128
QK_ROPE = 64
V_HEAD = 128
ROPE_THETA = 10000.0
ATTN_SCALE = (QK_NOPE + QK_ROPE) ** -0.5
Q_BLOCK = 128
D_FF = 5632
CONV_W = 3
N_BRANCH = 2
RWKV_IN = 3 * RWKV_DIM + N_DIR * DECAY_LORA + N_DIR * AAA_LORA + GATE_LORA
MLA_IN = Q_LORA + KV_LORA + QK_ROPE
GATE_IN = N_BRANCH * D_MODEL
D_IN = RWKV_IN + MLA_IN + GATE_IN
RWKV_SPLITS = [RWKV_DIM, 2 * RWKV_DIM, 3 * RWKV_DIM,
               3 * RWKV_DIM + N_DIR * DECAY_LORA,
               3 * RWKV_DIM + N_DIR * (DECAY_LORA + AAA_LORA)]


def rms_norm(x, g, eps=EPS):
    xf = x.astype(jnp.float32)
    y = xf * lax.rsqrt(jnp.mean(xf * xf, axis=-1, keepdims=True) + eps)
    return (y * g.astype(jnp.float32)).astype(x.dtype)

def modulate(h, shift, scale):
    return h * (1.0 + scale) + shift

def centred_shift(x):
    xp = jnp.pad(x, ((0, 0), (1, 1), (0, 0)))
    return 0.5 * (xp[:, :-2] + xp[:, 2:])

def depthwise_conv(x, w, b):
    T = x.shape[1]
    pad = CONV_W // 2
    xp = jnp.pad(x, ((0, 0), (pad, pad), (0, 0)))
    y = b
    for j in range(CONV_W):
        y = y + xp[:, j:j + T] * w[j]
    return y

def axial_angles(n_tok):
    rows = n_tok // GRID_W
    row = jnp.repeat(jnp.arange(rows), GRID_W).astype(jnp.float32)
    col = jnp.tile(jnp.arange(GRID_W), rows).astype(jnp.float32)
    half = QK_ROPE // 2
    freqs = ROPE_THETA ** (-jnp.arange(0, half, 2, dtype=jnp.float32) / half)
    return row[:, None] * freqs, col[:, None] * freqs

def rotate(x, ang):
    x1, x2 = jnp.split(x, 2, axis=-1)
    cs, sn = jnp.cos(ang).astype(x.dtype), jnp.sin(ang).astype(x.dtype)
    return jnp.concatenate([x1 * cs - x2 * sn, x1 * sn + x2 * cs], axis=-1)

def rope_2d(x, ang_row, ang_col):
    xr, xc = jnp.split(x, 2, axis=-1)
    return jnp.concatenate([rotate(xr, ang_row), rotate(xc, ang_col)], axis=-1)

def wkv7_scan(r, w, k, v, kk, a, s0, reverse, emit):
    def step(S, inp):
        r_t, w_t, k_t, v_t, kk_t, a_t = inp
        sa = jnp.einsum('bhvk,bhk->bhv', S, -kk_t)
        S = (S * w_t[:, :, None, :] + sa[..., None] * (kk_t * a_t)[:, :, None, :]
             + v_t[..., None] * k_t[:, :, None, :])
        y = jnp.einsum('bhvk,bhk->bhv', S, r_t) if emit else None
        return S, y
    xs = tuple(jnp.moveaxis(t, 1, 0) for t in (r, w, k, v, kk, a))
    s_fin, ys = lax.scan(step, s0, xs, reverse=reverse)
    return (jnp.moveaxis(ys, 0, 1) if emit else None), s_fin

def rwkv_branch(p, s0, P, emit):
    B, T, _ = p.shape
    f32 = jnp.float32
    heads = lambda t: t.reshape(B, T, RWKV_HEADS, RWKV_HEAD).astype(f32)
    p = p + P['rwkv_mu'] * (centred_shift(p) - p)
    r, k, v, wl, al, gl = jnp.split(p, RWKV_SPLITS, axis=-1)
    wl = wl.reshape(B, T, N_DIR, DECAY_LORA)
    al = al.reshape(B, T, N_DIR, AAA_LORA)
    w_raw = P['rwkv_w0'] + jnp.einsum('btdr,drc->btdc', jnp.tanh(wl), P['rwkv_w2'])
    decay = jnp.exp(-DECAY_SCALE * jax.nn.sigmoid(w_raw.astype(f32)))
    a = jax.nn.sigmoid((P['rwkv_a0'] + jnp.einsum('btdr,drc->btdc', al, P['rwkv_a2'])).astype(f32))
    kk = heads(k * P['rwkv_k_k'])
    kk = kk / jnp.maximum(jnp.sqrt(jnp.sum(kk * kk, axis=-1, keepdims=True)), 1e-12)
    k_dir = k[:, :, None, :].astype(f32) * (1.0 + (a - 1.0) * P['rwkv_k_a'].astype(f32))
    r_h, v_h = heads(r), heads(v)
    ys, states = [], []
    for d in range(N_DIR):
        y_d, s_d = wkv7_scan(r_h, heads(decay[:, :, d]), heads(k_dir[:, :, d]), v_h, kk,
                             heads(a[:, :, d]), s0[d], reverse=(d == 1), emit=emit)
        ys.append(y_d)
        states.append(s_d)
    s_fin = jnp.stack(states)
    if not emit:
        return None, s_fin
    y = ys[0] + ys[1]
    mu = jnp.mean(y, axis=-1, keepdims=True)
    var = jnp.mean(jnp.square(y - mu), axis=-1, keepdims=True)
    yn = ((y - mu) * lax.rsqrt(var + LNX_EPS)).reshape(B, T, RWKV_DIM)
    yn = yn * P['rwkv_lnx_w'] + P['rwkv_lnx_b']
    k_bar = heads(0.5 * (k_dir[:, :, 0] + k_dir[:, :, 1]))
    bonus = (jnp.sum(r_h * k_bar * P['rwkv_r_k'].astype(f32), axis=-1, keepdims=True) * v_h).reshape(B, T, RWKV_DIM)
    g = jax.nn.sigmoid(gl) @ P['rwkv_g2']
    return ((yn + bonus).astype(p.dtype) * g), s_fin

def mla_kv(p_mla, P, ang):
    B, T, _ = p_mla.shape
    ckv = rms_norm(p_mla[..., Q_LORA:Q_LORA + KV_LORA], P['mla_kv_norm'])
    kpe = p_mla[..., Q_LORA + KV_LORA:]
    kv = (ckv @ P['mla_w_ukv']).reshape(B, T, MLA_HEADS, QK_NOPE + V_HEAD)
    k_nope, v = kv[..., :QK_NOPE], kv[..., QK_NOPE:]
    if ang is not None:
        kpe = rope_2d(kpe, ang[0], ang[1])
    k = jnp.concatenate([k_nope, jnp.broadcast_to(kpe[:, :, None, :], (B, T, MLA_HEADS, QK_ROPE))], axis=-1)
    return k, v

def mla_q(p_mla, P, ang):
    B, T, _ = p_mla.shape
    cq = rms_norm(p_mla[..., :Q_LORA], P['mla_q_norm'])
    q = (cq @ P['mla_w_uq']).reshape(B, T, MLA_HEADS, QK_NOPE + QK_ROPE)
    if ang is not None:
        q = jnp.concatenate([q[..., :QK_NOPE], rope_2d(q[..., QK_NOPE:], ang[0][:, None], ang[1][:, None])], axis=-1)
    return q

def softmax_attend(q, k, v):
    s = jnp.einsum('bqhd,bkhd->bhqk', q, k).astype(jnp.float32) * ATTN_SCALE
    pr = jax.nn.softmax(s, axis=-1).astype(v.dtype)
    return jnp.einsum('bhqk,bkhd->bqhd', pr, v)

def blocked_attention(q, k, v):
    B, T, H, Dk = q.shape
    nb = T // Q_BLOCK
    qb = jnp.moveaxis(q.reshape(B, nb, Q_BLOCK, H, Dk), 1, 0)
    ob = lax.map(lambda qi: softmax_attend(qi, k, v), qb)
    return jnp.moveaxis(ob, 0, 1).reshape(B, T, H, v.shape[-1])

def token_mixer(h, s0, ang, kv_prefix, P, emit):
    B, T, _ = h.shape
    p = h @ P['w_in']
    p_rwkv, p_mla, p_gate = jnp.split(p, [RWKV_IN, RWKV_IN + MLA_IN], axis=-1)
    y_rwkv, s_fin = rwkv_branch(p_rwkv, s0, P, emit)
    k, v = mla_kv(p_mla, P, ang)
    if not emit:
        return None, s_fin, (k, v)
    q = mla_q(p_mla, P, ang)
    if kv_prefix is not None:
        k_all = jnp.concatenate([kv_prefix[0], k], axis=1)
        v_all = jnp.concatenate([kv_prefix[1], v], axis=1)
    else:
        k_all, v_all = k, v
    o = blocked_attention(q, k_all, v_all).reshape(B, T, MLA_HEADS * V_HEAD)
    g_rwkv, g_mla = jnp.split(jax.nn.sigmoid(p_gate + P['gate_b']), N_BRANCH, axis=-1)
    merged = g_rwkv * (y_rwkv @ P['w_rwkv_proj']) + g_mla * (o @ P['w_mla_proj'])
    return merged @ P['w_out'], s_fin, (k, v)

def conv_ffn(h, P):
    u = depthwise_conv(h @ P['ffn_w_gate'], P['ffn_conv_w'], P['ffn_conv_b'])
    return (jax.nn.gelu(u, approximate=True) * (h @ P['ffn_w_val'])) @ P['ffn_w_down']

def first_inputs(seed: int = 0) -> dict:
    key = jax.random.key(seed)
    ks = jax.random.split(key, 40)
    L, D, C, H = DEPTH, D_MODEL, RWKV_DIM, MLA_HEADS
    nrm = lambda k, shape, s: jax.random.normal(k, shape, jnp.float32) * s
    gain = lambda k, shape: 1.0 + 0.02 * jax.random.normal(k, shape, jnp.float32)
    return {
        'x': nrm(ks[0], (BATCH, SEQ, D), 1.0),
        'c': nrm(ks[1], (BATCH, D), 1.0),
        'ctx': nrm(ks[2], (BATCH, CTX_LEN, D), 1.0),
        'c_ctx': nrm(ks[3], (D,), 1.0),
        'w_ada': nrm(ks[4], (L, D, 6 * D), 0.5 * D ** -0.5),
        'b_ada': nrm(ks[5], (L, 6 * D), 0.02),
        'norm_mix_pre': gain(ks[6], (L, D)),
        'norm_mix_post': gain(ks[7], (L, D)),
        'norm_ffn_pre': gain(ks[8], (L, D)),
        'norm_ffn_post': gain(ks[9], (L, D)),
        'w_in': nrm(ks[10], (L, D, D_IN), D ** -0.5),
        'rwkv_mu': jax.random.uniform(ks[11], (L, RWKV_IN), jnp.float32),
        'rwkv_w0': nrm(ks[12], (L, N_DIR, C), 0.5),
        'rwkv_w2': nrm(ks[13], (L, N_DIR, DECAY_LORA, C), 0.5 * DECAY_LORA ** -0.5),
        'rwkv_a0': nrm(ks[14], (L, N_DIR, C), 0.5),
        'rwkv_a2': nrm(ks[15], (L, N_DIR, AAA_LORA, C), 0.5 * AAA_LORA ** -0.5),
        'rwkv_k_k': 0.85 + 0.05 * jax.random.normal(ks[16], (L, C), jnp.float32),
        'rwkv_k_a': gain(ks[17], (L, C)),
        'rwkv_r_k': nrm(ks[18], (L, RWKV_HEADS, RWKV_HEAD), 0.1),
        'rwkv_lnx_w': gain(ks[19], (L, C)),
        'rwkv_lnx_b': nrm(ks[20], (L, C), 0.02),
        'rwkv_g2': nrm(ks[21], (L, GATE_LORA, C), GATE_LORA ** -0.5),
        'w_rwkv_proj': nrm(ks[22], (L, C, D), C ** -0.5),
        'mla_q_norm': gain(ks[23], (L, Q_LORA)),
        'mla_kv_norm': gain(ks[24], (L, KV_LORA)),
        'mla_w_uq': nrm(ks[25], (L, Q_LORA, H * (QK_NOPE + QK_ROPE)), Q_LORA ** -0.5),
        'mla_w_ukv': nrm(ks[26], (L, KV_LORA, H * (QK_NOPE + V_HEAD)), KV_LORA ** -0.5),
        'w_mla_proj': nrm(ks[27], (L, H * V_HEAD, D), (H * V_HEAD) ** -0.5),
        'gate_b': nrm(ks[28], (L, GATE_IN), 0.02),
        'w_out': nrm(ks[29], (L, D, D), D ** -0.5),
        'ffn_w_gate': nrm(ks[30], (L, D, D_FF), D ** -0.5),
        'ffn_w_val': nrm(ks[31], (L, D, D_FF), D ** -0.5),
        'ffn_conv_w': nrm(ks[32], (L, CONV_W, D_FF), CONV_W ** -0.5),
        'ffn_conv_b': nrm(ks[33], (L, D_FF), 0.02),
        'ffn_w_down': nrm(ks[34], (L, D_FF, D), D_FF ** -0.5),
    }

def first_block(x, c, ctx, c_ctx, w_ada, b_ada, norm_mix_pre, norm_mix_post, norm_ffn_pre, norm_ffn_post,
              w_in, rwkv_mu, rwkv_w0, rwkv_w2, rwkv_a0, rwkv_a2, rwkv_k_k, rwkv_k_a, rwkv_r_k,
              rwkv_lnx_w, rwkv_lnx_b, rwkv_g2, w_rwkv_proj, mla_q_norm, mla_kv_norm, mla_w_uq, mla_w_ukv,
              w_mla_proj, gate_b, w_out, ffn_w_gate, ffn_w_val, ffn_conv_w, ffn_conv_b, ffn_w_down):
    B = x.shape[0]
    ang = axial_angles(x.shape[1])
    xc = ctx
    for l in range(DEPTH):
        last = l == DEPTH - 1
        P = {
            'w_in': w_in[l], 'rwkv_mu': rwkv_mu[l], 'rwkv_w0': rwkv_w0[l], 'rwkv_w2': rwkv_w2[l],
            'rwkv_a0': rwkv_a0[l], 'rwkv_a2': rwkv_a2[l], 'rwkv_k_k': rwkv_k_k[l], 'rwkv_k_a': rwkv_k_a[l],
            'rwkv_r_k': rwkv_r_k[l], 'rwkv_lnx_w': rwkv_lnx_w[l], 'rwkv_lnx_b': rwkv_lnx_b[l],
            'rwkv_g2': rwkv_g2[l], 'w_rwkv_proj': w_rwkv_proj[l], 'mla_q_norm': mla_q_norm[l],
            'mla_kv_norm': mla_kv_norm[l], 'mla_w_uq': mla_w_uq[l], 'mla_w_ukv': mla_w_ukv[l],
            'w_mla_proj': w_mla_proj[l], 'gate_b': gate_b[l], 'w_out': w_out[l],
            'ffn_w_gate': ffn_w_gate[l], 'ffn_w_val': ffn_w_val[l], 'ffn_conv_w': ffn_conv_w[l],
            'ffn_conv_b': ffn_conv_b[l], 'ffn_w_down': ffn_w_down[l],
        }
        sh1, sc1, g1, sh2, sc2, g2 = [m[:, None, :] for m in jnp.split(jax.nn.silu(c) @ w_ada[l] + b_ada[l], 6, axis=-1)]
        ch1, cs1, cg1, ch2, cs2, cg2 = jnp.split(jax.nn.silu(c_ctx) @ w_ada[l] + b_ada[l], 6, axis=-1)
        h_ctx = modulate(rms_norm(xc, norm_mix_pre[l]), ch1, cs1)
        s0 = jnp.zeros((N_DIR, B, RWKV_HEADS, RWKV_HEAD, RWKV_HEAD), jnp.float32)
        out_ctx, s_ctx, kv_ctx = token_mixer(h_ctx, s0, None, None, P, emit=not last)
        h_lat = modulate(rms_norm(x, norm_mix_pre[l]), sh1, sc1)
        out_lat, _, _ = token_mixer(h_lat, s_ctx, ang, kv_ctx, P, emit=True)
        x = x + g1 * rms_norm(out_lat, norm_mix_post[l])
        h = modulate(rms_norm(x, norm_ffn_pre[l]), sh2, sc2)
        x = x + g2 * rms_norm(conv_ffn(h, P), norm_ffn_post[l])
        if not last:
            xc = xc + cg1 * rms_norm(out_ctx, norm_mix_post[l])
            hc = modulate(rms_norm(xc, norm_ffn_pre[l]), ch2, cs2)
            xc = xc + cg2 * rms_norm(conv_ffn(hc, P), norm_ffn_post[l])
    return x


DEPTH_2 = 2

D_POOL = D_MODEL // 2
D_ATTN = D_MODEL // 2
D_MIX = D_POOL + D_ATTN
POOL_WINDOWS = (2, 4, 8, 16)
N_POOL_GROUPS = len(POOL_WINDOWS)
POOL_GROUP = D_POOL // N_POOL_GROUPS
DIFF_HEAD_DIM = 64
N_DIFF_HEADS = D_ATTN // (2 * DIFF_HEAD_DIM)
V_HEAD_DIM = 2 * DIFF_HEAD_DIM
ROPE_PAIRS = DIFF_HEAD_DIM // 4
ROPE_BASE = 10000.0
O_POOL_V = 0
O_POOL_G = O_POOL_V + D_POOL
O_Q = O_POOL_G + D_POOL
O_K = O_Q + D_ATTN
O_V = O_K + D_ATTN
O_ATTN_G = O_V + D_ATTN
D_IN_2 = O_ATTN_G + D_ATTN


def rms_norm_2(x, w):
    xf = x.astype(jnp.float32)
    y = xf * lax.rsqrt(jnp.mean(xf * xf, axis=-1, keepdims=True) + EPS)
    return (y * w.astype(jnp.float32)).astype(x.dtype)

def adaln_params(cond, w_ada, b_ada):
    mod = jax.nn.silu(cond) @ w_ada + b_ada
    shift, scale, gate = jnp.split(mod, 3, axis=-1)
    return shift[:, None, :], scale[:, None, :], gate[:, None, :]

def multiscale_pool(v, pool_w, pool_scale):
    B, L, _ = v.shape
    vf = v.astype(jnp.float32)
    csum = jnp.concatenate([jnp.zeros((B, 1, D_POOL), jnp.float32), jnp.cumsum(vf, axis=1)], axis=1)
    t = jnp.arange(L)
    outs = []
    for g, w in enumerate(POOL_WINDOWS):
        sl = slice(g * POOL_GROUP, (g + 1) * POOL_GROUP)
        lo = jnp.clip(t - w // 2, 0, L)
        hi = jnp.clip(t + w // 2, 0, L)
        cs = csum[:, :, sl]
        cnt = (hi - lo).astype(jnp.float32)[None, :, None]
        mean = (jnp.take(cs, hi, axis=1) - jnp.take(cs, lo, axis=1)) / cnt
        outs.append(mean - vf[:, :, sl])
    pooled = jnp.stack(outs, axis=2)
    mixed = jnp.einsum('blgc,gcd->blgd', pooled, pool_w.astype(jnp.float32))
    return (mixed.reshape(B, L, D_POOL) * pool_scale.astype(jnp.float32)).astype(v.dtype)

def axial_rope_tables(L, dtype):
    rows = L // GRID_W
    row = jnp.broadcast_to(jnp.arange(rows)[:, None], (rows, GRID_W)).reshape(-1).astype(jnp.float32)
    col = jnp.broadcast_to(jnp.arange(GRID_W)[None, :], (rows, GRID_W)).reshape(-1).astype(jnp.float32)
    inv_freq = ROPE_BASE ** (-jnp.arange(ROPE_PAIRS, dtype=jnp.float32) / ROPE_PAIRS)
    ang_r = row[:, None] * inv_freq
    ang_c = col[:, None] * inv_freq
    shape = (1, L, 1, 1, ROPE_PAIRS)
    cos_r = jnp.cos(ang_r).reshape(shape).astype(dtype)
    sin_r = jnp.sin(ang_r).reshape(shape).astype(dtype)
    cos_c = jnp.cos(ang_c).reshape(shape).astype(dtype)
    sin_c = jnp.sin(ang_c).reshape(shape).astype(dtype)
    return (cos_r, sin_r, cos_c, sin_c)

def rotate_half(x, cos, sin):
    x1, x2 = jnp.split(x, 2, axis=-1)
    return jnp.concatenate([x1 * cos - x2 * sin, x2 * cos + x1 * sin], axis=-1)

def apply_axial_rope(x, tables):
    cos_r, sin_r, cos_c, sin_c = tables
    half = DIFF_HEAD_DIM // 2
    return jnp.concatenate([rotate_half(x[..., :half], cos_r, sin_r),
                            rotate_half(x[..., half:], cos_c, sin_c)], axis=-1)

def diff_attend(q, k, v, lam):
    s = jnp.einsum('bqhnd,bkhnd->bhnqk', q, k).astype(jnp.float32) * (DIFF_HEAD_DIM ** -0.5)
    p = jax.nn.softmax(s, axis=-1)
    a = p[:, :, 0] - lam * p[:, :, 1]
    return jnp.einsum('bhqk,bkhe->bqhe', a.astype(v.dtype), v)

def merge_branches(p, o_attn, lam_init, pool_w, pool_scale, subln_w, w_out):
    B, L = p.shape[:2]
    pool_o = multiscale_pool(p[..., O_POOL_V:O_POOL_G], pool_w, pool_scale) * jax.nn.silu(p[..., O_POOL_G:O_Q])
    attn_o = (rms_norm_2(o_attn, subln_w).reshape(B, L, D_ATTN) * (1.0 - lam_init)
              * jax.nn.silu(p[..., O_ATTN_G:D_IN_2]))
    return jnp.concatenate([pool_o, attn_o], axis=-1) @ w_out

def hybrid_layer(x, ctx, c, c_ctx, rope_tables, layer_idx, update_ctx,
                 norm_w, w_ada, b_ada, w_in, pool_w, pool_scale, q_norm_w, k_norm_w,
                 lambda_q1, lambda_k1, lambda_q2, lambda_k2, subln_w, w_out):
    B, L, _ = x.shape
    C = ctx.shape[1]
    f32 = jnp.float32
    lam_init = 0.8 - 0.6 * math.exp(-0.3 * layer_idx)
    lam = (jnp.exp(jnp.sum(lambda_q1.astype(f32) * lambda_k1.astype(f32)))
           - jnp.exp(jnp.sum(lambda_q2.astype(f32) * lambda_k2.astype(f32))) + lam_init)

    shift, scale, gate = adaln_params(c, w_ada, b_ada)
    shift_c, scale_c, gate_c = adaln_params(c_ctx[None, :], w_ada, b_ada)
    h = rms_norm_2(x, norm_w) * (1 + scale) + shift
    hc = rms_norm_2(ctx, norm_w) * (1 + scale_c) + shift_c

    ctx_cols = slice(0, D_IN_2) if update_ctx else slice(O_K, O_ATTN_G)
    base = ctx_cols.start
    pc = hc @ w_in[:, ctx_cols]
    kc = rms_norm_2(pc[..., O_K - base:O_V - base].reshape(B, C, N_DIFF_HEADS, 2, DIFF_HEAD_DIM), k_norm_w)
    vc = pc[..., O_V - base:O_ATTN_G - base].reshape(B, C, N_DIFF_HEADS, V_HEAD_DIM)

    p = h @ w_in
    q = apply_axial_rope(rms_norm_2(p[..., O_Q:O_K].reshape(B, L, N_DIFF_HEADS, 2, DIFF_HEAD_DIM), q_norm_w), rope_tables)
    k = apply_axial_rope(rms_norm_2(p[..., O_K:O_V].reshape(B, L, N_DIFF_HEADS, 2, DIFF_HEAD_DIM), k_norm_w), rope_tables)
    v = p[..., O_V:O_ATTN_G].reshape(B, L, N_DIFF_HEADS, V_HEAD_DIM)
    k_all = jnp.concatenate([kc, k], axis=1)
    v_all = jnp.concatenate([vc, v], axis=1)
    nb = L // Q_BLOCK
    qb = q.reshape(B, nb, Q_BLOCK, N_DIFF_HEADS, 2, DIFF_HEAD_DIM).swapaxes(0, 1)
    o = lax.map(lambda qi: diff_attend(qi, k_all, v_all, lam), qb)
    o = o.swapaxes(0, 1).reshape(B, L, N_DIFF_HEADS, V_HEAD_DIM)
    x_new = x + gate * merge_branches(p, o, lam_init, pool_w, pool_scale, subln_w, w_out)

    if update_ctx:
        qc = rms_norm_2(pc[..., O_Q:O_K].reshape(B, C, N_DIFF_HEADS, 2, DIFF_HEAD_DIM), q_norm_w)
        oc = diff_attend(qc, kc, vc, lam)
        ctx_new = ctx + gate_c * merge_branches(pc, oc, lam_init, pool_w, pool_scale, subln_w, w_out)
    else:
        ctx_new = ctx
    return x_new, ctx_new

def second_inputs(seed: int = 0) -> dict:
    key = jax.random.key(seed)
    ks = jax.random.split(key, 18)
    f32 = jnp.float32

    def nrm(k, shape, s):
        return jax.random.normal(k, shape, f32) * s

    def gain(k, shape):
        return 1.0 + 0.02 * jax.random.normal(k, shape, f32)

    return {
        'x': nrm(ks[0], (BATCH, SEQ, D_MODEL), 1.0),
        'c': nrm(ks[1], (BATCH, D_MODEL), 1.0),
        'ctx': nrm(ks[2], (BATCH, CTX_LEN, D_MODEL), 1.0),
        'c_ctx': nrm(ks[3], (D_MODEL,), 1.0),
        'norm_w': gain(ks[4], (DEPTH_2, D_MODEL)),
        'w_ada': nrm(ks[5], (DEPTH_2, D_MODEL, 3 * D_MODEL), D_MODEL ** -0.5),
        'b_ada': nrm(ks[6], (DEPTH_2, 3 * D_MODEL), 0.02),
        'w_in': nrm(ks[7], (DEPTH_2, D_MODEL, D_IN_2), D_MODEL ** -0.5),
        'pool_w': nrm(ks[8], (DEPTH_2, N_POOL_GROUPS, POOL_GROUP, POOL_GROUP), POOL_GROUP ** -0.5),
        'pool_scale': gain(ks[9], (DEPTH_2, D_POOL)),
        'q_norm_w': gain(ks[10], (DEPTH_2, DIFF_HEAD_DIM)),
        'k_norm_w': gain(ks[11], (DEPTH_2, DIFF_HEAD_DIM)),
        'lambda_q1': nrm(ks[12], (DEPTH_2, DIFF_HEAD_DIM), 0.1),
        'lambda_k1': nrm(ks[13], (DEPTH_2, DIFF_HEAD_DIM), 0.1),
        'lambda_q2': nrm(ks[14], (DEPTH_2, DIFF_HEAD_DIM), 0.1),
        'lambda_k2': nrm(ks[15], (DEPTH_2, DIFF_HEAD_DIM), 0.1),
        'subln_w': gain(ks[16], (DEPTH_2, V_HEAD_DIM)),
        'w_out': nrm(ks[17], (DEPTH_2, D_MIX, D_MODEL), D_MIX ** -0.5),
    }

def second_block(x, c, ctx, c_ctx, norm_w, w_ada, b_ada, w_in, pool_w, pool_scale,
              q_norm_w, k_norm_w, lambda_q1, lambda_k1, lambda_q2, lambda_k2, subln_w, w_out):
    rope_tables = axial_rope_tables(x.shape[1], x.dtype)
    for l in range(DEPTH_2):
        x, ctx = hybrid_layer(x, ctx, c, c_ctx, rope_tables, l, l < DEPTH_2 - 1,
                              norm_w[l], w_ada[l], b_ada[l], w_in[l], pool_w[l], pool_scale[l],
                              q_norm_w[l], k_norm_w[l], lambda_q1[l], lambda_k1[l],
                              lambda_q2[l], lambda_k2[l], subln_w[l], w_out[l])
    return x


def setup_inputs(seed=0):
    out = dict(first_inputs(seed))
    for name, value in second_inputs(seed + 1).items():
        if name != "x":
            out[name + "_2"] = value
    return out


def reference(
    x, c, ctx, c_ctx, w_ada, b_ada, norm_mix_pre, norm_mix_post, norm_ffn_pre, norm_ffn_post,
    w_in, rwkv_mu, rwkv_w0, rwkv_w2, rwkv_a0, rwkv_a2, rwkv_k_k, rwkv_k_a, rwkv_r_k, rwkv_lnx_w,
    rwkv_lnx_b, rwkv_g2, w_rwkv_proj, mla_q_norm, mla_kv_norm, mla_w_uq, mla_w_ukv, w_mla_proj,
    gate_b, w_out, ffn_w_gate, ffn_w_val, ffn_conv_w, ffn_conv_b, ffn_w_down, c_2, ctx_2,
    c_ctx_2, norm_w_2, w_ada_2, b_ada_2, w_in_2, pool_w_2, pool_scale_2, q_norm_w_2, k_norm_w_2,
    lambda_q1_2, lambda_k1_2, lambda_q2_2, lambda_k2_2, subln_w_2, w_out_2,
):
    x = first_block(
        x, c, ctx, c_ctx, w_ada, b_ada, norm_mix_pre, norm_mix_post, norm_ffn_pre,
        norm_ffn_post, w_in, rwkv_mu, rwkv_w0, rwkv_w2, rwkv_a0, rwkv_a2, rwkv_k_k, rwkv_k_a,
        rwkv_r_k, rwkv_lnx_w, rwkv_lnx_b, rwkv_g2, w_rwkv_proj, mla_q_norm, mla_kv_norm,
        mla_w_uq, mla_w_ukv, w_mla_proj, gate_b, w_out, ffn_w_gate, ffn_w_val, ffn_conv_w,
        ffn_conv_b, ffn_w_down,
    )
    return second_block(
        x, c_2, ctx_2, c_ctx_2, norm_w_2, w_ada_2, b_ada_2, w_in_2, pool_w_2, pool_scale_2,
        q_norm_w_2, k_norm_w_2, lambda_q1_2, lambda_k1_2, lambda_q2_2, lambda_k2_2, subln_w_2,
        w_out_2,
    )


_drawn_inputs = setup_inputs


def setup_inputs(seed=0):
    import zlib

    import numpy as np

    out = dict(_drawn_inputs(seed))
    spreads = {}
    factors = {'norm_mix_pre': 4.66,
     'norm_mix_post': 8.0,
     'norm_ffn_pre': 6.715,
     'norm_ffn_post': 8.0,
     'rwkv_k_k': 46.211,
     'rwkv_k_a': 6.018,
     'rwkv_lnx_w': 38.494,
     'rwkv_lnx_b': 37.079,
     'mla_q_norm': 8.0,
     'mla_kv_norm': 8.0,
     'gate_b': 8.0,
     'ffn_conv_b': 8.0,
     'norm_w_2': 4.159,
     'pool_scale_2': 6.495,
     'q_norm_w_2': 8.0,
     'k_norm_w_2': 8.0,
     'lambda_q1_2': 3.711,
     'lambda_k1_2': 23.709,
     'lambda_k2_2': 7.969,
     'subln_w_2': 42.324}
    for name, (base, spread) in spreads.items():
        noise = np.random.default_rng([zlib.crc32(name.encode()), seed]).standard_normal(out[name].shape)
        drawn = base * np.exp(spread * noise) if base else spread * noise
        out[name] = __import__('jax').numpy.asarray(drawn.astype(out[name].dtype))
    for name, factor in factors.items():
        out[name] = (out[name] * factor).astype(out[name].dtype)
    return out
```

```python
from contextlib import ExitStack

import numpy as np

import concourse.bass as bass
from concourse import mybir

F32 = mybir.dt.float32
F32R = mybir.dt.float32r
ACT = mybir.ActivationFunctionType
ALU = mybir.AluOpType
AX = mybir.AxisListType

P = 128
D = 2048
DC = D // P
TOK = 256
T2 = 2 * TOK
N = 512
EPS = 1e-6
RW = 1024
LORA = 96
MLA0 = 3 * RW + 4 * LORA + 256
GATE0 = MLA0 + 512 + 512 + 64
ATTN_SCALE = (128 + 64) ** -0.5
DECAY_SCALE = float(np.exp(-0.5))
LNX_EPS = 64e-5
CH = 64
FF = 5632
DIFF_SCALE = 64 ** -0.5
LAM_INIT = [0.8 - 0.6 * float(np.exp(-0.3 * l)) for l in range(2)]
POOL_WINDOWS = (2, 4, 8, 16)

RAW = 4
HL = 4
LA = 3
ADA_RAW = 2
ADA_AT = [0, 2, 3, 5, 6, 8, 9, 11]

PHASES = [("ckv", 1, 16, 4, 3, 1), ("cq", 1, 16, 4, 3, 0), ("kpe", 1, 16, 1, 0, 1), ("mla", 8, 8, 7, 7, 1),
          ("kv", 4, 16, 4, 3, 1), ("r", 2, 16, 4, 3, 0), ("lora", 1, 16, 4, 3, 1), ("gl", 1, 16, 2, 1, 1),
          ("rwkv", 8, 0, 0, 0, 3), ("gate", 8, 16, 4, 3, 0), ("rproj", 4, 8, 4, 3, 0), ("mproj", 4, 16, 4, 3, 0),
          ("wout", 4, 16, 4, 3, 0), ("ffn0", 1, 32, 8, 6, 0), ("ffn", 10, 48, 8, 18, 0), ("ffn1", 1, 16, 0, 12, 0)]
for _l in range(2):
    PHASES += [(f"poolv{_l}", 2, 16, 4, 3, 0), (f"qkv{_l}", 2, 48, 12, 9, 0), (f"poolg{_l}", 2, 16, 4, 3, 0),
               (f"attng{_l}", 2, 16, 4, 3, 0), (f"out{_l}", 4, 16, 4, 3, 0)]
ADA_HEAD = 8
RW_OWN = 73
AT_OWN = [92, 60]


def _bases():
    chunk, block, done, ada = {}, {}, {}, {}
    c = b = d = 0
    a = ADA_HEAD
    for name, n, nc_, nb, nd, na in PHASES:
        chunk[name], block[name], done[name], ada[name] = c, b, d, a
        c, b, d, a = c + n * nc_, b + n * nb, d + n * nd, a + n * na
    return chunk, block, done, ada


C0, B0, D1, A0 = _bases()

VEC = [("b_ada", 96), ("mix_pre", 16), ("mix_post", 16), ("ffn_pre", 16), ("ffn_post", 16), ("gate_b", 32),
       ("conv_w0", 44), ("conv_w1", 44), ("conv_w2", 44), ("conv_b", 44), ("q_norm", 4), ("kv_norm", 4),
       ("mu", 30), ("b_ada_2", 96), ("norm_2", 32), ("pool_scale", 16), ("qn_2", 2), ("kn_2", 2),
       ("subln", 2), ("lambda", 8)]
VOFF, _o = {}, 0
for _n, _w in VEC:
    VOFF[_n] = _o
    _o += _w
VCOLS = _o
PAIR_VEC = ["w0_0", "w0_1", "a0_0", "a0_1", "k_k", "k_a", "r_k", "lnx_w", "lnx_b"]

CONST = [("ident", 128), ("ones", 128), ("bones", 128), ("bmean", 128), ("sel", 4), ("eps", 2), ("one", 1),
         ("rot", 128), ("cos", 256), ("sin", 256), ("masks", 16 * 128), ("restart", 512), ("eye64", 64),
         ("invcnt", 1024)]
COFF, _o = {}, 0
for _n, _w in CONST:
    COFF[_n] = _o
    _o += _w
CCOLS = _o
LEVELS = [1, 2, 4, 8, 16, 32]
M_LEVEL, M_LEVEL_T, M_STRICT, M_INCL = 0, 6, 12, 14


def constants():
    c = np.zeros((P, CCOLS), np.float32)

    def put(name, a):
        c[:, COFF[name]:COFF[name] + a.shape[1]] = a

    i = np.arange(P)
    same = (i[:, None] // 64 == i[None, :] // 64).astype(np.float32)
    put("ident", np.eye(P, dtype=np.float32))
    put("ones", np.ones((P, P), np.float32))
    put("bones", same)
    put("bmean", same / 64)
    sel = np.zeros((P, 4), np.float32)
    for kk in range(2):
        for nh in range(2):
            for j in range(2):
                sel[32 * (2 * kk + nh) + j, 2 * nh + j] = 1
    put("sel", sel)
    put("eps", np.tile(np.array([[EPS, LNX_EPS]], np.float32), (P, 1)))
    put("one", np.ones((P, 1), np.float32))
    t = np.arange(TOK)
    freq = (np.float32(10000.0) ** (-np.arange(0, 32, 2, dtype=np.float32) / np.float32(32))).astype(np.float32)
    rot = np.zeros((P, P), np.float32)
    ang = np.zeros((P, TOK), np.float32)
    for p in range(P):
        pos = (t // 64 if p % 64 < 32 else t % 64).astype(np.float32)
        ang[p] = pos * freq[p % 16]
        if p % 32 < 16:
            rot[p + 16, p] = -1
        else:
            rot[p - 16, p] = 1
    put("rot", rot)
    put("cos", np.cos(ang))
    put("sin", np.sin(ang))
    r, q = i[:, None], i[None, :]
    masks = []
    for b in LEVELS:
        masks.append((r // (2 * b) == q // (2 * b)) & ((r // b) % 2 == 1) & ((q // b) % 2 == 0))
    masks += [m.T for m in masks]
    chunk = r // CH == q // CH
    masks += [chunk & (q < r), chunk & (q > r), chunk & (q <= r), chunk & (q >= r)]
    put("masks", np.concatenate([m.astype(np.float32) for m in masks], 1))
    put("restart", np.tile((np.arange(T2) % CH != 0).astype(np.float32), (P, 1)))
    put("eye64", np.tile(np.eye(64, dtype=np.float32), (2, 1)))
    cnt = [np.clip(t + w // 2, 0, TOK) - np.clip(t - w // 2, 0, TOK) for w in POOL_WINDOWS]
    put("invcnt", np.tile(np.concatenate([(1 / x.astype(np.float32)) for x in cnt])[None], (P, 1)).astype(np.float32))
    return c


def at(labels, label, it=0, base=0):
    return base + it * len(labels) + labels.index(label) + 1


class Own:

    def __init__(self, eng, sem):
        self.eng, self.sem, self.n, self.it, self.per, self.n0 = eng, sem, 0, 0, 0, 0

    def then(self, ins):
        ins.then_inc(self.sem, 1)
        self.n += 1
        self.eng.wait_ge(self.sem, self.it * self.per + self.n)

    def loop(self, it, per):
        self.it, self.per, self.n0 = it, per, self.n

    def end(self, times):
        assert self.n - self.n0 == self.per, (self.n - self.n0, self.per)
        self.n = self.n0 + times * self.per
        self.it, self.per = 0, 0


def build(nc, A, out):
    ctx = ExitStack()
    with ctx:
        def sem(name):
            return ctx.enter_context(nc.semaphore(name))

        SBUF0 = 16512

        def sb(name, shape, kb, dt=F32):
            return nc.alloc_sbuf_tensor_at(name, shape, dt, offset=SBUF0 + int(kb * 1024))

        psum = ctx.enter_context(nc.psum_tensor("psum", [P, 8, 512], F32))
        PS = [psum[:, i, :] for i in range(8)]

        raw = sb("raw", [P, RAW, 2, N], 0)
        whi = sb("whi", [P, HL, N], 16, F32R)
        wlo = sb("wlo", [P, HL, N], 24, F32R)
        ada_raw = sb("ada_raw", [P, ADA_RAW, 2, N], 32)
        ada_head = sb("ada_head", [P, 2, 8, 2, N], 70)
        ada_sb = sb("ada_sb", [P, 256], 40)
        sc1 = sb("sc1", [P, DC, 32], 41)
        sc2 = sb("sc2", [P, DC, 32], 43)
        con = sb("con", [P, CCOLS], 45)
        vec = sb("vec", [P, VCOLS], 64.75)
        mod1 = sb("mod1", [P, 96, 2], 67)
        mod2 = sb("mod2", [P, 96, 2], 67.75)
        gain = sb("gain", [P, DC, 2], 68.5)
        cT = sb("cT", [P, 2, DC, 2], 68.75)
        mu_keep = sb("mu_keep", [P, 30], 69)
        mu_half = sb("mu_half", [P, 30], 69.125)
        lam = sb("lam", [P, 6], 69.25)
        smx = sb("smx", [P, 16], 69.375)
        D0 = 70
        hhi = sb("hhi", [P, 2, DC, TOK], D0 + 0, F32R)
        hlo = sb("hlo", [P, 2, DC, TOK], D0 + 32, F32R)
        xrow = sb("xrow", [P, 4, D], D0 + 64)
        xT = sb("xT", [P, DC, T2], D0 + 96)
        nsq0 = sb("nsq0", [P, 2, T2], D0 + 128)
        nrs0 = sb("nrs0", [P, T2], D0 + 132)
        nap0 = sb("nap0", [P, 3, T2], D0 + 64)
        ckvhi = sb("ckvhi", [P, 4, T2], D0 + 64, F32R)
        ckvlo = sb("ckvlo", [P, 4, T2], D0 + 72, F32R)
        cqhi = sb("cqhi", [P, 4, TOK], D0 + 80, F32R)
        cqlo = sb("cqlo", [P, 4, TOK], D0 + 84, F32R)
        kpe = sb("kpe", [P, T2], D0 + 88)
        oT = sb("oT", [P, 16, TOK], D0 + 90)
        ckv = sb("ckv", [P, 4, T2], D0 + 106)
        cq = sb("cq", [P, 4, TOK], D0 + 114)
        nsq1 = sb("nsq1", [P, 2, T2], D0 + 118)
        nrs1 = sb("nrs1", [P, T2], D0 + 122)
        nap1 = sb("nap1", [P, 3, T2], D0 + 124)
        ropet = sb("ropet", [P, 2, TOK], D0 + 135)
        nrs2 = sb("nrs2", [P, TOK], D0 + 136)
        k_sb = sb("k_sb", [P, 2, T2], D0 + 106)
        v_sb = sb("v_sb", [P, 4, 256], D0 + 110)
        qn = sb("qn", [P, 2, TOK], D0 + 114)
        qraw = sb("qraw", [P, TOK], D0 + 116)
        qpad = sb("qpad", [P, 2, TOK], D0 + 117)
        prob = sb("prob", [P, 4, T2], D0 + 119)
        probT = sb("probT", [P, 4, TOK], D0 + 127)
        probT2 = sb("probT2", [P, 4, TOK], D0 + 131)

        pad = sb("pad", [P, 2, 2, TOK + 2], D0 + 106)
        sh_a = sb("sh_a", [P, 2, TOK], D0 + 110.5)
        sh_out = sb("sh_out", [P, 2, T2], D0 + 112.5)
        wl = sb("wl", [P, 2, T2], D0 + 64)
        al = sb("al", [P, 2, T2], D0 + 68)
        gl = sb("gl", [P, 2, TOK], D0 + 72)
        atok_r = sb("rhs", [P, 2, 4, P], D0 + 8)
        r_s = sb("r_s", [P, TOK], D0 + 0)
        dec = sb("dec", [P, 8], D0 + 1)
        tot = sb("tot", [P, 8], D0 + 1.125)
        zs = sb("zs", [P, 8, CH], D0 + 2)
        b_tok = sb("b_tok", [P, 4, P], D0 + 4)
        k_tok = sb("k_tok", [P, 4, P], D0 + 6)
        akT = sb("akT", [P, 2, 4, P], D0 + 12)
        wu = sb("wu", [P, 2, 4, P], D0 + 12)
        bm = sb("bm", [P, 2, 4, P], D0 + 32)
        aT = sb("aT", [P, 2, 4, P], D0 + 36)
        inv = sb("inv", [P, 2, 4, P], D0 + 40)
        invT = sb("invT", [P, 2, 4, P], D0 + 44)
        v_tok = sb("v_tok", [P, 4, P], D0 + 74)
        l_in = sb("l_in", [P, T2], D0 + 76)
        l_ex = sb("l_ex", [P, T2], D0 + 78)
        e_ex = sb("e_ex", [P, T2], D0 + 80)
        e_in = sb("e_in", [P, T2], D0 + 82)
        a_s = sb("a_s", [P, T2], D0 + 84)
        b_s = sb("b_s", [P, T2], D0 + 86)
        k_s = sb("k_s", [P, T2], D0 + 88)
        arx = sb("arx", [P, 2, 2, 2, P], D0 + 76)
        g1t = sb("g1t", [P, 8, CH], D0 + 80)
        hd = sb("hd", [P, 8, CH], D0 + 82)
        qt = sb("qt", [P, TOK], D0 + 84)
        fin = sb("fin", [P, 3, TOK], D0 + 86)
        k_t = sb("k_t", [P, T2], D0 + 106)
        v_t = sb("v_t", [P, T2], D0 + 108)
        r_t = sb("r_t", [P, TOK], D0 + 110)
        lw2 = sb("lw2", [P, 4, P], D0 + 111)
        g2s = sb("g2s", [P, 2, P], D0 + 113)
        pv = sb("pv", [P, 9], D0 + 114)
        yacc = sb("yacc", [P, TOK], D0 + 1.25)
        kk = sb("kk", [P, T2], D0 + 115)
        sig = sb("sig", [P, 2, T2], D0 + 117)
        icl = sb("icl", [P, 2, T2], D0 + 121)
        kdir = sb("kdir", [P, 2, T2], D0 + 125)
        y_all = sb("y_all", [P, 8, TOK], D0 + 129)

        g_rwkv = sb("g_rwkv", [P, DC, TOK], D0 + 0)
        g_mla = sb("g_mla", [P, DC, TOK], D0 + 32)
        yhi = sb("yhi", [P, 8, TOK], D0 + 64, F32R)
        ylo = sb("ylo", [P, 8, TOK], D0 + 72, F32R)
        ohi = sb("ohi", [P, DC, TOK], D0 + 16, F32R)
        olo = sb("olo", [P, DC, TOK], D0 + 48, F32R)
        mrg = sb("mrg", [P, DC, TOK], D0 + 106)
        mhi = sb("mhi", [P, DC, TOK], D0 + 0, F32R)
        mlo = sb("mlo", [P, DC, TOK], D0 + 32, F32R)
        wo = sb("wo", [P, DC, TOK], D0 + 64)
        cf = sb("cf", [P, DC], 69.4375)
        nsq3 = sb("nsq3", [P, 2, TOK], D0 + 80)
        nrs3 = sb("nrs3", [P, TOK], D0 + 82)
        nap3 = sb("nap3", [P, 3, TOK], D0 + 83)
        x1 = sb("x1", [P, DC, TOK], D0 + 88)
        fhi = sb("fhi", [P, DC, TOK], D0 + 16, F32R)
        flo = sb("flo", [P, DC, TOK], D0 + 48, F32R)
        gpad = sb("gpad", [P, 4, TOK + 2], D0 + 0)
        ge = sb("ge", [P, 4, TOK], D0 + 4.25)
        uhi = sb("uhi", [P, 4, TOK], D0 + 32, F32R)
        ulo = sb("ulo", [P, 4, TOK], D0 + 36, F32R)
        yffn = sb("yffn", [P, DC, TOK], D0 + 64)
        crow = sb("crow", [P, 2, D], D0 + 0)
        xall = sb("xall", [P, DC, T2], D0 + 104)
        nap6 = sb("nap6", [P, 3, T2], D0 + 64)
        nsq6 = sb("nsq6", [P, 2, T2], D0 + 70)
        nrs6 = sb("nrs6", [P, T2], D0 + 74)
        mix = sb("mix", [P, DC, T2], D0 + 64)
        mixhi = sb("mixhi", [P, DC, T2], D0 + 0, F32R)
        mixlo = sb("mixlo", [P, DC, T2], D0 + 32, F32R)
        qk = sb("qk", [P, 8, T2], D0 + 96)
        v2 = sb("v2", [P, 4, N], D0 + 112)
        sq2 = sb("sq2", [P, 2, T2], D0 + 120)
        rs2 = sb("rs2", [P, 2, T2], D0 + 124)
        pr = sb("pr", [P, 2, 2, T2], D0 + 120)
        aTs = sb("aTs", [P, 2, 4, P], D0 + 128)
        rope2 = sb("rope2", [P, 2, TOK], D0 + 132)
        ors = sb("ors", [P, T2], D0 + 132)
        osq = sb("osq", [P, T2], D0 + 134)
        sub2 = sb("sub2", [P, 2], 69.28125)
        pl = sb("pl", [P, 4, T2], D0 + 96)
        stmp = sb("stmp", [P, 2, T2], D0 + 96)
        pw = sb("pw", [P, 4, 2, 256], D0 + 120)
        xp = sb("xp", [P, 2, 2, TOK + 32], D0 + 128)
        sw = sb("sw", [P, 2, 2, TOK + 32], D0 + 132.5)
        orow = sb("orow", [P, 2, D], D0 + 0)

        def C(name, a=0, b=None):
            w = dict(CONST)[name]
            return con[:, COFF[name] + a:COFF[name] + (w if b is None else b)]

        def V(name, i=0, n=1):
            return vec[:, VOFF[name] + i:VOFF[name] + i + n]

        def Vd(name, i, n=1):
            return vec[:, bass.ds(VOFF[name] + i, n)]

        ident, ones, bones, bmean, rot = C("ident"), C("ones"), C("bones"), C("bmean"), C("rot")
        cos, sin = C("cos"), C("sin")

        const_in = sem("const_in")
        rows_in = sem("rows_in")
        raw_in = [sem(f"raw_in{i}") for i in range(RAW)]
        w_hi = sem("w_hi")
        w_lo = sem("w_lo")
        w_used = sem("w_used")
        blk_done = sem("blk_done")
        blk_free = sem("blk_free")
        ada_in = [sem(f"ada_in{i}") for i in range(ADA_RAW)]
        ada_hin = [sem(f"ada_hin{i}") for i in range(2)]
        ada_used = sem("ada_used")
        ada_out = sem("ada_out")
        ada_fin = sem("ada_fin")
        mod_ready = sem("mod_ready")
        sc_zero = sem("sc_zero")
        sc_ready = sem("sc_ready")
        tr_done = sem("tr_done")
        tr_out = sem("tr_out")
        n_sq = sem("n_sq")
        n_mm = sem("n_mm")
        n_std = sem("n_std")
        n_f32 = sem("n_f32")
        n_hi = sem("n_hi")
        n_lo = sem("n_lo")
        dve_own = sem("dve_own")
        act_own = sem("act_own")
        mla_pe = sem("mla_pe")
        mla_act = sem("mla_act")
        mla_dve = sem("mla_dve")
        rope_mm = sem("rope_mm")
        x_saved = sem("x_saved")

        w_in = A["w_in"]
        MLA_PE = ["rot", "S0", "S1", "T0", "T1", "S2", "S3", "PV0", "T2", "T3", "PV1"]
        MLA_DVE = ["q", "nmx0", "nmx1", "pn0", "pn1", "nmx2", "nmx3", "o0", "pn2", "pn3", "o1"]
        MLA_ACT = ["exp0", "exp1", "pT0", "pT1", "exp2", "exp3", "pT2", "pT3"]

        sh_zero = sem("sh_zero")
        sh_done = sem("sh_done")
        sh_st = [sem(f"sh_st{i}") for i in range(2)]
        lora_act = sem("lora_act")
        pool_gate = sem("pool_gate")
        pe_gate = sem("pe_gate")
        rw_in = sem("rw_in")
        rw_pe = sem("rw_pe")
        rw_act = sem("rw_act")
        rw_dve = sem("rw_dve")
        RW_PE, RW_ACT, RW_DVE = ["w0", "w1", "a0", "a1", "kksum"], ["w0", "w1", "a0", "a1", "kkrt"], ["kksq"]
        for d in range(2):
            RW_PE += [f"{n}{d}" for n in ("tr", "A", "AT", "Ak", "Ar", "P1")]
            RW_ACT += [f"E{d}", f"tr{d}", f"P1{d}", f"WU{d}"]
            RW_DVE += [f"{n}{d}" for n in ("L", "abk", "I", "A", "Ak", "Ar")]
            for l in range(1, len(LEVELS)):
                RW_PE += [f"{n}{d}{l}{h}" for n in "BG" for h in range(2)]
                RW_DVE += [f"{n}{d}{l}{h}" for n in "BX" for h in range(2)]
            RW_PE += [f"WU{d}", f"GH{d}", f"Q{d}", f"YL{d}"] + [f"Z{d}{i}" for i in range(1, 7)] + [f"YZ{d}"]
            RW_DVE += [f"GH{d}", f"Q{d}"] + [f"Z{d}{i}" for i in range(1, 7)] + [f"Y{d}"]
        RW_PE += ["mean", "var", "bon", "g"]
        RW_ACT += ["sd"]
        RW_DVE += ["bt", "sq", "out"]
        SCAN = [[0, 1, 2, 3, 4, 5, 6, 7], [3, 2, 1, 0, 7, 6, 5, 4]]

        s_hi = sem("s_hi")
        s_lo = sem("s_lo")
        mg_done = sem("mg_done")
        x1_in = sem("x1_in")
        x1_done = sem("x1_done")
        dn_free = sem("dn_free")
        ff_zero = sem("ff_zero")
        cv_done = sem("cv_done")
        ge_done = sem("ge_done")
        u_hi = sem("u_hi")
        u_lo = sem("u_lo")
        crow_in = sem("crow_in")
        x2_saved = sem("x2_saved")
        x2_in = sem("x2_in")
        pw_in = sem("pw_in")
        lam_pr, lam_mm, lam_e, lam_ok = sem("lam_pr"), sem("lam_mm"), sem("lam_e"), sem("lam_ok")
        xp_zero = sem("xp_zero")
        pl_done = sem("pl_done")
        pw_mm = sem("pw_mm")
        pm_done = sem("pm_done")
        sg_done = sem("sg_done")
        at_pe = [sem(f"at_pe{l}") for l in range(2)]
        at_act = [sem(f"at_act{l}") for l in range(2)]
        at_dve = [sem(f"at_dve{l}") for l in range(2)]
        fin_tr, fin_cp, out_st = sem("fin_tr"), sem("fin_cp"), sem("out_st")
        TILES = [[0, 1, 2, 3], [2, 3]]
        UNITS = [[(h, t) for h in range(4) for t in TILES[l]] for l in range(2)]
        last_of = lambda l, u: UNITS[l][u][1] == 3
        AT_PE, AT_ACT, AT_DVE = [[], []], [[], []], [[], []]
        for l in range(2):
            nu = len(UNITS[l])
            for b in range(9):
                AT_PE[l] += ([f"n{b}"] if b < 8 else []) + ([f"r{b - 1}"] if b else [])
                AT_ACT[l] += ([f"sq{b}"] if b < 8 else []) + ([f"rt{b - 1}"] if b else [])
                AT_DVE[l] += ([f"w{b}"] if b < 8 else []) + ([f"f{b - 1}"] if b else [])
            for u in range(-1, nu + 1):
                nxt = [str(u + 1)] if u + 1 < nu else []
                now = [str(u)] if 0 <= u < nu else []
                end = [str(UNITS[l][u - 1][0])] if u >= 1 and last_of(l, u - 1) else []
                AT_PE[l] += ["S" + n for n in nxt] + ([f"PV{u - 1}"] if u >= 1 else []) + ["T" + n for n in now] + ["o" + n for n in end]
                AT_ACT[l] += ["e" + n for n in nxt] + ["osq" + n for n in end] + ["aT" + n for n in now] + ["ort" + n for n in end]
                AT_DVE[l] += ["mx" + n for n in nxt] + ["a" + n for n in now] + ["o" + n for n in end]

        nsq_of = [nsq0, nsq1, nsq1, nsq3, nsq3, nsq3, nsq6, nsq6]
        nrs_of = [nrs0, nrs1, nrs2, nrs3, nrs3, nrs3, nrs6, nrs6]
        nt_of = [T2, T2, TOK, TOK, TOK, TOK, T2, T2]

        def like(buf, dst):
            return buf.rearrange("p (s t) -> p s t", t=TOK) if len(dst.shape) == 3 else buf

        x_keep = nc.dram_tensor("x_keep", (P, DC, TOK), F32, kind="Internal").ap()

        rkv = nc.dram_tensor("rkv", (24, P, T2), F32, kind="Internal").ap()

        x2_keep = nc.dram_tensor("x2_keep", (P, DC, T2), F32, kind="Internal").ap()

        block = ctx.enter_context(nc.Block())

        @block.sync
        def _(sp):
            def seg(view, c0, lc0, nch):
                for r in range(nch // 2):
                    lc = lc0 + 2 * r
                    src = view(r)
                    c = c0 + lc
                    if not isinstance(c, int) or c >= 2 * RAW:
                        sp.wait_ge(w_lo, c - 2 * RAW + 2)
                    slot = (lc // 2) % RAW
                    sp.dma_start(raw[:, slot, :, 0:src.shape[2]], src).then_inc(raw_in[slot], 16)

            def cols(w, col, n=N):
                return lambda r: w[256 * r:256 * r + 256, bass.ds(col, n)].rearrange("(a p) n -> p a n", p=P)

            sp.dma_start(con[:, :], A["consts"]).then_inc(const_in, 16)
            sp.dma_start(vec[:, :], A["vec"]).then_inc(const_in, 16)
            sp.dma_start(cT[:, :, :, :], A["cT"]).then_inc(const_in, 16)
            for t in range(2):
                sp.dma_start(xrow[:, t, :], A["ctx"][P * t:P * t + P, :]).then_inc(rows_in, 16)
                sp.dma_start(xrow[:, 2 + t, :], A["x"][P * t:P * t + P, :]).then_inc(rows_in, 16)
            def ada_group(p, col, it=None):
                for kh in range(8):
                    if it is not None:
                        sp.wait_ge(ada_used, it * 16 + 8 * p - 15 + kh)
                    sp.dma_start(ada_head[:, p, kh, :, :], A["w_ada"][256 * kh:256 * kh + 256, bass.ds(col, N)].rearrange("(a p) n -> p a n", p=P)).then_inc(ada_hin[p], 16)
            for p in range(2):
                ada_group(p, p * N)
            with sp.Fori(1, ADA_HEAD // 2) as it:
                c0, c1 = sp.snap(it * 2 * N), sp.snap(it * 2 * N + N)
                ada_group(0, c0, it)
                ada_group(1, c1, it)
            seg(cols(w_in, MLA0 + 512), C0["ckv"], 0, 16)
            seg(cols(w_in, MLA0), C0["cq"], 0, 16)
            seg(cols(A["w_kpe"], 0, P), C0["kpe"], 0, 16)
            with sp.Fori(0, 8) as it:
                cu, cq_ = sp.snap(it * N), sp.snap(it * 384)
                seg(cols(A["w_ukv"], cu), C0["mla"] + it * 8, 0, 4)
                seg(cols(A["w_uq"], cq_, 384), C0["mla"] + it * 8, 4, 4)
            with sp.Fori(0, 4) as it:
                col = sp.snap(it * N + RW)
                seg(cols(w_in, col), C0["kv"] + it * 16, 0, 16)
            with sp.Fori(0, 2) as it:
                col = sp.snap(it * N)
                seg(cols(w_in, col), C0["r"] + it * 16, 0, 16)
            seg(cols(w_in, 3 * RW), C0["lora"], 0, 16)
            seg(cols(w_in, 3 * RW + 4 * LORA, 256), C0["gl"], 0, 16)
            with sp.Fori(0, 8) as it:
                col = sp.snap(it * N + GATE0)
                seg(cols(w_in, col), C0["gate"] + it * 16, 0, 16)
            for name, w in (("rproj", "w_rwkv_proj"), ("mproj", "w_mla_proj"), ("wout", "w_out")):
                n = 8 if name == "rproj" else 16
                with sp.Fori(0, 4) as it:
                    col = sp.snap(it * N)
                    seg(cols(A[w], col), C0[name] + it * n, 0, n)

            def down(row0, row1, c0, lc0):
                for n in range(4):
                    seg(lambda r: A["w_down"][bass.ds((row0, row1)[r], 256), n * N:n * N + N].rearrange("(a p) n -> p a n", p=P),
                        c0, lc0 + 4 * n, 4)
            seg(cols(A["w_gate"], 0), C0["ffn0"], 0, 16)
            seg(cols(A["w_val"], 0), C0["ffn0"], 16, 16)
            with sp.Fori(0, 10) as it:
                c = C0["ffn"] + it * 48
                col, r0, r1 = sp.snap(it * N + N), sp.snap(it * N), sp.snap(it * N + 256)
                seg(cols(A["w_gate"], col), c, 0, 16)
                down(r0, r1, c, 16)
                seg(cols(A["w_val"], col), c, 32, 16)
            down(10 * N, 10 * N + 256, C0["ffn1"], 0)
            for l in range(2):
                w = A["w_in_2"][l]
                def pairs(name, col0):
                    with sp.Fori(0, 2) as it:
                        col = sp.snap(it * N + col0)
                        seg(cols(w, col), C0[f"{name}{l}"] + it * 16, 0, 16)

                pairs("poolv", 0)
                with sp.Fori(0, 2) as it:
                    c = C0[f"qkv{l}"] + it * 48
                    cq_, ck, cv = sp.snap(it * N + 2048), sp.snap(it * N + 3072), sp.snap(it * N + 4096)
                    for i, col in enumerate((cq_, ck, cv)):
                        seg(cols(w, col), c, 16 * i, 16)
                pairs("poolg", 1024)
                pairs("attng", 5120)
                with sp.Fori(0, 4) as it:
                    col = sp.snap(it * N)
                    seg(cols(A["w_out_2"][l], col), C0[f"out{l}"] + it * 16, 0, 16)
            for t in range(2):
                sp.wait_ge(fin_cp, 32)
                sp.dma_start(out[P * t:P * t + P, :], orow[:, t, :]).then_inc(out_st, 16)
            sp.wait_ge(out_st, 32)

        @block.gpsimd
        def _(pool):
            pool.wait_ge(tr_out, DC)
            pool.dma_start(x_keep, xT[:, :, TOK:T2]).then_inc(x_saved, 16)
            pool.wait_ge(x_saved, 16)
            def ada_group(w, col, a):
                for kh in range(8):
                    if not isinstance(a, int) or a + kh >= 8 * ADA_HEAD + ADA_RAW:
                        pool.wait_ge(ada_used, a + kh - ADA_RAW + 1)
                    if not isinstance(a, int):
                        pool.sem_inc(pool_gate, 1)
                    pool.dma_start(ada_raw[:, kh % ADA_RAW, :, :], A[w][256 * kh:256 * kh + 256, bass.ds(col, N)].rearrange("(a p) n -> p a n", p=P)).then_inc(ada_in[kh % ADA_RAW], 16)

            for name in ("ckv", "kpe"):
                ada_group("w_ada", A0[name] * N, A0[name] * 8)
            with pool.Fori(0, 8) as it:
                col = pool.snap(it * N + A0["mla"] * N)
                ada_group("w_ada", col, it * 8 + A0["mla"] * 8)
            with pool.Fori(0, 4) as it:
                col = pool.snap(it * N + A0["kv"] * N)
                ada_group("w_ada", col, it * 8 + A0["kv"] * 8)
                for m in range(4):
                    dst = pool.snap(it * 4 + 8 + m)
                    pool.wait_ge(sh_done, it * 4 + m + 1)
                    pool.sem_inc(pool_gate, 1)
                    pool.dma_start(rkv[bass.ds(dst, 1), :, :].rearrange("o p t -> p (o t)"), sh_out[:, m % 2, :]).then_inc(sh_st[m % 2], 16)
            with pool.Fori(0, 2) as it:
                for m in range(4):
                    dst = pool.snap(it * 4 + m)
                    pool.wait_ge(sh_done, it * 4 + 16 + m + 1)
                    pool.sem_inc(pool_gate, 1)
                    pool.dma_start(rkv[bass.ds(dst, 1), :, TOK:T2].rearrange("o p t -> p (o t)"), sh_out[:, m % 2, 0:TOK]).then_inc(sh_st[m % 2], 16)
            for name in ("lora", "gl"):
                ada_group("w_ada", A0[name] * N, A0[name] * 8)
            pool.wait_ge(sh_done, 30)
            for slot in range(2):
                pool.wait_ge(sh_st[slot], 12 * 16)
            with pool.Fori(0, 8) as it:
                f0, r0, k0, v0 = pool.snap(it * P), pool.snap(it), pool.snap(it + 8), pool.snap(it + 16)
                chunk = lambda i: rkv[bass.ds(i, 1), :, :].rearrange("o p t -> p (o t)")
                pool.dma_start(k_t[:, :], chunk(k0)).then_inc(rw_in, 16)
                pool.dma_start(pv[:, :], A["pvec"][bass.ds(r0, 1), :, :].rearrange("o p t -> p (o t)")).then_inc(rw_in, 16)
                pool.dma_start(lw2[0:LORA, 0:2, :], A["w2"][:, :, bass.ds(f0, P)]).then_inc(rw_in, 16)
                pool.dma_start(lw2[0:LORA, 2:4, :], A["a2"][:, :, bass.ds(f0, P)]).then_inc(rw_in, 16)
                pool.dma_start(v_t[:, :], chunk(v0)).then_inc(rw_in, 16)
                pool.dma_start(r_t[:, :], rkv[bass.ds(r0, 1), :, TOK:T2].rearrange("o p t -> p (o t)")).then_inc(rw_in, 16)
                pool.dma_start(g2s[:, :, :], A["g2"][:, bass.ds(f0, P)].rearrange("(k p) n -> p k n", p=P)).then_inc(rw_in, 16)
                for j in range(3):
                    col = pool.snap(it * 3 * N + j * N)
                    ada_group("w_ada_2", col, (it * 3 + A0["rwkv"] + j) * 8)
                pool.wait_ge(rw_dve, it * len(RW_DVE) + len(RW_DVE))
            pool.wait_ge(rw_in, 8 * 7 * 16)
            pool.wait_ge(s_lo, 2 + 4)
            pool.dma_start(x1[:, :, :], x_keep).then_inc(x1_in, 16)
            pool.wait_ge(x1_in, 16)
            pool.wait_ge(u_lo, 44)
            for t in range(2):
                pool.dma_start(crow[:, t, :], A["ctx_2"][P * t:P * t + P, :]).then_inc(crow_in, 16)
            pool.wait_ge(crow_in, 32)
            for l in range(2):
                if l == 0:
                    pool.wait_ge(tr_out, 2 * DC)
                    pool.wait_ge(x1_done, 2 * DC)
                else:
                    pool.wait_ge(blk_free, B0["poolv1"])
                pool.dma_start(x2_keep, xall[:, :, :]).then_inc(x2_saved, 16)
                pool.wait_ge(x2_saved, 16 * l + 16)
                pool.wait_ge(n_lo, (3 + l) * DC + 8)
                pool.dma_start(pw[:, :, :, :], A["pool_w"][l].rearrange("g (k p) n -> p g k n", p=P)).then_inc(pw_in, 16)
                pool.wait_ge(pw_in, 16 * l + 16)
                pool.wait_ge(at_dve[l], 2 * len(AT_DVE[l]))
                pool.dma_start(xall[:, :, :], x2_keep).then_inc(x2_in, 16)
                pool.wait_ge(x2_in, 16 * l + 16)

        @block.tensor
        def _(pe):
            def ada_mm(sc, kh, src):
                for kk in range(2):
                    for nh in range(2):
                        t = 32 * (2 * kk + nh)
                        mm = pe.matmul(PS[4][t:t + 32, 0:256], sc[:, 2 * kh + kk, :], src[:, kk, nh * 256:nh * 256 + 256],
                                       start=(kh == 0), stop=(kh == 7), tile_position=(0, t))
                mm.then_inc(ada_used, 1)

            def ada_half(sc, kh, g):
                pe.wait_ge(ada_in[kh % ADA_RAW], (g - ADA_HEAD) * (8 // ADA_RAW * 16) + (kh // ADA_RAW + 1) * 16)
                if kh == 0:
                    pe.wait_ge(mod_ready, g)
                ada_mm(sc, kh, ada_raw[:, kh % ADA_RAW, :, :])

            def ada_final(g):
                pe.wait_ge(ada_out, g + 1)
                for m in range(4):
                    mm = pe.matmul(PS[4][:, 256 + 2 * m:258 + 2 * m], ada_sb[:, (m % 2) * P:(m % 2) * P + P],
                                   C("sel", 2 * (m // 2), 2 * (m // 2) + 2), start=True, stop=True)
                mm.then_inc(ada_fin, 1)

            def seg(c0, lc0, nch, b0, nblk, product, ada=None, each=True, ready=None):
                for k in range(nch):
                    slot = (lc0 + k) % HL
                    pe.wait_ge(w_lo, c0 + lc0 + k + 1)
                    if ready is not None:
                        pe.wait_ge(n_lo, ready + k + 1)
                    for m in range(nblk):
                        if k == 0 and callable(each):
                            each(m)
                        elif k == 0 and each:
                            pe.wait_ge(blk_free, b0 + m - 3)
                        pairs, dst, first = product(m, k, slot)
                        for i, (l, r) in enumerate(pairs):
                            mm = pe.matmul(dst, l, r, start=(k == 0 and i == 0 and first), stop=(k == nch - 1 and i == 2),
                                           skip_group_check=True)
                        if k == nch - 1 and m < nblk - 1:
                            mm.then_inc(blk_done, 1)
                    mm.then_inc(w_used, 1)
                    if ada and k in ADA_AT:
                        kh = ADA_AT.index(k)
                        ada_half(ada[0], kh, ada[1])
                if ada:
                    ada_final(ada[1])

            def rows(xhi, xlo, T):
                def product(m, k, slot):
                    wh, wl = whi[:, slot, m * P:m * P + P], wlo[:, slot, m * P:m * P + P]
                    return [(wh, xhi(k)), (wh, xlo(k)), (wl, xhi(k))], PS[m][:, 0:T], True
                return product

            h2 = rows(lambda k: hhi[:, :, k, :], lambda k: hlo[:, :, k, :], T2)
            h1 = rows(lambda k: hhi[:, 1, k, :], lambda k: hlo[:, 1, k, :], TOK)
            nq = [0]
            nn = [0]

            def norm(n, T):
                for k in range(n):
                    pe.wait_ge(n_sq, nq[0] + 1)
                    if k == 0 and nn[0] > 0:
                        pe.wait_ge(n_std, nn[0])
                    pe.matmul(PS[5][:, 0:T], ones, nsq_of[nn[0]][:, nq[0] % 2, 0:T], start=(k == 0),
                              stop=(k == n - 1)).then_inc(n_mm, 1)
                    nq[0] += 1
                nn[0] += 1

            pe.wait_ge(const_in, 48)
            pe.wait_ge(rows_in, 64)
            for d in range(DC):
                if d >= 2:
                    pe.wait_ge(tr_out, d - 1)
                for t in range(4):
                    tr = pe.transpose(PS[6 + d % 2][:, t * P:t * P + P], xrow[:, t, d * P:d * P + P], ident)
                tr.then_inc(tr_done, 1)
            norm(DC, T2)
            pe.wait_ge(sc_ready, 2)
            with pe.Fori(0, ADA_HEAD // 2) as it:
                for p in range(2):
                    g = it * 2 + p
                    pe.wait_ge(ada_hin[p], it * 128 + 128)
                    if p == 1:
                        pe.wait_ge(mod_ready, g)
                    for kh in range(8):
                        ada_mm(sc1, kh, ada_head[:, p, kh, :, :])
                    ada_final(g)
                pe.wait_ge(mod_ready, it * 2 + 2)
            seg(C0["ckv"], 0, 16, 0, 4, h2, (sc1, A0["ckv"]), each=False, ready=0)
            pe.wait_ge(blk_free, B0["cq"])
            seg(C0["cq"], 0, 16, 0, 4, h1, None, each=False)
            pe.wait_ge(blk_free, B0["kpe"])
            seg(C0["kpe"], 0, 16, 0, 1, h2, (sc1, A0["kpe"]), each=False)
            norm(4, T2)
            norm(4, TOK)
            pe.wait_ge(blk_free, B0["mla"])
            pe.matmul(PS[6][:, 0:TOK], rot, kpe[:, TOK:T2], start=True, stop=True).then_inc(rope_mm, 1)
            pe.wait_ge(n_lo, DC + 8)

            def ukv(m, k, slot):
                if m < 2:
                    wh, wl = whi[:, slot, m * P:m * P + P], wlo[:, slot, m * P:m * P + P]
                    return [(wh, ckvhi[:, k, :]), (wh, ckvlo[:, k, :]), (wl, ckvhi[:, k, :])], PS[m][:, :], True
                t = m - 2
                wh, wl = whi[:, slot, 256:512], wlo[:, slot, 256:512]
                xh, xl = ckvhi[:, k, t * P:t * P + P], ckvlo[:, k, t * P:t * P + P]
                return [(xh, wh), (xh, wl), (xl, wh)], PS[2 + t // 2][:, (t % 2) * 256:(t % 2) * 256 + 256], t % 2 == 0

            uq = rows(lambda k: cqhi[:, k, :], lambda k: cqlo[:, k, :], TOK)
            with pe.Fori(0, 8) as it:
                pe.wait_ge(blk_free, B0["mla"] + it * 7)
                seg(C0["mla"] + it * 8, 0, 4, 0, 6, ukv, None, each=False)
                pe.wait_ge(blk_free, B0["mla"] + it * 7 + 4)
                seg(C0["mla"] + it * 8, 4, 4, 0, 3, uq, None, each=False)
                pe.wait_ge(blk_free, B0["mla"] + it * 7 + 7)
                pe.matmul(PS[3][:, 0:TOK], rot, qraw[:, :], start=True, stop=True).then_inc(mla_pe, 1)

                def scores(u):
                    h, q0 = u // 2, (u % 2) * P
                    if u == 0:
                        pe.wait_ge(mla_dve, at(MLA_DVE, "q", it))
                    if u >= 2:
                        pe.wait_ge(mla_act, at(MLA_ACT, f"exp{u - 2}", it))
                    pe.matmul(PS[u % 2][:, :], qn[:, h, q0:q0 + P], k_sb[:, h, :], start=True, stop=False)
                    pe.matmul(PS[u % 2][:, :], qpad[:, h, q0:q0 + P], kpe[:, :], start=False, stop=True).then_inc(mla_pe, 1)

                def turn(u):
                    pe.wait_ge(mla_dve, at(MLA_DVE, f"pn{u}", it))
                    if u >= 1:
                        pe.wait_ge(mla_act, at(MLA_ACT, f"pT{u - 1}", it))
                    for kt in range(4):
                        tr = pe.transpose(PS[6][:, kt * P:kt * P + P], prob[:, u, kt * P:kt * P + P], ident)
                    tr.then_inc(mla_pe, 1)

                def values(h):
                    pe.wait_ge(mla_act, at(MLA_ACT, f"pT{2 * h + 1}", it))
                    if h == 1:
                        pe.wait_ge(mla_dve, at(MLA_DVE, "o0", it))
                    for kt in range(4):
                        mm = pe.matmul(PS[7][:, 0:TOK], v_sb[:, kt, h * P:h * P + P], (probT, probT2)[h][:, kt, :],
                                       start=(kt == 0), stop=(kt == 3))
                    mm.then_inc(mla_pe, 1)

                def ada(*khs):
                    for kh in khs:
                        ada_half(sc1, kh, A0["mla"] + it)

                ada(0, 1)
                scores(0)
                scores(1)
                ada(2, 3)
                turn(0)
                turn(1)
                scores(2)
                scores(3)
                ada(4, 5)
                values(0)
                turn(2)
                turn(3)
                ada(6, 7)
                values(1)
                ada_final(A0["mla"] + it)
            with pe.Fori(0, 4) as it:
                seg(C0["kv"] + it * 16, 0, 16, B0["kv"] + it * 4, 4, h2, (sc1, A0["kv"] + it))
            with pe.Fori(0, 2) as it:
                seg(C0["r"] + it * 16, 0, 16, B0["r"] + it * 4, 4, h1)

            def lora(m, k, slot):
                wh, wl_ = whi[:, slot, m * LORA:m * LORA + P], wlo[:, slot, m * LORA:m * LORA + P]
                return [(wh, hhi[:, :, k, :]), (wh, hlo[:, :, k, :]), (wl_, hhi[:, :, k, :])], PS[m][:, :], True
            seg(C0["lora"], 0, 16, B0["lora"], 4, lora, (sc1, A0["lora"]))
            seg(C0["gl"], 0, 16, B0["gl"], 2, h1, (sc1, A0["gl"]))

            pe.wait_ge(blk_free, B0["gate"])
            pe.wait_ge(mod_ready, A0["rwkv"])
            pe.wait_ge(lora_act, 4)
            pe.wait_ge(sh_done, 30)
            LF = [slice(TOK, TOK + P), slice(TOK + P, T2)]
            with pe.Fori(0, 8) as it:
                dve_at = lambda n: pe.wait_ge(rw_dve, at(RW_DVE, n, it))
                act_at = lambda n: pe.wait_ge(rw_act, at(RW_ACT, n, it))
                pe.wait_ge(rw_in, it * 112 + 112)
                for i in range(4):
                    pe.matmul(PS[i][:, :], lw2[0:LORA, i, :], (wl if i < 2 else al)[0:LORA, i % 2, :], start=True, stop=True).then_inc(rw_pe, 1)
                dve_at("kksq")
                pe.matmul(PS[5][:, :], bones, e_ex[:, :], start=True, stop=True).then_inc(rw_pe, 1)

                def ada(j, *khs):
                    for kh in khs:
                        ada_half(sc2, kh, it * 3 + A0["rwkv"] + j)

                ada(0, *range(8))
                for d in range(2):
                    hs = [slice(0, 64), slice(64, P)]
                    blk = lambda b: slice(b * P, b * P + P)
                    dve_at(f"abk{d}")
                    if d == 0:
                        act_at("kkrt")
                    for i, src in enumerate((a_s, b_s, k_s, v_t)[0:4 if d == 0 else 3]):
                        for b in range(4):
                            mm = pe.transpose(PS[(5, 6, 7, 3)[i]][:, blk(b)], src[:, blk(b)], ident)
                    mm.then_inc(rw_pe, 1)

                    def pairs(bank, l, r, label):
                        pe.sem_inc(pe_gate, 1)
                        for h in range(2):
                            for b in range(4):
                                mm = pe.matmul(PS[bank + h][:, blk(b)], l[hs[h], blk(b)], r[hs[h], blk(b)], start=True, stop=True)
                        mm.then_inc(rw_pe, 1)

                    pairs(0, a_s, b_s, "A")
                    act_at(f"tr{d}")
                    pairs(2, b_s, a_s, "AT")
                    pairs(5, k_s, a_s, "Ak")
                    ada_final(it * 3 + A0["rwkv"] + d)
                    dve_at(f"I{d}")
                    for h in range(2):
                        for i, l in enumerate((b_s, k_s)):
                            for b in range(2):
                                mm = pe.matmul(PS[h][:, (2 * i + b) * P:(2 * i + b) * P + P], l[hs[h], LF[b]], r_s[hs[h], blk(b)], start=True, stop=True)
                    mm.then_inc(rw_pe, 1)
                    dve_at(f"Ak{d}")
                    for h in range(2):
                        for b in range(4):
                            mm = pe.matmul(PS[5 + h][:, blk(b)], akT[:, h, b, :], v_tok[:, b, :], start=True, stop=True)
                    mm.then_inc(rw_pe, 1)
                    for l in range(1, len(LEVELS)):
                        for h in range(2):
                            if l == 1:
                                dve_at(f"Ar{d}")
                            else:
                                dve_at(f"X{d}{l - 1}{h}")
                            for b in range(4):
                                mm = pe.matmul(PS[h][:, blk(b)], aT[:, h, b, :], inv[:, h, b, :], start=True, stop=True)
                            mm.then_inc(rw_pe, 1)
                        if l == 1:
                            act_at(f"P1{d}")
                        for h in range(2):
                            dve_at(f"B{d}{l}{h}")
                            for b in range(4):
                                mm = pe.matmul(PS[2 + h][:, blk(b)], bm[:, h, b, :], invT[:, h, b, :], start=True, stop=True)
                                if l < len(LEVELS) - 1:
                                    mm = pe.matmul(PS[6 + h][:, blk(b)], invT[:, h, b, :], bm[:, h, b, :], start=True, stop=True)
                            mm.then_inc(rw_pe, 1)
                    for h in range(2):
                        dve_at(f"X{d}{len(LEVELS) - 1}{h}")
                        for b in range(4):
                            mm = pe.matmul(PS[h][:, blk(b)], invT[:, h, b, :], atok_r[:, h, b, :], start=True, stop=True)
                    mm.then_inc(rw_pe, 1)
                    act_at(f"WU{d}")
                    pe.sem_inc(pe_gate, 1)
                    for e in range(2):
                        t = hs[e]
                        for h in range(2):
                            for b in range(4):
                                o = PS[2 + e][hs[h], b * CH:b * CH + CH]
                                pe.matmul(o, wu[t, h, b, 0:64], b_tok[t, b, hs[h]], start=True, stop=True)
                                o = PS[2 + e][hs[h], 256 + b * CH:256 + b * CH + CH]
                                pe.matmul(o, b_tok[t, b, hs[h]], wu[t, h, b, 64:P], start=True, stop=False)
                                mm = pe.matmul(o, k_tok[t, b, hs[h]], v_tok[t, b, hs[h]], start=False, stop=True)
                    mm.then_inc(rw_pe, 1)
                    for h in range(2):
                        for b in range(2):
                            mm = pe.matmul(PS[6][hs[h], blk(b)], wu[:, h, 2 + b, 0:64], arx[:, h, 0, b, :], start=True, stop=True)
                    mm.then_inc(rw_pe, 1)
                    for h in range(2):
                        for b in range(2):
                            pe.matmul(PS[7][hs[h], blk(b)], v_tok[:, 2 + b, hs[h]], arx[:, h, 1, b, :], start=True, stop=False)
                            mm = pe.matmul(PS[7][hs[h], blk(b)], wu[:, h, 2 + b, 64:P], arx[:, h, 0, b, :], start=False, stop=True)
                    mm.then_inc(rw_pe, 1)
                    state = lambda i: hd[:, SCAN[d][0], :] if i == 1 else zs[:, i, :]
                    for i in range(1, 7):
                        dve_at(f"Q{d}" if i == 1 else f"Z{d}{i - 1}")
                        pe.sem_inc(pe_gate, 1)
                        for h in range(2):
                            mm = pe.matmul(PS[5][hs[h], (i % 2) * CH:(i % 2) * CH + CH], g1t[hs[h], SCAN[d][i], :], state(i)[hs[h], :], start=True, stop=True)
                        mm.then_inc(rw_pe, 1)
                        ada(1 + d, i - 1)
                    dve_at(f"Z{d}6")
                    pe.sem_inc(pe_gate, 1)
                    for i in range(4, 8):
                        c = (SCAN[d][i] - 4) * CH
                        for h in range(2):
                            mm = pe.matmul(PS[0][hs[h], c:c + CH], state(i)[hs[h], :], qt[hs[h], c:c + CH], start=True, stop=True)
                    mm.then_inc(rw_pe, 1)
                    ada(1 + d, 6, 7)
                dve_at("Y1")
                pe.matmul(PS[0][:, 0:TOK], bmean, yacc[:, :], start=True, stop=True).then_inc(rw_pe, 1)
                dve_at("sq")
                pe.matmul(PS[1][:, 0:TOK], bmean, fin[:, 1, :], start=True, stop=True).then_inc(rw_pe, 1)
                pe.matmul(PS[2][:, 0:TOK], bones, fin[:, 2, :], start=True, stop=True).then_inc(rw_pe, 1)
                for k in range(2):
                    mm = pe.matmul(PS[3][:, 0:TOK], g2s[:, k, :], gl[:, k, :], start=(k == 0), stop=(k == 1))
                mm.then_inc(rw_pe, 1)
                ada_final(it * 3 + A0["rwkv"] + 2)
            pe.wait_ge(rw_dve, 8 * len(RW_DVE))
            with pe.Fori(0, 8) as it:
                seg(C0["gate"] + it * 16, 0, 16, B0["gate"] + it * 4, 4, h1)
            for name, n, xh, xl, split in (("rproj", 8, yhi, ylo, 2), ("mproj", 16, ohi, olo, 6), ("wout", 16, mhi, mlo, 10)):
                pe.wait_ge(s_lo, split)
                x_ = rows(lambda k: xh[:, k, :], lambda k: xl[:, k, :], TOK)
                with pe.Fori(0, 4) as it:
                    seg(C0[name] + it * n, 0, n, B0[name] + it * 4, 4, x_)
            norm(DC, TOK)
            norm(DC, TOK)

            f1 = rows(lambda k: fhi[:, k, :], lambda k: flo[:, k, :], TOK)
            ud = rows(lambda k: uhi[:, k, :], lambda k: ulo[:, k, :], TOK)

            def down(c0, lc0, g, gate_b=None):
                pe.wait_ge(u_lo, g * 4 + 4)
                for n in range(4):
                    if n == 0:
                        free = (lambda m: pe.wait_ge(blk_free, gate_b + m + 1))
                    else:
                        free = (lambda m: pe.wait_ge(dn_free, g * 16 + 4 * (n - 1) + m + 1))
                    seg(c0, lc0 + 4 * n, 4, 0, 4, ud, None, free)

            seg(C0["ffn0"], 0, 16, B0["ffn0"], 4, f1, ready=DC + 8)
            seg(C0["ffn0"], 16, 16, B0["ffn0"] + 4, 4, f1)
            with pe.Fori(0, 10) as it:
                c, b = C0["ffn"] + it * 48, B0["ffn"] + it * 8
                seg(c, 0, 16, b, 4, f1)
                down(c, 16, it, b)
                seg(c, 32, 16, b + 4, 4, f1, None, lambda m: pe.wait_ge(dn_free, it * 16 + 12 + m + 1))
            down(C0["ffn1"], 0, 10, B0["ffn1"] - 4)

            pe.wait_ge(crow_in, 32)
            for d in range(DC):
                if d >= 2:
                    pe.wait_ge(tr_out, DC + d - 1)
                for t in range(2):
                    tr = pe.transpose(PS[6 + d % 2][:, t * P:t * P + P], crow[:, t, d * P:d * P + P], ident)
                tr.then_inc(tr_done, 1)
            norm(DC, TOK)
            pe.wait_ge(lam_pr, 1)
            pe.matmul(PS[7][:, 256:260], ones, lam[:, 0:4], start=True, stop=True).then_inc(lam_mm, 1)
            for l in range(2):
                norm(DC, T2)
                hl = h2 if l == 0 else h1
                T = T2 if l == 0 else TOK
                t0 = T2 - T
                if l == 0:
                    pe.wait_ge(dn_free, 176)

                def v_rows(m, k, slot):
                    xh, xl = hhi[:, m // 2, k, (m % 2) * P:(m % 2) * P + P], hlo[:, m // 2, k, (m % 2) * P:(m % 2) * P + P]
                    return [(xh, whi[:, slot, :]), (xh, wlo[:, slot, :]), (xl, whi[:, slot, :])], PS[m][:, :], True

                for it in range(2):
                    seg(C0[f"poolv{l}"] + it * 16, 0, 16, B0[f"poolv{l}"] + it * 4, 4, hl, ready=(2 + l) * DC + 8 if it == 0 else None)
                    pe.wait_ge(pw_in, 16 * l + 16)
                    for g in range(2):
                        pe.wait_ge(pl_done, 8 * l + it * 4 + g * 2 + 2)
                        if 4 * l + it * 2 + g > 0:
                            pe.wait_ge(pm_done, 8 * l + it * 4 + g * 2)
                        for j in range(2):
                            for k in range(2):
                                mm = pe.matmul(PS[5 + j][:, 0:T], pw[:, it * 2 + g, k, j * P:j * P + P], pl[:, 2 * g + k, 0:T], start=(k == 0), stop=(k == 1))
                        mm.then_inc(pw_mm, 1)
                with pe.Fori(0, 2) as it:
                    c, b = C0[f"qkv{l}"] + it * 48, B0[f"qkv{l}"] + it * 12
                    done = lambda ins: ins.then_inc(at_pe[l], 1)
                    dve_at = lambda n: pe.wait_ge(at_dve[l], at(AT_DVE[l], n, it))
                    act_at = lambda n: pe.wait_ge(at_act[l], at(AT_ACT[l], n, it))
                    seg(c, 0, 16, b, 4, hl)
                    seg(c, 16, 16, b + 4, 4, h2)
                    seg(c, 32, 16, b + 8, 4, v_rows)
                    pe.wait_ge(blk_free, b + 12)
                    for i in range(9):
                        if i < 8:
                            act_at(f"sq{i}")
                            if i > 0:
                                act_at(f"rt{i - 1}")
                            ts = slice(t0 if i < 4 else 0, T2)
                            done(pe.matmul(PS[5][:, ts], bones, sq2[:, i % 2, ts], start=True, stop=True))
                        if i > 0:
                            dve_at(f"w{i - 1}")
                            if i > 1:
                                dve_at(f"f{i - 2}")
                            done(pe.matmul(PS[6][:, 0:TOK], rot, qk[:, i - 1, TOK:T2], start=True, stop=True))
                    units = UNITS[l]
                    o_bank = lambda h: PS[(7, 4)[h % 2]]

                    def scores(u):
                        h, t = units[u]
                        if u == 0:
                            dve_at("f7")
                        if u >= 2:
                            act_at(f"e{u - 2}")
                        pe.sem_inc(pe_gate, 1)
                        nk = TOK if t < 2 else T2
                        for n in range(2):
                            r = slice(64 * n, 64 * n + 64)
                            mm = pe.matmul(PS[2 * (u % 2) + n][:, 0:nk], qk[r, h, t * P:t * P + P], qk[r, 4 + h, 0:nk], start=True, stop=True)
                        done(mm)

                    def turn(u):
                        dve_at(f"a{u}")
                        for kt in range(2 if units[u][1] < 2 else 4):
                            tr = pe.transpose(PS[6][:, kt * P:kt * P + P], pr[:, u % 2, 0, kt * P:kt * P + P], ident)
                        done(tr)

                    def values(u):
                        h, t = units[u]
                        nk = 2 if t < 2 else 4
                        act_at(f"aT{u}")
                        if t == TILES[l][0] and h >= 2:
                            dve_at(f"o{h - 2}")
                        for kt in range(nk):
                            mm = pe.matmul(o_bank(h)[:, t * P:t * P + P], v2[:, kt, h * P:h * P + P], aTs[:, u % 2, kt, :], start=(kt == 0), stop=(kt == nk - 1))
                        done(mm)

                    for u in range(-1, len(units) + 1):
                        if u + 1 < len(units):
                            scores(u + 1)
                        if u >= 1:
                            values(u - 1)
                        if 0 <= u < len(units):
                            turn(u)
                        if u >= 1 and last_of(l, u - 1):
                            h = units[u - 1][0]
                            act_at(f"osq{h}")
                            done(pe.matmul(PS[5][:, t0:T2], ones, osq[:, t0:T2], start=True, stop=True))
                    pe.wait_ge(at_dve[l], it * len(AT_DVE[l]) + len(AT_DVE[l]))
                for name in ("poolg", "attng"):
                    with pe.Fori(0, 2) as it:
                        seg(C0[f"{name}{l}"] + it * 16, 0, 16, B0[f"{name}{l}"] + it * 4, 4, hl)
                pe.wait_ge(s_lo, 10 + 8 * l + 8)
                xm = rows(lambda k: mixhi[:, k, t0:T2], lambda k: mixlo[:, k, t0:T2], T)
                with pe.Fori(0, 4) as it:
                    seg(C0[f"out{l}"] + it * 16, 0, 16, B0[f"out{l}"] + it * 4, 4, xm)
            pe.wait_ge(blk_free, B0["out1"] + 16)
            for d in range(DC):
                for t in range(2):
                    i = 2 * d + t
                    if i >= 2:
                        pe.wait_ge(fin_cp, i - 1)
                    pe.transpose(PS[6 + t][:, 0:P], xall[:, d, TOK + t * P:TOK + t * P + P], ident).then_inc(fin_tr, 1)

        @block.scalar
        def _(act):
            own = Own(act, act_own)

            def hi(c0, lcs, width=N):
                for lc in lcs:
                    c = c0 + lc
                    if lc % 2 == 0:
                        act.wait_ge(raw_in[(lc // 2) % RAW], 2 * c0 + 16 * (lc // 8 + 1))
                    if not isinstance(c, int) or c >= HL:
                        act.wait_ge(w_used, c - HL + 1)
                    act.activation(whi[:, lc % HL, 0:width], raw[:, (lc // 2) % RAW, lc % 2, 0:width], ACT.Copy).then_inc(w_hi, 1)

            def ada_take(g):
                act.wait_ge(ada_used, g * 8 + 8)
                act.activation(ada_sb[:, :], PS[4][:, 0:256], ACT.Copy).then_inc(ada_out, 1)

            def block_done(c_end, d0, m, nblk):
                if m < nblk - 1:
                    act.wait_ge(blk_done, d0 + m + 1)
                else:
                    act.wait_ge(w_used, c_end)

            nq, nn, na = [0], [0], [0]

            def norm(src, n, T, width, ready=None):
                sq, rs = nsq_of[nn[0]], nrs_of[nn[0]]
                for k in range(n):
                    if ready:
                        ready(k)
                    if nq[0] >= 2:
                        act.wait_ge(n_mm, nq[0] - 1)
                    act.activation(sq[:, nq[0] % 2, 0:T], src(k), ACT.Square).then_inc(n_sq, 1)
                    nq[0] += 1
                act.wait_ge(n_mm, nq[0])
                act.activation(rs[:, 0:T], PS[5][:, 0:T], ACT.Sqrt, bias=C("eps", 0, 1), scale=1.0 / width).then_inc(n_std, 1)
                nn[0] += 1

            def split(n, T, buf, dst, after=None):
                for k in range(n):
                    act.wait_ge(n_f32, na[0] + 1)
                    act.activation(dst(k), like(buf[:, 1 + na[0] % 2, 0:T], dst(k)), ACT.Copy).then_inc(n_hi, 1)
                    na[0] += 1
                    if after is not None and k >= 2:
                        hi(after, [LA + k - 2])

            act.wait_ge(const_in, 48)
            act.wait_ge(sc_zero, 2)
            act.activation(sc1[:, :, 0:2], cT[:, 0, :, :], ACT.Silu).then_inc(sc_ready, 1)
            act.activation(sc2[:, :, 0:2], cT[:, 1, :, :], ACT.Silu).then_inc(sc_ready, 1)
            for d in range(DC):
                act.wait_ge(tr_done, d + 1)
                act.activation(xT[:, d, :], PS[6 + d % 2][:, :], ACT.Copy).then_inc(tr_out, 1)
            norm(lambda k: xT[:, k, :], DC, T2, D, lambda k: act.wait_ge(tr_out, k + 1))
            with act.Fori(0, ADA_HEAD) as it:
                ada_take(it)
            hi(0, range(LA))
            c = C0["ckv"]
            split(DC, T2, nap0, lambda k: hhi[:, :, k, :], c)

            hi(c, range(LA + 14, 16 + LA))
            ada_take(A0["ckv"])
            act.wait_ge(x_saved, 16)
            for m in range(4):
                block_done(c + 16, D1["ckv"], m, 4)
                act.activation(ckv[:, m, :], PS[m][:, :], ACT.Copy).then_inc(blk_free, 1)
            c = C0["cq"]
            hi(c, range(LA, 16))
            hi(c, range(16, 16 + LA), P)
            for m in range(4):
                block_done(c + 16, D1["cq"], m, 4)
                act.activation(cq[:, m, :], PS[m][:, 0:TOK], ACT.Copy).then_inc(blk_free, 1)
            c = C0["kpe"]
            hi(c, range(LA, 16), P)
            hi(c, range(16, 16 + LA))
            ada_take(A0["kpe"])
            norm(lambda k: ckv[:, k, :], 4, T2, 512, lambda k: act.wait_ge(blk_free, B0["ckv"] + k + 1))
            act.wait_ge(w_used, c + 16)
            act.activation(kpe[:, :], PS[0][:, :], ACT.Copy).then_inc(blk_free, 1)
            norm(lambda k: cq[:, k, :], 4, TOK, 512, lambda k: act.wait_ge(blk_free, B0["cq"] + k + 1))
            split(4, T2, nap1, lambda k: ckvhi[:, k, :])
            split(4, TOK, nap1, lambda k: cqhi[:, k, :])

            with act.Fori(0, 8) as it:
                c = C0["mla"] + it * 8
                d0 = D1["mla"] + it * 7
                hi(c, range(LA, 4))
                hi(c, range(4, 4 + LA), 384)
                act.wait_ge(n_lo, DC + 8)
                for m, dst in enumerate((k_sb[:, 0, :], k_sb[:, 1, :], v_sb[:, 0:2, :], v_sb[:, 2:4, :])):
                    if m == 3:
                        act.wait_ge(w_used, c + 4)
                    else:
                        act.wait_ge(blk_done, d0 + (1, 2, 4)[m])
                    act.activation(dst, PS[m][:, :], ACT.Copy).then_inc(blk_free, 1)
                hi(c, range(4 + LA, 8), 384)
                hi(c, range(8, 8 + LA))
                for m, dst in enumerate((qn[:, 0, :], qn[:, 1, :], qraw[:, :])):
                    if m == 2:
                        act.wait_ge(w_used, c + 8)
                    else:
                        act.wait_ge(blk_done, d0 + 5 + m + 1)
                    act.activation(dst, PS[m][:, 0:TOK], ACT.Copy).then_inc(blk_free, 1)

                def exp(u):
                    act.wait_ge(mla_dve, at(MLA_DVE, f"nmx{u}", it))
                    act.activation(prob[:, u, :], PS[u % 2][:, :], ACT.Exp, bias=smx[:, 4 + u:5 + u], scale=ATTN_SCALE,
                                   accum_out=smx[:, 8 + u:9 + u]).then_inc(mla_act, 1)

                def turned(u):
                    act.wait_ge(mla_pe, at(MLA_PE, f"T{u}", it))
                    act.activation((probT, probT2)[u // 2][:, :, (u % 2) * P:(u % 2) * P + P],
                                   PS[6][:, :].rearrange("p (k q) -> p k q", q=P), ACT.Copy).then_inc(mla_act, 1)

                exp(0)
                exp(1)
                turned(0)
                turned(1)
                exp(2)
                exp(3)
                turned(2)
                turned(3)
                ada_take(A0["mla"] + it)

            def shifted(c, d0, m, nblk, latents=False, end=16, n=None):
                block_done(c + end, d0, m, nblk)
                if m >= 2:
                    act.wait_ge(sh_done, n - 1)
                if latents:
                    act.activation(pad[:, m % 2, 1, 1:TOK + 1], PS[m][:, 0:TOK], ACT.Copy).then_inc(blk_free, 1)
                else:
                    act.activation(pad[:, m % 2, :, 1:TOK + 1], PS[m][:, :].rearrange("p (s t) -> p s t", t=TOK), ACT.Copy).then_inc(blk_free, 1)

            act.wait_ge(sh_zero, 1)
            with act.Fori(0, 4) as it:
                c = C0["kv"] + it * 16
                hi(c, range(LA, 16 + LA))
                ada_take(A0["kv"] + it)
                for m in range(4):
                    shifted(c, D1["kv"] + it * 3, m, 4, n=it * 4 + m)
                act.wait_ge(sh_done, it * 4 + 4)
            with act.Fori(0, 2) as it:
                c = C0["r"] + it * 16
                hi(c, range(LA, 16 + LA))
                for m in range(4):
                    shifted(c, D1["r"] + it * 3, m, 4, True, n=it * 4 + 16 + m)
                act.wait_ge(sh_done, it * 4 + 20)
            c = C0["lora"]
            hi(c, range(LA, 16))
            hi(c, range(16, 16 + LA), 256)
            ada_take(A0["lora"])
            for m in range(4):
                shifted(c, D1["lora"], m, 4, n=24 + m)
            act.wait_ge(sh_done, 28)
            c = C0["gl"]
            hi(c, range(LA, 16), 256)
            hi(c, range(16, 16 + LA))
            ada_take(A0["gl"])
            for m in range(2):
                shifted(c, D1["gl"], m, 2, True, n=28 + m)
            act.wait_ge(sh_done, 30)
            for d in range(2):
                act.activation(wl[0:LORA, d, :], wl[0:LORA, d, :], ACT.Tanh).then_inc(lora_act, 1)
            for m in range(2):
                act.activation(gl[:, m, :], gl[:, m, :], ACT.Sigmoid).then_inc(lora_act, 1)

            with act.Fori(0, 8) as it:
                pe_at = lambda n: act.wait_ge(rw_pe, at(RW_PE, n, it))
                dve_at = lambda n: act.wait_ge(rw_dve, at(RW_DVE, n, it))
                done = lambda ins: ins.then_inc(rw_act, 1)
                act.wait_ge(rw_in, it * 112 + 112)
                for i in range(4):
                    pe_at(("w0", "w1", "a0", "a1")[i])
                    done(act.activation((sig if i < 2 else icl)[:, i % 2, :], PS[i][:, :], ACT.Sigmoid, bias=pv[:, i:i + 1]))
                pe_at("kksum")
                done(act.activation(e_in[:, :], PS[5][:, :], ACT.Sqrt))
                for d in range(2):
                    dve_at(f"L{d}")
                    act.activation(e_ex[:, :], l_ex[:, :], ACT.Exp, scale=-DECAY_SCALE)
                    act.activation(e_in[:, :], l_in[:, :], ACT.Exp, scale=DECAY_SCALE)
                    act.activation(r_s[:, :], l_in[:, TOK:T2], ACT.Exp, scale=-DECAY_SCALE)
                    done(act.activation(dec[:, :], tot[:, :], ACT.Exp, scale=-DECAY_SCALE))
                    ada_take(it * 3 + A0["rwkv"] + d)
                    pe_at(f"tr{d}")
                    if d == 0:
                        act.activation(v_tok[:, :, :], PS[3][:, :].rearrange("p (b c) -> p b c", c=P), ACT.Copy)
                    act.activation(atok_r[:, :, :, 0:64].rearrange("p h b c -> p b h c"), PS[5][:, :].rearrange("p (b h c) -> p b h c", h=2, c=64), ACT.Copy)
                    act.activation(b_tok[:, :, :], PS[6][:, :].rearrange("p (b c) -> p b c", c=P), ACT.Copy)
                    done(act.activation(k_tok[:, :, :], PS[7][:, :].rearrange("p (b c) -> p b c", c=P), ACT.Copy))
                    pe_at(f"P1{d}")
                    act.activation(atok_r[:, 0, :, 64:P], PS[5][:, :].rearrange("p (b c) -> p b c", c=P)[:, :, 0:64], ACT.Copy)
                    done(act.activation(atok_r[:, 1, :, 64:P], PS[6][:, :].rearrange("p (b c) -> p b c", c=P)[:, :, 64:P], ACT.Copy))
                    pe_at(f"WU{d}")
                    act.activation(wu[:, 0, :, :], PS[0][:, :].rearrange("p (b c) -> p b c", c=P), ACT.Copy)
                    done(act.activation(wu[:, 1, :, :], PS[1][:, :].rearrange("p (b c) -> p b c", c=P), ACT.Copy))
                ada_take(it * 3 + A0["rwkv"] + 2)
                pe_at("var")
                done(act.activation(yacc[:, :], PS[1][:, 0:TOK], ACT.Sqrt, bias=C("eps", 1, 2)))

            def split_hi(src, dst, ready=None, n=4):
                for g in range(src.shape[1] // n):
                    if ready:
                        ready(g)
                    act.activation(dst[:, n * g:n * g + n, :], src[:, n * g:n * g + n, :], ACT.Copy).then_inc(s_hi, 1)

            act.wait_ge(rw_dve, 8 * len(RW_DVE))
            split_hi(y_all, yhi)
            for half, dst in enumerate((g_rwkv, g_mla)):
                with act.Fori(0, 4) as it:
                    c, d0 = C0["gate"] + half * 64 + it * 16, D1["gate"] + half * 12 + it * 3
                    hi(c, range(LA, 16 + LA))
                    for m in range(4):
                        block_done(c + 16, d0, m, 4)
                        act.activation(dst[:, bass.ds(it * 4 + m, 1), :], PS[m][:, 0:TOK].unsqueeze(1), ACT.Sigmoid,
                                       bias=Vd("gate_b", it * 4 + 16 * half + m)).then_inc(blk_free, 1)
            act.wait_ge(w_used, C0["rproj"])
            split_hi(oT, ohi)
            for name, n in (("rproj", 8), ("mproj", 16)):
                with act.Fori(0, 4) as it:
                    hi(C0[name] + it * n, range(LA, n + LA))
            split_hi(mrg, mhi, lambda g: act.wait_ge(mg_done, g + 1 if g < 3 else 4))
            with act.Fori(0, 4) as it:
                c = C0["wout"] + it * 16
                hi(c, range(LA, 16 + LA))
                for m in range(4):
                    block_done(c + 16, D1["wout"] + it * 3, m, 4)
                    act.activation(wo[:, bass.ds(it * 4 + m, 1), :], PS[m][:, 0:TOK].unsqueeze(1), ACT.Copy).then_inc(blk_free, 1)
            norm(lambda k: wo[:, k, :], DC, TOK, D, lambda k: act.wait_ge(blk_free, B0["wout"] + k + 1))
            norm(lambda k: x1[:, k, :], DC, TOK, D, lambda k: act.wait_ge(x1_done, k + 1))
            split(DC, TOK, nap3, lambda k: fhi[:, k, :], C0["ffn0"])

            def gate_out(c_end, d0):
                for m in range(4):
                    block_done(c_end, d0, m, 4)
                    act.activation(gpad[:, m, 1:TOK + 1], PS[m][:, 0:TOK], ACT.Copy).then_inc(blk_free, 1)

            def gelu(g):
                for m in range(4):
                    act.wait_ge(cv_done, g * 4 + m + 1)
                    act.activation(ge[:, m, :], ge[:, m, :], ACT.Gelu_apprx_tanh, bias=Vd("conv_b", g * 4 + m)).then_inc(ge_done, 1)

            def u_split(b):
                for m in range(4):
                    act.wait_ge(blk_free, b + m + 1)
                    act.activation(uhi[:, m, :], ge[:, m, :], ACT.Copy).then_inc(u_hi, 1)

            c, d0 = C0["ffn0"], D1["ffn0"]
            hi(c, range(LA + 14, 16 + LA))
            act.wait_ge(ff_zero, 1)
            gate_out(c + 16, d0)
            gelu(0)
            hi(c, range(16 + LA, 32 + LA))
            u_split(B0["ffn0"] + 4)
            with act.Fori(0, 10) as it:
                c, d0 = C0["ffn"] + it * 48, D1["ffn"] + it * 18
                hi(c, range(LA, 16 + LA))
                gate_out(c + 16, d0)
                hi(c, range(16 + LA, 20 + LA))
                gelu(it + 1)
                hi(c, range(20 + LA, 48 + LA))
                u_split(B0["ffn"] + it * 8 + 4)
            hi(C0["ffn1"], range(LA, 16 + LA))

            for d in range(DC):
                act.wait_ge(tr_done, DC + d + 1)
                act.activation(xall[:, d, 0:TOK], PS[6 + d % 2][:, 0:TOK], ACT.Copy).then_inc(tr_out, 1)
            norm(lambda k: yffn[:, k, :], DC, TOK, D, lambda k: act.wait_ge(dn_free, 160 + k + 1))
            act.wait_ge(lam_mm, 1)
            act.activation(lam[:, 0:4], PS[7][:, 256:260], ACT.Exp).then_inc(lam_e, 1)
            act.wait_ge(tr_out, 2 * DC)
            for l in range(2):
                if l == 0:
                    norm(lambda k: xall[:, k, :], DC, T2, D, lambda k: act.wait_ge(x1_done, 2 * DC))
                else:
                    norm(lambda k: xall[:, k, :], DC, T2, D, lambda k: act.wait_ge(blk_free, B0["out0"] + k + 1))
                split(DC, T2, nap6, lambda k: hhi[:, :, k, :], C0[f"poolv{l}"])
                T = T2 if l == 0 else TOK
                t0 = T2 - T
                units = UNITS[l]
                act.wait_ge(x2_saved, 16 * l + 16)
                act.wait_ge(xp_zero, l + 1)
                for it in range(2):
                    c = C0[f"poolv{l}"] + it * 16
                    hi(c, range(LA if it else LA + 14, 16 + LA))
                    for m in range(4):
                        n = 8 * l + it * 4 + m
                        block_done(c + 16, D1[f"poolv{l}"] + 3 * it, m, 4)
                        if it * 4 + m >= 2:
                            act.wait_ge(pl_done, n - 1)
                        if l == 0:
                            act.activation(xp[:, m % 2, :, 16:16 + TOK], PS[m][:, :].rearrange("p (s t) -> p s t", t=TOK), ACT.Copy).then_inc(blk_free, 1)
                        else:
                            act.activation(xp[:, m % 2, 1, 16:16 + TOK], PS[m][:, 0:TOK], ACT.Copy).then_inc(blk_free, 1)
                act.wait_ge(pm_done, 8 * l + 8)
                with act.Fori(0, 2) as it:
                    c, d0, b = C0[f"qkv{l}"] + it * 48, D1[f"qkv{l}"] + it * 9, B0[f"qkv{l}"] + it * 12
                    done = lambda ins: ins.then_inc(at_act[l], 1)
                    pe_at = lambda n: act.wait_ge(at_pe[l], at(AT_PE[l], n, it))
                    dve_at = lambda n: act.wait_ge(at_dve[l], at(AT_DVE[l], n, it))
                    for i in range(3):
                        hi(c, range(16 * i + LA, 16 * i + 16 + LA))
                        for m in range(4):
                            block_done(c + 16 * i + 16, d0 + 3 * i, m, 4)
                            ts = slice(t0 if i == 0 else 0, T2)
                            dst = qk[:, 4 * i + m, ts] if i < 2 else v2[:, m, :]
                            act.activation(dst, PS[m][:, 0:dst.shape[1]], ACT.Copy).then_inc(blk_free, 1)
                    act.wait_ge(blk_free, b + 12)
                    for i in range(9):
                        if i < 8:
                            ts = slice(t0 if i < 4 else 0, T2)
                            if i >= 2:
                                pe_at(f"n{i - 2}")
                            done(act.activation(sq2[:, i % 2, ts], qk[:, i, ts], ACT.Square))
                        if i > 0:
                            ts = slice(t0 if i - 1 < 4 else 0, T2)
                            pe_at(f"n{i - 1}")
                            if i >= 3:
                                dve_at(f"w{i - 3}")
                            done(act.activation(rs2[:, (i - 1) % 2, ts], PS[5][:, ts], ACT.Sqrt, bias=C("eps", 0, 1), scale=1.0 / 64))

                    def exp(u):
                        nk = TOK if units[u][1] < 2 else T2
                        dve_at(f"mx{u}")
                        if u >= 2:
                            pe_at(f"T{u - 2}")
                        s = 8 * (u % 2)
                        act.activation(pr[:, u % 2, 0, 0:nk], PS[2 * (u % 2)][:, 0:nk], ACT.Exp, bias=smx[:, s + 2:s + 3], scale=DIFF_SCALE,
                                       accum_out=smx[:, s + 4:s + 5])
                        done(act.activation(pr[:, u % 2, 1, 0:nk], PS[2 * (u % 2) + 1][:, 0:nk], ACT.Exp, bias=smx[:, s + 3:s + 4], scale=DIFF_SCALE,
                                            accum_out=smx[:, s + 5:s + 6]))

                    for u in range(-1, len(units) + 1):
                        if u + 1 < len(units):
                            exp(u + 1)
                        end = u >= 1 and last_of(l, u - 1)
                        if end:
                            h = units[u - 1][0]
                            pe_at(f"PV{u - 1}")
                            if h > 0:
                                dve_at(f"o{h - 1}")
                            done(act.activation(osq[:, t0:T2], PS[(7, 4)[h % 2]][:, t0:T2], ACT.Square))
                        if 0 <= u < len(units):
                            nk = 2 if units[u][1] < 2 else 4
                            pe_at(f"T{u}")
                            done(act.activation(aTs[:, u % 2, 0:nk, :], PS[6][:, 0:nk * P].rearrange("p (k q) -> p k q", q=P), ACT.Copy))
                        if end:
                            pe_at(f"o{h}")
                            done(act.activation(ors[:, t0:T2], PS[5][:, t0:T2], ACT.Sqrt, bias=C("eps", 0, 1), scale=1.0 / P))
                act.wait_ge(at_dve[l], 2 * len(AT_DVE[l]))
                for i, name in enumerate(("poolg", "attng")):
                    with act.Fori(0, 2) as it:
                        c = C0[f"{name}{l}"] + it * 16
                        hi(c, range(LA, 16 + LA))
                        for m in range(4):
                            block_done(c + 16, D1[f"{name}{l}"] + 3 * it, m, 4)
                            if m >= 2:
                                act.wait_ge(sg_done, it * 4 + 16 * l + 8 * i + m - 1)
                            act.activation(stmp[:, m % 2, 0:T], PS[m][:, 0:T], ACT.Silu).then_inc(blk_free, 1)
                        act.wait_ge(sg_done, it * 4 + 16 * l + 8 * i + 4)
                act.wait_ge(w_used, C0[f"out{l}"])
                split_hi(mix[:, :, t0:T2], mixhi[:, :, t0:T2], lambda g: act.wait_ge(sg_done, 16 * l + 16), 2)
                with act.Fori(0, 4 if l == 0 else 3) as it:
                    hi(C0[f"out{l}"] + it * 16, range(LA, 16 + LA))
            hi(C0["out1"] + 48, range(LA, 16))
            for d in range(DC):
                for t in range(2):
                    act.wait_ge(fin_tr, 2 * d + t + 1)
                    act.activation(orow[:, t, d * P:d * P + P], PS[6 + t][:, 0:P], ACT.Copy).then_inc(fin_cp, 1)

        @block.vector
        def _(dve):
            own = Own(dve, dve_own)

            def lo(c0, lcs, width=N):
                for lc in lcs:
                    dve.wait_ge(w_hi, c0 + lc + 1)
                    dve.tensor_tensor(wlo[:, lc % HL, 0:width], raw[:, (lc // 2) % RAW, lc % 2, 0:width],
                                      whi[:, lc % HL, 0:width].bitcast(F32), ALU.subtract).then_inc(w_lo, 1)

            def ada_bias(g, mod, bias, n):
                dve.wait_ge(ada_fin, g + 1)
                dve.tensor_tensor(mod[:, bass.ds(n, 4), :], PS[4][:, 256:264].rearrange("p (m j) -> p m j", j=2),
                                  Vd(bias, n, 4).unsqueeze(2).to_broadcast([P, 4, 2]), ALU.add).then_inc(mod_ready, 1)

            nn, na = [0], [0]

            def norm_scale():
                rs = nrs_of[nn[0]]
                dve.wait_ge(n_std, nn[0] + 1)
                own.then(dve.reciprocal(rs[:, 0:nt_of[nn[0]]], rs[:, 0:nt_of[nn[0]]]))
                nn[0] += 1
                return rs

            def rest(T, buf, dst, upto_):
                while rest.n < upto_:
                    k = rest.n
                    dve.wait_ge(n_hi, k + 1)
                    d = rest.dst[k]
                    dve.tensor_tensor(d[0], like(buf[:, 1 + k % 2, 0:T], d[0]), d[1].bitcast(F32), ALU.subtract).then_inc(n_lo, 1)
                    rest.n += 1
            rest.n, rest.dst = 0, {}

            def modulated(n, T, src, buf, rs, shift, hi_of, lo_of, after=None):
                for k in range(n):
                    i = na[0]
                    if i - rest.n >= 2:
                        rest(T, buf, None, i - 1)
                    if i >= 2:
                        dve.wait_ge(n_lo, i - 1)
                    if i >= 1:
                        dve.wait_ge(n_f32, i)
                    own.then(dve.tensor_tensor(buf[:, 0, 0:T], src(k), rs[:, 0:T], ALU.mult))
                    if T == T2:
                        own.then(dve.tensor_scalar(buf[:, 1 + i % 2, 0:TOK], buf[:, 0, 0:TOK], gain[:, k, 1:2], shift(k, 1), ALU.mult, ALU.add))
                        dve.tensor_scalar(buf[:, 1 + i % 2, TOK:T2], buf[:, 0, TOK:T2], gain[:, k, 0:1], shift(k, 0), ALU.mult, ALU.add).then_inc(n_f32, 1)
                    else:
                        dve.tensor_scalar(buf[:, 1 + i % 2, 0:T], buf[:, 0, 0:T], gain[:, k, 0:1], shift(k, 0), ALU.mult, ALU.add).then_inc(n_f32, 1)
                    rest.dst[i] = (lo_of(k), hi_of(k))
                    na[0] += 1
                    if after is not None and k >= 2:
                        lo(after, [LA + k - 2])
                rest(T, buf, None, na[0])

            def gained(n, T, src, buf, rs, g, hi_of, lo_of):
                for k in range(n):
                    i = na[0]
                    if i - rest.n >= 2:
                        rest(T, buf, None, i - 1)
                    if i >= 2:
                        dve.wait_ge(n_lo, i - 1)
                    dve.scalar_tensor_tensor(buf[:, 1 + i % 2, 0:T], src(k), g(k), rs[:, 0:T], ALU.mult, ALU.mult).then_inc(n_f32, 1)
                    rest.dst[i] = (lo_of(k), hi_of(k))
                    na[0] += 1
                rest(T, buf, None, na[0])

            dve.memset(sc1[:, :, :], 0.0).then_inc(sc_zero, 1)
            dve.memset(sc2[:, :, :], 0.0).then_inc(sc_zero, 1)
            dve.wait_ge(const_in, 48)
            dve.tensor_scalar(mu_keep[:, :], V("mu", 0, 30), -1.0, 1.0, ALU.mult, ALU.add)
            dve.tensor_scalar(mu_half[:, :], V("mu", 0, 30), 0.5, None, ALU.mult)
            rs = norm_scale()
            with dve.Fori(0, ADA_HEAD) as it:
                ada_bias(it, mod1, "b_ada", it * 4)
            dve.wait_ge(mod_ready, ADA_HEAD)
            own.then(dve.scalar_tensor_tensor(gain[:, :, :], mod1[:, 16:32, :], 1.0, V("mix_pre", 0, 16).unsqueeze(2).to_broadcast([P, 16, 2]),
                                              ALU.add, ALU.mult))
            c = C0["ckv"]
            lo(0, range(LA))
            modulated(DC, T2, lambda k: xT[:, k, :], nap0, rs, lambda k, j: mod1[:, k, j:j + 1],
                      lambda k: hhi[:, :, k, :], lambda k: hlo[:, :, k, :], c)
            lo(c, range(LA + 14, 16 + LA))
            ada_bias(A0["ckv"], mod1, "b_ada", A0["ckv"] * 4)
            c = C0["cq"]
            lo(c, range(LA, 16))
            lo(c, range(16, 16 + LA), P)
            c = C0["kpe"]
            lo(c, range(LA, 16), P)
            lo(c, range(16, 16 + LA))
            ada_bias(A0["kpe"], mod1, "b_ada", A0["kpe"] * 4)
            rs = norm_scale()
            gained(4, T2, lambda k: ckv[:, k, :], nap1, rs, lambda k: V("kv_norm", k), lambda k: ckvhi[:, k, :], lambda k: ckvlo[:, k, :])
            rs = norm_scale()
            gained(4, TOK, lambda k: cq[:, k, :], nap1, rs, lambda k: V("q_norm", k), lambda k: cqhi[:, k, :], lambda k: cqlo[:, k, :])
            dve.wait_ge(rope_mm, 1)
            dve.tensor_tensor(ropet[:, 0, :], kpe[:, TOK:T2], cos, ALU.mult)
            own.then(dve.tensor_tensor(ropet[:, 1, :], PS[6][:, 0:TOK], sin, ALU.mult))
            own.then(dve.tensor_tensor(kpe[:, TOK:T2], ropet[:, 0, :], ropet[:, 1, :], ALU.add))
            own.then(dve.memset(qpad[:, :, :], 0.0))
            with dve.Fori(0, 8) as it:
                own.loop(it, 9)
                c = C0["mla"] + it * 8
                lo(c, range(LA, 4))
                lo(c, range(4, 4 + LA), 384)
                lo(c, range(4 + LA, 8), 384)
                lo(c, range(8, 8 + LA))
                dve.wait_ge(mla_pe, at(MLA_PE, "rot", it))
                dve.tensor_tensor(ropet[:, 0, :], qraw[:, :], cos, ALU.mult)
                own.then(dve.tensor_tensor(ropet[:, 1, :], PS[3][:, 0:TOK], sin, ALU.mult))
                dve.tensor_tensor(qpad[0:64, 0, :], ropet[0:64, 0, :], ropet[0:64, 1, :], ALU.add)
                dve.tensor_tensor(qpad[64:P, 1, :], ropet[64:P, 0, :], ropet[64:P, 1, :], ALU.add).then_inc(mla_dve, 1)

                def maximum(u):
                    dve.wait_ge(mla_pe, at(MLA_PE, f"S{u}", it))
                    own.then(dve.reduce_max(smx[:, u:u + 1], PS[u % 2][:, :], axis=AX.X))
                    dve.tensor_scalar(smx[:, 4 + u:5 + u], smx[:, u:u + 1], -ATTN_SCALE, None, ALU.mult).then_inc(mla_dve, 1)

                def normalise(u):
                    dve.wait_ge(mla_act, at(MLA_ACT, f"exp{u}", it))
                    own.then(dve.reciprocal(smx[:, 12 + u:13 + u], smx[:, 8 + u:9 + u]))
                    dve.tensor_scalar(prob[:, u, :], prob[:, u, :], smx[:, 12 + u:13 + u], None, ALU.mult).then_inc(mla_dve, 1)

                def head(h):
                    dve.wait_ge(mla_pe, at(MLA_PE, f"PV{h}", it))
                    dve.tensor_scalar(oT[:, bass.ds(it * 2 + h, 1), :], PS[7][:, 0:TOK].unsqueeze(1), 1.0, None, ALU.mult).then_inc(mla_dve, 1)

                maximum(0)
                maximum(1)
                normalise(0)
                normalise(1)
                maximum(2)
                maximum(3)
                head(0)
                normalise(2)
                normalise(3)
                head(1)
                ada_bias(A0["mla"] + it, mod1, "b_ada", it * 4 + A0["mla"] * 4)
            own.end(8)

            def shift(m, mu, n, dst, latents=False):
                s = slice(1, 2) if latents else slice(0, 2)
                dve.wait_ge(blk_free, n[0])
                src = pad[:, m % 2, s, :]
                own.then(dve.tensor_tensor(sh_a[:, s, :], src[:, :, 0:TOK], src[:, :, 2:TOK + 2], ALU.add))
                own.then(dve.tensor_scalar(sh_a[:, s, :], sh_a[:, s, :], mu_half[:, bass.ds(mu, 1)], None, ALU.mult))
                dve.scalar_tensor_tensor(dst, src[:, :, 1:TOK + 1], mu_keep[:, bass.ds(mu, 1)], sh_a[:, s, :], ALU.mult, ALU.add).then_inc(sh_done, 1)
                dve.wait_ge(sh_done, n[1])

            both = lambda b: b.rearrange("p (s t) -> p s t", t=TOK)
            own.then(dve.memset(sh_a[:, 0, 0:1], 0.0))
            dve.memset(pad[:, :, :, :], 0.0).then_inc(sh_zero, 1)
            with dve.Fori(0, 4) as it:
                own.loop(it, 8)
                c = C0["kv"] + it * 16
                lo(c, range(LA, 16 + LA))
                ada_bias(A0["kv"] + it, mod1, "b_ada", it * 4 + A0["kv"] * 4)
                for m in range(4):
                    if m >= 2:
                        dve.wait_ge(sh_st[m % 2], it * 32 + 16)
                    shift(m, it * 4 + 8 + m, (B0["kv"] + it * 4 + m + 1, it * 4 + m + 1), both(sh_out[:, m % 2, :]))
                for slot in range(2):
                    dve.wait_ge(sh_st[slot], it * 32 + 32)
            own.end(4)
            with dve.Fori(0, 2) as it:
                own.loop(it, 8)
                c = C0["r"] + it * 16
                lo(c, range(LA, 16 + LA))
                for m in range(4):
                    if m >= 2:
                        dve.wait_ge(sh_st[m % 2], it * 32 + 144)
                    shift(m, it * 4 + m, (B0["r"] + it * 4 + m + 1, it * 4 + 16 + m + 1), sh_out[:, m % 2, 0:TOK].unsqueeze(1), True)
                for slot in range(2):
                    dve.wait_ge(sh_st[slot], it * 32 + 160)
            own.end(2)
            c = C0["lora"]
            lo(c, range(LA, 16))
            lo(c, range(16, 16 + LA), 256)
            ada_bias(A0["lora"], mod1, "b_ada", A0["lora"] * 4)
            for m in range(4):
                shift(m, 24 + m, (B0["lora"] + m + 1, 24 + m + 1), both((wl if m < 2 else al)[:, m % 2, :]))
            c = C0["gl"]
            lo(c, range(LA, 16), 256)
            lo(c, range(16, 16 + LA))
            ada_bias(A0["gl"], mod1, "b_ada", A0["gl"] * 4)
            for m in range(2):
                shift(m, 28 + m, (B0["gl"] + m + 1, 28 + m + 1), gl[:, m, :].unsqueeze(1), True)

            with dve.Fori(0, 8) as it:
                own.loop(it, RW_OWN)
                step = [0]
                pe_at = lambda n: dve.wait_ge(rw_pe, at(RW_PE, n, it))
                act_at = lambda n: dve.wait_ge(rw_act, at(RW_ACT, n, it))

                def done(ins, label):
                    assert RW_DVE[step[0]] == label, (RW_DVE[step[0]], label)
                    step[0] += 1
                    ins.then_inc(rw_dve, 1)
                    dve.wait_ge(rw_dve, at(RW_DVE, label, it))

                pb = lambda n, h: PS[n + h][:, :].rearrange("p (b c) -> p b c", c=P)
                mask = lambda i: C("masks", i * P, i * P + P).unsqueeze(1).to_broadcast([P, 4, P])
                eye = ident.unsqueeze(1).to_broadcast([P, 4, P])
                TT, TS, STT = dve.tensor_tensor, dve.tensor_scalar, dve.scalar_tensor_tensor
                dve.wait_ge(rw_in, it * 112 + 112)
                own.then(TS(kk[:, :], k_t[:, :], pv[:, 4:5], None, ALU.mult))
                done(TT(e_ex[:, :], kk[:, :], kk[:, :], ALU.mult), "kksq")
                act_at("kkrt")
                own.then(TS(e_in[:, :], e_in[:, :], 1e-12, None, ALU.max))
                own.then(dve.reciprocal(e_in[:, :], e_in[:, :]))
                own.then(TT(kk[:, :], kk[:, :], e_in[:, :], ALU.mult))
                for d in range(2):
                    own.then(TS(kdir[:, d, :], icl[:, d, :], 1.0, pv[:, 5:6], ALU.subtract, ALU.mult))
                    own.then(STT(kdir[:, d, :], kdir[:, d, :], 1.0, k_t[:, :], ALU.add, ALU.mult))
                for d in range(2):
                    s3 = sig[:, d, :].rearrange("p (c t) -> p c t", t=CH)
                    in3, ex3 = l_in[:, :].rearrange("p (c t) -> p c t", t=CH), l_ex[:, :].rearrange("p (c t) -> p c t", t=CH)
                    own.then(dve.tensor_tensor_scan(l_in[:, :], C("restart"), sig[:, d, :], 0.0, ALU.mult, ALU.add))
                    own.then(TS(tot[:, :], in3[:, :, CH - 1], 1.0, None, ALU.mult))
                    if d == 0:
                        done(TT(l_ex[:, :], l_in[:, :], sig[:, d, :], ALU.subtract), f"L{d}")
                    else:
                        own.then(TT(ex3, tot[:, :].unsqueeze(2).to_broadcast([P, 8, CH]), in3, ALU.subtract))
                        done(TT(l_in[:, :], l_ex[:, :], sig[:, d, :], ALU.add), f"L{d}")
                    act_at(f"E{d}")
                    own.then(STT(a_s[:, :], kk[:, :], -1.0, e_ex[:, :], ALU.mult, ALU.mult))
                    own.then(TT(b_s[:, :], kk[:, :], icl[:, d, :], ALU.mult))
                    own.then(TT(b_s[:, :], b_s[:, :], e_in[:, :], ALU.mult))
                    own.then(TT(k_s[:, :], kdir[:, d, :], e_in[:, :], ALU.mult))
                    done(TT(r_s[:, :], r_t[:, :], r_s[:, :], ALU.mult), f"abk{d}")
                    lv, lvT = (M_LEVEL, M_LEVEL_T) if d == 0 else (M_LEVEL_T, M_LEVEL)
                    pe_at(f"A{d}")
                    for h in range(2):
                        own.then(TT(inv[:, h, :, :], pb(0, h), mask(lv), ALU.mult))
                        t = TT(inv[:, h, :, :], inv[:, h, :, :], eye, ALU.add)
                        if h == 0:
                            own.then(t)
                    done(t, f"I{d}")
                    pe_at(f"AT{d}")
                    for h in range(2):
                        own.then(TT(aT[:, h, :, :], pb(2, h), mask(M_STRICT + 1 - d), ALU.mult))
                        own.then(TT(invT[:, h, :, :], aT[:, h, :, :], mask(lvT), ALU.mult))
                        t = TT(invT[:, h, :, :], invT[:, h, :, :], eye, ALU.add)
                        if h == 0:
                            own.then(t)
                    done(t, f"A{d}")
                    pe_at(f"Ak{d}")
                    own.then(TT(akT[:, 0, :, :], pb(5, 0), mask(M_STRICT + 1 - d), ALU.mult))
                    done(TT(akT[:, 1, :, :], pb(5, 1), mask(M_STRICT + 1 - d), ALU.mult), f"Ak{d}")
                    pe_at(f"Ar{d}")
                    ar4 = lambda h: arx[:, h, :, :, :].rearrange("p i b c -> p (i b) c")
                    own.then(TT(ar4(0), pb(0, 0), mask(M_INCL + 1 - d), ALU.mult))
                    done(TT(ar4(1), pb(0, 1), mask(M_INCL + 1 - d), ALU.mult), f"Ar{d}")
                    ada_bias(it * 3 + A0["rwkv"] + d, mod2, "b_ada_2", it * 12 + 4 * d)
                    for l in range(1, len(LEVELS)):
                        for h in range(2):
                            pe_at(f"B{d}{l}{h}")
                            done(TT(bm[:, h, :, :], pb(0, h), mask(lv + l), ALU.mult), f"B{d}{l}{h}")
                        for h in range(2):
                            pe_at(f"G{d}{l}{h}")
                            t = TT(invT[:, h, :, :], invT[:, h, :, :], pb(2, h), ALU.add)
                            if l < len(LEVELS) - 1:
                                own.then(t)
                                t = TT(inv[:, h, :, :], inv[:, h, :, :], pb(6, h), ALU.add)
                            done(t, f"X{d}{l}{h}")
                    pe_at(f"GH{d}")
                    for e in range(2):
                        g = lambda i: PS[2 + e][:, i * 256:i * 256 + 256].rearrange("p (b c) -> p b c", c=CH)
                        own.then(TT(g1t[:, e::2, :], g(0), C("eye64").unsqueeze(1).to_broadcast([P, 4, CH]), ALU.add))
                        t = TT(hd[:, e::2, :], g(1), dec[:, e::2].unsqueeze(2).to_broadcast([P, 4, CH]), ALU.mult)
                        if e == 0:
                            own.then(t)
                    done(t, f"GH{d}")
                    pe_at(f"Q{d}")
                    done(TT(qt[:, :], PS[6][:, 0:TOK], r_s[:, :], ALU.add), f"Q{d}")
                    for i in range(1, 7):
                        c = SCAN[d][i]
                        pe_at(f"Z{d}{i}")
                        done(STT(zs[:, i + 1, :], PS[5][:, (i % 2) * CH:(i % 2) * CH + CH], dec[:, c:c + 1], hd[:, c, :], ALU.mult, ALU.add), f"Z{d}{i}")
                    pe_at(f"YZ{d}")
                    if d == 0:
                        own.then(TS(yacc[:, :], PS[7][:, 0:TOK], 1.0, None, ALU.mult))
                    else:
                        own.then(TT(yacc[:, :], yacc[:, :], PS[7][:, 0:TOK], ALU.add))
                    done(TT(yacc[:, :], yacc[:, :], PS[0][:, 0:TOK], ALU.add), f"Y{d}")
                own.then(TT(fin[:, 2, :], kdir[:, 0, TOK:T2], kdir[:, 1, TOK:T2], ALU.add))
                own.then(TT(fin[:, 2, :], fin[:, 2, :], r_t[:, :], ALU.mult))
                done(TS(fin[:, 2, :], fin[:, 2, :], pv[:, 6:7], 0.5, ALU.mult, ALU.mult), "bt")
                pe_at("mean")
                own.then(TT(fin[:, 0, :], yacc[:, :], PS[0][:, 0:TOK], ALU.subtract))
                done(TT(fin[:, 1, :], fin[:, 0, :], fin[:, 0, :], ALU.mult), "sq")
                act_at("sd")
                own.then(dve.reciprocal(yacc[:, :], yacc[:, :]))
                own.then(TT(fin[:, 0, :], fin[:, 0, :], yacc[:, :], ALU.mult))
                own.then(TS(fin[:, 0, :], fin[:, 0, :], pv[:, 7:8], pv[:, 8:9], ALU.mult, ALU.add))
                pe_at("g")
                own.then(TT(fin[:, 1, :], PS[2][:, 0:TOK], v_t[:, TOK:T2], ALU.mult))
                own.then(TT(fin[:, 0, :], fin[:, 0, :], fin[:, 1, :], ALU.add))
                done(TT(y_all[:, bass.ds(it, 1), :], fin[:, 0, :].unsqueeze(1), PS[3][:, 0:TOK].unsqueeze(1), ALU.mult), "out")
                ada_bias(it * 3 + A0["rwkv"] + 2, mod2, "b_ada_2", it * 12 + 8)
            own.end(8)
            TT, TS, STT = dve.tensor_tensor, dve.tensor_scalar, dve.scalar_tensor_tensor
            ns = [0]

            def split_lo(src, hi_, lo_, n=4):
                for g in range(src.shape[1] // n):
                    s = slice(n * g, n * g + n)
                    ns[0] += 1
                    dve.wait_ge(s_hi, ns[0])
                    TT(lo_[:, s, :], src[:, s, :], hi_[:, s, :].bitcast(F32), ALU.subtract).then_inc(s_lo, 1)

            def block_done(c_end, d0, m, nblk):
                if m < nblk - 1:
                    dve.wait_ge(blk_done, d0 + m + 1)
                else:
                    dve.wait_ge(w_used, c_end)

            split_lo(y_all, yhi, ylo)
            with dve.Fori(0, 8) as it:
                lo(C0["gate"] + it * 16, range(LA, 16 + LA))
            split_lo(oT, ohi, olo)
            dve.wait_ge(blk_free, B0["rproj"])
            with dve.Fori(0, 4) as it:
                c = C0["rproj"] + it * 8
                lo(c, range(LA, 8 + LA))
                for m in range(4):
                    block_done(c + 8, D1["rproj"] + it * 3, m, 4)
                    n = bass.ds(it * 4 + m, 1)
                    TT(mrg[:, n, :], PS[m][:, 0:TOK].unsqueeze(1), g_rwkv[:, n, :], ALU.mult).then_inc(blk_free, 1)
            dve.wait_ge(blk_free, B0["mproj"])
            with dve.Fori(0, 4) as it:
                own.loop(it, 3)
                c = C0["mproj"] + it * 16
                lo(c, range(LA, 16 + LA))
                for m in range(4):
                    block_done(c + 16, D1["mproj"] + it * 3, m, 4)
                    n = bass.ds(it * 4 + m, 1)
                    TT(g_mla[:, n, :], PS[m][:, 0:TOK].unsqueeze(1), g_mla[:, n, :], ALU.mult).then_inc(blk_free, 1)
                    dve.wait_ge(blk_free, B0["mproj"] + it * 4 + m + 1)
                    t = TT(mrg[:, n, :], mrg[:, n, :], g_mla[:, n, :], ALU.add)
                    if m < 3:
                        own.then(t)
                t.then_inc(mg_done, 1)
            own.end(4)
            split_lo(mrg, mhi, mlo)
            with dve.Fori(0, 4) as it:
                lo(C0["wout"] + it * 16, range(LA, 16 + LA))

            def residual(dst, src, g0, post, ready):
                own.then(TT(cf[:, :], mod1[:, g0:g0 + 16, 0], V(post, 0, 16), ALU.mult))
                rs = norm_scale()
                own.then(TT(src[:, :, :], src[:, :, :], rs[:, 0:TOK].unsqueeze(1).to_broadcast([P, DC, TOK]), ALU.mult))
                if ready:
                    ready()
                for k in range(DC):
                    STT(dst(k), src[:, k, :], cf[:, k:k + 1], x1[:, k, :], ALU.mult, ALU.add).then_inc(x1_done, 1)

            def gains(mod, s, g, n=DC):
                own.then(STT(gain[:, :, :], mod[:, s:s + DC, :], 1.0, g.unsqueeze(2).to_broadcast([P, DC, 2]), ALU.add, ALU.mult))

            dve.wait_ge(mod_ready, A0["ffn0"])
            residual(lambda k: x1[:, k, :], wo, 32, "mix_post", lambda: dve.wait_ge(x1_in, 16))
            gains(mod1, 64, V("ffn_pre", 0, 16))
            rs = norm_scale()
            modulated(DC, TOK, lambda k: x1[:, k, :], nap3, rs, lambda k, j: mod1[:, 48 + k, j:j + 1],
                      lambda k: fhi[:, k, :], lambda k: flo[:, k, :], C0["ffn0"])

            def conv(b, g):
                for m in range(4):
                    w = lambda j: Vd(f"conv_w{j}", g * 4 + m)
                    dve.wait_ge(blk_free, b + m + 1)
                    own.then(TS(ge[:, m, :], gpad[:, m, 0:TOK], w(0), None, ALU.mult))
                    own.then(STT(ge[:, m, :], gpad[:, m, 1:TOK + 1], w(1), ge[:, m, :], ALU.mult, ALU.add))
                    STT(ge[:, m, :], gpad[:, m, 2:TOK + 2], w(2), ge[:, m, :], ALU.mult, ALU.add).then_inc(cv_done, 1)

            def gated(c_end, d0, g):
                for m in range(4):
                    block_done(c_end, d0, m, 4)
                    dve.wait_ge(ge_done, g * 4 + m + 1)
                    TT(ge[:, m, :], ge[:, m, :], PS[m][:, 0:TOK], ALU.mult).then_inc(blk_free, 1)
                for m in range(4):
                    dve.wait_ge(u_hi, g * 4 + m + 1)
                    TT(ulo[:, m, :], ge[:, m, :], uhi[:, m, :].bitcast(F32), ALU.subtract).then_inc(u_lo, 1)

            def down(c0, lc0, d0):
                for n in range(4):
                    lo(c0, range(lc0 + 4 * n + LA, lc0 + 4 * n + 4 + LA))
                    for m in range(4):
                        block_done(c0 + lc0 + 4 * n + 4, d0 + 3 * n, m, 4)
                        k = 4 * n + m
                        TT(yffn[:, k, :], yffn[:, k, :], PS[m][:, 0:TOK], ALU.add).then_inc(dn_free, 1)

            own.then(dve.memset(yffn[:, :, :], 0.0))
            dve.memset(gpad[:, :, :], 0.0).then_inc(ff_zero, 1)
            c, d0 = C0["ffn0"], D1["ffn0"]
            lo(c, range(LA + 14, 16 + LA))
            conv(B0["ffn0"], 0)
            lo(c, range(16 + LA, 32 + LA))
            gated(c + 32, d0 + 3, 0)
            with dve.Fori(0, 10) as it:
                own.loop(it, 8)
                c, d0 = C0["ffn"] + it * 48, D1["ffn"] + it * 18
                lo(c, range(LA, 16 + LA))
                conv(B0["ffn"] + it * 8, it + 1)
                down(c, 16, d0 + 3)
                dve.wait_ge(dn_free, it * 16 + 16)
                lo(c, range(32 + LA, 48 + LA))
                gated(c + 48, d0 + 15, it + 1)
            own.end(10)
            down(C0["ffn1"], 0, D1["ffn1"])

            dve.wait_ge(dn_free, 176)
            own.then(TT(lam[:, 0:4].rearrange("p (a b) -> p a b", b=1), V("lambda", 0, 8).rearrange("p (a b) -> p a b", b=2)[:, :, 0:1],
                        V("lambda", 0, 8).rearrange("p (a b) -> p a b", b=2)[:, :, 1:2], ALU.mult))
            for l in range(2):
                t = TS(sub2[:, l:l + 1], V("subln", l), 1.0 - LAM_INIT[l], None, ALU.mult)
                if l == 0:
                    own.then(t)
            t.then_inc(lam_pr, 1)
            residual(lambda k: xall[:, k, TOK:T2], yffn, 80, "ffn_post", None)
            dve.wait_ge(lam_e, 1)
            for l in range(2):
                own.then(TT(lam[:, 4 + l:5 + l], lam[:, 2 * l:2 * l + 1], lam[:, 2 * l + 1:2 * l + 2], ALU.subtract))
                own.then(TS(lam[:, 4 + l:5 + l], lam[:, 4 + l:5 + l], LAM_INIT[l], None, ALU.add))
            dve.wait_ge(mod_ready, A0["ffn1"])
            for l in range(2):
                gains(mod2, 48 * l + 16, V("norm_2", 16 * l, 16))
                rs = norm_scale()
                modulated(DC, T2, lambda k: xall[:, k, :], nap6, rs, lambda k, j: mod2[:, 48 * l + k, j:j + 1],
                          lambda k: hhi[:, :, k, :], lambda k: hlo[:, :, k, :], C0[f"poolv{l}"])
                T = T2 if l == 0 else TOK
                t0 = T2 - T
                units = UNITS[l]
                dve.wait_ge(n_lo, (3 + l) * DC + 8)
                dve.wait_ge(x2_saved, 16 * l + 16)
                dve.memset(xp[:, :, :, :], 0.0).then_inc(xp_zero, 1)
                sq_ = slice(0, 2) if l == 0 else slice(1, 2)
                L = TOK + 32
                for it in range(2):
                    lo(C0[f"poolv{l}"] + it * 16, range(LA if it else LA + 14, 16 + LA))
                    for m in range(4):
                        n = 8 * l + it * 4 + m
                        g = it * 2 + m // 2
                        dve.wait_ge(blk_free, B0[f"poolv{l}"] + it * 4 + m + 1)
                        x_ = xp[:, m % 2, sq_, :]
                        own.then(TT(sw[:, 0, sq_, 1:L], x_[:, :, 0:L - 1], x_[:, :, 1:L], ALU.add))
                        a, cur = 1, 0
                        for j in range(g):
                            s = 1 << j
                            own.then(TT(sw[:, 1 - cur, sq_, a + s:L - a - s], sw[:, cur, sq_, a:L - a - 2 * s], sw[:, cur, sq_, a + 2 * s:L - a], ALU.add))
                            a, cur = a + s, 1 - cur
                        inv_ = C("invcnt", g * TOK, g * TOK + TOK).unsqueeze(1).to_broadcast([P, T // TOK, TOK])
                        own.then(TT(sw[:, 1 - cur, sq_, 16:16 + TOK], sw[:, cur, sq_, 16:16 + TOK], inv_, ALU.mult))
                        if it == 1 and m < 2:
                            dve.wait_ge(pw_mm, 4 * l + 2)
                        TT(pl[:, m, 0:T].rearrange("p (s t) -> p s t", t=TOK), sw[:, 1 - cur, sq_, 16:16 + TOK], x_[:, :, 16:16 + TOK], ALU.subtract).then_inc(pl_done, 1)
                        dve.wait_ge(pl_done, n + 1)
                    for g in range(2):
                        dve.wait_ge(pw_mm, 4 * l + it * 2 + g + 1)
                        for j in range(2):
                            k = it * 4 + g * 2 + j
                            TS(mix[:, k, t0:T2], PS[5 + j][:, 0:T], V("pool_scale", 8 * l + k), None, ALU.mult).then_inc(pm_done, 1)
                with dve.Fori(0, 2) as it:
                    own.loop(it, AT_OWN[l])
                    c = C0[f"qkv{l}"] + it * 48
                    lo(c, range(LA, 48 + LA))
                    step = [0]
                    pe_at = lambda n: dve.wait_ge(at_pe[l], at(AT_PE[l], n, it))
                    act_at = lambda n: dve.wait_ge(at_act[l], at(AT_ACT[l], n, it))

                    def done(ins, label):
                        assert AT_DVE[l][step[0]] == label, (AT_DVE[l][step[0]], label)
                        step[0] += 1
                        ins.then_inc(at_dve[l], 1)
                        dve.wait_ge(at_dve[l], at(AT_DVE[l], label, it))

                    for i in range(9):
                        if i < 8:
                            ts = slice(t0 if i < 4 else 0, T2)
                            act_at(f"rt{i}")
                            own.then(dve.reciprocal(rs2[:, i % 2, ts], rs2[:, i % 2, ts]))
                            done(STT(qk[:, i, ts], qk[:, i, ts], V("qn_2" if i < 4 else "kn_2", l), rs2[:, i % 2, ts], ALU.mult, ALU.mult), f"w{i}")
                        if i > 0:
                            pe_at(f"r{i - 1}")
                            own.then(TT(rope2[:, 0, :], qk[:, i - 1, TOK:T2], cos, ALU.mult))
                            own.then(TT(rope2[:, 1, :], PS[6][:, 0:TOK], sin, ALU.mult))
                            done(TT(qk[:, i - 1, TOK:T2], rope2[:, 0, :], rope2[:, 1, :], ALU.add), f"f{i - 1}")

                    def maxima(u):
                        nk = TOK if units[u][1] < 2 else T2
                        pe_at(f"S{u}")
                        s, b = 8 * (u % 2), 2 * (u % 2)
                        own.then(dve.reduce_max(smx[:, s:s + 2], psum[:, b:b + 2, 0:nk], axis=AX.X))
                        done(TS(smx[:, s + 2:s + 4], smx[:, s:s + 2], -DIFF_SCALE, None, ALU.mult), f"mx{u}")

                    for u in range(-1, len(units) + 1):
                        if u + 1 < len(units):
                            maxima(u + 1)
                        if 0 <= u < len(units):
                            nk = TOK if units[u][1] < 2 else T2
                            s = 8 * (u % 2)
                            act_at(f"e{u}")
                            own.then(dve.reciprocal(smx[:, s + 6:s + 8], smx[:, s + 4:s + 6]))
                            own.then(TT(smx[:, s + 7:s + 8], smx[:, s + 7:s + 8], lam[:, 4 + l:5 + l], ALU.mult))
                            own.then(TS(pr[:, u % 2, 1, 0:nk], pr[:, u % 2, 1, 0:nk], smx[:, s + 7:s + 8], None, ALU.mult))
                            done(STT(pr[:, u % 2, 0, 0:nk], pr[:, u % 2, 0, 0:nk], smx[:, s + 6:s + 7], pr[:, u % 2, 1, 0:nk], ALU.mult, ALU.subtract), f"a{u}")
                        if u >= 1 and last_of(l, u - 1):
                            h = units[u - 1][0]
                            act_at(f"ort{h}")
                            own.then(dve.reciprocal(ors[:, t0:T2], ors[:, t0:T2]))
                            done(STT(mix[:, bass.ds(it * 4 + 8 + h, 1), t0:T2], PS[(7, 4)[h % 2]][:, t0:T2].unsqueeze(1), sub2[:, l:l + 1], ors[:, t0:T2].unsqueeze(1),
                                     ALU.mult, ALU.mult), f"o{h}")
                own.end(2)
                dve.wait_ge(pm_done, 8 * l + 8)
                for i, name in enumerate(("poolg", "attng")):
                    with dve.Fori(0, 2) as it:
                        lo(C0[f"{name}{l}"] + it * 16, range(LA, 16 + LA))
                        for m in range(4):
                            dve.wait_ge(blk_free, B0[f"{name}{l}"] + it * 4 + m + 1)
                            n = bass.ds(it * 4 + 8 * i + m, 1)
                            TT(mix[:, n, t0:T2], mix[:, n, t0:T2], stmp[:, m % 2, 0:T].unsqueeze(1), ALU.mult).then_inc(sg_done, 1)
                dve.wait_ge(sg_done, 16 * l + 16)
                split_lo(mix[:, :, t0:T2], mixhi[:, :, t0:T2], mixlo[:, :, t0:T2], 2)
                dve.wait_ge(x2_in, 16 * l + 16)

                def out_add(it, ahead):
                    own.loop(it, 4 if l == 0 else 0)
                    c = C0[f"out{l}"] + it * 16
                    lo(c, range(LA, 16 + ahead))
                    for m in range(4):
                        block_done(c + 16, D1[f"out{l}"] + it * 3, m, 4)
                        n = bass.ds(it * 4 + m, 1)
                        gate = lambda j: mod2[:, bass.ds(it * 4 + 48 * l + 32 + m, 1), j:j + 1].rearrange("p a b -> p (a b)")
                        if l == 0:
                            own.then(STT(xall[:, n, 0:TOK], PS[m][:, 0:TOK].unsqueeze(1), gate(1), xall[:, n, 0:TOK], ALU.mult, ALU.add))
                        STT(xall[:, n, TOK:T2], PS[m][:, T - TOK:T].unsqueeze(1), gate(0), xall[:, n, TOK:T2], ALU.mult, ALU.add).then_inc(blk_free, 1)

                with dve.Fori(0, 4 if l == 0 else 3) as it:
                    out_add(it, LA)
                own.end(4)
                if l == 1:
                    out_add(3, 0)
                dve.wait_ge(blk_free, B0[f"out{l}"] + 16)



def layout(x):
    def fm(v, n=P):
        v = v.reshape(-1, n).T
        return v if n == P else np.concatenate([v, np.zeros((P - n, v.shape[1]), np.float32)], 0)

    mu = x["rwkv_mu"][0]
    lams = [x[f"lambda_{n}_2"][l] for l in range(2) for n in ("q1", "k1", "q2", "k2")]
    vec = [fm(x["b_ada"][0]), fm(x["norm_mix_pre"][0]), fm(x["norm_mix_post"][0]), fm(x["norm_ffn_pre"][0]),
           fm(x["norm_ffn_post"][0]), fm(x["gate_b"][0]), fm(x["ffn_conv_w"][0, 0]), fm(x["ffn_conv_w"][0, 1]),
           fm(x["ffn_conv_w"][0, 2]), fm(x["ffn_conv_b"][0]), fm(x["mla_q_norm"][0]), fm(x["mla_kv_norm"][0]),
           fm(mu[:3 * RW]), fm(mu[3 * RW:3 * RW + 4 * LORA], LORA), fm(mu[3 * RW + 4 * LORA:]),
           fm(x["b_ada_2"]), fm(x["norm_w_2"]), fm(x["pool_scale_2"]),
           np.concatenate([fm(x["q_norm_w_2"], 64)[:64]] * 2, 0), np.concatenate([fm(x["k_norm_w_2"], 64)[:64]] * 2, 0),
           fm(x["subln_w_2"]), fm(np.stack(lams), 64)]
    vec = np.ascontiguousarray(np.concatenate(vec, 1))
    assert vec.shape == (P, VCOLS)
    pair = [x["rwkv_w0"][0, 0], x["rwkv_w0"][0, 1], x["rwkv_a0"][0, 0], x["rwkv_a0"][0, 1], x["rwkv_k_k"][0],
            x["rwkv_k_a"][0], x["rwkv_r_k"][0].reshape(-1), x["rwkv_lnx_w"][0], x["rwkv_lnx_b"][0]]
    pvec = np.ascontiguousarray(np.stack([fm(v).T for v in pair], 2))

    def two(a, b):
        return np.stack([a.reshape(DC, P).T, b.reshape(DC, P).T], 2)

    cT = np.ascontiguousarray(np.stack([two(x["c"], x["c_ctx"]), two(x["c_2"], x["c_ctx_2"])], 1))
    uq = x["mla_w_uq"][0].reshape(512, 8, 2, 192)
    uq = np.concatenate([uq[..., :128].reshape(512, 8, 256), uq[..., 128:].reshape(512, 8, 128)], 2).reshape(512, 8 * 384)
    ukv = x["mla_w_ukv"][0].reshape(512, 8, 2, 2, 128).transpose(0, 1, 3, 2, 4).reshape(512, 8 * 512)
    w_in = x["w_in"][0]
    kpe = w_in[:, MLA0 + 1024:MLA0 + 1088]
    lora = lambda w: np.ascontiguousarray(w[0].transpose(1, 0, 2))
    return {"consts": constants(), "vec": vec, "pvec": pvec, "cT": cT, "x": x["x"][0], "ctx": x["ctx"][0], "ctx_2": x["ctx_2"][0],
            "w_ada": x["w_ada"][0], "w_in": w_in, "w_kpe": np.ascontiguousarray(np.concatenate([kpe, kpe], 1)),
            "w_uq": np.ascontiguousarray(uq), "w_ukv": np.ascontiguousarray(ukv), "w2": lora(x["rwkv_w2"]), "a2": lora(x["rwkv_a2"]),
            "g2": x["rwkv_g2"][0], "w_rwkv_proj": x["w_rwkv_proj"][0], "w_mla_proj": x["w_mla_proj"][0], "w_out": x["w_out"][0],
            "w_gate": x["ffn_w_gate"][0], "w_val": x["ffn_w_val"][0], "w_down": x["ffn_w_down"][0],
            "w_ada_2": np.ascontiguousarray(np.concatenate(list(x["w_ada_2"]), 1)), "w_in_2": x["w_in_2"], "pool_w": x["pool_w_2"], "w_out_2": x["w_out_2"]}


def kernel(**inputs):
    import concourse.bacc as bacc
    from concourse.bass_utils import run_bass_kernel_spmd

    arrays = layout({k: np.asarray(v) for k, v in inputs.items()})
    nc = bacc.Bacc("TRN2", target_bir_lowering=False, num_devices=1)
    A = {k: nc.dram_tensor(f"in_{k}", a.shape, F32, kind="ExternalInput").ap() for k, a in arrays.items()}
    out = nc.dram_tensor("out", (TOK, D), F32, kind="ExternalOutput").ap()
    build(nc, A, out)
    r = run_bass_kernel_spmd(nc, [{f"in_{k}": a for k, a in arrays.items()}], core_ids=[0])
    return r.results[0]["out"].reshape(1, TOK, D)
```

```python
from contextlib import ExitStack

import numpy as np

import concourse.bass as bass
from concourse import mybir

F32 = mybir.dt.float32
F32R = mybir.dt.float32r
ACT = mybir.ActivationFunctionType
ALU = mybir.AluOpType
AX = mybir.AxisListType

P = 128
D = 2048
DC = D // P
TOK = 256
T2 = 2 * TOK
N = 512
EPS = 1e-6
RW = 1024
LORA = 96
MLA0 = 3 * RW + 4 * LORA + 256
GATE0 = MLA0 + 512 + 512 + 64
ATTN_SCALE = (128 + 64) ** -0.5
DECAY_SCALE = float(np.exp(-0.5))
LNX_EPS = 64e-5
CH = 64
FF = 5632
DIFF_SCALE = 64 ** -0.5
LAM_INIT = [0.8 - 0.6 * float(np.exp(-0.3 * l)) for l in range(2)]
POOL_WINDOWS = (2, 4, 8, 16)

RAW = 4
HL = 4
LA = 3
ADA_RAW = 2
ADA_AT = [1, 2, 5, 6, 8, 9, 11, 12]

PHASES = [("ckv", 1, 16, 4, 3, 1), ("cq", 1, 16, 4, 3, 0), ("kpe", 1, 16, 1, 0, 1), ("mla", 8, 8, 7, 7, 1),
          ("kv", 4, 16, 4, 3, 1), ("r", 2, 16, 4, 3, 0), ("lora", 1, 16, 4, 3, 1), ("gl", 1, 16, 2, 1, 1),
          ("rwkv", 8, 0, 0, 0, 3), ("gate", 8, 16, 4, 3, 0), ("rproj", 4, 8, 4, 3, 0), ("mproj", 4, 16, 4, 3, 0),
          ("wout", 4, 16, 4, 3, 0), ("ffn0", 1, 32, 8, 6, 0), ("ffn", 10, 48, 8, 18, 0), ("ffn1", 1, 16, 0, 12, 0)]
for _l in range(2):
    PHASES += [(f"poolv{_l}", 2, 16, 4, 3, 0), (f"qkv{_l}", 2, 48, 12, 9, 0), (f"poolg{_l}", 2, 16, 4, 3, 0),
               (f"attng{_l}", 2, 16, 4, 3, 0), (f"out{_l}", 4, 16, 4, 3, 0)]
ADA_HEAD = 8
RW_OWN = 73
AT_OWN = [88, 52]


def _bases():
    chunk, block, done, ada = {}, {}, {}, {}
    c = b = d = 0
    a = ADA_HEAD
    for name, n, nc_, nb, nd, na in PHASES:
        chunk[name], block[name], done[name], ada[name] = c, b, d, a
        c, b, d, a = c + n * nc_, b + n * nb, d + n * nd, a + n * na
    return chunk, block, done, ada


C0, B0, D1, A0 = _bases()

VEC = [("b_ada", 96), ("mix_pre", 16), ("mix_post", 16), ("ffn_pre", 16), ("ffn_post", 16), ("gate_b", 32),
       ("conv_w0", 44), ("conv_w1", 44), ("conv_w2", 44), ("conv_b", 44), ("q_norm", 4), ("kv_norm", 4),
       ("mu", 30), ("b_ada_2", 96), ("norm_2", 32), ("pool_scale", 16), ("qn_2", 2), ("kn_2", 2),
       ("subln", 2), ("lambda", 8)]
VOFF, _o = {}, 0
for _n, _w in VEC:
    VOFF[_n] = _o
    _o += _w
VCOLS = _o
PAIR_VEC = ["w0_0", "w0_1", "a0_0", "a0_1", "k_k", "k_a", "r_k", "lnx_w", "lnx_b"]

CONST = [("ident", 128), ("ones", 128), ("bones", 128), ("bmean", 128), ("sel", 4), ("eps", 2), ("one", 1),
         ("rot", 128), ("cos", 256), ("sin", 256), ("masks", 16 * 128), ("restart", 512), ("eye64", 64),
         ("invcnt", 1024)]
COFF, _o = {}, 0
for _n, _w in CONST:
    COFF[_n] = _o
    _o += _w
CCOLS = _o
HEAD_CONST = [("sum_q", 32), ("sum_k", 32), ("sum_o", 32), ("spread_q", 128), ("spread_k", 128), ("spread_o", 128)]
HOFF, _o = {}, 0
for _n, _w in HEAD_CONST:
    HOFF[_n] = _o
    _o += _w
HCOLS = _o
LEVELS = [1, 2, 4, 8, 16, 32]
M_LEVEL, M_LEVEL_T, M_STRICT, M_INCL = 0, 6, 12, 14


def constants():
    c = np.zeros((P, CCOLS), np.float32)

    def put(name, a):
        c[:, COFF[name]:COFF[name] + a.shape[1]] = a

    i = np.arange(P)
    same = (i[:, None] // 64 == i[None, :] // 64).astype(np.float32)
    put("ident", np.eye(P, dtype=np.float32))
    put("ones", np.ones((P, P), np.float32))
    put("bones", same)
    put("bmean", same / 64)
    sel = np.zeros((P, 4), np.float32)
    for kk in range(2):
        for nh in range(2):
            for j in range(2):
                sel[32 * (2 * kk + nh) + j, 2 * nh + j] = 1
    put("sel", sel)
    put("eps", np.tile(np.array([[EPS, LNX_EPS]], np.float32), (P, 1)))
    put("one", np.ones((P, 1), np.float32))
    t = np.arange(TOK)
    freq = (np.float32(10000.0) ** (-np.arange(0, 32, 2, dtype=np.float32) / np.float32(32))).astype(np.float32)
    rot = np.zeros((P, P), np.float32)
    ang = np.zeros((P, TOK), np.float32)
    for p in range(P):
        pos = (t // 64 if p % 64 < 32 else t % 64).astype(np.float32)
        ang[p] = pos * freq[p % 16]
        if p % 32 < 16:
            rot[p + 16, p] = -1
        else:
            rot[p - 16, p] = 1
    put("rot", rot)
    put("cos", np.cos(ang))
    put("sin", np.sin(ang))
    r, q = i[:, None], i[None, :]
    masks = []
    for b in LEVELS:
        masks.append((r // (2 * b) == q // (2 * b)) & ((r // b) % 2 == 1) & ((q // b) % 2 == 0))
    masks += [m.T for m in masks]
    chunk = r // CH == q // CH
    masks += [chunk & (q < r), chunk & (q > r), chunk & (q <= r), chunk & (q >= r)]
    put("masks", np.concatenate([m.astype(np.float32) for m in masks], 1))
    put("restart", np.tile((np.arange(T2) % CH != 0).astype(np.float32), (P, 1)))
    put("eye64", np.tile(np.eye(64, dtype=np.float32), (2, 1)))
    cnt = [np.clip(t + w // 2, 0, TOK) - np.clip(t - w // 2, 0, TOK) for w in POOL_WINDOWS]
    put("invcnt", np.tile(np.concatenate([(1 / x.astype(np.float32)) for x in cnt])[None], (P, 1)).astype(np.float32))
    return c


def head_constants():
    c = np.zeros((P, HCOLS), np.float32)
    half, row = np.arange(P) // 64, np.arange(P) % 32
    for i, n in enumerate("qk"):
        c[np.arange(P), HOFF["sum_" + n] + 2 * i + half] = 1
        c[:, HOFF["spread_" + n]:HOFF["spread_" + n] + P] = row[:, None] == 2 * i + half[None, :]
    c[:, HOFF["sum_o"]] = 1
    c[:, HOFF["spread_o"]:HOFF["spread_o"] + P] = (row == 0)[:, None]
    return c


def at(labels, label, it=0, base=0):
    return base + it * len(labels) + labels.index(label) + 1


class Own:

    def __init__(self, eng, sem):
        self.eng, self.sem, self.n, self.it, self.per, self.n0 = eng, sem, 0, 0, 0, 0

    def then(self, ins):
        ins.then_inc(self.sem, 1)
        self.n += 1
        self.eng.wait_ge(self.sem, self.it * self.per + self.n)

    def loop(self, it, per):
        self.it, self.per, self.n0 = it, per, self.n

    def end(self, times):
        assert self.n - self.n0 == self.per, (self.n - self.n0, self.per)
        self.n = self.n0 + times * self.per
        self.it, self.per = 0, 0


def build(nc, A, out):
    ctx = ExitStack()
    with ctx:
        def sem(name):
            return ctx.enter_context(nc.semaphore(name))

        SBUF0 = 16512

        def sb(name, shape, kb, dt=F32):
            return nc.alloc_sbuf_tensor_at(name, shape, dt, offset=SBUF0 + int(kb * 1024))

        psum = ctx.enter_context(nc.psum_tensor("psum", [P, 8, 512], F32))
        PS = [psum[:, i, :] for i in range(8)]

        raw = sb("raw", [P, RAW, 2, N], 0)
        whi = sb("whi", [P, HL, N], 16, F32R)
        wlo = sb("wlo", [P, HL, N], 24, F32R)
        ada_raw = sb("ada_raw", [P, ADA_RAW, 2, N], 32)
        ada_head = sb("ada_head", [P, 2, 8, 2, N], 70)
        ada_sb = sb("ada_sb", [P, 256], 40)
        sc1 = sb("sc1", [P, DC, 32], 41)
        sc2 = sb("sc2", [P, DC, 32], 43)
        con = sb("con", [P, CCOLS], 45)
        vec = sb("vec", [P, VCOLS], 64.75)
        mod1 = sb("mod1", [P, 96, 2], 67)
        mod2 = sb("mod2", [P, 96, 2], 67.75)
        gain = sb("gain", [P, DC, 2], 68.5)
        cT = sb("cT", [P, 2, DC, 2], 68.75)
        mu_keep = sb("mu_keep", [P, 30], 69)
        mu_half = sb("mu_half", [P, 30], 69.125)
        lam = sb("lam", [P, 6], 69.25)
        smx = sb("smx", [P, 16], 69.375)
        D0 = 70
        hhi = sb("hhi", [P, 2, DC, TOK], D0 + 0, F32R)
        hlo = sb("hlo", [P, 2, DC, TOK], D0 + 32, F32R)
        xrow = sb("xrow", [P, 4, D], D0 + 64)
        xT = sb("xT", [P, DC, T2], D0 + 96)
        nsq0 = sb("nsq0", [P, 2, T2], D0 + 128)
        nrs0 = sb("nrs0", [P, T2], D0 + 132)
        nap0 = sb("nap0", [P, 3, T2], D0 + 64)
        ckvhi = sb("ckvhi", [P, 4, T2], D0 + 64, F32R)
        ckvlo = sb("ckvlo", [P, 4, T2], D0 + 72, F32R)
        cqhi = sb("cqhi", [P, 4, TOK], D0 + 80, F32R)
        cqlo = sb("cqlo", [P, 4, TOK], D0 + 84, F32R)
        kpe = sb("kpe", [P, T2], D0 + 88)
        oT = sb("oT", [P, 16, TOK], D0 + 90)
        ckv = sb("ckv", [P, 4, T2], D0 + 106)
        cq = sb("cq", [P, 4, TOK], D0 + 114)
        nsq1 = sb("nsq1", [P, 2, T2], D0 + 118)
        nrs1 = sb("nrs1", [P, T2], D0 + 122)
        nap1 = sb("nap1", [P, 3, T2], D0 + 124)
        ropet = sb("ropet", [P, 2, TOK], D0 + 135)
        nrs2 = sb("nrs2", [P, TOK], D0 + 136)
        k_sb = sb("k_sb", [P, 2, T2], D0 + 106)
        v_sb = sb("v_sb", [P, 4, 256], D0 + 110)
        qn = sb("qn", [P, 2, TOK], D0 + 114)
        qraw = sb("qraw", [P, TOK], D0 + 116)
        qpad = sb("qpad", [P, 2, TOK], D0 + 117)
        prob = sb("prob", [P, 4, T2], D0 + 119)
        probT = sb("probT", [P, 4, TOK], D0 + 127)
        probT2 = sb("probT2", [P, 4, TOK], D0 + 131)

        pad = sb("pad", [P, 4, 2, TOK + 2], D0 + 106)
        sh_a = sb("sh_a", [P, 2, TOK], D0 + 115)
        sh_out = sb("sh_out", [P, 4, T2], D0 + 117)
        wl = sb("wl", [P, 2, T2], D0 + 64)
        al = sb("al", [P, 2, T2], D0 + 68)
        gl = sb("gl", [P, 2, TOK], D0 + 72)
        atok_r = sb("rhs", [P, 2, 4, P], D0 + 8)
        r_s = [sb("r_s", [P, TOK], D0 + 0), sb("r_s1", [P, TOK], D0 + 104)]
        dec = [sb("dec", [P, 8], D0 + 1), sb("dec1", [P, 8], D0 + 105)]
        tot = [sb("tot", [P, 8], D0 + 1.125), sb("tot1", [P, 8], D0 + 105.125)]
        zs = sb("zs", [P, 8, CH], D0 + 2)
        b_tok = sb("b_tok", [P, 4, P], D0 + 4)
        k_tok = sb("k_tok", [P, 4, P], D0 + 6)
        akT = sb("akT", [P, 2, 4, P], D0 + 12)
        wu = sb("wu", [P, 2, 4, P], D0 + 12)
        bm = sb("bm", [P, 2, 4, P], D0 + 32)
        aT = sb("aT", [P, 2, 4, P], D0 + 36)
        inv = sb("inv", [P, 2, 4, P], D0 + 40)
        invT = sb("invT", [P, 2, 4, P], D0 + 44)
        v_tok = sb("v_tok", [P, 4, P], D0 + 74)
        l_in = [sb("l_in", [P, T2], D0 + 76), sb("l_in1", [P, T2], D0 + 90)]
        l_ex = [sb("l_ex", [P, T2], D0 + 78), sb("l_ex1", [P, T2], D0 + 92)]
        e_ex = [sb("e_ex", [P, T2], D0 + 80), sb("e_ex1", [P, T2], D0 + 94)]
        e_in = [sb("e_in", [P, T2], D0 + 82), sb("e_in1", [P, T2], D0 + 96)]
        a_s = [sb("a_s", [P, T2], D0 + 84), sb("a_s1", [P, T2], D0 + 98)]
        b_s = [sb("b_s", [P, T2], D0 + 86), sb("b_s1", [P, T2], D0 + 100)]
        k_s = [sb("k_s", [P, T2], D0 + 88), sb("k_s1", [P, T2], D0 + 102)]
        arx = sb("arx", [P, 2, 2, 2, P], D0 + 76)
        g1t = sb("g1t", [P, 8, CH], D0 + 80)
        hd = sb("hd", [P, 8, CH], D0 + 82)
        qt = sb("qt", [P, TOK], D0 + 84)
        fin = sb("fin", [P, 3, TOK], D0 + 86)
        k_t = sb("k_t", [P, T2], D0 + 106)
        v_t = sb("v_t", [P, T2], D0 + 108)
        r_t = sb("r_t", [P, TOK], D0 + 110)
        lw2 = sb("lw2", [P, 4, P], D0 + 111)
        g2s = sb("g2s", [P, 2, P], D0 + 113)
        pv = sb("pv", [P, 6], D0 + 114)
        pv2 = sb("pv2", [P, 3], D0 + 114.125)
        yacc = sb("yacc", [P, TOK], D0 + 1.25)
        kk = sb("kk", [P, T2], D0 + 115)
        sig = sb("sig", [P, 2, T2], D0 + 117)
        icl = sb("icl", [P, 2, T2], D0 + 121)
        kdir = sb("kdir", [P, 2, T2], D0 + 125)
        y_all = sb("y_all", [P, 8, TOK], D0 + 129)

        g_rwkv = sb("g_rwkv", [P, DC, TOK], D0 + 0)
        g_mla = sb("g_mla", [P, DC, TOK], D0 + 32)
        yhi = sb("yhi", [P, 8, TOK], D0 + 64, F32R)
        ylo = sb("ylo", [P, 8, TOK], D0 + 72, F32R)
        ohi = sb("ohi", [P, DC, TOK], D0 + 16, F32R)
        olo = sb("olo", [P, DC, TOK], D0 + 48, F32R)
        mrg = sb("mrg", [P, DC, TOK], D0 + 106)
        mhi = sb("mhi", [P, DC, TOK], D0 + 0, F32R)
        mlo = sb("mlo", [P, DC, TOK], D0 + 32, F32R)
        wo = sb("wo", [P, DC, TOK], D0 + 64)
        cf = sb("cf", [P, DC], 69.4375)
        nsq3 = sb("nsq3", [P, 2, TOK], D0 + 80)
        nrs3 = sb("nrs3", [P, TOK], D0 + 82)
        nap3 = sb("nap3", [P, 3, TOK], D0 + 83)
        x1 = sb("x1", [P, DC, TOK], D0 + 88)
        fhi = sb("fhi", [P, DC, TOK], D0 + 16, F32R)
        flo = sb("flo", [P, DC, TOK], D0 + 48, F32R)
        gpad = sb("gpad", [P, 4, TOK + 2], D0 + 0)
        ge = sb("ge", [P, 4, TOK], D0 + 4.25)
        uhi = sb("uhi", [P, 4, TOK], D0 + 32, F32R)
        ulo = sb("ulo", [P, 4, TOK], D0 + 36, F32R)
        yffn = sb("yffn", [P, DC, TOK], D0 + 64)
        crow = sb("crow", [P, 2, D], D0 + 0)
        xall = sb("xall", [P, DC, T2], D0 + 104)
        nap6 = sb("nap6", [P, 3, T2], D0 + 64)
        nsq6 = sb("nsq6", [P, 2, T2], D0 + 70)
        nrs6 = sb("nrs6", [P, T2], D0 + 74)
        mix = sb("mix", [P, DC, T2], D0 + 64)
        mixhi = sb("mixhi", [P, DC, T2], D0 + 0, F32R)
        mixlo = sb("mixlo", [P, DC, T2], D0 + 32, F32R)
        qk = sb("qk", [P, 8, T2], D0 + 96)
        v2 = sb("v2", [P, 4, N], D0 + 112)
        pr = sb("pr", [P, 3, 2, T2], D0 + 120)
        aTs = sb("aTs", [P, 2, 4, P], D0 + 132)
        sq2 = sb("sq2", [P, 4, T2], D0 + 120)
        rope2 = sb("rope2", [P, 2, TOK], D0 + 128)
        rs2 = sb("rs2", [P, T2], D0 + 130)
        hcon = sb("hcon", [P, HCOLS], 41)
        rotw = sb("rotw", [P, 2, P], 43)
        smx2 = sb("smx2", [P, 24], 69.5)
        sub2 = sb("sub2", [P, 2], 69.28125)
        pl = sb("pl", [P, 4, T2], D0 + 96)
        stmp = sb("stmp", [P, 2, T2], D0 + 96)
        pw = sb("pw", [P, 4, 2, 256], D0 + 120)
        xp = sb("xp", [P, 2, 2, TOK + 32], D0 + 128)
        sw = sb("sw", [P, 2, 2, TOK + 32], D0 + 132.5)
        orow = sb("orow", [P, 2, D], D0 + 0)

        def C(name, a=0, b=None):
            w = dict(CONST)[name]
            return con[:, COFF[name] + a:COFF[name] + (w if b is None else b)]

        def H(name, rows=slice(0, P)):
            return hcon[rows, HOFF[name]:HOFF[name] + dict(HEAD_CONST)[name]]

        def V(name, i=0, n=1):
            return vec[:, VOFF[name] + i:VOFF[name] + i + n]

        def Vd(name, i, n=1):
            return vec[:, bass.ds(VOFF[name] + i, n)]

        ident, ones, bones, bmean, rot = C("ident"), C("ones"), C("bones"), C("bmean"), C("rot")
        cos, sin = C("cos"), C("sin")

        const_in = sem("const_in")
        rows_in = sem("rows_in")
        raw_in = [sem(f"raw_in{i}") for i in range(RAW)]
        w_hi = sem("w_hi")
        w_lo = sem("w_lo")
        w_used = sem("w_used")
        blk_done = sem("blk_done")
        blk_free = sem("blk_free")
        ada_in = [sem(f"ada_in{i}") for i in range(ADA_RAW)]
        ada_hin = [sem(f"ada_hin{i}") for i in range(2)]
        ada_used = sem("ada_used")
        ada_out = sem("ada_out")
        ada_fin = sem("ada_fin")
        mod_ready = sem("mod_ready")
        sc_zero = sem("sc_zero")
        sc_ready = sem("sc_ready")
        tr_done = sem("tr_done")
        tr_out = sem("tr_out")
        n_sq = sem("n_sq")
        n_mm = sem("n_mm")
        n_std = sem("n_std")
        n_f32 = sem("n_f32")
        n_hi = sem("n_hi")
        n_lo = sem("n_lo")
        dve_own = sem("dve_own")
        act_own = sem("act_own")
        mla_pe = sem("mla_pe")
        mla_act = sem("mla_act")
        mla_dve = sem("mla_dve")
        rope_mm = sem("rope_mm")
        x_saved = sem("x_saved")

        w_in = A["w_in"]
        MLA_PE = ["rot", "S0", "S1", "T0", "T1", "S2", "S3", "PV0", "T2", "T3", "PV1"]
        MLA_DVE = ["q", "nmx0", "nmx1", "pn0", "pn1", "nmx2", "nmx3", "o0", "pn2", "pn3", "o1"]
        MLA_ACT = ["exp0", "exp1", "pT0", "pT1", "exp2", "exp3", "pT2", "pT3"]

        sh_done = sem("sh_done")
        sh_st = [sem(f"sh_st{i}") for i in range(4)]
        sh_free = sem("sh_free")
        lora_act = sem("lora_act")
        pool_gate = sem("pool_gate")
        pe_gate = sem("pe_gate")
        rw_in = sem("rw_in")
        rw_in2 = sem("rw_in2")
        o_saved = sem("o_saved")
        o_in = sem("o_in")
        rw_pe = sem("rw_pe")
        rw_act = sem("rw_act")
        rw_dve = sem("rw_dve")
        def levels(d, names):
            return [[f"{n}{d}{l}{h}" for n in names for h in range(2)] for l in range(1, len(LEVELS))]

        z = [[f"Z{d}{i}" for i in range(1, 7)] for d in range(2)]
        RW_PE = ["w0", "w1", "a0", "a1", "kksum", "tr0", "A0", "AT0", "Ak0", "Ar0", "P10"] + sum(levels(0, "BG"), [])
        RW_PE += ["WU0", "GH0", "Q0", "YL0", "Z01", "A1", "Z02", "AT1"] + z[0][2:] + ["YZ0", "tr1", "Ak1", "Ar1", "P11"]
        RW_PE += sum(levels(1, "BG"), []) + ["WU1", "GH1", "Q1", "YL1"] + z[1] + ["YZ1", "mean", "var", "bon", "g"]
        RW_ACT = ["w0", "w1", "a0", "a1", "kkrt", "E0", "trv", "tr0", "P10", "E1", "WU0", "tr1", "P11", "WU1", "sd"]
        lv0, lv1 = levels(0, "BX"), levels(1, "BX")
        RW_DVE = ["kksq", "L0", "abk0", "I0", "A0", "Ak0", "Ar0"] + lv0[0] + ["L1"] + lv0[1] + lv0[2] + ["abk1"] + sum(lv0[3:], [])
        RW_DVE += ["W0", "GH0", "Q0", "Z01", "Z02", "Z03", "I1", "Z04", "Z05", "A1", "Z06", "Y0", "Ak1", "Ar1"] + sum(lv1, [])
        RW_DVE += ["W1", "GH1", "Q1"] + z[1] + ["Y1", "bt", "sq", "out"]
        SCAN = [[0, 1, 2, 3, 4, 5, 6, 7], [3, 2, 1, 0, 7, 6, 5, 4]]

        s_hi = sem("s_hi")
        s_lo = sem("s_lo")
        mg_done = sem("mg_done")
        x1_in = sem("x1_in")
        x1_done = sem("x1_done")
        dn_free = sem("dn_free")
        ff_zero = sem("ff_zero")
        cv_done = sem("cv_done")
        ge_done = sem("ge_done")
        u_hi = sem("u_hi")
        u_lo = sem("u_lo")
        crow_in = sem("crow_in")
        hcon_in = sem("hcon_in")
        rotw_ok = sem("rotw_ok")
        x2_saved = sem("x2_saved")
        x2_in = sem("x2_in")
        pw_in = sem("pw_in")
        lam_pr, lam_mm, lam_e, lam_ok = sem("lam_pr"), sem("lam_mm"), sem("lam_e"), sem("lam_ok")
        xp_zero = sem("xp_zero")
        pl_done = sem("pl_done")
        pw_mm = sem("pw_mm")
        pm_done = sem("pm_done")
        sg_done = sem("sg_done")
        at_pe = [sem(f"at_pe{l}") for l in range(2)]
        at_act = [sem(f"at_act{l}") for l in range(2)]
        at_dve = [sem(f"at_dve{l}") for l in range(2)]
        fin_tr, fin_cp, out_st = sem("fin_tr"), sem("fin_cp"), sem("out_st")
        TILES = [[0, 1, 2, 3], [2, 3]]
        UNITS = [[(h, t) for h in range(4) for t in TILES[l]] for l in range(2)]
        last_of = lambda l, u: UNITS[l][u][1] == 3
        QK_HEADS = [0, 4, 1, 5, 2, 6, 3, 7]
        AT_PE, AT_ACT, AT_DVE = [[], []], [[], []], [[], []]
        for l in range(2):
            nu = len(UNITS[l])
            AT_DVE[l] += ["z"] if l else []
            for b in range(8):
                AT_PE[l] += [f"r{b}", f"n{b}"]
                AT_ACT[l] += [f"sq{b}"]
                AT_DVE[l] += [f"t{b}"]
            AT_PE[l] += [f"c{b}" for b in QK_HEADS]
            AT_ACT[l] += ["rt"]
            AT_DVE[l] += ["rc"] + [f"f{b}" for b in QK_HEADS]
            for u in range(-2, nu + 1):
                nxt = [str(u + 2)] if u + 2 < nu else []
                now = [str(u)] if 0 <= u < nu else []
                end = [str(UNITS[l][u - 1][0])] if u >= 1 and last_of(l, u - 1) else []
                AT_PE[l] += ["S" + n for n in nxt] + ([f"PV{u - 1}"] if u >= 1 else []) + ["T" + n for n in now]
                AT_ACT[l] += ["o" + n for n in end] + ["aT" + n for n in now] + ["e" + n for n in nxt]
                AT_DVE[l] += ["a" + n for n in now] + ["mx" + n for n in nxt]
            AT_PE[l] += ["no"] + [f"co{h}" for h in range(4)]
            AT_ACT[l] += ["rto"]
            AT_DVE[l] += ["rco"] + [f"fo{h}" for h in range(4)]

        nsq_of = [nsq0, nsq1, nsq1, nsq3, nsq3, nsq3, nsq6, nsq6]
        nrs_of = [nrs0, nrs1, nrs2, nrs3, nrs3, nrs3, nrs6, nrs6]
        nt_of = [T2, T2, TOK, TOK, TOK, TOK, T2, T2]

        def like(buf, dst):
            return buf.rearrange("p (s t) -> p s t", t=TOK) if len(dst.shape) == 3 else buf

        x_keep = nc.dram_tensor("x_keep", (P, DC, TOK), F32, kind="Internal").ap()

        rkv = nc.dram_tensor("rkv", (24, P, T2), F32, kind="Internal").ap()

        o_keep = nc.dram_tensor("o_keep", (P, 16, TOK), F32, kind="Internal").ap()
        x2_keep = nc.dram_tensor("x2_keep", (P, DC, T2), F32, kind="Internal").ap()

        block = ctx.enter_context(nc.Block())

        @block.sync
        def _(sp):
            def seg(view, c0, lc0, nch):
                for r in range(nch // 2):
                    lc = lc0 + 2 * r
                    src = view(r)
                    c = c0 + lc
                    if not isinstance(c, int) or c >= 2 * RAW:
                        sp.wait_ge(w_lo, c - 2 * RAW + 2)
                    slot = (lc // 2) % RAW
                    sp.dma_start(raw[:, slot, :, 0:src.shape[2]], src).then_inc(raw_in[slot], 16)

            def cols(w, col, n=N):
                return lambda r: w[256 * r:256 * r + 256, bass.ds(col, n)].rearrange("(a p) n -> p a n", p=P)

            sp.dma_start(con[:, :], A["consts"]).then_inc(const_in, 16)
            sp.dma_start(vec[:, :], A["vec"]).then_inc(const_in, 16)
            sp.dma_start(cT[:, :, :, :], A["cT"]).then_inc(const_in, 16)
            for t in range(2):
                sp.dma_start(xrow[:, t, :], A["ctx"][P * t:P * t + P, :]).then_inc(rows_in, 16)
                sp.dma_start(xrow[:, 2 + t, :], A["x"][P * t:P * t + P, :]).then_inc(rows_in, 16)
            def ada_group(p, col, it=None):
                for kh in range(8):
                    if it is not None:
                        sp.wait_ge(ada_used, it * 16 + 8 * p - 15 + kh)
                    sp.dma_start(ada_head[:, p, kh, :, :], A["w_ada"][256 * kh:256 * kh + 256, bass.ds(col, N)].rearrange("(a p) n -> p a n", p=P)).then_inc(ada_hin[p], 16)
            for p in range(2):
                ada_group(p, p * N)
            with sp.Fori(1, ADA_HEAD // 2) as it:
                c0, c1 = sp.snap(it * 2 * N), sp.snap(it * 2 * N + N)
                ada_group(0, c0, it)
                ada_group(1, c1, it)
            seg(cols(w_in, MLA0 + 512), C0["ckv"], 0, 16)
            seg(cols(w_in, MLA0), C0["cq"], 0, 16)
            seg(cols(A["w_kpe"], 0, P), C0["kpe"], 0, 16)
            with sp.Fori(0, 8) as it:
                cu, cq_ = sp.snap(it * N), sp.snap(it * 384)
                seg(cols(A["w_ukv"], cu), C0["mla"] + it * 8, 0, 4)
                seg(cols(A["w_uq"], cq_, 384), C0["mla"] + it * 8, 4, 4)
            with sp.Fori(0, 4) as it:
                col = sp.snap(it * N + RW)
                seg(cols(w_in, col), C0["kv"] + it * 16, 0, 16)
            with sp.Fori(0, 2) as it:
                col = sp.snap(it * N)
                seg(cols(w_in, col), C0["r"] + it * 16, 0, 16)
            seg(cols(w_in, 3 * RW), C0["lora"], 0, 16)
            seg(cols(w_in, 3 * RW + 4 * LORA, 256), C0["gl"], 0, 16)
            with sp.Fori(0, 8) as it:
                col = sp.snap(it * N + GATE0)
                seg(cols(w_in, col), C0["gate"] + it * 16, 0, 16)
            for name, w in (("rproj", "w_rwkv_proj"), ("mproj", "w_mla_proj"), ("wout", "w_out")):
                n = 8 if name == "rproj" else 16
                with sp.Fori(0, 4) as it:
                    col = sp.snap(it * N)
                    seg(cols(A[w], col), C0[name] + it * n, 0, n)

            def down(row0, row1, c0, lc0):
                for n in range(4):
                    seg(lambda r: A["w_down"][bass.ds((row0, row1)[r], 256), n * N:n * N + N].rearrange("(a p) n -> p a n", p=P),
                        c0, lc0 + 4 * n, 4)
            seg(cols(A["w_gate"], 0), C0["ffn0"], 0, 16)
            seg(cols(A["w_val"], 0), C0["ffn0"], 16, 16)
            with sp.Fori(0, 10) as it:
                c = C0["ffn"] + it * 48
                col, r0, r1 = sp.snap(it * N + N), sp.snap(it * N), sp.snap(it * N + 256)
                seg(cols(A["w_gate"], col), c, 0, 16)
                down(r0, r1, c, 16)
                seg(cols(A["w_val"], col), c, 32, 16)
            down(10 * N, 10 * N + 256, C0["ffn1"], 0)
            for l in range(2):
                w = A["w_in_2"][l]
                def pairs(name, col0):
                    with sp.Fori(0, 2) as it:
                        col = sp.snap(it * N + col0)
                        seg(cols(w, col), C0[f"{name}{l}"] + it * 16, 0, 16)

                pairs("poolv", 0)
                with sp.Fori(0, 2) as it:
                    c = C0[f"qkv{l}"] + it * 48
                    cq_, ck, cv = sp.snap(it * N + 2048), sp.snap(it * N + 3072), sp.snap(it * N + 4096)
                    for i, col in enumerate((cq_, ck, cv)):
                        seg(cols(w, col), c, 16 * i, 16)
                pairs("poolg", 1024)
                pairs("attng", 5120)
                with sp.Fori(0, 4) as it:
                    col = sp.snap(it * N)
                    seg(cols(A["w_out_2"][l], col), C0[f"out{l}"] + it * 16, 0, 16)
            for t in range(2):
                sp.wait_ge(fin_cp, 32)
                sp.dma_start(out[P * t:P * t + P, :], orow[:, t, :]).then_inc(out_st, 16)
            sp.wait_ge(out_st, 32)

        @block.gpsimd
        def _(pool):
            pool.wait_ge(tr_out, DC)
            pool.dma_start(x_keep, xT[:, :, TOK:T2]).then_inc(x_saved, 16)
            pool.wait_ge(x_saved, 16)
            def ada_group(w, col, a, khs=range(8)):
                for kh in khs:
                    if not isinstance(a, int) or a + kh >= 8 * ADA_HEAD + ADA_RAW:
                        pool.wait_ge(ada_used, a + kh - ADA_RAW + 1)
                    if not isinstance(a, int):
                        pool.sem_inc(pool_gate, 1)
                    pool.dma_start(ada_raw[:, kh % ADA_RAW, :, :], A[w][256 * kh:256 * kh + 256, bass.ds(col, N)].rearrange("(a p) n -> p a n", p=P)).then_inc(ada_in[kh % ADA_RAW], 16)

            for name in ("ckv", "kpe"):
                ada_group("w_ada", A0[name] * N, A0[name] * 8)
            with pool.Fori(0, 8) as it:
                col = pool.snap(it * N + A0["mla"] * N)
                ada_group("w_ada", col, it * 8 + A0["mla"] * 8)
            pool.wait_ge(mla_dve, 8 * len(MLA_DVE))
            pool.dma_start(o_keep, oT[:, :, :]).then_inc(o_saved, 16)
            pool.sem_inc(sh_free, 1)
            ada_group("w_ada", A0["kv"] * N, A0["kv"] * 8, range(2))
            with pool.Fori(0, 4) as it:
                col, col1 = pool.snap(it * N + A0["kv"] * N), pool.snap(it * N + A0["kv"] * N + N)
                ada_group("w_ada", col, it * 8 + A0["kv"] * 8, range(2, 8))
                ada_group("w_ada", col1, it * 8 + A0["kv"] * 8 + 8, range(2))
                for m in range(4):
                    dst = pool.snap(it * 4 + 8 + m)
                    pool.wait_ge(sh_done, it * 4 + m + 2)
                    pool.sem_inc(pool_gate, 1)
                    pool.dma_start(rkv[bass.ds(dst, 1), :, :].rearrange("o p t -> p (o t)"), sh_out[:, m, :]).then_inc(sh_st[m], 16)
                for m in range(4):
                    pool.wait_ge(sh_st[m], it * 16 + 16)
                pool.sem_inc(sh_free, 1)
            with pool.Fori(0, 2) as it:
                for m in range(4):
                    dst = pool.snap(it * 4 + m)
                    pool.wait_ge(sh_done, it * 4 + 16 + m + 2)
                    pool.sem_inc(pool_gate, 1)
                    pool.dma_start(rkv[bass.ds(dst, 1), :, TOK:T2].rearrange("o p t -> p (o t)"), sh_out[:, m, 0:TOK]).then_inc(sh_st[m], 16)
                for m in range(4):
                    pool.wait_ge(sh_st[m], it * 16 + 80)
                pool.sem_inc(sh_free, 1)
            ada_group("w_ada", A0["lora"] * N, A0["lora"] * 8, range(2, 8))
            ada_group("w_ada", A0["gl"] * N, A0["gl"] * 8)
            pool.wait_ge(o_saved, 16)
            pool.wait_ge(sh_done, 31)
            def first_inputs(p, r0, k0, f0):
                pool.dma_start(k_t[:, :], rkv[bass.ds(k0, 1), :, :].rearrange("o p t -> p (o t)")).then_inc(rw_in, 16)
                pool.dma_start(pv[:, :], A["pvec"][bass.ds(r0, 1), :, 0:6].rearrange("o p t -> p (o t)")).then_inc(rw_in, 16)
                pool.dma_start(lw2[0:LORA, 0:2, :], A["w2"][:, :, bass.ds(f0, P)]).then_inc(rw_in, 16)
                pool.dma_start(lw2[0:LORA, 2:4, :], A["a2"][:, :, bass.ds(f0, P)]).then_inc(rw_in, 16)

            def pair(it, r0, v0, f0):
                pool.dma_start(v_t[:, :], rkv[bass.ds(v0, 1), :, :].rearrange("o p t -> p (o t)")).then_inc(rw_in2, 16)
                pool.dma_start(r_t[:, :], rkv[bass.ds(r0, 1), :, TOK:T2].rearrange("o p t -> p (o t)")).then_inc(rw_in2, 16)
                pool.dma_start(g2s[:, :, :], A["g2"][:, bass.ds(f0, P)].rearrange("(k p) n -> p k n", p=P)).then_inc(rw_in2, 16)
                pool.dma_start(pv2[:, :], A["pvec"][bass.ds(r0, 1), :, 6:9].rearrange("o p t -> p (o t)")).then_inc(rw_in2, 16)
                for j in range(3):
                    col = it * 3 * N + j * N
                    ada_group("w_ada_2", col if isinstance(it, int) else pool.snap(col), (it * 3 + A0["rwkv"] + j) * 8)

            first_inputs(0, 0, 8, 0)
            with pool.Fori(0, 7) as it:
                f0, r0, v0 = pool.snap(it * P), pool.snap(it), pool.snap(it + 16)
                f1, r1, k1 = pool.snap(it * P + P), pool.snap(it + 1), pool.snap(it + 9)
                pair(it, r0, v0, f0)
                pool.wait_ge(rw_dve, at(RW_DVE, "abk1", it))
                pool.sem_inc(pool_gate, 1)
                first_inputs(it + 1, r1, k1, f1)
                pool.wait_ge(rw_dve, it * len(RW_DVE) + len(RW_DVE))
                pool.sem_inc(pool_gate, 1)
            pair(7, 7, 23, 7 * P)
            pool.wait_ge(rw_in, 8 * 4 * 16)
            pool.wait_ge(rw_in2, 8 * 4 * 16)
            pool.wait_ge(rw_dve, 8 * len(RW_DVE))
            pool.dma_start(oT[:, :, :], o_keep).then_inc(o_in, 16)
            pool.wait_ge(o_in, 16)
            pool.wait_ge(s_lo, 2 + 4)
            pool.dma_start(x1[:, :, :], x_keep).then_inc(x1_in, 16)
            pool.wait_ge(x1_in, 16)
            pool.wait_ge(u_lo, 44)
            for t in range(2):
                pool.dma_start(crow[:, t, :], A["ctx_2"][P * t:P * t + P, :]).then_inc(crow_in, 16)
            pool.dma_start(hcon[:, :], A["hconsts"]).then_inc(hcon_in, 16)
            pool.wait_ge(hcon_in, 16)
            pool.wait_ge(crow_in, 32)
            for l in range(2):
                if l == 0:
                    pool.wait_ge(tr_out, 2 * DC)
                    pool.wait_ge(x1_done, 2 * DC)
                else:
                    pool.wait_ge(blk_free, B0["poolv1"])
                pool.dma_start(x2_keep, xall[:, :, :]).then_inc(x2_saved, 16)
                pool.wait_ge(x2_saved, 16 * l + 16)
                pool.wait_ge(n_lo, (3 + l) * DC + 8)
                pool.dma_start(pw[:, :, :, :], A["pool_w"][l].rearrange("g (k p) n -> p g k n", p=P)).then_inc(pw_in, 16)
                pool.wait_ge(pw_in, 16 * l + 16)
                pool.wait_ge(at_dve[l], 2 * len(AT_DVE[l]))
                pool.dma_start(xall[:, :, :], x2_keep).then_inc(x2_in, 16)
                pool.wait_ge(x2_in, 16 * l + 16)

        @block.tensor
        def _(pe):
            def ada_mm(sc, kh, src):
                for kk in range(2):
                    for nh in range(2):
                        t = 32 * (2 * kk + nh)
                        mm = pe.matmul(PS[4][t:t + 32, 0:256], sc[:, 2 * kh + kk, :], src[:, kk, nh * 256:nh * 256 + 256],
                                       start=(kh == 0), stop=(kh == 7), tile_position=(0, t))
                mm.then_inc(ada_used, 1)

            def ada_half(sc, kh, g):
                pe.wait_ge(ada_in[kh % ADA_RAW], (g - ADA_HEAD) * (8 // ADA_RAW * 16) + (kh // ADA_RAW + 1) * 16)
                if kh == 0:
                    pe.wait_ge(mod_ready, g)
                ada_mm(sc, kh, ada_raw[:, kh % ADA_RAW, :, :])

            def ada_final(g):
                pe.wait_ge(ada_out, g + 1)
                for m in range(4):
                    mm = pe.matmul(PS[4][:, 256 + 2 * m:258 + 2 * m], ada_sb[:, (m % 2) * P:(m % 2) * P + P],
                                   C("sel", 2 * (m // 2), 2 * (m // 2) + 2), start=True, stop=True)
                mm.then_inc(ada_fin, 1)

            def seg(c0, lc0, nch, b0, nblk, product, ada=None, each=True, ready=None, between=None):
                for k in range(nch):
                    slot = (lc0 + k) % HL
                    pe.wait_ge(w_lo, c0 + lc0 + k + 1)
                    if ready is not None:
                        pe.wait_ge(n_lo, ready + k + 1)
                    for m in range(nblk):
                        if k == 0 and callable(each):
                            each(m)
                        elif k == 0 and each:
                            pe.wait_ge(blk_free, b0 + m - 3)
                        pairs, dst, first = product(m, k, slot)
                        for i, (l, r) in enumerate(pairs):
                            mm = pe.matmul(dst, l, r, start=(k == 0 and i == 0 and first), stop=(k == nch - 1 and i == 2),
                                           skip_group_check=True)
                        if k == nch - 1 and m < nblk - 1:
                            mm.then_inc(blk_done, 1)
                    mm.then_inc(w_used, 1)
                    if between:
                        between(k)
                    if ada and k in ADA_AT:
                        kh = ADA_AT.index(k)
                        ada_half(ada[0], kh, ada[1])
                if ada:
                    ada_final(ada[1])

            def rows(xhi, xlo, T):
                def product(m, k, slot):
                    wh, wl = whi[:, slot, m * P:m * P + P], wlo[:, slot, m * P:m * P + P]
                    return [(wh, xhi(k)), (wh, xlo(k)), (wl, xhi(k))], PS[m][:, 0:T], True
                return product

            h2 = rows(lambda k: hhi[:, :, k, :], lambda k: hlo[:, :, k, :], T2)
            h1 = rows(lambda k: hhi[:, 1, k, :], lambda k: hlo[:, 1, k, :], TOK)
            nq = [0]
            nn = [0]

            def norm(n, T):
                for k in range(n):
                    pe.wait_ge(n_sq, nq[0] + 1)
                    if k == 0 and nn[0] > 0:
                        pe.wait_ge(n_std, nn[0])
                    pe.matmul(PS[5][:, 0:T], ones, nsq_of[nn[0]][:, nq[0] % 2, 0:T], start=(k == 0),
                              stop=(k == n - 1)).then_inc(n_mm, 1)
                    nq[0] += 1
                nn[0] += 1

            pe.wait_ge(const_in, 48)
            pe.wait_ge(rows_in, 64)
            for d in range(DC):
                if d >= 2:
                    pe.wait_ge(tr_out, d - 1)
                for t in range(4):
                    tr = pe.transpose(PS[6 + d % 2][:, t * P:t * P + P], xrow[:, t, d * P:d * P + P], ident)
                tr.then_inc(tr_done, 1)
            norm(DC, T2)
            pe.wait_ge(sc_ready, 2)
            with pe.Fori(0, ADA_HEAD // 2) as it:
                for p in range(2):
                    g = it * 2 + p
                    pe.wait_ge(ada_hin[p], it * 128 + 128)
                    if p == 1:
                        pe.wait_ge(mod_ready, g)
                    for kh in range(8):
                        ada_mm(sc1, kh, ada_head[:, p, kh, :, :])
                    ada_final(g)
                pe.wait_ge(mod_ready, it * 2 + 2)
            seg(C0["ckv"], 0, 16, 0, 4, h2, (sc1, A0["ckv"]), each=False, ready=0)
            pe.wait_ge(blk_free, B0["cq"])
            seg(C0["cq"], 0, 16, 0, 4, h1, None, each=False)
            pe.wait_ge(blk_free, B0["kpe"])
            seg(C0["kpe"], 0, 16, 0, 1, h2, (sc1, A0["kpe"]), each=False)
            norm(4, T2)
            norm(4, TOK)
            pe.wait_ge(blk_free, B0["mla"])
            pe.matmul(PS[6][:, 0:TOK], rot, kpe[:, TOK:T2], start=True, stop=True).then_inc(rope_mm, 1)
            pe.wait_ge(n_lo, DC + 8)

            def ukv(m, k, slot):
                if m < 2:
                    wh, wl = whi[:, slot, m * P:m * P + P], wlo[:, slot, m * P:m * P + P]
                    return [(wh, ckvhi[:, k, :]), (wh, ckvlo[:, k, :]), (wl, ckvhi[:, k, :])], PS[m][:, :], True
                t = m - 2
                wh, wl = whi[:, slot, 256:512], wlo[:, slot, 256:512]
                xh, xl = ckvhi[:, k, t * P:t * P + P], ckvlo[:, k, t * P:t * P + P]
                return [(xh, wh), (xh, wl), (xl, wh)], PS[2 + t // 2][:, (t % 2) * 256:(t % 2) * 256 + 256], t % 2 == 0

            uq = rows(lambda k: cqhi[:, k, :], lambda k: cqlo[:, k, :], TOK)
            with pe.Fori(0, 8) as it:
                pe.wait_ge(blk_free, B0["mla"] + it * 7)
                seg(C0["mla"] + it * 8, 0, 4, 0, 6, ukv, None, each=False)
                pe.wait_ge(blk_free, B0["mla"] + it * 7 + 4)
                seg(C0["mla"] + it * 8, 4, 4, 0, 3, uq, None, each=False)
                pe.wait_ge(blk_free, B0["mla"] + it * 7 + 7)
                pe.matmul(PS[3][:, 0:TOK], rot, qraw[:, :], start=True, stop=True).then_inc(mla_pe, 1)

                def scores(u):
                    h, q0 = u // 2, (u % 2) * P
                    if u == 0:
                        pe.wait_ge(mla_dve, at(MLA_DVE, "q", it))
                    if u >= 2:
                        pe.wait_ge(mla_act, at(MLA_ACT, f"exp{u - 2}", it))
                    pe.matmul(PS[u % 2][:, :], qn[:, h, q0:q0 + P], k_sb[:, h, :], start=True, stop=False)
                    pe.matmul(PS[u % 2][:, :], qpad[:, h, q0:q0 + P], kpe[:, :], start=False, stop=True).then_inc(mla_pe, 1)

                def turn(u):
                    pe.wait_ge(mla_dve, at(MLA_DVE, f"pn{u}", it))
                    if u >= 1:
                        pe.wait_ge(mla_act, at(MLA_ACT, f"pT{u - 1}", it))
                    for kt in range(4):
                        tr = pe.transpose(PS[6][:, kt * P:kt * P + P], prob[:, u, kt * P:kt * P + P], ident)
                    tr.then_inc(mla_pe, 1)

                def values(h):
                    pe.wait_ge(mla_act, at(MLA_ACT, f"pT{2 * h + 1}", it))
                    if h == 1:
                        pe.wait_ge(mla_dve, at(MLA_DVE, "o0", it))
                    for kt in range(4):
                        mm = pe.matmul(PS[7][:, 0:TOK], v_sb[:, kt, h * P:h * P + P], (probT, probT2)[h][:, kt, :],
                                       start=(kt == 0), stop=(kt == 3))
                    mm.then_inc(mla_pe, 1)

                def ada(*khs):
                    for kh in khs:
                        ada_half(sc1, kh, A0["mla"] + it)

                ada(0, 1)
                scores(0)
                scores(1)
                ada(2, 3)
                turn(0)
                turn(1)
                scores(2)
                scores(3)
                ada(4, 5)
                values(0)
                turn(2)
                turn(3)
                ada(6, 7)
                values(1)
                ada_final(A0["mla"] + it)
            with pe.Fori(0, 4) as it:
                seg(C0["kv"] + it * 16, 0, 16, B0["kv"] + it * 4, 4, h2, (sc1, A0["kv"] + it))
            with pe.Fori(0, 2) as it:
                seg(C0["r"] + it * 16, 0, 16, B0["r"] + it * 4, 4, h1)

            def lora(m, k, slot):
                wh, wl_ = whi[:, slot, m * LORA:m * LORA + P], wlo[:, slot, m * LORA:m * LORA + P]
                return [(wh, hhi[:, :, k, :]), (wh, hlo[:, :, k, :]), (wl_, hhi[:, :, k, :])], PS[m][:, :], True
            seg(C0["lora"], 0, 16, B0["lora"], 4, lora, (sc1, A0["lora"]))
            seg(C0["gl"], 0, 16, B0["gl"], 2, h1, (sc1, A0["gl"]))

            pe.wait_ge(blk_free, B0["gate"])
            pe.wait_ge(mod_ready, A0["rwkv"])
            pe.wait_ge(lora_act, 4)
            pe.wait_ge(sh_done, 31)
            LF = [slice(TOK, TOK + P), slice(TOK + P, T2)]
            ADA_LEVEL = [[[(0, 4), (0, 5)], [(0, 6), (0, 7)], [(0, None)], [(1, 0), (1, 1)], [(1, 2), (1, 3)]],
                         [[(2, 0), (2, 1)], [(2, 2), (2, 3)], [(2, 4), (2, 5)], [(2, 6), (2, 7)], []]]
            with pe.Fori(0, 8) as it:
                dve_at = lambda n: pe.wait_ge(rw_dve, at(RW_DVE, n, it))
                act_at = lambda n: pe.wait_ge(rw_act, at(RW_ACT, n, it))
                done = lambda ins: ins.then_inc(rw_pe, 1)
                hs = [slice(0, 64), slice(64, P)]
                blk = lambda b: slice(b * P, b * P + P)

                def ada(j, *khs):
                    for kh in khs:
                        ada_half(sc2, kh, it * 3 + A0["rwkv"] + j)

                def turn(banks, srcs):
                    for bank, src in zip(banks, srcs):
                        for b in range(4):
                            mm = pe.transpose(PS[bank][:, blk(b)], src[:, blk(b)], ident)
                    done(mm)

                def pairs(bank, l, r):
                    pe.sem_inc(pe_gate, 1)
                    for h in range(2):
                        for b in range(4):
                            mm = pe.matmul(PS[bank + h][:, blk(b)], l[hs[h], blk(b)], r[hs[h], blk(b)], start=True, stop=True)
                    done(mm)

                def from_keys(d):
                    pairs(5, k_s[d], a_s[d])
                    if d == 1:
                        ada_final(it * 3 + A0["rwkv"] + 1)
                    dve_at(f"I{d}")
                    pe.sem_inc(pe_gate, 1)
                    for h in range(2):
                        for i, l in enumerate((b_s[d], k_s[d])):
                            for b in range(2):
                                mm = pe.matmul(PS[h][:, (2 * i + b) * P:(2 * i + b) * P + P], l[hs[h], TOK + b * P:TOK + b * P + P], r_s[d][hs[h], blk(b)], start=True, stop=True)
                    done(mm)
                    dve_at(f"Ak{d}")
                    for h in range(2):
                        for b in range(4):
                            mm = pe.matmul(PS[5 + h][:, blk(b)], akT[:, h, b, :], v_tok[:, b, :], start=True, stop=True)
                    done(mm)

                def inverse(d):
                    for l in range(1, len(LEVELS)):
                        for h in range(2):
                            if l == 1:
                                dve_at(f"Ar{d}")
                            else:
                                dve_at(f"X{d}{l - 1}{h}")
                            for b in range(4):
                                mm = pe.matmul(PS[h][:, blk(b)], aT[:, h, b, :], inv[:, h, b, :], start=True, stop=True)
                            done(mm)
                        if l == 1:
                            act_at(f"P1{d}")
                        for h in range(2):
                            dve_at(f"B{d}{l}{h}")
                            for b in range(4):
                                mm = pe.matmul(PS[2 + h][:, blk(b)], bm[:, h, b, :], invT[:, h, b, :], start=True, stop=True)
                                if l < len(LEVELS) - 1:
                                    mm = pe.matmul(PS[6 + h][:, blk(b)], invT[:, h, b, :], bm[:, h, b, :], start=True, stop=True)
                            done(mm)
                        for step in ADA_LEVEL[d][l - 1]:
                            if step[1] is None:
                                ada_final(it * 3 + A0["rwkv"] + step[0])
                            else:
                                ada(*step)
                    for h in range(2):
                        dve_at(f"X{d}{len(LEVELS) - 1}{h}")
                        for b in range(4):
                            mm = pe.matmul(PS[h][:, blk(b)], invT[:, h, b, :], atok_r[:, h, b, :], start=True, stop=True)
                    done(mm)

                def chunks(d):
                    act_at(f"WU{d}")
                    dve_at(f"W{d}")
                    pe.sem_inc(pe_gate, 1)
                    for e in range(2):
                        t = hs[e]
                        for h in range(2):
                            for b in range(4):
                                o = PS[2 + e][hs[h], b * CH:b * CH + CH]
                                pe.matmul(o, wu[t, h, b, 0:64], b_tok[t, b, hs[h]], start=True, stop=True)
                                o = PS[2 + e][hs[h], 256 + b * CH:256 + b * CH + CH]
                                pe.matmul(o, b_tok[t, b, hs[h]], wu[t, h, b, 64:P], start=True, stop=False)
                                mm = pe.matmul(o, k_tok[t, b, hs[h]], v_tok[t, b, hs[h]], start=False, stop=True)
                    done(mm)
                    for h in range(2):
                        for b in range(2):
                            mm = pe.matmul(PS[6][hs[h], blk(b)], wu[:, h, 2 + b, 0:64], arx[:, h, 0, b, :], start=True, stop=True)
                    done(mm)
                    for h in range(2):
                        for b in range(2):
                            pe.matmul(PS[7][hs[h], blk(b)], v_tok[:, 2 + b, hs[h]], arx[:, h, 1, b, :], start=True, stop=False)
                            mm = pe.matmul(PS[7][hs[h], blk(b)], wu[:, h, 2 + b, 64:P], arx[:, h, 0, b, :], start=False, stop=True)
                    done(mm)
                    if d == 1:
                        ada_final(it * 3 + A0["rwkv"] + 2)

                def scan(d, between=None):
                    state = lambda i: hd[:, SCAN[d][0], :] if i == 1 else zs[:, i, :]
                    for i in range(1, 7):
                        dve_at(f"Q{d}" if i == 1 else f"Z{d}{i - 1}")
                        pe.sem_inc(pe_gate, 1)
                        for h in range(2):
                            mm = pe.matmul(PS[5][hs[h], (i % 2) * CH:(i % 2) * CH + CH], g1t[hs[h], SCAN[d][i], :], state(i)[hs[h], :], start=True, stop=True)
                        done(mm)
                        if between:
                            between(i)
                    dve_at(f"Z{d}6")
                    pe.sem_inc(pe_gate, 1)
                    for i in range(4, 8):
                        c = (SCAN[d][i] - 4) * CH
                        for h in range(2):
                            mm = pe.matmul(PS[6][hs[h], TOK + c:TOK + c + CH], state(i)[hs[h], :], qt[hs[h], c:c + CH], start=True, stop=True)
                    done(mm)

                def next_direction(i):
                    if i == 1:
                        pairs(0, a_s[1], b_s[1])
                    if i == 2:
                        pairs(2, b_s[1], a_s[1])
                    if i > 4:
                        ada(1, i - 1)

                pe.wait_ge(rw_in, it * 64 + 64)
                for i in range(4):
                    done(pe.matmul(PS[i][:, :], lw2[0:LORA, i, :], (wl if i < 2 else al)[0:LORA, i % 2, :], start=True, stop=True))
                dve_at("kksq")
                done(pe.matmul(PS[5][:, :], bones, e_ex[0][:, :], start=True, stop=True))
                ada(0, 0, 1, 2, 3)
                dve_at("abk0")
                turn((3, 5, 6, 7), (v_t, a_s[0], b_s[0], k_s[0]))
                pairs(0, a_s[0], b_s[0])
                act_at("trv")
                pairs(2, b_s[0], a_s[0])
                act_at("tr0")
                from_keys(0)
                inverse(0)
                chunks(0)
                scan(0, next_direction)
                dve_at("Y0")
                turn((5, 7, 0), (a_s[1], b_s[1], k_s[1]))
                ada(1, 6, 7)
                act_at("tr1")
                from_keys(1)
                inverse(1)
                chunks(1)
                scan(1)
                dve_at("Y1")
                done(pe.matmul(PS[5][:, 0:TOK], bmean, yacc[:, :], start=True, stop=True))
                dve_at("sq")
                done(pe.matmul(PS[6][:, 0:TOK], bmean, fin[:, 1, :], start=True, stop=True))
                done(pe.matmul(PS[7][:, 0:TOK], bones, fin[:, 2, :], start=True, stop=True))
                for k in range(2):
                    mm = pe.matmul(PS[7][:, TOK:T2], g2s[:, k, :], gl[:, k, :], start=(k == 0), stop=(k == 1))
                done(mm)
            pe.wait_ge(rw_dve, 8 * len(RW_DVE))
            with pe.Fori(0, 8) as it:
                seg(C0["gate"] + it * 16, 0, 16, B0["gate"] + it * 4, 4, h1)
            for name, n, xh, xl, split in (("rproj", 8, yhi, ylo, 2), ("mproj", 16, ohi, olo, 6), ("wout", 16, mhi, mlo, 10)):
                pe.wait_ge(s_lo, split)
                x_ = rows(lambda k: xh[:, k, :], lambda k: xl[:, k, :], TOK)
                with pe.Fori(0, 4) as it:
                    seg(C0[name] + it * n, 0, n, B0[name] + it * 4, 4, x_)
            norm(DC, TOK)
            norm(DC, TOK)

            f1 = rows(lambda k: fhi[:, k, :], lambda k: flo[:, k, :], TOK)
            ud = rows(lambda k: uhi[:, k, :], lambda k: ulo[:, k, :], TOK)

            def down(c0, lc0, g, gate_b=None):
                pe.wait_ge(u_lo, g * 4 + 4)
                for n in range(4):
                    if n == 0:
                        free = (lambda m: pe.wait_ge(blk_free, gate_b + m + 1))
                    else:
                        free = (lambda m: pe.wait_ge(dn_free, g * 16 + 4 * (n - 1) + m + 1))
                    seg(c0, lc0 + 4 * n, 4, 0, 4, ud, None, free)

            seg(C0["ffn0"], 0, 16, B0["ffn0"], 4, f1, ready=DC + 8)
            seg(C0["ffn0"], 16, 16, B0["ffn0"] + 4, 4, f1)
            with pe.Fori(0, 10) as it:
                c, b = C0["ffn"] + it * 48, B0["ffn"] + it * 8
                seg(c, 0, 16, b, 4, f1)
                down(c, 16, it, b)
                seg(c, 32, 16, b + 4, 4, f1, None, lambda m: pe.wait_ge(dn_free, it * 16 + 12 + m + 1))
            down(C0["ffn1"], 0, 10, B0["ffn1"] - 4)

            pe.wait_ge(crow_in, 32)
            for d in range(DC):
                if d >= 2:
                    pe.wait_ge(tr_out, DC + d - 1)
                for t in range(2):
                    tr = pe.transpose(PS[6 + d % 2][:, t * P:t * P + P], crow[:, t, d * P:d * P + P], ident)
                tr.then_inc(tr_done, 1)
            norm(DC, TOK)
            pe.wait_ge(lam_pr, 1)
            pe.matmul(PS[7][:, 256:260], ones, lam[:, 0:4], start=True, stop=True).then_inc(lam_mm, 1)
            for l in range(2):
                norm(DC, T2)
                hl = h2 if l == 0 else h1
                T = T2 if l == 0 else TOK
                t0 = T2 - T
                if l == 0:
                    pe.wait_ge(dn_free, 176)

                def v_rows(m, k, slot):
                    xh, xl = hhi[:, m // 2, k, (m % 2) * P:(m % 2) * P + P], hlo[:, m // 2, k, (m % 2) * P:(m % 2) * P + P]
                    return [(xh, whi[:, slot, :]), (xh, wlo[:, slot, :]), (xl, whi[:, slot, :])], PS[m][:, :], True

                for it in range(2):
                    seg(C0[f"poolv{l}"] + it * 16, 0, 16, B0[f"poolv{l}"] + it * 4, 4, hl, ready=(2 + l) * DC + 8 if it == 0 else None)
                    pe.wait_ge(pw_in, 16 * l + 16)
                    for g in range(2):
                        pe.wait_ge(pl_done, 8 * l + it * 4 + g * 2 + 2)
                        if 4 * l + it * 2 + g > 0:
                            pe.wait_ge(pm_done, 8 * l + it * 4 + g * 2)
                        for j in range(2):
                            for k in range(2):
                                mm = pe.matmul(PS[5 + j][:, 0:T], pw[:, it * 2 + g, k, j * P:j * P + P], pl[:, 2 * g + k, 0:T], start=(k == 0), stop=(k == 1))
                        mm.then_inc(pw_mm, 1)
                with pe.Fori(0, 2) as it:
                    c, b = C0[f"qkv{l}"] + it * 48, B0[f"qkv{l}"] + it * 12
                    done = lambda ins: ins.then_inc(at_pe[l], 1)
                    dve_at = lambda n: pe.wait_ge(at_dve[l], at(AT_DVE[l], n, it))
                    act_at = lambda n: pe.wait_ge(at_act[l], at(AT_ACT[l], n, it))
                    seg(c, 0, 16, b, 4, hl)
                    seg(c, 16, 16, b + 4, 4, h2)
                    def norms(k):
                        for b in {4: (0, 1, 2), 8: (3, 4, 5), 12: (6, 7)}.get(k, ()):
                            pe.wait_ge(blk_free, B0[f"qkv{l}"] + it * 12 + b + 1)
                            if b >= 3:
                                dve_at(f"t{b - 3}")
                            done(pe.matmul(PS[(4, 6, 7)[b % 3]][:, 0:TOK], rotw[:, b // 4, :], qk[:, b, TOK:T2], start=True, stop=True))
                            act_at(f"sq{b}")
                            j = 32 * (b % 4)
                            done(pe.matmul(PS[5][j:j + 32, :], H("sum_k" if b >= 4 else "sum_q"), sq2[:, b % 4, :], start=b < 4, stop=b >= 4,
                                           tile_position=(0, j), skip_group_check=True))
                    pe.wait_ge(hcon_in, 16)
                    pe.wait_ge(rotw_ok, l + 1)
                    seg(c, 32, 16, b + 8, 4, v_rows, between=norms)
                    pe.wait_ge(blk_free, b + 12)
                    dve_at("rc")
                    for i, b in enumerate(QK_HEADS):
                        ts = slice(t0 if b < 4 else 0, T2)
                        rows_ = slice(32 * (b % 4), 32 * (b % 4) + 32)
                        if i >= 4:
                            dve_at(f"f{QK_HEADS[i - 4]}")
                        done(pe.matmul(PS[4 + i % 4][:, ts], H("spread_k" if b >= 4 else "spread_q", rows_), rs2[rows_, ts], start=True, stop=True,
                                       tile_position=(32 * (b % 4), 0)))
                    units = UNITS[l]

                    def scores(u):
                        h, t = units[u]
                        if t == TILES[l][0]:
                            dve_at(f"f{4 + h}")
                        if u == 2:
                            dve_at("f7")
                        if u >= 3:
                            act_at(f"e{u - 3}")
                        pe.sem_inc(pe_gate, 1)
                        nk = TOK if t < 2 else T2
                        for n in range(2):
                            r = slice(64 * n, 64 * n + 64)
                            mm = pe.matmul(PS[2 * (u % 3) + n][:, 0:nk], qk[r, h, t * P:t * P + P], qk[r, 4 + h, 0:nk], start=True, stop=True)
                        done(mm)

                    def turn(u):
                        dve_at(f"a{u}")
                        for kt in range(2 if units[u][1] < 2 else 4):
                            tr = pe.transpose(PS[6][:, kt * P:kt * P + P], pr[:, u % 3, 0, kt * P:kt * P + P], ident)
                        done(tr)

                    def values(u):
                        h, t = units[u]
                        nk = 2 if t < 2 else 4
                        act_at(f"aT{u}")
                        if t == TILES[l][0] and h >= 1:
                            act_at(f"o{h - 1}")
                        for kt in range(nk):
                            mm = pe.matmul(PS[7][:, t * P:t * P + P], v2[:, kt, h * P:h * P + P], aTs[:, u % 2, kt, :], start=(kt == 0), stop=(kt == nk - 1))
                        done(mm)

                    for u in range(-2, len(units) + 1):
                        if u + 2 < len(units):
                            scores(u + 2)
                        if u >= 1:
                            values(u - 1)
                        if 0 <= u < len(units):
                            turn(u)
                    act_at("o3")
                    for h in range(4):
                        mm = pe.matmul(PS[4][32 * h:32 * h + 32, t0:T2], H("sum_o"), qk[:, h, t0:T2], start=True, stop=True, tile_position=(0, 32 * h))
                    done(mm)
                    dve_at("rco")
                    for h in range(4):
                        rows_ = slice(32 * h, 32 * h + 32)
                        done(pe.matmul(PS[h][:, t0:T2], H("spread_o", rows_), rs2[rows_, t0:T2], start=True, stop=True, tile_position=(32 * h, 0)))
                    pe.wait_ge(at_dve[l], it * len(AT_DVE[l]) + len(AT_DVE[l]))
                for name in ("poolg", "attng"):
                    with pe.Fori(0, 2) as it:
                        seg(C0[f"{name}{l}"] + it * 16, 0, 16, B0[f"{name}{l}"] + it * 4, 4, hl)
                pe.wait_ge(s_lo, 10 + 8 * l + 8)
                xm = rows(lambda k: mixhi[:, k, t0:T2], lambda k: mixlo[:, k, t0:T2], T)
                with pe.Fori(0, 4) as it:
                    seg(C0[f"out{l}"] + it * 16, 0, 16, B0[f"out{l}"] + it * 4, 4, xm)
            pe.wait_ge(blk_free, B0["out1"] + 16)
            for d in range(DC):
                for t in range(2):
                    i = 2 * d + t
                    if i >= 2:
                        pe.wait_ge(fin_cp, i - 1)
                    pe.transpose(PS[6 + t][:, 0:P], xall[:, d, TOK + t * P:TOK + t * P + P], ident).then_inc(fin_tr, 1)

        @block.scalar
        def _(act):
            own = Own(act, act_own)

            def hi(c0, lcs, width=N):
                for lc in lcs:
                    c = c0 + lc
                    if lc % 2 == 0:
                        act.wait_ge(raw_in[(lc // 2) % RAW], 2 * c0 + 16 * (lc // 8 + 1))
                    if not isinstance(c, int) or c >= HL:
                        act.wait_ge(w_used, c - HL + 1)
                    act.activation(whi[:, lc % HL, 0:width], raw[:, (lc // 2) % RAW, lc % 2, 0:width], ACT.Copy).then_inc(w_hi, 1)

            def ada_take(g):
                act.wait_ge(ada_used, g * 8 + 8)
                act.activation(ada_sb[:, :], PS[4][:, 0:256], ACT.Copy).then_inc(ada_out, 1)

            def block_done(c_end, d0, m, nblk):
                if m < nblk - 1:
                    act.wait_ge(blk_done, d0 + m + 1)
                else:
                    act.wait_ge(w_used, c_end)

            nq, nn, na = [0], [0], [0]

            def norm(src, n, T, width, ready=None):
                sq, rs = nsq_of[nn[0]], nrs_of[nn[0]]
                for k in range(n):
                    if ready:
                        ready(k)
                    if nq[0] >= 2:
                        act.wait_ge(n_mm, nq[0] - 1)
                    act.activation(sq[:, nq[0] % 2, 0:T], src(k), ACT.Square).then_inc(n_sq, 1)
                    nq[0] += 1
                act.wait_ge(n_mm, nq[0])
                act.activation(rs[:, 0:T], PS[5][:, 0:T], ACT.Sqrt, bias=C("eps", 0, 1), scale=1.0 / width).then_inc(n_std, 1)
                nn[0] += 1

            def split(n, T, buf, dst, after=None):
                for k in range(n):
                    act.wait_ge(n_f32, na[0] + 1)
                    act.activation(dst(k), like(buf[:, 1 + na[0] % 2, 0:T], dst(k)), ACT.Copy).then_inc(n_hi, 1)
                    na[0] += 1
                    if after is not None and k >= 2:
                        hi(after, [LA + k - 2])

            act.wait_ge(const_in, 48)
            act.wait_ge(sc_zero, 2)
            act.activation(sc1[:, :, 0:2], cT[:, 0, :, :], ACT.Silu).then_inc(sc_ready, 1)
            act.activation(sc2[:, :, 0:2], cT[:, 1, :, :], ACT.Silu).then_inc(sc_ready, 1)
            for d in range(DC):
                act.wait_ge(tr_done, d + 1)
                act.activation(xT[:, d, :], PS[6 + d % 2][:, :], ACT.Copy).then_inc(tr_out, 1)
            norm(lambda k: xT[:, k, :], DC, T2, D, lambda k: act.wait_ge(tr_out, k + 1))
            with act.Fori(0, ADA_HEAD) as it:
                ada_take(it)
            hi(0, range(LA))
            c = C0["ckv"]
            split(DC, T2, nap0, lambda k: hhi[:, :, k, :], c)

            hi(c, range(LA + 14, 16 + LA))
            ada_take(A0["ckv"])
            act.wait_ge(x_saved, 16)
            for m in range(4):
                block_done(c + 16, D1["ckv"], m, 4)
                act.activation(ckv[:, m, :], PS[m][:, :], ACT.Copy).then_inc(blk_free, 1)
            c = C0["cq"]
            hi(c, range(LA, 16))
            hi(c, range(16, 16 + LA), P)
            for m in range(4):
                block_done(c + 16, D1["cq"], m, 4)
                act.activation(cq[:, m, :], PS[m][:, 0:TOK], ACT.Copy).then_inc(blk_free, 1)
            c = C0["kpe"]
            hi(c, range(LA, 16), P)
            hi(c, range(16, 16 + LA))
            ada_take(A0["kpe"])
            norm(lambda k: ckv[:, k, :], 4, T2, 512, lambda k: act.wait_ge(blk_free, B0["ckv"] + k + 1))
            act.wait_ge(w_used, c + 16)
            act.activation(kpe[:, :], PS[0][:, :], ACT.Copy).then_inc(blk_free, 1)
            norm(lambda k: cq[:, k, :], 4, TOK, 512, lambda k: act.wait_ge(blk_free, B0["cq"] + k + 1))
            split(4, T2, nap1, lambda k: ckvhi[:, k, :])
            split(4, TOK, nap1, lambda k: cqhi[:, k, :])

            with act.Fori(0, 8) as it:
                c = C0["mla"] + it * 8
                d0 = D1["mla"] + it * 7
                hi(c, range(LA, 4))
                hi(c, range(4, 4 + LA), 384)
                act.wait_ge(n_lo, DC + 8)
                for m, dst in enumerate((k_sb[:, 0, :], k_sb[:, 1, :], v_sb[:, 0:2, :], v_sb[:, 2:4, :])):
                    if m == 3:
                        act.wait_ge(w_used, c + 4)
                    else:
                        act.wait_ge(blk_done, d0 + (1, 2, 4)[m])
                    act.activation(dst, PS[m][:, :], ACT.Copy).then_inc(blk_free, 1)
                hi(c, range(4 + LA, 8), 384)
                hi(c, range(8, 8 + LA))
                for m, dst in enumerate((qn[:, 0, :], qn[:, 1, :], qraw[:, :])):
                    if m == 2:
                        act.wait_ge(w_used, c + 8)
                    else:
                        act.wait_ge(blk_done, d0 + 5 + m + 1)
                    act.activation(dst, PS[m][:, 0:TOK], ACT.Copy).then_inc(blk_free, 1)

                def exp(u):
                    act.wait_ge(mla_dve, at(MLA_DVE, f"nmx{u}", it))
                    act.activation(prob[:, u, :], PS[u % 2][:, :], ACT.Exp, bias=smx[:, 4 + u:5 + u], scale=ATTN_SCALE,
                                   accum_out=smx[:, 8 + u:9 + u]).then_inc(mla_act, 1)

                def turned(u):
                    act.wait_ge(mla_pe, at(MLA_PE, f"T{u}", it))
                    act.activation((probT, probT2)[u // 2][:, :, (u % 2) * P:(u % 2) * P + P],
                                   PS[6][:, :].rearrange("p (k q) -> p k q", q=P), ACT.Copy).then_inc(mla_act, 1)

                exp(0)
                exp(1)
                turned(0)
                turned(1)
                exp(2)
                exp(3)
                turned(2)
                turned(3)
                ada_take(A0["mla"] + it)

            def shifted(c, d0, m, nblk, latents=False, end=16, n=None):
                block_done(c + end, d0, m, nblk)
                act.wait_ge(sh_done, n + 1 - (m if nblk == 4 else 2 + m))
                if latents:
                    act.activation(pad[:, m, 1, 1:TOK + 1], PS[m][:, 0:TOK], ACT.Copy).then_inc(blk_free, 1)
                else:
                    act.activation(pad[:, m, :, 1:TOK + 1], PS[m][:, :].rearrange("p (s t) -> p s t", t=TOK), ACT.Copy).then_inc(blk_free, 1)

            with act.Fori(0, 4) as it:
                c = C0["kv"] + it * 16
                hi(c, range(LA, 16 + LA))
                ada_take(A0["kv"] + it)
                for m in range(4):
                    shifted(c, D1["kv"] + it * 3, m, 4, n=it * 4 + m)
            with act.Fori(0, 2) as it:
                c = C0["r"] + it * 16
                hi(c, range(LA, 16 + LA))
                for m in range(4):
                    shifted(c, D1["r"] + it * 3, m, 4, True, n=it * 4 + 16 + m)
            c = C0["lora"]
            hi(c, range(LA, 16))
            hi(c, range(16, 16 + LA), 256)
            ada_take(A0["lora"])
            for m in range(4):
                shifted(c, D1["lora"], m, 4, n=24 + m)
            c = C0["gl"]
            hi(c, range(LA, 16), 256)
            hi(c, range(16, 16 + LA))
            ada_take(A0["gl"])
            for m in range(2):
                shifted(c, D1["gl"], m, 2, True, n=28 + m)
            act.wait_ge(sh_done, 31)
            for d in range(2):
                act.activation(wl[0:LORA, d, :], wl[0:LORA, d, :], ACT.Tanh).then_inc(lora_act, 1)
            for m in range(2):
                act.activation(gl[:, m, :], gl[:, m, :], ACT.Sigmoid).then_inc(lora_act, 1)

            with act.Fori(0, 8) as it:
                pe_at = lambda n: act.wait_ge(rw_pe, at(RW_PE, n, it))
                dve_at = lambda n: act.wait_ge(rw_dve, at(RW_DVE, n, it))
                done = lambda ins: ins.then_inc(rw_act, 1)
                b4 = lambda bank: PS[bank][:, :].rearrange("p (b c) -> p b c", c=P)

                def decays(d):
                    dve_at(f"L{d}")
                    act.activation(e_ex[d][:, :], l_ex[d][:, :], ACT.Exp, scale=-DECAY_SCALE)
                    act.activation(e_in[d][:, :], l_in[d][:, :], ACT.Exp, scale=DECAY_SCALE)
                    act.activation(r_s[d][:, :], l_in[d][:, TOK:T2], ACT.Exp, scale=-DECAY_SCALE)
                    done(act.activation(dec[d][:, :], tot[d][:, :], ACT.Exp, scale=-DECAY_SCALE))

                def turned(d, a, b, k):
                    pe_at(f"tr{d}")
                    if d == 0:
                        done(act.activation(v_tok[:, :, :], b4(3), ACT.Copy))
                    act.activation(atok_r[:, :, :, 0:64].rearrange("p h b c -> p b h c"), PS[a][:, :].rearrange("p (b h c) -> p b h c", h=2, c=64), ACT.Copy)
                    act.activation(b_tok[:, :, :], b4(b), ACT.Copy)
                    done(act.activation(k_tok[:, :, :], b4(k), ACT.Copy))
                    if d == 1:
                        ada_take(it * 3 + A0["rwkv"] + 1)
                    pe_at(f"P1{d}")
                    act.activation(atok_r[:, 0, :, 64:P], b4(5)[:, :, 0:64], ACT.Copy)
                    done(act.activation(atok_r[:, 1, :, 64:P], b4(6)[:, :, 64:P], ACT.Copy))

                def solved(d):
                    pe_at(f"WU{d}")
                    done(act.activation(wu[:, 0, :, :], b4(0), ACT.Copy))

                act.wait_ge(rw_in, it * 64 + 64)
                for i in range(4):
                    pe_at(("w0", "w1", "a0", "a1")[i])
                    done(act.activation((sig if i < 2 else icl)[:, i % 2, :], PS[i][:, :], ACT.Sigmoid, bias=pv[:, i:i + 1]))
                pe_at("kksum")
                done(act.activation(e_in[1][:, :], PS[5][:, :], ACT.Sqrt))
                decays(0)
                turned(0, 5, 6, 7)
                decays(1)
                ada_take(it * 3 + A0["rwkv"])
                solved(0)
                turned(1, 5, 7, 0)
                ada_take(it * 3 + A0["rwkv"] + 2)
                solved(1)
                pe_at("var")
                done(act.activation(yacc[:, :], PS[6][:, 0:TOK], ACT.Sqrt, bias=C("eps", 1, 2)))

            def split_hi(src, dst, ready=None, n=4):
                for g in range(src.shape[1] // n):
                    if ready:
                        ready(g)
                    act.activation(dst[:, n * g:n * g + n, :], src[:, n * g:n * g + n, :], ACT.Copy).then_inc(s_hi, 1)

            act.wait_ge(rw_dve, 8 * len(RW_DVE))
            split_hi(y_all, yhi)
            for half, dst in enumerate((g_rwkv, g_mla)):
                with act.Fori(0, 4) as it:
                    c, d0 = C0["gate"] + half * 64 + it * 16, D1["gate"] + half * 12 + it * 3
                    hi(c, range(LA, 16 + LA))
                    for m in range(4):
                        block_done(c + 16, d0, m, 4)
                        act.activation(dst[:, bass.ds(it * 4 + m, 1), :], PS[m][:, 0:TOK].unsqueeze(1), ACT.Sigmoid,
                                       bias=Vd("gate_b", it * 4 + 16 * half + m)).then_inc(blk_free, 1)
            act.wait_ge(w_used, C0["rproj"])
            act.wait_ge(o_in, 16)
            split_hi(oT, ohi)
            for name, n in (("rproj", 8), ("mproj", 16)):
                with act.Fori(0, 4) as it:
                    hi(C0[name] + it * n, range(LA, n + LA))
            split_hi(mrg, mhi, lambda g: act.wait_ge(mg_done, g + 1 if g < 3 else 4))
            with act.Fori(0, 4) as it:
                c = C0["wout"] + it * 16
                hi(c, range(LA, 16 + LA))
                for m in range(4):
                    block_done(c + 16, D1["wout"] + it * 3, m, 4)
                    act.activation(wo[:, bass.ds(it * 4 + m, 1), :], PS[m][:, 0:TOK].unsqueeze(1), ACT.Copy).then_inc(blk_free, 1)
            norm(lambda k: wo[:, k, :], DC, TOK, D, lambda k: act.wait_ge(blk_free, B0["wout"] + k + 1))
            norm(lambda k: x1[:, k, :], DC, TOK, D, lambda k: act.wait_ge(x1_done, k + 1))
            split(DC, TOK, nap3, lambda k: fhi[:, k, :], C0["ffn0"])

            def gate_out(c_end, d0):
                for m in range(4):
                    block_done(c_end, d0, m, 4)
                    act.activation(gpad[:, m, 1:TOK + 1], PS[m][:, 0:TOK], ACT.Copy).then_inc(blk_free, 1)

            def gelu(g):
                for m in range(4):
                    act.wait_ge(cv_done, g * 4 + m + 1)
                    act.activation(ge[:, m, :], ge[:, m, :], ACT.Gelu_apprx_tanh, bias=Vd("conv_b", g * 4 + m)).then_inc(ge_done, 1)

            def u_split(b):
                for m in range(4):
                    act.wait_ge(blk_free, b + m + 1)
                    act.activation(uhi[:, m, :], ge[:, m, :], ACT.Copy).then_inc(u_hi, 1)

            c, d0 = C0["ffn0"], D1["ffn0"]
            hi(c, range(LA + 14, 16 + LA))
            act.wait_ge(ff_zero, 1)
            gate_out(c + 16, d0)
            gelu(0)
            hi(c, range(16 + LA, 32 + LA))
            u_split(B0["ffn0"] + 4)
            with act.Fori(0, 10) as it:
                c, d0 = C0["ffn"] + it * 48, D1["ffn"] + it * 18
                hi(c, range(LA, 16 + LA))
                gate_out(c + 16, d0)
                hi(c, range(16 + LA, 20 + LA))
                gelu(it + 1)
                hi(c, range(20 + LA, 48 + LA))
                u_split(B0["ffn"] + it * 8 + 4)
            hi(C0["ffn1"], range(LA, 16 + LA))

            for d in range(DC):
                act.wait_ge(tr_done, DC + d + 1)
                act.activation(xall[:, d, 0:TOK], PS[6 + d % 2][:, 0:TOK], ACT.Copy).then_inc(tr_out, 1)
            norm(lambda k: yffn[:, k, :], DC, TOK, D, lambda k: act.wait_ge(dn_free, 160 + k + 1))
            act.wait_ge(lam_mm, 1)
            act.activation(lam[:, 0:4], PS[7][:, 256:260], ACT.Exp).then_inc(lam_e, 1)
            act.wait_ge(tr_out, 2 * DC)
            for l in range(2):
                if l == 0:
                    norm(lambda k: xall[:, k, :], DC, T2, D, lambda k: act.wait_ge(x1_done, 2 * DC))
                else:
                    norm(lambda k: xall[:, k, :], DC, T2, D, lambda k: act.wait_ge(blk_free, B0["out0"] + k + 1))
                split(DC, T2, nap6, lambda k: hhi[:, :, k, :], C0[f"poolv{l}"])
                T = T2 if l == 0 else TOK
                t0 = T2 - T
                units = UNITS[l]
                act.wait_ge(x2_saved, 16 * l + 16)
                act.wait_ge(xp_zero, l + 1)
                for it in range(2):
                    c = C0[f"poolv{l}"] + it * 16
                    hi(c, range(LA if it else LA + 14, 16 + LA))
                    for m in range(4):
                        n = 8 * l + it * 4 + m
                        block_done(c + 16, D1[f"poolv{l}"] + 3 * it, m, 4)
                        if it * 4 + m >= 2:
                            act.wait_ge(pl_done, n - 1)
                        if l == 0:
                            act.activation(xp[:, m % 2, :, 16:16 + TOK], PS[m][:, :].rearrange("p (s t) -> p s t", t=TOK), ACT.Copy).then_inc(blk_free, 1)
                        else:
                            act.activation(xp[:, m % 2, 1, 16:16 + TOK], PS[m][:, 0:TOK], ACT.Copy).then_inc(blk_free, 1)
                act.wait_ge(pm_done, 8 * l + 8)
                with act.Fori(0, 2) as it:
                    c, d0, b = C0[f"qkv{l}"] + it * 48, D1[f"qkv{l}"] + it * 9, B0[f"qkv{l}"] + it * 12
                    done = lambda ins: ins.then_inc(at_act[l], 1)
                    pe_at = lambda n: act.wait_ge(at_pe[l], at(AT_PE[l], n, it))
                    dve_at = lambda n: act.wait_ge(at_dve[l], at(AT_DVE[l], n, it))
                    def squares(ns):
                        for n in ns:
                            ts = slice(t0 if n < 4 else 0, T2)
                            act.wait_ge(blk_free, b + n + 1)
                            if n >= 4:
                                pe_at(f"n{n - 4}")
                            done(act.activation(sq2[:, n % 4, ts], qk[:, n, ts], ACT.Square))

                    for i in range(3):
                        if i < 2:
                            hi(c, range(16 * i + LA, 16 * i + 16 + LA))
                        else:
                            if l:
                                dve_at("z")
                            squares(range(4))
                            hi(c, range(32 + LA, 41))
                            squares((4, 5))
                            hi(c, range(41, 45))
                            squares((6, 7))
                            hi(c, range(45, 48))
                            pe_at("n7")
                            done(act.activation(rs2[:, :], PS[5][:, :], ACT.Sqrt, bias=C("eps", 0, 1), scale=1.0 / 64))
                            hi(c, range(48, 48 + LA))
                        for m in range(4):
                            block_done(c + 16 * i + 16, d0 + 3 * i, m, 4)
                            ts = slice(t0 if i == 0 else 0, T2)
                            dst = qk[:, 4 * i + m, ts] if i < 2 else v2[:, m, :]
                            act.activation(dst, PS[m][:, 0:dst.shape[1]], ACT.Copy).then_inc(blk_free, 1)
                    act.wait_ge(blk_free, b + 12)

                    def exp(u):
                        nk = TOK if units[u][1] < 2 else T2
                        dve_at(f"mx{u}")
                        if u >= 3:
                            pe_at(f"T{u - 3}")
                        s, k = 8 * (u % 3), u % 3
                        act.activation(pr[:, k, 0, 0:nk], PS[2 * k][:, 0:nk], ACT.Exp, bias=smx2[:, s + 2:s + 3], scale=DIFF_SCALE,
                                       accum_out=smx2[:, s + 4:s + 5])
                        done(act.activation(pr[:, k, 1, 0:nk], PS[2 * k + 1][:, 0:nk], ACT.Exp, bias=smx2[:, s + 3:s + 4], scale=DIFF_SCALE,
                                            accum_out=smx2[:, s + 5:s + 6]))

                    for u in range(-2, len(units) + 1):
                        if u >= 1 and last_of(l, u - 1):
                            h = units[u - 1][0]
                            pe_at(f"PV{u - 1}")
                            act.activation(mix[:, bass.ds(it * 4 + 8 + h, 1), t0:T2], PS[7][:, t0:T2].unsqueeze(1), ACT.Copy)
                            done(act.activation(qk[:, h, t0:T2], PS[7][:, t0:T2], ACT.Square))
                        if 0 <= u < len(units):
                            nk = 2 if units[u][1] < 2 else 4
                            pe_at(f"T{u}")
                            done(act.activation(aTs[:, u % 2, 0:nk, :], PS[6][:, 0:nk * P].rearrange("p (k q) -> p k q", q=P), ACT.Copy))
                        if u + 2 < len(units):
                            exp(u + 2)
                    pe_at("no")
                    done(act.activation(rs2[:, t0:T2], PS[4][:, t0:T2], ACT.Sqrt, bias=C("eps", 0, 1), scale=1.0 / P))
                act.wait_ge(at_dve[l], 2 * len(AT_DVE[l]))
                for i, name in enumerate(("poolg", "attng")):
                    with act.Fori(0, 2) as it:
                        c = C0[f"{name}{l}"] + it * 16
                        hi(c, range(LA, 16 + LA))
                        for m in range(4):
                            block_done(c + 16, D1[f"{name}{l}"] + 3 * it, m, 4)
                            if m >= 2:
                                act.wait_ge(sg_done, it * 4 + 16 * l + 8 * i + m - 1)
                            act.activation(stmp[:, m % 2, 0:T], PS[m][:, 0:T], ACT.Silu).then_inc(blk_free, 1)
                        act.wait_ge(sg_done, it * 4 + 16 * l + 8 * i + 4)
                act.wait_ge(w_used, C0[f"out{l}"])
                split_hi(mix[:, :, t0:T2], mixhi[:, :, t0:T2], lambda g: act.wait_ge(sg_done, 16 * l + 16), 2)
                with act.Fori(0, 4 if l == 0 else 3) as it:
                    hi(C0[f"out{l}"] + it * 16, range(LA, 16 + LA))
            hi(C0["out1"] + 48, range(LA, 16))
            for d in range(DC):
                for t in range(2):
                    act.wait_ge(fin_tr, 2 * d + t + 1)
                    act.activation(orow[:, t, d * P:d * P + P], PS[6 + t][:, 0:P], ACT.Copy).then_inc(fin_cp, 1)

        @block.vector
        def _(dve):
            own = Own(dve, dve_own)

            def lo(c0, lcs, width=N):
                for lc in lcs:
                    dve.wait_ge(w_hi, c0 + lc + 1)
                    dve.tensor_tensor(wlo[:, lc % HL, 0:width], raw[:, (lc // 2) % RAW, lc % 2, 0:width],
                                      whi[:, lc % HL, 0:width].bitcast(F32), ALU.subtract).then_inc(w_lo, 1)

            def ada_bias(g, mod, bias, n):
                dve.wait_ge(ada_fin, g + 1)
                dve.tensor_tensor(mod[:, bass.ds(n, 4), :], PS[4][:, 256:264].rearrange("p (m j) -> p m j", j=2),
                                  Vd(bias, n, 4).unsqueeze(2).to_broadcast([P, 4, 2]), ALU.add).then_inc(mod_ready, 1)

            nn, na = [0], [0]

            def norm_scale():
                rs = nrs_of[nn[0]]
                dve.wait_ge(n_std, nn[0] + 1)
                own.then(dve.reciprocal(rs[:, 0:nt_of[nn[0]]], rs[:, 0:nt_of[nn[0]]]))
                nn[0] += 1
                return rs

            def rest(T, buf, dst, upto_):
                while rest.n < upto_:
                    k = rest.n
                    dve.wait_ge(n_hi, k + 1)
                    d = rest.dst[k]
                    dve.tensor_tensor(d[0], like(buf[:, 1 + k % 2, 0:T], d[0]), d[1].bitcast(F32), ALU.subtract).then_inc(n_lo, 1)
                    rest.n += 1
            rest.n, rest.dst = 0, {}

            def modulated(n, T, src, buf, rs, shift, hi_of, lo_of, after=None):
                for k in range(n):
                    i = na[0]
                    if i - rest.n >= 2:
                        rest(T, buf, None, i - 1)
                    if i >= 2:
                        dve.wait_ge(n_lo, i - 1)
                    if i >= 1:
                        dve.wait_ge(n_f32, i)
                    own.then(dve.tensor_tensor(buf[:, 0, 0:T], src(k), rs[:, 0:T], ALU.mult))
                    if T == T2:
                        own.then(dve.tensor_scalar(buf[:, 1 + i % 2, 0:TOK], buf[:, 0, 0:TOK], gain[:, k, 1:2], shift(k, 1), ALU.mult, ALU.add))
                        dve.tensor_scalar(buf[:, 1 + i % 2, TOK:T2], buf[:, 0, TOK:T2], gain[:, k, 0:1], shift(k, 0), ALU.mult, ALU.add).then_inc(n_f32, 1)
                    else:
                        dve.tensor_scalar(buf[:, 1 + i % 2, 0:T], buf[:, 0, 0:T], gain[:, k, 0:1], shift(k, 0), ALU.mult, ALU.add).then_inc(n_f32, 1)
                    rest.dst[i] = (lo_of(k), hi_of(k))
                    na[0] += 1
                    if after is not None and k >= 2:
                        lo(after, [LA + k - 2])
                rest(T, buf, None, na[0])

            def gained(n, T, src, buf, rs, g, hi_of, lo_of):
                for k in range(n):
                    i = na[0]
                    if i - rest.n >= 2:
                        rest(T, buf, None, i - 1)
                    if i >= 2:
                        dve.wait_ge(n_lo, i - 1)
                    dve.scalar_tensor_tensor(buf[:, 1 + i % 2, 0:T], src(k), g(k), rs[:, 0:T], ALU.mult, ALU.mult).then_inc(n_f32, 1)
                    rest.dst[i] = (lo_of(k), hi_of(k))
                    na[0] += 1
                rest(T, buf, None, na[0])

            dve.memset(sc1[:, :, :], 0.0).then_inc(sc_zero, 1)
            dve.memset(sc2[:, :, :], 0.0).then_inc(sc_zero, 1)
            dve.wait_ge(const_in, 48)
            dve.tensor_scalar(mu_keep[:, :], V("mu", 0, 30), -1.0, 1.0, ALU.mult, ALU.add)
            dve.tensor_scalar(mu_half[:, :], V("mu", 0, 30), 0.5, None, ALU.mult)
            rs = norm_scale()
            with dve.Fori(0, ADA_HEAD) as it:
                ada_bias(it, mod1, "b_ada", it * 4)
            dve.wait_ge(mod_ready, ADA_HEAD)
            own.then(dve.scalar_tensor_tensor(gain[:, :, :], mod1[:, 16:32, :], 1.0, V("mix_pre", 0, 16).unsqueeze(2).to_broadcast([P, 16, 2]),
                                              ALU.add, ALU.mult))
            c = C0["ckv"]
            lo(0, range(LA))
            modulated(DC, T2, lambda k: xT[:, k, :], nap0, rs, lambda k, j: mod1[:, k, j:j + 1],
                      lambda k: hhi[:, :, k, :], lambda k: hlo[:, :, k, :], c)
            lo(c, range(LA + 14, 16 + LA))
            ada_bias(A0["ckv"], mod1, "b_ada", A0["ckv"] * 4)
            c = C0["cq"]
            lo(c, range(LA, 16))
            lo(c, range(16, 16 + LA), P)
            c = C0["kpe"]
            lo(c, range(LA, 16), P)
            lo(c, range(16, 16 + LA))
            ada_bias(A0["kpe"], mod1, "b_ada", A0["kpe"] * 4)
            rs = norm_scale()
            gained(4, T2, lambda k: ckv[:, k, :], nap1, rs, lambda k: V("kv_norm", k), lambda k: ckvhi[:, k, :], lambda k: ckvlo[:, k, :])
            rs = norm_scale()
            gained(4, TOK, lambda k: cq[:, k, :], nap1, rs, lambda k: V("q_norm", k), lambda k: cqhi[:, k, :], lambda k: cqlo[:, k, :])
            dve.wait_ge(rope_mm, 1)
            dve.tensor_tensor(ropet[:, 0, :], kpe[:, TOK:T2], cos, ALU.mult)
            own.then(dve.tensor_tensor(ropet[:, 1, :], PS[6][:, 0:TOK], sin, ALU.mult))
            own.then(dve.tensor_tensor(kpe[:, TOK:T2], ropet[:, 0, :], ropet[:, 1, :], ALU.add))
            own.then(dve.memset(qpad[:, :, :], 0.0))
            with dve.Fori(0, 8) as it:
                own.loop(it, 9)
                c = C0["mla"] + it * 8
                lo(c, range(LA, 4))
                lo(c, range(4, 4 + LA), 384)
                lo(c, range(4 + LA, 8), 384)
                lo(c, range(8, 8 + LA))
                dve.wait_ge(mla_pe, at(MLA_PE, "rot", it))
                dve.tensor_tensor(ropet[:, 0, :], qraw[:, :], cos, ALU.mult)
                own.then(dve.tensor_tensor(ropet[:, 1, :], PS[3][:, 0:TOK], sin, ALU.mult))
                dve.tensor_tensor(qpad[0:64, 0, :], ropet[0:64, 0, :], ropet[0:64, 1, :], ALU.add)
                dve.tensor_tensor(qpad[64:P, 1, :], ropet[64:P, 0, :], ropet[64:P, 1, :], ALU.add).then_inc(mla_dve, 1)

                def maximum(u):
                    dve.wait_ge(mla_pe, at(MLA_PE, f"S{u}", it))
                    own.then(dve.reduce_max(smx[:, u:u + 1], PS[u % 2][:, :], axis=AX.X))
                    dve.tensor_scalar(smx[:, 4 + u:5 + u], smx[:, u:u + 1], -ATTN_SCALE, None, ALU.mult).then_inc(mla_dve, 1)

                def normalise(u):
                    dve.wait_ge(mla_act, at(MLA_ACT, f"exp{u}", it))
                    own.then(dve.reciprocal(smx[:, 12 + u:13 + u], smx[:, 8 + u:9 + u]))
                    dve.tensor_scalar(prob[:, u, :], prob[:, u, :], smx[:, 12 + u:13 + u], None, ALU.mult).then_inc(mla_dve, 1)

                def head(h):
                    dve.wait_ge(mla_pe, at(MLA_PE, f"PV{h}", it))
                    dve.tensor_scalar(oT[:, bass.ds(it * 2 + h, 1), :], PS[7][:, 0:TOK].unsqueeze(1), 1.0, None, ALU.mult).then_inc(mla_dve, 1)

                maximum(0)
                maximum(1)
                normalise(0)
                normalise(1)
                maximum(2)
                maximum(3)
                head(0)
                normalise(2)
                normalise(3)
                head(1)
                ada_bias(A0["mla"] + it, mod1, "b_ada", it * 4 + A0["mla"] * 4)
            own.end(8)

            def shift(m, mu, n, dst, latents=False):
                s = slice(1, 2) if latents else slice(0, 2)
                dve.wait_ge(blk_free, n[0])
                src = pad[:, m, s, :]
                own.then(dve.tensor_tensor(sh_a[:, s, :], src[:, :, 0:TOK], src[:, :, 2:TOK + 2], ALU.add))
                own.then(dve.tensor_scalar(sh_a[:, s, :], sh_a[:, s, :], mu_half[:, bass.ds(mu, 1)], None, ALU.mult))
                dve.scalar_tensor_tensor(dst, src[:, :, 1:TOK + 1], mu_keep[:, bass.ds(mu, 1)], sh_a[:, s, :], ALU.mult, ALU.add).then_inc(sh_done, 1)
                dve.wait_ge(sh_done, n[1] + 1)

            both = lambda b: b.rearrange("p (s t) -> p s t", t=TOK)
            own.then(dve.memset(sh_a[:, 0, 0:1], 0.0))
            dve.memset(pad[:, :, :, :], 0.0).then_inc(sh_done, 1)
            with dve.Fori(0, 4) as it:
                own.loop(it, 8)
                c = C0["kv"] + it * 16
                lo(c, range(LA, 16 + LA))
                ada_bias(A0["kv"] + it, mod1, "b_ada", it * 4 + A0["kv"] * 4)
                for m in range(4):
                    if m == 0:
                        dve.wait_ge(sh_free, it + 1)
                    shift(m, it * 4 + 8 + m, (B0["kv"] + it * 4 + m + 1, it * 4 + m + 1), both(sh_out[:, m, :]))
            own.end(4)
            with dve.Fori(0, 2) as it:
                own.loop(it, 8)
                c = C0["r"] + it * 16
                lo(c, range(LA, 16 + LA))
                for m in range(4):
                    if m == 0:
                        dve.wait_ge(sh_free, it + 5)
                    shift(m, it * 4 + m, (B0["r"] + it * 4 + m + 1, it * 4 + 16 + m + 1), sh_out[:, m, 0:TOK].unsqueeze(1), True)
            own.end(2)
            c = C0["lora"]
            lo(c, range(LA, 16))
            lo(c, range(16, 16 + LA), 256)
            ada_bias(A0["lora"], mod1, "b_ada", A0["lora"] * 4)
            for m in range(4):
                shift(m, 24 + m, (B0["lora"] + m + 1, 24 + m + 1), both((wl if m < 2 else al)[:, m % 2, :]))
            c = C0["gl"]
            lo(c, range(LA, 16), 256)
            lo(c, range(16, 16 + LA))
            ada_bias(A0["gl"], mod1, "b_ada", A0["gl"] * 4)
            for m in range(2):
                shift(m, 28 + m, (B0["gl"] + m + 1, 28 + m + 1), gl[:, m, :].unsqueeze(1), True)

            with dve.Fori(0, 8) as it:
                own.loop(it, RW_OWN)
                step = [0]
                pe_at = lambda n: dve.wait_ge(rw_pe, at(RW_PE, n, it))
                act_at = lambda n: dve.wait_ge(rw_act, at(RW_ACT, n, it))

                def done(ins, label):
                    assert RW_DVE[step[0]] == label, (RW_DVE[step[0]], label)
                    step[0] += 1
                    ins.then_inc(rw_dve, 1)
                    dve.wait_ge(rw_dve, at(RW_DVE, label, it))

                pb = lambda n, h: PS[n + h][:, :].rearrange("p (b c) -> p b c", c=P)
                mask = lambda i: C("masks", i * P, i * P + P).unsqueeze(1).to_broadcast([P, 4, P])
                eye = ident.unsqueeze(1).to_broadcast([P, 4, P])
                TT, TS, STT = dve.tensor_tensor, dve.tensor_scalar, dve.scalar_tensor_tensor
                def sums(d):
                    in3, ex3 = [x[d][:, :].rearrange("p (c t) -> p c t", t=CH) for x in (l_in, l_ex)]
                    own.then(dve.tensor_tensor_scan(l_in[d][:, :], C("restart"), sig[:, d, :], 0.0, ALU.mult, ALU.add))
                    own.then(TS(tot[d][:, :], in3[:, :, CH - 1], 1.0, None, ALU.mult))
                    if d == 0:
                        done(TT(l_ex[d][:, :], l_in[d][:, :], sig[:, d, :], ALU.subtract), f"L{d}")
                    else:
                        own.then(TT(ex3, tot[d][:, :].unsqueeze(2).to_broadcast([P, 8, CH]), in3, ALU.subtract))
                        done(TT(l_in[d][:, :], l_ex[d][:, :], sig[:, d, :], ALU.add), f"L{d}")

                def scaled(d):
                    act_at(f"E{d}")
                    dve.wait_ge(rw_in2, it * 64 + 64)
                    own.then(STT(a_s[d][:, :], kk[:, :], -1.0, e_ex[d][:, :], ALU.mult, ALU.mult))
                    own.then(TT(b_s[d][:, :], kk[:, :], icl[:, d, :], ALU.mult))
                    own.then(TT(b_s[d][:, :], b_s[d][:, :], e_in[d][:, :], ALU.mult))
                    own.then(TT(k_s[d][:, :], kdir[:, d, :], e_in[d][:, :], ALU.mult))
                    done(TT(r_s[d][:, :], r_t[:, :], r_s[d][:, :], ALU.mult), f"abk{d}")

                def mask_a(d, h):
                    if h == 0:
                        pe_at(f"A{d}")
                    own.then(TT(inv[:, h, :, :], pb(0, h), mask(M_LEVEL_T if d else M_LEVEL), ALU.mult))
                    t = TT(inv[:, h, :, :], inv[:, h, :, :], eye, ALU.add)
                    if h == 0:
                        own.then(t)
                    else:
                        done(t, f"I{d}")

                def mask_at(d, h):
                    if h == 0:
                        pe_at(f"AT{d}")
                    own.then(TT(aT[:, h, :, :], pb(2, h), mask(M_STRICT + 1 - d), ALU.mult))
                    own.then(TT(invT[:, h, :, :], aT[:, h, :, :], mask(M_LEVEL if d else M_LEVEL_T), ALU.mult))
                    t = TT(invT[:, h, :, :], invT[:, h, :, :], eye, ALU.add)
                    if h == 0:
                        own.then(t)
                    else:
                        done(t, f"A{d}")

                def mask_keys(d):
                    pe_at(f"Ak{d}")
                    own.then(TT(akT[:, 0, :, :], pb(5, 0), mask(M_STRICT + 1 - d), ALU.mult))
                    done(TT(akT[:, 1, :, :], pb(5, 1), mask(M_STRICT + 1 - d), ALU.mult), f"Ak{d}")
                    pe_at(f"Ar{d}")
                    ar4 = lambda h: arx[:, h, :, :, :].rearrange("p i b c -> p (i b) c")
                    own.then(TT(ar4(0), pb(0, 0), mask(M_INCL + 1 - d), ALU.mult))
                    done(TT(ar4(1), pb(0, 1), mask(M_INCL + 1 - d), ALU.mult), f"Ar{d}")

                def level(d, l):
                    for h in range(2):
                        pe_at(f"B{d}{l}{h}")
                        done(TT(bm[:, h, :, :], pb(0, h), mask((M_LEVEL_T if d else M_LEVEL) + l), ALU.mult), f"B{d}{l}{h}")
                    for h in range(2):
                        pe_at(f"G{d}{l}{h}")
                        t = TT(invT[:, h, :, :], invT[:, h, :, :], pb(2, h), ALU.add)
                        if l < len(LEVELS) - 1:
                            own.then(t)
                            t = TT(inv[:, h, :, :], inv[:, h, :, :], pb(6, h), ALU.add)
                        done(t, f"X{d}{l}{h}")

                def chunks(d):
                    pe_at(f"WU{d}")
                    done(TS(wu[:, 1, :, :], pb(0, 1), 1.0, None, ALU.mult), f"W{d}")
                    pe_at(f"GH{d}")
                    for e in range(2):
                        g = lambda i: PS[2 + e][:, i * 256:i * 256 + 256].rearrange("p (b c) -> p b c", c=CH)
                        own.then(TT(g1t[:, e::2, :], g(0), C("eye64").unsqueeze(1).to_broadcast([P, 4, CH]), ALU.add))
                        t = TT(hd[:, e::2, :], g(1), dec[d][:, e::2].unsqueeze(2).to_broadcast([P, 4, CH]), ALU.mult)
                        if e == 0:
                            own.then(t)
                    done(t, f"GH{d}")
                    pe_at(f"Q{d}")
                    done(TT(qt[:, :], PS[6][:, 0:TOK], r_s[d][:, :], ALU.add), f"Q{d}")

                def within(d):
                    pe_at(f"YL{d}")
                    if d == 0:
                        own.then(TS(yacc[:, :], PS[7][:, 0:TOK], 1.0, None, ALU.mult))
                    else:
                        own.then(TT(yacc[:, :], yacc[:, :], PS[7][:, 0:TOK], ALU.add))

                def state(d, i):
                    c = SCAN[d][i]
                    pe_at(f"Z{d}{i}")
                    done(STT(zs[:, i + 1, :], PS[5][:, (i % 2) * CH:(i % 2) * CH + CH], dec[d][:, c:c + 1], hd[:, c, :], ALU.mult, ALU.add), f"Z{d}{i}")

                def outputs(d):
                    pe_at(f"YZ{d}")
                    done(TT(yacc[:, :], yacc[:, :], PS[6][:, TOK:T2], ALU.add), f"Y{d}")

                def ada(j):
                    ada_bias(it * 3 + A0["rwkv"] + j, mod2, "b_ada_2", it * 12 + 4 * j)

                dve.wait_ge(rw_in, it * 64 + 64)
                own.then(TS(kk[:, :], k_t[:, :], pv[:, 4:5], None, ALU.mult))
                done(TT(e_ex[0][:, :], kk[:, :], kk[:, :], ALU.mult), "kksq")
                act_at("w0")
                sums(0)
                act_at("kkrt")
                own.then(TS(e_in[1][:, :], e_in[1][:, :], 1e-12, None, ALU.max))
                own.then(dve.reciprocal(e_in[1][:, :], e_in[1][:, :]))
                own.then(TT(kk[:, :], kk[:, :], e_in[1][:, :], ALU.mult))
                act_at("a1")
                for d in range(2):
                    own.then(TS(kdir[:, d, :], icl[:, d, :], 1.0, pv[:, 5:6], ALU.subtract, ALU.mult))
                    own.then(STT(kdir[:, d, :], kdir[:, d, :], 1.0, k_t[:, :], ALU.add, ALU.mult))
                scaled(0)
                mask_a(0, 0)
                mask_a(0, 1)
                mask_at(0, 0)
                mask_at(0, 1)
                mask_keys(0)
                level(0, 1)
                sums(1)
                level(0, 2)
                level(0, 3)
                ada(0)
                scaled(1)
                level(0, 4)
                level(0, 5)
                chunks(0)
                state(0, 1)
                within(0)
                state(0, 2)
                mask_a(1, 0)
                state(0, 3)
                mask_a(1, 1)
                state(0, 4)
                mask_at(1, 0)
                state(0, 5)
                mask_at(1, 1)
                state(0, 6)
                outputs(0)
                mask_keys(1)
                ada(1)
                for l in range(1, len(LEVELS)):
                    level(1, l)
                chunks(1)
                state(1, 1)
                within(1)
                ada(2)
                for i in range(2, 7):
                    state(1, i)
                outputs(1)
                own.then(TT(fin[:, 2, :], kdir[:, 0, TOK:T2], kdir[:, 1, TOK:T2], ALU.add))
                own.then(TT(fin[:, 2, :], fin[:, 2, :], r_t[:, :], ALU.mult))
                done(TS(fin[:, 2, :], fin[:, 2, :], pv2[:, 0:1], 0.5, ALU.mult, ALU.mult), "bt")
                pe_at("mean")
                own.then(TT(fin[:, 0, :], yacc[:, :], PS[5][:, 0:TOK], ALU.subtract))
                done(TT(fin[:, 1, :], fin[:, 0, :], fin[:, 0, :], ALU.mult), "sq")
                act_at("sd")
                own.then(dve.reciprocal(yacc[:, :], yacc[:, :]))
                own.then(TT(fin[:, 0, :], fin[:, 0, :], yacc[:, :], ALU.mult))
                own.then(TS(fin[:, 0, :], fin[:, 0, :], pv2[:, 1:2], pv2[:, 2:3], ALU.mult, ALU.add))
                pe_at("g")
                own.then(TT(fin[:, 1, :], PS[7][:, 0:TOK], v_t[:, TOK:T2], ALU.mult))
                own.then(TT(fin[:, 0, :], fin[:, 0, :], fin[:, 1, :], ALU.add))
                done(TT(y_all[:, bass.ds(it, 1), :], fin[:, 0, :].unsqueeze(1), PS[7][:, TOK:T2].unsqueeze(1), ALU.mult), "out")
            own.end(8)
            TT, TS, STT = dve.tensor_tensor, dve.tensor_scalar, dve.scalar_tensor_tensor
            ns = [0]

            def split_lo(src, hi_, lo_, n=4):
                for g in range(src.shape[1] // n):
                    s = slice(n * g, n * g + n)
                    ns[0] += 1
                    dve.wait_ge(s_hi, ns[0])
                    TT(lo_[:, s, :], src[:, s, :], hi_[:, s, :].bitcast(F32), ALU.subtract).then_inc(s_lo, 1)

            def block_done(c_end, d0, m, nblk):
                if m < nblk - 1:
                    dve.wait_ge(blk_done, d0 + m + 1)
                else:
                    dve.wait_ge(w_used, c_end)

            split_lo(y_all, yhi, ylo)
            with dve.Fori(0, 8) as it:
                lo(C0["gate"] + it * 16, range(LA, 16 + LA))
            split_lo(oT, ohi, olo)
            dve.wait_ge(blk_free, B0["rproj"])
            with dve.Fori(0, 4) as it:
                c = C0["rproj"] + it * 8
                lo(c, range(LA, 8 + LA))
                for m in range(4):
                    block_done(c + 8, D1["rproj"] + it * 3, m, 4)
                    n = bass.ds(it * 4 + m, 1)
                    TT(mrg[:, n, :], PS[m][:, 0:TOK].unsqueeze(1), g_rwkv[:, n, :], ALU.mult).then_inc(blk_free, 1)
            dve.wait_ge(blk_free, B0["mproj"])
            with dve.Fori(0, 4) as it:
                own.loop(it, 3)
                c = C0["mproj"] + it * 16
                lo(c, range(LA, 16 + LA))
                for m in range(4):
                    block_done(c + 16, D1["mproj"] + it * 3, m, 4)
                    n = bass.ds(it * 4 + m, 1)
                    TT(g_mla[:, n, :], PS[m][:, 0:TOK].unsqueeze(1), g_mla[:, n, :], ALU.mult).then_inc(blk_free, 1)
                    dve.wait_ge(blk_free, B0["mproj"] + it * 4 + m + 1)
                    t = TT(mrg[:, n, :], mrg[:, n, :], g_mla[:, n, :], ALU.add)
                    if m < 3:
                        own.then(t)
                t.then_inc(mg_done, 1)
            own.end(4)
            split_lo(mrg, mhi, mlo)
            with dve.Fori(0, 4) as it:
                lo(C0["wout"] + it * 16, range(LA, 16 + LA))

            def residual(dst, src, g0, post, ready):
                own.then(TT(cf[:, :], mod1[:, g0:g0 + 16, 0], V(post, 0, 16), ALU.mult))
                rs = norm_scale()
                own.then(TT(src[:, :, :], src[:, :, :], rs[:, 0:TOK].unsqueeze(1).to_broadcast([P, DC, TOK]), ALU.mult))
                if ready:
                    ready()
                for k in range(DC):
                    STT(dst(k), src[:, k, :], cf[:, k:k + 1], x1[:, k, :], ALU.mult, ALU.add).then_inc(x1_done, 1)

            def gains(mod, s, g, n=DC):
                own.then(STT(gain[:, :, :], mod[:, s:s + DC, :], 1.0, g.unsqueeze(2).to_broadcast([P, DC, 2]), ALU.add, ALU.mult))

            dve.wait_ge(mod_ready, A0["ffn0"])
            residual(lambda k: x1[:, k, :], wo, 32, "mix_post", lambda: dve.wait_ge(x1_in, 16))
            gains(mod1, 64, V("ffn_pre", 0, 16))
            rs = norm_scale()
            modulated(DC, TOK, lambda k: x1[:, k, :], nap3, rs, lambda k, j: mod1[:, 48 + k, j:j + 1],
                      lambda k: fhi[:, k, :], lambda k: flo[:, k, :], C0["ffn0"])

            def conv(b, g):
                for m in range(4):
                    w = lambda j: Vd(f"conv_w{j}", g * 4 + m)
                    dve.wait_ge(blk_free, b + m + 1)
                    own.then(TS(ge[:, m, :], gpad[:, m, 0:TOK], w(0), None, ALU.mult))
                    own.then(STT(ge[:, m, :], gpad[:, m, 1:TOK + 1], w(1), ge[:, m, :], ALU.mult, ALU.add))
                    STT(ge[:, m, :], gpad[:, m, 2:TOK + 2], w(2), ge[:, m, :], ALU.mult, ALU.add).then_inc(cv_done, 1)

            def gated(c_end, d0, g):
                for m in range(4):
                    block_done(c_end, d0, m, 4)
                    dve.wait_ge(ge_done, g * 4 + m + 1)
                    TT(ge[:, m, :], ge[:, m, :], PS[m][:, 0:TOK], ALU.mult).then_inc(blk_free, 1)
                for m in range(4):
                    dve.wait_ge(u_hi, g * 4 + m + 1)
                    TT(ulo[:, m, :], ge[:, m, :], uhi[:, m, :].bitcast(F32), ALU.subtract).then_inc(u_lo, 1)

            def down(c0, lc0, d0):
                for n in range(4):
                    lo(c0, range(lc0 + 4 * n + LA, lc0 + 4 * n + 4 + LA))
                    for m in range(4):
                        block_done(c0 + lc0 + 4 * n + 4, d0 + 3 * n, m, 4)
                        k = 4 * n + m
                        TT(yffn[:, k, :], yffn[:, k, :], PS[m][:, 0:TOK], ALU.add).then_inc(dn_free, 1)

            own.then(dve.memset(yffn[:, :, :], 0.0))
            dve.memset(gpad[:, :, :], 0.0).then_inc(ff_zero, 1)
            c, d0 = C0["ffn0"], D1["ffn0"]
            lo(c, range(LA + 14, 16 + LA))
            conv(B0["ffn0"], 0)
            lo(c, range(16 + LA, 32 + LA))
            gated(c + 32, d0 + 3, 0)
            with dve.Fori(0, 10) as it:
                own.loop(it, 8)
                c, d0 = C0["ffn"] + it * 48, D1["ffn"] + it * 18
                lo(c, range(LA, 16 + LA))
                conv(B0["ffn"] + it * 8, it + 1)
                down(c, 16, d0 + 3)
                dve.wait_ge(dn_free, it * 16 + 16)
                lo(c, range(32 + LA, 48 + LA))
                gated(c + 48, d0 + 15, it + 1)
            own.end(10)
            down(C0["ffn1"], 0, D1["ffn1"])

            dve.wait_ge(dn_free, 176)
            own.then(TT(lam[:, 0:4].rearrange("p (a b) -> p a b", b=1), V("lambda", 0, 8).rearrange("p (a b) -> p a b", b=2)[:, :, 0:1],
                        V("lambda", 0, 8).rearrange("p (a b) -> p a b", b=2)[:, :, 1:2], ALU.mult))
            for l in range(2):
                t = TS(sub2[:, l:l + 1], V("subln", l), 1.0 - LAM_INIT[l], None, ALU.mult)
                if l == 0:
                    own.then(t)
            t.then_inc(lam_pr, 1)
            residual(lambda k: xall[:, k, TOK:T2], yffn, 80, "ffn_post", None)
            dve.wait_ge(lam_e, 1)
            for l in range(2):
                own.then(TT(lam[:, 4 + l:5 + l], lam[:, 2 * l:2 * l + 1], lam[:, 2 * l + 1:2 * l + 2], ALU.subtract))
                own.then(TS(lam[:, 4 + l:5 + l], lam[:, 4 + l:5 + l], LAM_INIT[l], None, ALU.add))
            dve.wait_ge(mod_ready, A0["ffn1"])
            for l in range(2):
                gains(mod2, 48 * l + 16, V("norm_2", 16 * l, 16))
                rs = norm_scale()
                modulated(DC, T2, lambda k: xall[:, k, :], nap6, rs, lambda k, j: mod2[:, 48 * l + k, j:j + 1],
                          lambda k: hhi[:, :, k, :], lambda k: hlo[:, :, k, :], C0[f"poolv{l}"])
                T = T2 if l == 0 else TOK
                t0 = T2 - T
                units = UNITS[l]
                dve.wait_ge(n_lo, (3 + l) * DC + 8)
                dve.wait_ge(x2_saved, 16 * l + 16)
                dve.memset(xp[:, :, :, :], 0.0).then_inc(xp_zero, 1)
                sq_ = slice(0, 2) if l == 0 else slice(1, 2)
                L = TOK + 32
                for it in range(2):
                    lo(C0[f"poolv{l}"] + it * 16, range(LA if it else LA + 14, 16 + LA))
                    for m in range(4):
                        n = 8 * l + it * 4 + m
                        g = it * 2 + m // 2
                        dve.wait_ge(blk_free, B0[f"poolv{l}"] + it * 4 + m + 1)
                        x_ = xp[:, m % 2, sq_, :]
                        own.then(TT(sw[:, 0, sq_, 1:L], x_[:, :, 0:L - 1], x_[:, :, 1:L], ALU.add))
                        a, cur = 1, 0
                        for j in range(g):
                            s = 1 << j
                            own.then(TT(sw[:, 1 - cur, sq_, a + s:L - a - s], sw[:, cur, sq_, a:L - a - 2 * s], sw[:, cur, sq_, a + 2 * s:L - a], ALU.add))
                            a, cur = a + s, 1 - cur
                        inv_ = C("invcnt", g * TOK, g * TOK + TOK).unsqueeze(1).to_broadcast([P, T // TOK, TOK])
                        own.then(TT(sw[:, 1 - cur, sq_, 16:16 + TOK], sw[:, cur, sq_, 16:16 + TOK], inv_, ALU.mult))
                        if it == 1 and m < 2:
                            dve.wait_ge(pw_mm, 4 * l + 2)
                        TT(pl[:, m, 0:T].rearrange("p (s t) -> p s t", t=TOK), sw[:, 1 - cur, sq_, 16:16 + TOK], x_[:, :, 16:16 + TOK], ALU.subtract).then_inc(pl_done, 1)
                        dve.wait_ge(pl_done, n + 1)
                    for g in range(2):
                        dve.wait_ge(pw_mm, 4 * l + it * 2 + g + 1)
                        for j in range(2):
                            k = it * 4 + g * 2 + j
                            TS(mix[:, k, t0:T2], PS[5 + j][:, 0:T], V("pool_scale", 8 * l + k), None, ALU.mult).then_inc(pm_done, 1)
                for i in range(2):
                    t = TS(rotw[:, i, :], rot, V(("qn_2", "kn_2")[i], l), None, ALU.mult)
                t.then_inc(rotw_ok, 1)
                with dve.Fori(0, 2) as it:
                    own.loop(it, AT_OWN[l])
                    c = C0[f"qkv{l}"] + it * 48
                    step = [0]
                    pe_at = lambda n: dve.wait_ge(at_pe[l], at(AT_PE[l], n, it))
                    act_at = lambda n: dve.wait_ge(at_act[l], at(AT_ACT[l], n, it))

                    def done(ins, label):
                        assert AT_DVE[l][step[0]] == label, (AT_DVE[l][step[0]], label)
                        step[0] += 1
                        ins.then_inc(at_dve[l], 1)
                        dve.wait_ge(at_dve[l], at(AT_DVE[l], label, it))

                    def ropes(bs):
                        for b in bs:
                            g = V("qn_2" if b < 4 else "kn_2", l)
                            act_at(f"sq{b}")
                            pe_at(f"r{b}")
                            own.then(STT(rope2[:, 0, :], qk[:, b, TOK:T2], g, cos, ALU.mult, ALU.mult))
                            own.then(TT(rope2[:, 1, :], PS[(4, 6, 7)[b % 3]][:, 0:TOK], sin, ALU.mult))
                            done(TT(qk[:, b, TOK:T2], rope2[:, 0, :], rope2[:, 1, :], ALU.add), f"t{b}")

                    if l:
                        done(dve.memset(sq2[:, :, 0:TOK], 0.0), "z")
                    lo(c, range(LA, 41))
                    ropes((0, 1, 2))
                    lo(c, range(41, 45))
                    ropes((3, 4, 5))
                    lo(c, range(45, 48))
                    ropes((6, 7))
                    lo(c, range(48, 48 + LA))
                    act_at("rt")
                    done(dve.reciprocal(rs2[:, :], rs2[:, :]), "rc")
                    for i, b in enumerate(QK_HEADS):
                        g = V("qn_2" if b < 4 else "kn_2", l)
                        pe_at(f"c{b}")
                        if b >= 4 or l == 0:
                            own.then(STT(qk[:, b, 0:TOK], qk[:, b, 0:TOK], g, PS[4 + i % 4][:, 0:TOK], ALU.mult, ALU.mult))
                        done(TT(qk[:, b, TOK:T2], qk[:, b, TOK:T2], PS[4 + i % 4][:, TOK:T2], ALU.mult), f"f{b}")

                    def maxima(u):
                        nk = TOK if units[u][1] < 2 else T2
                        pe_at(f"S{u}")
                        s, k = 8 * (u % 3), 2 * (u % 3)
                        own.then(dve.reduce_max(smx2[:, s:s + 2], psum[:, k:k + 2, 0:nk], axis=AX.X))
                        done(TS(smx2[:, s + 2:s + 4], smx2[:, s:s + 2], -DIFF_SCALE, None, ALU.mult), f"mx{u}")

                    for u in range(-2, len(units) + 1):
                        if 0 <= u < len(units):
                            nk = TOK if units[u][1] < 2 else T2
                            s, k = 8 * (u % 3), u % 3
                            act_at(f"e{u}")
                            own.then(dve.reciprocal(smx2[:, s + 6:s + 8], smx2[:, s + 4:s + 6]))
                            own.then(TT(smx2[:, s + 7:s + 8], smx2[:, s + 7:s + 8], lam[:, 4 + l:5 + l], ALU.mult))
                            own.then(TS(pr[:, k, 1, 0:nk], pr[:, k, 1, 0:nk], smx2[:, s + 7:s + 8], None, ALU.mult))
                            done(STT(pr[:, k, 0, 0:nk], pr[:, k, 0, 0:nk], smx2[:, s + 6:s + 7], pr[:, k, 1, 0:nk], ALU.mult, ALU.subtract), f"a{u}")
                        if u + 2 < len(units):
                            maxima(u + 2)
                    act_at("rto")
                    done(dve.reciprocal(rs2[:, t0:T2], rs2[:, t0:T2]), "rco")
                    for h in range(4):
                        n = bass.ds(it * 4 + 8 + h, 1)
                        pe_at(f"co{h}")
                        done(STT(mix[:, n, t0:T2], mix[:, n, t0:T2], sub2[:, l:l + 1], PS[h][:, t0:T2].unsqueeze(1), ALU.mult, ALU.mult), f"fo{h}")
                own.end(2)
                dve.wait_ge(pm_done, 8 * l + 8)
                for i, name in enumerate(("poolg", "attng")):
                    with dve.Fori(0, 2) as it:
                        lo(C0[f"{name}{l}"] + it * 16, range(LA, 16 + LA))
                        for m in range(4):
                            dve.wait_ge(blk_free, B0[f"{name}{l}"] + it * 4 + m + 1)
                            n = bass.ds(it * 4 + 8 * i + m, 1)
                            TT(mix[:, n, t0:T2], mix[:, n, t0:T2], stmp[:, m % 2, 0:T].unsqueeze(1), ALU.mult).then_inc(sg_done, 1)
                dve.wait_ge(sg_done, 16 * l + 16)
                split_lo(mix[:, :, t0:T2], mixhi[:, :, t0:T2], mixlo[:, :, t0:T2], 2)
                dve.wait_ge(x2_in, 16 * l + 16)

                def out_add(it, ahead):
                    own.loop(it, 4 if l == 0 else 0)
                    c = C0[f"out{l}"] + it * 16
                    lo(c, range(LA, 16 + ahead))
                    for m in range(4):
                        block_done(c + 16, D1[f"out{l}"] + it * 3, m, 4)
                        n = bass.ds(it * 4 + m, 1)
                        gate = lambda j: mod2[:, bass.ds(it * 4 + 48 * l + 32 + m, 1), j:j + 1].rearrange("p a b -> p (a b)")
                        if l == 0:
                            own.then(STT(xall[:, n, 0:TOK], PS[m][:, 0:TOK].unsqueeze(1), gate(1), xall[:, n, 0:TOK], ALU.mult, ALU.add))
                        STT(xall[:, n, TOK:T2], PS[m][:, T - TOK:T].unsqueeze(1), gate(0), xall[:, n, TOK:T2], ALU.mult, ALU.add).then_inc(blk_free, 1)

                with dve.Fori(0, 4 if l == 0 else 3) as it:
                    out_add(it, LA)
                own.end(4)
                if l == 1:
                    out_add(3, 0)
                dve.wait_ge(blk_free, B0[f"out{l}"] + 16)



def layout(x):
    def fm(v, n=P):
        v = v.reshape(-1, n).T
        return v if n == P else np.concatenate([v, np.zeros((P - n, v.shape[1]), np.float32)], 0)

    mu = x["rwkv_mu"][0]
    lams = [x[f"lambda_{n}_2"][l] for l in range(2) for n in ("q1", "k1", "q2", "k2")]
    vec = [fm(x["b_ada"][0]), fm(x["norm_mix_pre"][0]), fm(x["norm_mix_post"][0]), fm(x["norm_ffn_pre"][0]),
           fm(x["norm_ffn_post"][0]), fm(x["gate_b"][0]), fm(x["ffn_conv_w"][0, 0]), fm(x["ffn_conv_w"][0, 1]),
           fm(x["ffn_conv_w"][0, 2]), fm(x["ffn_conv_b"][0]), fm(x["mla_q_norm"][0]), fm(x["mla_kv_norm"][0]),
           fm(mu[:3 * RW]), fm(mu[3 * RW:3 * RW + 4 * LORA], LORA), fm(mu[3 * RW + 4 * LORA:]),
           fm(x["b_ada_2"]), fm(x["norm_w_2"]), fm(x["pool_scale_2"]),
           np.concatenate([fm(x["q_norm_w_2"], 64)[:64]] * 2, 0), np.concatenate([fm(x["k_norm_w_2"], 64)[:64]] * 2, 0),
           fm(x["subln_w_2"]), fm(np.stack(lams), 64)]
    vec = np.ascontiguousarray(np.concatenate(vec, 1))
    assert vec.shape == (P, VCOLS)
    pair = [x["rwkv_w0"][0, 0], x["rwkv_w0"][0, 1], x["rwkv_a0"][0, 0], x["rwkv_a0"][0, 1], x["rwkv_k_k"][0],
            x["rwkv_k_a"][0], x["rwkv_r_k"][0].reshape(-1), x["rwkv_lnx_w"][0], x["rwkv_lnx_b"][0]]
    pvec = np.ascontiguousarray(np.stack([fm(v).T for v in pair], 2))

    def two(a, b):
        return np.stack([a.reshape(DC, P).T, b.reshape(DC, P).T], 2)

    cT = np.ascontiguousarray(np.stack([two(x["c"], x["c_ctx"]), two(x["c_2"], x["c_ctx_2"])], 1))
    uq = x["mla_w_uq"][0].reshape(512, 8, 2, 192)
    uq = np.concatenate([uq[..., :128].reshape(512, 8, 256), uq[..., 128:].reshape(512, 8, 128)], 2).reshape(512, 8 * 384)
    ukv = x["mla_w_ukv"][0].reshape(512, 8, 2, 2, 128).transpose(0, 1, 3, 2, 4).reshape(512, 8 * 512)
    w_in = x["w_in"][0]
    kpe = w_in[:, MLA0 + 1024:MLA0 + 1088]
    lora = lambda w: np.ascontiguousarray(w[0].transpose(1, 0, 2))
    return {"consts": constants(), "hconsts": head_constants(), "vec": vec, "pvec": pvec, "cT": cT, "x": x["x"][0], "ctx": x["ctx"][0], "ctx_2": x["ctx_2"][0],
            "w_ada": x["w_ada"][0], "w_in": w_in, "w_kpe": np.ascontiguousarray(np.concatenate([kpe, kpe], 1)),
            "w_uq": np.ascontiguousarray(uq), "w_ukv": np.ascontiguousarray(ukv), "w2": lora(x["rwkv_w2"]), "a2": lora(x["rwkv_a2"]),
            "g2": x["rwkv_g2"][0], "w_rwkv_proj": x["w_rwkv_proj"][0], "w_mla_proj": x["w_mla_proj"][0], "w_out": x["w_out"][0],
            "w_gate": x["ffn_w_gate"][0], "w_val": x["ffn_w_val"][0], "w_down": x["ffn_w_down"][0],
            "w_ada_2": np.ascontiguousarray(np.concatenate(list(x["w_ada_2"]), 1)), "w_in_2": x["w_in_2"], "pool_w": x["pool_w_2"], "w_out_2": x["w_out_2"]}


def kernel(**inputs):
    import concourse.bacc as bacc
    from concourse.bass_utils import run_bass_kernel_spmd

    arrays = layout({k: np.asarray(v) for k, v in inputs.items()})
    nc = bacc.Bacc("TRN2", target_bir_lowering=False, num_devices=1)
    A = {k: nc.dram_tensor(f"in_{k}", a.shape, F32, kind="ExternalInput").ap() for k, a in arrays.items()}
    out = nc.dram_tensor("out", (TOK, D), F32, kind="ExternalOutput").ap()
    build(nc, A, out)
    r = run_bass_kernel_spmd(nc, [{f"in_{k}": a for k, a in arrays.items()}], core_ids=[0])
    return r.results[0]["out"].reshape(1, TOK, D)
```

```python
from contextlib import ExitStack

import numpy as np

import concourse.bass as bass
from concourse import mybir

F32 = mybir.dt.float32
F32R = mybir.dt.float32r
ACT = mybir.ActivationFunctionType
ALU = mybir.AluOpType
AX = mybir.AxisListType

P = 128
D = 2048
DC = D // P
TOK = 256
T2 = 2 * TOK
N = 512
EPS = 1e-6
RW = 1024
LORA = 96
MLA0 = 3 * RW + 4 * LORA + 256
GATE0 = MLA0 + 512 + 512 + 64
ATTN_SCALE = (128 + 64) ** -0.5
DECAY_SCALE = float(np.exp(-0.5))
LNX_EPS = 64e-5
CH = 64
FF = 5632
DIFF_SCALE = 64 ** -0.5
LAM_INIT = [0.8 - 0.6 * float(np.exp(-0.3 * l)) for l in range(2)]
POOL_WINDOWS = (2, 4, 8, 16)

RAW = 4
HL = 4
LA = 3
ADA_RAW = 2
ADA_AT = [1, 2, 5, 6, 8, 9, 11, 12]

PHASES = [("ckv", 1, 16, 4, 3, 1), ("cq", 1, 16, 4, 3, 0), ("kpe", 1, 16, 1, 0, 1), ("mla", 8, 8, 7, 7, 1),
          ("kv", 4, 16, 4, 3, 1), ("r", 2, 16, 4, 3, 0), ("lora", 1, 16, 4, 3, 1), ("gl", 1, 16, 2, 1, 1),
          ("rwkv", 8, 0, 0, 0, 3), ("gate", 8, 16, 4, 3, 0), ("rproj", 4, 8, 4, 3, 0), ("mproj", 4, 16, 4, 3, 0),
          ("wout", 4, 16, 4, 3, 0), ("ffn0", 1, 32, 8, 6, 0), ("ffn", 10, 48, 8, 18, 0), ("ffn1", 1, 16, 0, 12, 0)]
for _l in range(2):
    PHASES += [(f"poolv{_l}", 2, 16, 4, 3, 0), (f"qkv{_l}", 2, 48, 12, 9, 0), (f"poolg{_l}", 2, 16, 4, 3, 0),
               (f"attng{_l}", 2, 16, 4, 3, 0), (f"out{_l}", 4, 16, 4, 3, 0)]
ADA_HEAD = 8
RW_OWN = 75
AT_OWN = [88, 52]


def _bases():
    chunk, block, done, ada = {}, {}, {}, {}
    c = b = d = 0
    a = ADA_HEAD
    for name, n, nc_, nb, nd, na in PHASES:
        chunk[name], block[name], done[name], ada[name] = c, b, d, a
        c, b, d, a = c + n * nc_, b + n * nb, d + n * nd, a + n * na
    return chunk, block, done, ada


C0, B0, D1, A0 = _bases()

VEC = [("b_ada", 96), ("mix_pre", 16), ("mix_post", 16), ("ffn_pre", 16), ("ffn_post", 16), ("gate_b", 32),
       ("conv_w0", 44), ("conv_w1", 44), ("conv_w2", 44), ("conv_b", 44), ("q_norm", 4), ("kv_norm", 4),
       ("mu", 30), ("b_ada_2", 96), ("norm_2", 32), ("pool_scale", 16), ("qn_2", 2), ("kn_2", 2),
       ("subln", 2), ("lambda", 8)]
VOFF, _o = {}, 0
for _n, _w in VEC:
    VOFF[_n] = _o
    _o += _w
VCOLS = _o
PAIR_VEC = ["w0_0", "w0_1", "a0_0", "a0_1", "k_k", "k_a", "r_k", "lnx_w", "lnx_b"]

CONST = [("ident", 128), ("ones", 128), ("bones", 128), ("bmean", 128), ("sel", 4), ("eps", 2), ("one", 1),
         ("rot", 128), ("cos", 256), ("sin", 256), ("masks", 16 * 128), ("restart", 512), ("eye64", 64),
         ("invcnt", 1024)]
COFF, _o = {}, 0
for _n, _w in CONST:
    COFF[_n] = _o
    _o += _w
CCOLS = _o
HEAD_CONST = [("sum_q", 32), ("sum_k", 32), ("sum_o", 32), ("spread_q", 128), ("spread_k", 128), ("spread_o", 128)]
HOFF, _o = {}, 0
for _n, _w in HEAD_CONST:
    HOFF[_n] = _o
    _o += _w
HCOLS = _o
LEVELS = [1, 2, 4, 8, 16, 32]
M_LEVEL, M_LEVEL_T, M_STRICT, M_INCL = 0, 6, 12, 14


def constants():
    c = np.zeros((P, CCOLS), np.float32)

    def put(name, a):
        c[:, COFF[name]:COFF[name] + a.shape[1]] = a

    i = np.arange(P)
    same = (i[:, None] // 64 == i[None, :] // 64).astype(np.float32)
    put("ident", np.eye(P, dtype=np.float32))
    put("ones", np.ones((P, P), np.float32))
    put("bones", same)
    put("bmean", same / 64)
    sel = np.zeros((P, 4), np.float32)
    for kk in range(2):
        for nh in range(2):
            for j in range(2):
                sel[32 * (2 * kk + nh) + j, 2 * nh + j] = 1
    put("sel", sel)
    put("eps", np.tile(np.array([[EPS, LNX_EPS]], np.float32), (P, 1)))
    put("one", np.ones((P, 1), np.float32))
    t = np.arange(TOK)
    freq = (np.float32(10000.0) ** (-np.arange(0, 32, 2, dtype=np.float32) / np.float32(32))).astype(np.float32)
    rot = np.zeros((P, P), np.float32)
    ang = np.zeros((P, TOK), np.float32)
    for p in range(P):
        pos = (t // 64 if p % 64 < 32 else t % 64).astype(np.float32)
        ang[p] = pos * freq[p % 16]
        if p % 32 < 16:
            rot[p + 16, p] = -1
        else:
            rot[p - 16, p] = 1
    put("rot", rot)
    put("cos", np.cos(ang))
    put("sin", np.sin(ang))
    r, q = i[:, None], i[None, :]
    masks = []
    for b in LEVELS:
        masks.append((r // (2 * b) == q // (2 * b)) & ((r // b) % 2 == 1) & ((q // b) % 2 == 0))
    masks += [m.T for m in masks]
    chunk = r // CH == q // CH
    masks += [chunk & (q < r), chunk & (q > r), chunk & (q <= r), chunk & (q >= r)]
    put("masks", np.concatenate([m.astype(np.float32) for m in masks], 1))
    put("restart", np.tile((np.arange(T2) % CH != 0).astype(np.float32), (P, 1)))
    put("eye64", np.tile(np.eye(64, dtype=np.float32), (2, 1)))
    cnt = [np.clip(t + w // 2, 0, TOK) - np.clip(t - w // 2, 0, TOK) for w in POOL_WINDOWS]
    put("invcnt", np.tile(np.concatenate([(1 / x.astype(np.float32)) for x in cnt])[None], (P, 1)).astype(np.float32))
    return c


def head_constants():
    c = np.zeros((P, HCOLS), np.float32)
    half, row = np.arange(P) // 64, np.arange(P) % 32
    for i, n in enumerate("qk"):
        c[np.arange(P), HOFF["sum_" + n] + 2 * i + half] = 1
        c[:, HOFF["spread_" + n]:HOFF["spread_" + n] + P] = row[:, None] == 2 * i + half[None, :]
    c[:, HOFF["sum_o"]] = 1
    c[:, HOFF["spread_o"]:HOFF["spread_o"] + P] = (row == 0)[:, None]
    return c


def at(labels, label, it=0, base=0):
    return base + it * len(labels) + labels.index(label) + 1


class Own:

    def __init__(self, eng, sem):
        self.eng, self.sem, self.n, self.it, self.per, self.n0 = eng, sem, 0, 0, 0, 0

    def then(self, ins):
        ins.then_inc(self.sem, 1)
        self.n += 1
        self.eng.wait_ge(self.sem, self.it * self.per + self.n)

    def loop(self, it, per):
        self.it, self.per, self.n0 = it, per, self.n

    def end(self, times):
        assert self.n - self.n0 == self.per, (self.n - self.n0, self.per)
        self.n = self.n0 + times * self.per
        self.it, self.per = 0, 0


def build(nc, A, out):
    ctx = ExitStack()
    with ctx:
        def sem(name):
            return ctx.enter_context(nc.semaphore(name))

        SBUF0 = 16512

        def sb(name, shape, kb, dt=F32):
            return nc.alloc_sbuf_tensor_at(name, shape, dt, offset=SBUF0 + int(kb * 1024))

        psum = ctx.enter_context(nc.psum_tensor("psum", [P, 8, 512], F32))
        PS = [psum[:, i, :] for i in range(8)]

        raw = sb("raw", [P, RAW, 2, N], 0)
        whi = sb("whi", [P, HL, N], 16, F32R)
        wlo = sb("wlo", [P, HL, N], 24, F32R)
        ada_raw = sb("ada_raw", [P, ADA_RAW, 2, N], 32)
        ada_head = sb("ada_head", [P, 2, 8, 2, N], 70)
        ada_sb = sb("ada_sb", [P, 256], 40)
        sc1 = sb("sc1", [P, DC, 32], 41)
        sc2 = sb("sc2", [P, DC, 32], 43)
        con = sb("con", [P, CCOLS], 45)
        vec = sb("vec", [P, VCOLS], 64.75)
        mod1 = sb("mod1", [P, 96, 2], 67)
        mod2 = sb("mod2", [P, 96, 2], 67.75)
        gain = sb("gain", [P, DC, 2], 68.5)
        cT = sb("cT", [P, 2, DC, 2], 68.75)
        mu_keep = sb("mu_keep", [P, 30], 69)
        mu_half = sb("mu_half", [P, 30], 69.125)
        lam = sb("lam", [P, 6], 69.25)
        smx = sb("smx", [P, 16], 69.375)
        D0 = 70
        hhi = sb("hhi", [P, 2, DC, TOK], D0 + 0, F32R)
        hlo = sb("hlo", [P, 2, DC, TOK], D0 + 32, F32R)
        xrow = sb("xrow", [P, 4, D], D0 + 64)
        xT = sb("xT", [P, DC, T2], D0 + 96)
        nsq0 = sb("nsq0", [P, 2, T2], D0 + 128)
        nrs0 = sb("nrs0", [P, T2], D0 + 132)
        nap0 = sb("nap0", [P, 3, T2], D0 + 64)
        ckvhi = sb("ckvhi", [P, 4, T2], D0 + 64, F32R)
        ckvlo = sb("ckvlo", [P, 4, T2], D0 + 72, F32R)
        cqhi = sb("cqhi", [P, 4, TOK], D0 + 80, F32R)
        cqlo = sb("cqlo", [P, 4, TOK], D0 + 84, F32R)
        kpe = sb("kpe", [P, T2], D0 + 88)
        oT = sb("oT", [P, 16, TOK], D0 + 90)
        ckv = sb("ckv", [P, 4, T2], D0 + 106)
        cq = sb("cq", [P, 4, TOK], D0 + 114)
        nsq1 = sb("nsq1", [P, 2, T2], D0 + 118)
        nrs1 = sb("nrs1", [P, T2], D0 + 122)
        nap1 = sb("nap1", [P, 3, T2], D0 + 124)
        ropet = sb("ropet", [P, 2, TOK], D0 + 135)
        nrs2 = sb("nrs2", [P, TOK], D0 + 136)
        k_sb = sb("k_sb", [P, 2, T2], D0 + 106)
        v_sb = sb("v_sb", [P, 4, 256], D0 + 110)
        qn = sb("qn", [P, 2, TOK], D0 + 114)
        qraw = sb("qraw", [P, TOK], D0 + 116)
        qpad = sb("qpad", [P, 2, TOK], D0 + 117)
        prob = sb("prob", [P, 4, T2], D0 + 119)
        probT = sb("probT", [P, 4, TOK], D0 + 127)
        probT2 = sb("probT2", [P, 4, TOK], D0 + 131)

        pad = sb("pad", [P, 4, 2, TOK + 2], D0 + 106)
        sh_a = sb("sh_a", [P, 2, TOK], D0 + 115)
        sh_out = sb("sh_out", [P, 4, T2], D0 + 117)
        wl = sb("wl", [P, 2, T2], D0 + 64)
        al = sb("al", [P, 2, T2], D0 + 68)
        gl = sb("gl", [P, 2, TOK], D0 + 72)
        atok_r = sb("rhs", [P, 2, 4, P], D0 + 8)
        r_s = [sb("r_s", [P, TOK], D0 + 0), sb("r_s1", [P, TOK], D0 + 104)]
        dec = [sb("dec", [P, 8], D0 + 1), sb("dec1", [P, 8], D0 + 105)]
        tot = [sb("tot", [P, 8], D0 + 1.125), sb("tot1", [P, 8], D0 + 105.125)]
        zs = sb("zs", [P, 8, CH], D0 + 2)
        b_tok = sb("b_tok", [P, 4, P], D0 + 4)
        k_tok = sb("k_tok", [P, 4, P], D0 + 6)
        akT = sb("akT", [P, 2, 4, P], D0 + 12)
        wu = sb("wu", [P, 2, 4, P], D0 + 12)
        bm = sb("bm", [P, 2, 4, P], D0 + 32)
        aT = sb("aT", [P, 2, 4, P], D0 + 36)
        inv = sb("inv", [P, 2, 4, P], D0 + 40)
        invT = sb("invT", [P, 2, 4, P], D0 + 44)
        v_tok = sb("v_tok", [P, 4, P], D0 + 74)
        l_in = [sb("l_in", [P, T2], D0 + 76), sb("l_in1", [P, T2], D0 + 90)]
        l_ex = [sb("l_ex", [P, T2], D0 + 78), sb("l_ex1", [P, T2], D0 + 92)]
        e_ex = [sb("e_ex", [P, T2], D0 + 80), sb("e_ex1", [P, T2], D0 + 94)]
        e_in = [sb("e_in", [P, T2], D0 + 82), sb("e_in1", [P, T2], D0 + 96)]
        a_s = [sb("a_s", [P, T2], D0 + 84), sb("a_s1", [P, T2], D0 + 98)]
        b_s = [sb("b_s", [P, T2], D0 + 86), sb("b_s1", [P, T2], D0 + 100)]
        k_s = [sb("k_s", [P, T2], D0 + 88), sb("k_s1", [P, T2], D0 + 102)]
        arx = [sb(f"arx{d}", [P, 2, 2, 2, P], D0 + (76, 90)[d]) for d in range(2)]
        g1t = [sb(f"g1t{d}", [P, 8, CH], D0 + (80, 94)[d]) for d in range(2)]
        hd = [sb(f"hd{d}", [P, 8, CH], D0 + (82, 96)[d]) for d in range(2)]
        qt = [sb(f"qt{d}", [P, TOK], D0 + (84, 98)[d]) for d in range(2)]
        fin = sb("fin", [P, 2, TOK], D0 + 100)
        bonus = sb("bonus", [P, TOK], 41)
        k_t = sb("k_t", [P, T2], D0 + 106)
        v_t = sb("v_t", [P, T2], D0 + 108)
        r_t = sb("r_t", [P, TOK], D0 + 110)
        lw2 = sb("lw2", [P, 4, P], D0 + 111)
        g2s = sb("g2s", [P, 2, P], D0 + 113)
        pv = sb("pv", [P, 6], D0 + 114)
        pv2 = sb("pv2", [P, 3], D0 + 114.125)
        yacc = sb("yacc", [P, TOK], D0 + 1.25)
        kk = sb("kk", [P, T2], D0 + 115)
        sig = sb("sig", [P, 2, T2], D0 + 117)
        icl = sb("icl", [P, 2, T2], D0 + 121)
        kdir = sb("kdir", [P, 2, T2], D0 + 125)
        y_all = sb("y_all", [P, 8, TOK], D0 + 129)

        g_rwkv = sb("g_rwkv", [P, DC, TOK], D0 + 0)
        g_mla = sb("g_mla", [P, DC, TOK], D0 + 32)
        yhi = sb("yhi", [P, 8, TOK], D0 + 64, F32R)
        ylo = sb("ylo", [P, 8, TOK], D0 + 72, F32R)
        ohi = sb("ohi", [P, DC, TOK], D0 + 16, F32R)
        olo = sb("olo", [P, DC, TOK], D0 + 48, F32R)
        mrg = sb("mrg", [P, DC, TOK], D0 + 106)
        mhi = sb("mhi", [P, DC, TOK], D0 + 0, F32R)
        mlo = sb("mlo", [P, DC, TOK], D0 + 32, F32R)
        wo = sb("wo", [P, DC, TOK], D0 + 64)
        cf = sb("cf", [P, DC], 69.4375)
        nsq3 = sb("nsq3", [P, 2, TOK], D0 + 80)
        nrs3 = sb("nrs3", [P, TOK], D0 + 82)
        nap3 = sb("nap3", [P, 3, TOK], D0 + 83)
        x1 = sb("x1", [P, DC, TOK], D0 + 88)
        fhi = sb("fhi", [P, DC, TOK], D0 + 16, F32R)
        flo = sb("flo", [P, DC, TOK], D0 + 48, F32R)
        gpad = sb("gpad", [P, 4, TOK + 2], D0 + 0)
        ge = sb("ge", [P, 4, TOK], D0 + 4.25)
        uhi = sb("uhi", [P, 4, TOK], D0 + 32, F32R)
        ulo = sb("ulo", [P, 4, TOK], D0 + 36, F32R)
        yffn = sb("yffn", [P, DC, TOK], D0 + 64)
        crow = sb("crow", [P, 2, D], D0 + 0)
        xall = sb("xall", [P, DC, T2], D0 + 104)
        nap6 = sb("nap6", [P, 3, T2], D0 + 64)
        nsq6 = sb("nsq6", [P, 2, T2], D0 + 84)
        nrs6 = sb("nrs6", [P, T2], D0 + 74)
        mix = sb("mix", [P, DC, T2], D0 + 64)
        mixhi = sb("mixhi", [P, DC, T2], D0 + 0, F32R)
        mixlo = sb("mixlo", [P, DC, T2], D0 + 32, F32R)
        qk = sb("qk", [P, 8, T2], D0 + 96)
        v2 = sb("v2", [P, 4, N], D0 + 112)
        pr = sb("pr", [P, 3, 2, T2], D0 + 120)
        aTs = sb("aTs", [P, 2, 4, P], D0 + 132)
        sq2 = sb("sq2", [P, 4, T2], D0 + 120)
        rope2 = sb("rope2", [P, 2, TOK], D0 + 128)
        rs2 = sb("rs2", [P, T2], D0 + 130)
        hcon = sb("hcon", [P, HCOLS], 41)
        rotw = sb("rotw", [P, 2, P], 43)
        smx2 = sb("smx2", [P, 24], 69.5)
        sub2 = sb("sub2", [P, 2], 69.28125)
        pl = sb("pl", [P, 4, T2], D0 + 96)
        stmp = sb("stmp", [P, 2, T2], D0 + 96)
        pw = sb("pw", [P, 4, 2, 256], D0 + 120)
        xp = sb("xp", [P, 2, 2, TOK + 32], D0 + 128)
        sw = sb("sw", [P, 2, 2, TOK + 32], D0 + 132.5)
        orow = sb("orow", [P, 2, D], D0 + 0)

        def C(name, a=0, b=None):
            w = dict(CONST)[name]
            return con[:, COFF[name] + a:COFF[name] + (w if b is None else b)]

        def H(name, rows=slice(0, P)):
            return hcon[rows, HOFF[name]:HOFF[name] + dict(HEAD_CONST)[name]]

        def V(name, i=0, n=1):
            return vec[:, VOFF[name] + i:VOFF[name] + i + n]

        def Vd(name, i, n=1):
            return vec[:, bass.ds(VOFF[name] + i, n)]

        ident, ones, bones, bmean, rot = C("ident"), C("ones"), C("bones"), C("bmean"), C("rot")
        cos, sin = C("cos"), C("sin")

        const_in = sem("const_in")
        rows_in = sem("rows_in")
        raw_in = [sem(f"raw_in{i}") for i in range(RAW)]
        w_hi = sem("w_hi")
        w_lo = sem("w_lo")
        w_used = sem("w_used")
        blk_done = sem("blk_done")
        blk_free = sem("blk_free")
        ada_in = [sem(f"ada_in{i}") for i in range(ADA_RAW)]
        ada_hin = [sem(f"ada_hin{i}") for i in range(2)]
        ada_used = sem("ada_used")
        ada_out = sem("ada_out")
        ada_fin = sem("ada_fin")
        mod_ready = sem("mod_ready")
        sc_zero = sem("sc_zero")
        sc_ready = sem("sc_ready")
        tr_done = sem("tr_done")
        tr_out = sem("tr_out")
        n_sq = sem("n_sq")
        n_mm = sem("n_mm")
        n_std = sem("n_std")
        n_f32 = sem("n_f32")
        n_hi = sem("n_hi")
        n_lo = sem("n_lo")
        dve_own = sem("dve_own")
        act_own = sem("act_own")
        mla_pe = sem("mla_pe")
        mla_act = sem("mla_act")
        mla_dve = sem("mla_dve")
        rope_mm = sem("rope_mm")
        x_saved = sem("x_saved")

        w_in = A["w_in"]
        MLA_PE = ["rot", "S0", "S1", "S2", "S3", "T0", "T1", "PV0", "T2", "T3", "PV1"]
        MLA_DVE = ["q", "nmx0", "nmx1", "pn0", "nmx2", "pn1", "nmx3", "pn2", "pn3", "o0", "o1"]
        MLA_ACT = ["exp0", "exp1", "exp2", "pT0", "exp3", "pT1", "pT2", "pT3"]

        sh_done = sem("sh_done")
        sh_st = [sem(f"sh_st{i}") for i in range(4)]
        sh_free = sem("sh_free")
        lora_act = sem("lora_act")
        pool_gate = sem("pool_gate")
        pe_gate = sem("pe_gate")
        rw_in = sem("rw_in")
        v_in = sem("v_in")
        rw_in2 = sem("rw_in2")
        o_saved = sem("o_saved")
        o_in = sem("o_in")
        rw_pe = sem("rw_pe")
        rw_act = sem("rw_act")
        rw_dve = sem("rw_dve")
        def levels(d, names):
            return [[f"{n}{d}{l}{h}" for n in names for h in range(2)] for l in range(1, len(LEVELS))]

        z = [[f"Z{d}{i}" for i in range(1, 7)] for d in range(2)]
        FIRST_PE, FIRST_ACT, FIRST_DVE = ["w0", "kksum", "a0", "a1", "w1", "A0", "AT0"], ["w0", "kkrt", "a0", "a1", "w1", "E0"], ["kksq", "L0", "kk", "abk0", "I0", "A0"]
        RW_PE = ["tr0", "Ak0", "Ar0", "trv", "P10"] + sum(levels(0, "BG"), [])
        RW_PE += ["WU0", "GH0", "Q0", "YL0", "Z01", "A1", "Z02", "AT1"] + z[0][2:] + ["YZ0", "tr1", "Ak1", "Ar1", "P11"]
        for lv, first in zip(levels(1, "BG"), FIRST_PE):
            RW_PE += lv + [first]
        RW_PE += ["WU1", "GH1", "Q1", "YL1", "Z11", "A0", "Z12", "AT0"] + z[1][2:] + ["YZ1", "mean", "var", "bon", "g"]
        RW_ACT = ["tr0", "v", "P10", "E1", "WU0", "tr1", "P11"] + FIRST_ACT[:-1] + ["WU1", "E0", "sd"]
        lv0, lv1 = levels(0, "BX"), levels(1, "BX")
        RW_DVE = ["Ak0", "Ar0"] + lv0[0] + ["L1"] + lv0[1] + lv0[2] + lv0[3] + lv0[4]
        RW_DVE += ["W0", "abk1", "bt", "GH0", "Q0", "Z01", "Z02", "Z03", "Z04", "Z05", "I1", "Z06", "Y0", "A1", "Ak1", "Ar1"]
        RW_DVE += lv1[0][:2] + ["kksq"] + lv1[0][2:] + lv1[1] + ["L0"] + lv1[2] + lv1[3] + lv1[4][:2] + ["kk"] + lv1[4][2:] + ["W1", "abk0", "GH1", "Q1"]
        RW_DVE += ["Z11", "Z12", "Z13", "Z14", "Z15", "I0", "Z16", "Y1", "sq", "out", "A0"]
        RW_END = len(FIRST_DVE) + 8 * len(RW_DVE)
        SCAN = [[0, 1, 2, 3, 4, 5, 6, 7], [3, 2, 1, 0, 7, 6, 5, 4]]

        s_hi = sem("s_hi")
        s_lo = sem("s_lo")
        mg_done = sem("mg_done")
        x1_in = sem("x1_in")
        x1_done = sem("x1_done")
        dn_free = sem("dn_free")
        ff_zero = sem("ff_zero")
        cv_done = sem("cv_done")
        ge_done = sem("ge_done")
        u_hi = sem("u_hi")
        u_lo = sem("u_lo")
        crow_in = sem("crow_in")
        hcon_in = sem("hcon_in")
        rotw_ok = sem("rotw_ok")
        x2_saved = sem("x2_saved")
        x2_in = sem("x2_in")
        pw_in = sem("pw_in")
        lam_pr, lam_mm, lam_e, lam_ok = sem("lam_pr"), sem("lam_mm"), sem("lam_e"), sem("lam_ok")
        xp_zero = sem("xp_zero")
        pl_done = sem("pl_done")
        pw_mm = sem("pw_mm")
        pm_done = sem("pm_done")
        sg_done = sem("sg_done")
        at_pe = [sem(f"at_pe{l}") for l in range(2)]
        at_act = [sem(f"at_act{l}") for l in range(2)]
        at_dve = [sem(f"at_dve{l}") for l in range(2)]
        fin_tr, fin_cp, out_st = sem("fin_tr"), sem("fin_cp"), sem("out_st")
        TILES = [[0, 1, 2, 3], [2, 3]]
        UNITS = [[(h, t) for h in range(4) for t in TILES[l]] for l in range(2)]
        last_of = lambda l, u: UNITS[l][u][1] == 3
        QK_HEADS = [0, 4, 1, 5, 2, 6, 3, 7]
        AT_PE, AT_ACT, AT_DVE = [[], []], [[], []], [[], []]
        for l in range(2):
            nu = len(UNITS[l])
            AT_DVE[l] += ["z"] if l else []
            for b in range(8):
                AT_PE[l] += [f"r{b}", f"n{b}"]
                AT_ACT[l] += [f"sq{b}"]
                AT_DVE[l] += [f"t{b}"]
            AT_PE[l] += [f"c{b}" for b in QK_HEADS]
            AT_ACT[l] += ["rt"]
            AT_DVE[l] += ["rc"] + [f"f{b}" for b in QK_HEADS]
            for u in range(-2, nu + 1):
                nxt = [str(u + 2)] if u + 2 < nu else []
                now = [str(u)] if 0 <= u < nu else []
                end = [str(UNITS[l][u - 1][0])] if u >= 1 and last_of(l, u - 1) else []
                AT_PE[l] += ["S" + n for n in nxt] + ([f"PV{u - 1}"] if u >= 1 else []) + ["T" + n for n in now]
                AT_ACT[l] += ["o" + n for n in end] + ["aT" + n for n in now] + ["e" + n for n in nxt]
                AT_DVE[l] += ["a" + n for n in now] + ["mx" + n for n in nxt]
            AT_PE[l] += ["no"] + [f"co{h}" for h in range(4)]
            AT_ACT[l] += ["rto"]
            AT_DVE[l] += ["rco"] + [f"fo{h}" for h in range(4)]

        nsq_of = [nsq0, nsq1, nsq1, nsq3, nsq3, nsq3, nsq6, nsq6]
        nrs_of = [nrs0, nrs1, nrs2, nrs3, nrs3, nrs3, nrs6, nrs6]
        nt_of = [T2, T2, TOK, TOK, TOK, TOK, T2, T2]

        def like(buf, dst):
            return buf.rearrange("p (s t) -> p s t", t=TOK) if len(dst.shape) == 3 else buf

        x_keep = nc.dram_tensor("x_keep", (P, DC, TOK), F32, kind="Internal").ap()

        rkv = nc.dram_tensor("rkv", (24, P, T2), F32, kind="Internal").ap()

        o_keep = nc.dram_tensor("o_keep", (P, 16, TOK), F32, kind="Internal").ap()
        x2_keep = nc.dram_tensor("x2_keep", (P, DC, T2), F32, kind="Internal").ap()

        block = ctx.enter_context(nc.Block())

        @block.sync
        def _(sp):
            def seg(view, c0, lc0, nch):
                for r in range(nch // 2):
                    lc = lc0 + 2 * r
                    src = view(r)
                    c = c0 + lc
                    if not isinstance(c, int) or c >= 2 * RAW:
                        sp.wait_ge(w_lo, c - 2 * RAW + 2)
                    slot = (lc // 2) % RAW
                    sp.dma_start(raw[:, slot, :, 0:src.shape[2]], src).then_inc(raw_in[slot], 16)

            def cols(w, col, n=N):
                return lambda r: w[256 * r:256 * r + 256, bass.ds(col, n)].rearrange("(a p) n -> p a n", p=P)

            sp.dma_start(con[:, :], A["consts"]).then_inc(const_in, 16)
            sp.dma_start(vec[:, :], A["vec"]).then_inc(const_in, 16)
            sp.dma_start(cT[:, :, :, :], A["cT"]).then_inc(const_in, 16)
            for t in range(2):
                sp.dma_start(xrow[:, t, :], A["ctx"][P * t:P * t + P, :]).then_inc(rows_in, 16)
                sp.dma_start(xrow[:, 2 + t, :], A["x"][P * t:P * t + P, :]).then_inc(rows_in, 16)
            def ada_group(p, col, it=None):
                for kh in range(8):
                    if it is not None:
                        sp.wait_ge(ada_used, it * 16 + 8 * p - 15 + kh)
                    sp.dma_start(ada_head[:, p, kh, :, :], A["w_ada"][256 * kh:256 * kh + 256, bass.ds(col, N)].rearrange("(a p) n -> p a n", p=P)).then_inc(ada_hin[p], 16)
            for p in range(2):
                ada_group(p, p * N)
            with sp.Fori(1, ADA_HEAD // 2) as it:
                c0, c1 = sp.snap(it * 2 * N), sp.snap(it * 2 * N + N)
                ada_group(0, c0, it)
                ada_group(1, c1, it)
            seg(cols(w_in, MLA0 + 512), C0["ckv"], 0, 16)
            seg(cols(w_in, MLA0), C0["cq"], 0, 16)
            seg(cols(A["w_kpe"], 0, P), C0["kpe"], 0, 16)
            with sp.Fori(0, 8) as it:
                cu, cq_ = sp.snap(it * N), sp.snap(it * 384)
                seg(cols(A["w_ukv"], cu), C0["mla"] + it * 8, 0, 4)
                seg(cols(A["w_uq"], cq_, 384), C0["mla"] + it * 8, 4, 4)
            with sp.Fori(0, 4) as it:
                col = sp.snap(it * N + RW)
                seg(cols(w_in, col), C0["kv"] + it * 16, 0, 16)
            with sp.Fori(0, 2) as it:
                col = sp.snap(it * N)
                seg(cols(w_in, col), C0["r"] + it * 16, 0, 16)
            seg(cols(w_in, 3 * RW), C0["lora"], 0, 16)
            seg(cols(w_in, 3 * RW + 4 * LORA, 256), C0["gl"], 0, 16)
            with sp.Fori(0, 8) as it:
                col = sp.snap(it * N + GATE0)
                seg(cols(w_in, col), C0["gate"] + it * 16, 0, 16)
            for name, w in (("rproj", "w_rwkv_proj"), ("mproj", "w_mla_proj"), ("wout", "w_out")):
                n = 8 if name == "rproj" else 16
                with sp.Fori(0, 4) as it:
                    col = sp.snap(it * N)
                    seg(cols(A[w], col), C0[name] + it * n, 0, n)

            def down(row0, row1, c0, lc0):
                for n in range(4):
                    seg(lambda r: A["w_down"][bass.ds((row0, row1)[r], 256), n * N:n * N + N].rearrange("(a p) n -> p a n", p=P),
                        c0, lc0 + 4 * n, 4)
            seg(cols(A["w_gate"], 0), C0["ffn0"], 0, 16)
            seg(cols(A["w_val"], 0), C0["ffn0"], 16, 16)
            with sp.Fori(0, 10) as it:
                c = C0["ffn"] + it * 48
                col, r0, r1 = sp.snap(it * N + N), sp.snap(it * N), sp.snap(it * N + 256)
                seg(cols(A["w_gate"], col), c, 0, 16)
                down(r0, r1, c, 16)
                seg(cols(A["w_val"], col), c, 32, 16)
            down(10 * N, 10 * N + 256, C0["ffn1"], 0)
            for l in range(2):
                w = A["w_in_2"][l]
                def pairs(name, col0):
                    with sp.Fori(0, 2) as it:
                        col = sp.snap(it * N + col0)
                        seg(cols(w, col), C0[f"{name}{l}"] + it * 16, 0, 16)

                pairs("poolv", 0)
                with sp.Fori(0, 2) as it:
                    c = C0[f"qkv{l}"] + it * 48
                    cq_, ck, cv = sp.snap(it * N + 2048), sp.snap(it * N + 3072), sp.snap(it * N + 4096)
                    for i, col in enumerate((cq_, ck, cv)):
                        seg(cols(w, col), c, 16 * i, 16)
                pairs("poolg", 1024)
                pairs("attng", 5120)
                with sp.Fori(0, 4) as it:
                    col = sp.snap(it * N)
                    seg(cols(A["w_out_2"][l], col), C0[f"out{l}"] + it * 16, 0, 16)
            for t in range(2):
                sp.wait_ge(fin_cp, 32)
                sp.dma_start(out[P * t:P * t + P, :], orow[:, t, :]).then_inc(out_st, 16)
            sp.wait_ge(out_st, 32)

        @block.gpsimd
        def _(pool):
            pool.wait_ge(tr_out, DC)
            pool.dma_start(x_keep, xT[:, :, TOK:T2]).then_inc(x_saved, 16)
            pool.wait_ge(x_saved, 16)
            def ada_group(w, col, a, khs=range(8)):
                for kh in khs:
                    if not isinstance(a, int) or a + kh >= 8 * ADA_HEAD + ADA_RAW:
                        pool.wait_ge(ada_used, a + kh - ADA_RAW + 1)
                    if not isinstance(a, int):
                        pool.sem_inc(pool_gate, 1)
                    pool.dma_start(ada_raw[:, kh % ADA_RAW, :, :], A[w][256 * kh:256 * kh + 256, bass.ds(col, N)].rearrange("(a p) n -> p a n", p=P)).then_inc(ada_in[kh % ADA_RAW], 16)

            for name in ("ckv", "kpe"):
                ada_group("w_ada", A0[name] * N, A0[name] * 8)
            with pool.Fori(0, 8) as it:
                col = pool.snap(it * N + A0["mla"] * N)
                ada_group("w_ada", col, it * 8 + A0["mla"] * 8)
            pool.wait_ge(mla_dve, 8 * len(MLA_DVE))
            pool.dma_start(o_keep, oT[:, :, :]).then_inc(o_saved, 16)
            pool.sem_inc(sh_free, 1)
            ada_group("w_ada", A0["kv"] * N, A0["kv"] * 8, range(2))
            with pool.Fori(0, 4) as it:
                col, col1 = pool.snap(it * N + A0["kv"] * N), pool.snap(it * N + A0["kv"] * N + N)
                ada_group("w_ada", col, it * 8 + A0["kv"] * 8, range(2, 8))
                ada_group("w_ada", col1, it * 8 + A0["kv"] * 8 + 8, range(2))
                for m in range(4):
                    dst = pool.snap(it * 4 + 8 + m)
                    pool.wait_ge(sh_done, it * 4 + m + 2)
                    pool.sem_inc(pool_gate, 1)
                    pool.dma_start(rkv[bass.ds(dst, 1), :, :].rearrange("o p t -> p (o t)"), sh_out[:, m, :]).then_inc(sh_st[m], 16)
                for m in range(4):
                    pool.wait_ge(sh_st[m], it * 16 + 16)
                pool.sem_inc(sh_free, 1)
            with pool.Fori(0, 2) as it:
                for m in range(4):
                    dst = pool.snap(it * 4 + m)
                    pool.wait_ge(sh_done, it * 4 + 16 + m + 2)
                    pool.sem_inc(pool_gate, 1)
                    pool.dma_start(rkv[bass.ds(dst, 1), :, TOK:T2].rearrange("o p t -> p (o t)"), sh_out[:, m, 0:TOK]).then_inc(sh_st[m], 16)
                for m in range(4):
                    pool.wait_ge(sh_st[m], it * 16 + 80)
                pool.sem_inc(sh_free, 1)
            ada_group("w_ada", A0["lora"] * N, A0["lora"] * 8, range(2, 8))
            ada_group("w_ada", A0["gl"] * N, A0["gl"] * 8)
            pool.wait_ge(o_saved, 16)
            pool.wait_ge(sh_done, 31)
            def first_inputs(r0, k0, f0):
                pool.dma_start(k_t[:, :], rkv[bass.ds(k0, 1), :, :].rearrange("o p t -> p (o t)")).then_inc(rw_in, 16)
                pool.dma_start(pv[:, :], A["pvec"][bass.ds(r0, 1), :, 0:6].rearrange("o p t -> p (o t)")).then_inc(rw_in, 16)
                pool.dma_start(lw2[0:LORA, 0:2, :], A["w2"][:, :, bass.ds(f0, P)]).then_inc(rw_in, 16)
                pool.dma_start(lw2[0:LORA, 2:4, :], A["a2"][:, :, bass.ds(f0, P)]).then_inc(rw_in, 16)
                pool.dma_start(r_t[:, :], rkv[bass.ds(r0, 1), :, TOK:T2].rearrange("o p t -> p (o t)")).then_inc(rw_in, 16)

            first_inputs(0, 8, 0)
            AHEAD = range(ADA_RAW)
            ada_group("w_ada_2", 0, A0["rwkv"] * 8, AHEAD)

            def pair(it, snap, last):
                f0, r0, v0 = snap(it * P), snap(it), snap(it + 16)
                f1, r1, k1 = snap(it * P + P), snap(it + 1), snap(it + 9)
                cols_ = [snap(it * 3 * N + j * N) for j in range(4)]
                pool.dma_start(v_t[:, :], rkv[bass.ds(v0, 1), :, :].rearrange("o p t -> p (o t)")).then_inc(v_in, 16)
                ada_group("w_ada_2", cols_[0], (it * 3 + A0["rwkv"]) * 8, range(ADA_RAW, 4))
                pool.dma_start(pv2[:, :], A["pvec"][bass.ds(r0, 1), :, 6:9].rearrange("o p t -> p (o t)")).then_inc(rw_in2, 16)
                pool.dma_start(g2s[:, :, :], A["g2"][:, bass.ds(f0, P)].rearrange("(k p) n -> p k n", p=P)).then_inc(rw_in2, 16)
                ada_group("w_ada_2", cols_[0], (it * 3 + A0["rwkv"]) * 8, range(4, 8))
                ada_group("w_ada_2", cols_[1], (it * 3 + A0["rwkv"] + 1) * 8)
                pool.wait_ge(rw_dve, at(RW_DVE, "bt", it, len(FIRST_DVE)))
                pool.sem_inc(pool_gate, 1)
                first_inputs(r1, k1, f1)
                ada_group("w_ada_2", cols_[2], (it * 3 + A0["rwkv"] + 2) * 8)
                if not last:
                    ada_group("w_ada_2", cols_[3], (it * 3 + A0["rwkv"] + 3) * 8, AHEAD)
                pool.wait_ge(rw_dve, at(RW_DVE, "out", it, len(FIRST_DVE)))
                pool.sem_inc(pool_gate, 1)

            with pool.Fori(0, 7) as it:
                pair(it, pool.snap, False)
            pair(7, int, True)
            pool.wait_ge(rw_in, 9 * 5 * 16)
            pool.wait_ge(v_in, 8 * 16)
            pool.wait_ge(rw_in2, 8 * 2 * 16)
            pool.wait_ge(rw_dve, RW_END)
            pool.dma_start(oT[:, :, :], o_keep).then_inc(o_in, 16)
            pool.wait_ge(o_in, 16)
            pool.wait_ge(s_lo, 2 + 4)
            pool.dma_start(x1[:, :, :], x_keep).then_inc(x1_in, 16)
            pool.wait_ge(x1_in, 16)
            pool.wait_ge(u_lo, 44)
            for t in range(2):
                pool.dma_start(crow[:, t, :], A["ctx_2"][P * t:P * t + P, :]).then_inc(crow_in, 16)
            pool.dma_start(hcon[:, :], A["hconsts"]).then_inc(hcon_in, 16)
            pool.wait_ge(hcon_in, 16)
            pool.wait_ge(crow_in, 32)
            for l in range(2):
                if l == 0:
                    pool.wait_ge(tr_out, 2 * DC)
                    pool.wait_ge(x1_done, 2 * DC)
                else:
                    pool.wait_ge(blk_free, B0["poolv1"])
                pool.dma_start(x2_keep, xall[:, :, :]).then_inc(x2_saved, 16)
                pool.wait_ge(x2_saved, 16 * l + 16)
                pool.wait_ge(n_lo, (3 + l) * DC + 8)
                pool.dma_start(pw[:, :, :, :], A["pool_w"][l].rearrange("g (k p) n -> p g k n", p=P)).then_inc(pw_in, 16)
                pool.wait_ge(pw_in, 16 * l + 16)
                pool.wait_ge(at_dve[l], 2 * len(AT_DVE[l]))
                pool.dma_start(xall[:, :, :], x2_keep).then_inc(x2_in, 16)
                pool.wait_ge(x2_in, 16 * l + 16)

        @block.tensor
        def _(pe):
            def ada_mm(sc, kh, src):
                for kk in range(2):
                    for nh in range(2):
                        t = 32 * (2 * kk + nh)
                        mm = pe.matmul(PS[4][t:t + 32, 0:256], sc[:, 2 * kh + kk, :], src[:, kk, nh * 256:nh * 256 + 256],
                                       start=(kh == 0), stop=(kh == 7), tile_position=(0, t))
                mm.then_inc(ada_used, 1)

            def ada_half(sc, kh, g):
                pe.wait_ge(ada_in[kh % ADA_RAW], (g - ADA_HEAD) * (8 // ADA_RAW * 16) + (kh // ADA_RAW + 1) * 16)
                if kh == 0:
                    pe.wait_ge(mod_ready, g)
                ada_mm(sc, kh, ada_raw[:, kh % ADA_RAW, :, :])

            def ada_final(g):
                pe.wait_ge(ada_out, g + 1)
                for m in range(4):
                    mm = pe.matmul(PS[4][:, 256 + 2 * m:258 + 2 * m], ada_sb[:, (m % 2) * P:(m % 2) * P + P],
                                   C("sel", 2 * (m // 2), 2 * (m // 2) + 2), start=True, stop=True)
                mm.then_inc(ada_fin, 1)

            def seg(c0, lc0, nch, b0, nblk, product, ada=None, each=True, ready=None, between=None, parts=None):
                for k in range(nch):
                    slot = (lc0 + k) % HL
                    pe.wait_ge(w_lo, c0 + lc0 + k + 1)
                    if ready is not None:
                        pe.wait_ge(n_lo, ready + k + 1)
                    if parts and k % parts[1] == 0:
                        pe.wait_ge(s_lo, parts[0] + k // parts[1] + 1)
                    for m in range(nblk):
                        if k == 0 and callable(each):
                            each(m)
                        elif k == 0 and each:
                            pe.wait_ge(blk_free, b0 + m - 3)
                        pairs, dst, first = product(m, k, slot)
                        for i, (l, r) in enumerate(pairs):
                            mm = pe.matmul(dst, l, r, start=(k == 0 and i == 0 and first), stop=(k == nch - 1 and i == 2),
                                           skip_group_check=True)
                        if k == nch - 1 and m < nblk - 1:
                            mm.then_inc(blk_done, 1)
                    mm.then_inc(w_used, 1)
                    if between:
                        between(k)
                    if ada and k in ADA_AT:
                        kh = ADA_AT.index(k)
                        ada_half(ada[0], kh, ada[1])
                if ada:
                    ada_final(ada[1])

            def rows(xhi, xlo, T, bank=0):
                def product(m, k, slot):
                    wh, wl = whi[:, slot, m * P:m * P + P], wlo[:, slot, m * P:m * P + P]
                    return [(wh, xhi(k)), (wh, xlo(k)), (wl, xhi(k))], PS[bank + m][:, 0:T], True
                return product

            h2 = rows(lambda k: hhi[:, :, k, :], lambda k: hlo[:, :, k, :], T2)
            h1 = rows(lambda k: hhi[:, 1, k, :], lambda k: hlo[:, 1, k, :], TOK)
            nq = [0]
            nn = [0]

            def norm(n, T):
                for k in range(n):
                    pe.wait_ge(n_sq, nq[0] + 1)
                    if k == 0 and nn[0] > 0:
                        pe.wait_ge(n_std, nn[0])
                    pe.matmul(PS[5][:, 0:T], ones, nsq_of[nn[0]][:, nq[0] % 2, 0:T], start=(k == 0),
                              stop=(k == n - 1)).then_inc(n_mm, 1)
                    nq[0] += 1
                nn[0] += 1

            pe.wait_ge(const_in, 48)
            pe.wait_ge(rows_in, 64)
            for d in range(DC):
                if d >= 2:
                    pe.wait_ge(tr_out, d - 1)
                for t in range(4):
                    tr = pe.transpose(PS[6 + d % 2][:, t * P:t * P + P], xrow[:, t, d * P:d * P + P], ident)
                tr.then_inc(tr_done, 1)
            norm(DC, T2)
            pe.wait_ge(sc_ready, 2)
            with pe.Fori(0, ADA_HEAD // 2) as it:
                for p in range(2):
                    g = it * 2 + p
                    pe.wait_ge(ada_hin[p], it * 128 + 128)
                    if p == 1:
                        pe.wait_ge(mod_ready, g)
                    for kh in range(8):
                        ada_mm(sc1, kh, ada_head[:, p, kh, :, :])
                    ada_final(g)
                pe.wait_ge(mod_ready, it * 2 + 2)
            seg(C0["ckv"], 0, 16, 0, 4, h2, (sc1, A0["ckv"]), each=False, ready=0)
            pe.wait_ge(blk_free, B0["cq"])
            seg(C0["cq"], 0, 16, 0, 4, h1, None, each=False)
            pe.wait_ge(blk_free, B0["kpe"])
            seg(C0["kpe"], 0, 16, 0, 1, h2, (sc1, A0["kpe"]), each=False)
            norm(4, T2)
            norm(4, TOK)
            pe.wait_ge(blk_free, B0["mla"])
            pe.matmul(PS[6][:, 0:TOK], rot, kpe[:, TOK:T2], start=True, stop=True).then_inc(rope_mm, 1)
            pe.wait_ge(n_lo, DC + 8)

            def ukv(m, k, slot):
                if m < 2:
                    wh, wl = whi[:, slot, m * P:m * P + P], wlo[:, slot, m * P:m * P + P]
                    return [(wh, ckvhi[:, k, :]), (wh, ckvlo[:, k, :]), (wl, ckvhi[:, k, :])], PS[m][:, :], True
                t = m - 2
                wh, wl = whi[:, slot, 256:512], wlo[:, slot, 256:512]
                xh, xl = ckvhi[:, k, t * P:t * P + P], ckvlo[:, k, t * P:t * P + P]
                return [(xh, wh), (xh, wl), (xl, wh)], PS[2 + t // 2][:, (t % 2) * 256:(t % 2) * 256 + 256], t % 2 == 0

            uq = rows(lambda k: cqhi[:, k, :], lambda k: cqlo[:, k, :], TOK)
            with pe.Fori(0, 8) as it:
                def ada(*khs):
                    for kh in khs:
                        ada_half(sc1, kh, A0["mla"] + it)

                pe.wait_ge(blk_free, B0["mla"] + it * 7)
                seg(C0["mla"] + it * 8, 0, 4, 0, 6, ukv, None, each=False, between=lambda k: k == 2 and ada(0))
                pe.wait_ge(blk_free, B0["mla"] + it * 7 + 4)
                seg(C0["mla"] + it * 8, 4, 4, 0, 3, uq, None, each=False, between=lambda k: k == 1 and ada(1))
                ada(2)
                pe.wait_ge(blk_free, B0["mla"] + it * 7 + 7)
                pe.matmul(PS[3][:, 0:TOK], rot, qraw[:, :], start=True, stop=True).then_inc(mla_pe, 1)

                def scores(u):
                    h, q0 = u // 2, (u % 2) * P
                    if u == 0:
                        pe.wait_ge(mla_dve, at(MLA_DVE, "q", it))
                    if u >= 2:
                        pe.wait_ge(mla_act, at(MLA_ACT, f"exp{u - 2}", it))
                    pe.matmul(PS[u % 2][:, :], qn[:, h, q0:q0 + P], k_sb[:, h, :], start=True, stop=False)
                    pe.matmul(PS[u % 2][:, :], qpad[:, h, q0:q0 + P], kpe[:, :], start=False, stop=True).then_inc(mla_pe, 1)

                def turn(u):
                    pe.wait_ge(mla_dve, at(MLA_DVE, f"pn{u}", it))
                    if u >= 1:
                        pe.wait_ge(mla_act, at(MLA_ACT, f"pT{u - 1}", it))
                    for kt in range(4):
                        tr = pe.transpose(PS[6][:, kt * P:kt * P + P], prob[:, u, kt * P:kt * P + P], ident)
                    tr.then_inc(mla_pe, 1)

                def values(h):
                    pe.wait_ge(mla_act, at(MLA_ACT, f"pT{2 * h + 1}", it))
                    if h == 1:
                        pe.wait_ge(mla_dve, at(MLA_DVE, "o0", it))
                    for kt in range(4):
                        mm = pe.matmul(PS[7][:, 0:TOK], v_sb[:, kt, h * P:h * P + P], (probT, probT2)[h][:, kt, :],
                                       start=(kt == 0), stop=(kt == 3))
                    mm.then_inc(mla_pe, 1)

                ada(3)
                scores(0)
                scores(1)
                ada(4)
                scores(2)
                scores(3)
                turn(0)
                ada(5)
                turn(1)
                values(0)
                ada(6)
                turn(2)
                turn(3)
                ada(7)
                values(1)
                ada_final(A0["mla"] + it)
            with pe.Fori(0, 4) as it:
                seg(C0["kv"] + it * 16, 0, 16, B0["kv"] + it * 4, 4, h2, (sc1, A0["kv"] + it))
            with pe.Fori(0, 2) as it:
                seg(C0["r"] + it * 16, 0, 16, B0["r"] + it * 4, 4, h1)

            def lora(m, k, slot):
                wh, wl_ = whi[:, slot, m * LORA:m * LORA + P], wlo[:, slot, m * LORA:m * LORA + P]
                return [(wh, hhi[:, :, k, :]), (wh, hlo[:, :, k, :]), (wl_, hhi[:, :, k, :])], PS[m][:, :], True
            seg(C0["lora"], 0, 16, B0["lora"], 4, lora, (sc1, A0["lora"]))
            seg(C0["gl"], 0, 16, B0["gl"], 2, h1, (sc1, A0["gl"]))

            pe.wait_ge(blk_free, B0["gate"])
            pe.wait_ge(mod_ready, A0["rwkv"])
            pe.wait_ge(lora_act, 4)
            pe.wait_ge(sh_done, 31)
            LF = [slice(TOK, TOK + P), slice(TOK + P, T2)]
            ADA_LEVEL = [[[(0, 4), (0, 5)], [(0, 6)], [(0, 7)], [(0, None)], [(1, 0)]],
                         [[(1, 7), (1, None)], [(2, 0), (2, 1)], [(2, 2)], [(2, 3)], []]]
            def first(step, p, dve_at, act_at):
                i = FIRST_PE.index(step)
                if i == 0:
                    pe.wait_ge(rw_in, p * 80 + 80)
                elif i == 1:
                    act_at("w0")
                    dve_at("kksq")
                    pe.matmul(PS[5][:, :], bones, e_ex[0][:, :], start=True, stop=True).then_inc(rw_pe, 1)
                    return
                else:
                    act_at({"a0": "kkrt", "a1": "a0", "w1": "a1"}[step])
                j = ("w0", "w1", "a0", "a1").index(step)
                pe.matmul(PS[5][:, :], lw2[0:LORA, j, :], (wl if j < 2 else al)[0:LORA, j % 2, :], start=True, stop=True).then_inc(rw_pe, 1)

            def pairs(bank, l, r):
                pe.sem_inc(pe_gate, 1)
                for h in range(2):
                    for b in range(4):
                        mm = pe.matmul(PS[bank + h][:, b * P:b * P + P], l[64 * h:64 * h + 64, b * P:b * P + P], r[64 * h:64 * h + 64, b * P:b * P + P], start=True, stop=True)
                mm.then_inc(rw_pe, 1)

            for step in FIRST_PE[:5]:
                first(step, 0, lambda n: pe.wait_ge(rw_dve, at(FIRST_DVE, n)), lambda n: pe.wait_ge(rw_act, at(FIRST_ACT, n)))
            pe.wait_ge(rw_dve, at(FIRST_DVE, "abk0"))
            pairs(0, a_s[0], b_s[0])
            pairs(2, b_s[0], a_s[0])
            pe.wait_ge(rw_dve, len(FIRST_DVE))
            with pe.Fori(0, 8) as it:
                dve_at = lambda n: pe.wait_ge(rw_dve, at(RW_DVE, n, it, len(FIRST_DVE)))
                act_at = lambda n: pe.wait_ge(rw_act, at(RW_ACT, n, it, len(FIRST_ACT)))
                done = lambda ins: ins.then_inc(rw_pe, 1)
                hs = [slice(0, 64), slice(64, P)]
                blk = lambda b: slice(b * P, b * P + P)

                def ada(j, *khs):
                    for kh in khs:
                        ada_half(sc2, kh, it * 3 + A0["rwkv"] + j)

                def turn(banks, srcs):
                    for bank, src in zip(banks, srcs):
                        for b in range(4):
                            mm = pe.transpose(PS[bank][:, blk(b)], src[:, blk(b)], ident)
                    done(mm)

                def from_keys(d):
                    pairs(5, k_s[d], a_s[d])
                    if d == 1:
                        ada(1, 5, 6)
                    else:
                        ada(0, 1)
                    if d == 1:
                        dve_at("I1")
                    else:
                        pe.wait_ge(rw_dve, it * len(RW_DVE) + len(FIRST_DVE) - 1)
                    pe.sem_inc(pe_gate, 1)
                    for h in range(2):
                        for i, l in enumerate((b_s[d], k_s[d])):
                            for b in range(2):
                                mm = pe.matmul(PS[h][:, (2 * i + b) * P:(2 * i + b) * P + P], l[hs[h], TOK + b * P:TOK + b * P + P], r_s[d][hs[h], blk(b)], start=True, stop=True)
                    done(mm)
                    if d == 0:
                        pe.wait_ge(v_in, it * 16 + 16)
                        turn((7,), (v_t,))
                        ada(0, 2, 3)
                    dve_at(f"Ak{d}")
                    if d == 0:
                        act_at("v")
                    for h in range(2):
                        for b in range(4):
                            mm = pe.matmul(PS[5 + h][:, blk(b)], akT[:, h, b, :], v_tok[:, b, :], start=True, stop=True)
                    done(mm)

                def inverse(d):
                    for l in range(1, len(LEVELS)):
                        for h in range(2):
                            if l == 1:
                                dve_at(f"Ar{d}")
                            else:
                                dve_at(f"X{d}{l - 1}{h}")
                            for b in range(4):
                                mm = pe.matmul(PS[h][:, blk(b)], aT[:, h, b, :], inv[:, h, b, :], start=True, stop=True)
                            done(mm)
                        if l == 1:
                            act_at(f"P1{d}")
                        for h in range(2):
                            dve_at(f"B{d}{l}{h}")
                            for b in range(4):
                                mm = pe.matmul(PS[2 + h][:, blk(b)], bm[:, h, b, :], invT[:, h, b, :], start=True, stop=True)
                                if l < len(LEVELS) - 1:
                                    mm = pe.matmul(PS[6 + h][:, blk(b)], invT[:, h, b, :], bm[:, h, b, :], start=True, stop=True)
                            done(mm)
                        for step in ADA_LEVEL[d][l - 1]:
                            if step[1] is None:
                                ada_final(it * 3 + A0["rwkv"] + step[0])
                            else:
                                ada(*step)
                        if d == 1:
                            first(FIRST_PE[l - 1], it + 1, dve_at, act_at)
                    for h in range(2):
                        dve_at(f"X{d}{len(LEVELS) - 1}{h}")
                        for b in range(4):
                            mm = pe.matmul(PS[h][:, blk(b)], invT[:, h, b, :], atok_r[:, h, b, :], start=True, stop=True)
                    done(mm)

                def chunks(d):
                    act_at(f"WU{d}")
                    dve_at(f"W{d}")
                    pe.sem_inc(pe_gate, 1)
                    for e in range(2):
                        t = hs[e]
                        for h in range(2):
                            for b in range(4):
                                o = PS[2 + e][hs[h], b * CH:b * CH + CH]
                                pe.matmul(o, wu[t, h, b, 0:64], b_tok[t, b, hs[h]], start=True, stop=True)
                                o = PS[2 + e][hs[h], 256 + b * CH:256 + b * CH + CH]
                                pe.matmul(o, b_tok[t, b, hs[h]], wu[t, h, b, 64:P], start=True, stop=False)
                                mm = pe.matmul(o, k_tok[t, b, hs[h]], v_tok[t, b, hs[h]], start=False, stop=True)
                    done(mm)
                    for h in range(2):
                        for b in range(2):
                            mm = pe.matmul(PS[6][hs[h], blk(b)], wu[:, h, 2 + b, 0:64], arx[d][:, h, 0, b, :], start=True, stop=True)
                    done(mm)
                    for h in range(2):
                        for b in range(2):
                            pe.matmul(PS[7][hs[h], blk(b)], v_tok[:, 2 + b, hs[h]], arx[d][:, h, 1, b, :], start=True, stop=False)
                            mm = pe.matmul(PS[7][hs[h], blk(b)], wu[:, h, 2 + b, 64:P], arx[d][:, h, 0, b, :], start=False, stop=True)
                    done(mm)

                def scan(d, between=None):
                    state = lambda i: hd[d][:, SCAN[d][0], :] if i == 1 else zs[:, i, :]
                    for i in range(1, 7):
                        dve_at(f"Q{d}" if i == 1 else f"Z{d}{i - 1}")
                        pe.sem_inc(pe_gate, 1)
                        for h in range(2):
                            mm = pe.matmul(PS[5][hs[h], (i % 2) * CH:(i % 2) * CH + CH], g1t[d][hs[h], SCAN[d][i], :], state(i)[hs[h], :], start=True, stop=True)
                        done(mm)
                        if between:
                            between(i)
                    dve_at(f"Z{d}6")
                    pe.sem_inc(pe_gate, 1)
                    for i in range(4, 8):
                        c = (SCAN[d][i] - 4) * CH
                        for h in range(2):
                            mm = pe.matmul(PS[6][hs[h], TOK + c:TOK + c + CH], state(i)[hs[h], :], qt[d][hs[h], c:c + CH], start=True, stop=True)
                    done(mm)

                def next_direction(d, i):
                    if i == 1:
                        pairs(0, a_s[d], b_s[d])
                    if i == 2:
                        pairs(2, b_s[d], a_s[d])
                    if i in (3, 6):
                        ada(1 if d == 1 else 2, (i // 3) if d == 1 else 3 + i // 3)

                turn((5, 6, 7), (a_s[0], b_s[0], k_s[0]))
                ada(0, 0)
                act_at("tr0")
                from_keys(0)
                inverse(0)
                chunks(0)
                scan(0, lambda i: next_direction(1, i))
                dve_at("Y0")
                turn((5, 7, 0), (a_s[1], b_s[1], k_s[1]))
                ada(1, 3, 4)
                act_at("tr1")
                from_keys(1)
                inverse(1)
                act_at("w1")
                chunks(1)
                scan(1, lambda i: next_direction(0, i))
                ada(2, 6)
                dve_at("Y1")
                done(pe.matmul(PS[0][:, 0:TOK], bmean, yacc[:, :], start=True, stop=True))
                ada(2, 7)
                ada_final(it * 3 + A0["rwkv"] + 2)
                dve_at("sq")
                done(pe.matmul(PS[1][:, 0:TOK], bmean, fin[:, 1, :], start=True, stop=True))
                done(pe.matmul(PS[0][:, 0:TOK], bones, bonus[:, :], start=True, stop=True))
                pe.wait_ge(rw_in2, it * 32 + 32)
                for k in range(2):
                    mm = pe.matmul(PS[0][:, TOK:T2], g2s[:, k, :], gl[:, k, :], start=(k == 0), stop=(k == 1))
                done(mm)
            pe.wait_ge(rw_dve, RW_END)
            with pe.Fori(0, 8) as it:
                seg(C0["gate"] + it * 16, 0, 16, B0["gate"] + it * 4, 4, h1)
            for name, n, xh, xl, split in (("rproj", 8, yhi, ylo, 0), ("mproj", 16, ohi, olo, 2), ("wout", 16, mhi, mlo, 6)):
                x_ = rows(lambda k: xh[:, k, :], lambda k: xl[:, k, :], TOK)
                with pe.Fori(0, 4) as it:
                    seg(C0[name] + it * n, 0, n, B0[name] + it * 4, 4, x_, parts=(split, 4))
            norm(DC, TOK)
            norm(DC, TOK)

            f1 = rows(lambda k: fhi[:, k, :], lambda k: flo[:, k, :], TOK)
            f1_up = rows(lambda k: fhi[:, k, :], lambda k: flo[:, k, :], TOK, 4)
            ud = [rows(lambda k: uhi[:, k, :], lambda k: ulo[:, k, :], TOK, b) for b in (4, 0)]

            def down(c0, lc0, g, gate_b=None):
                pe.wait_ge(u_lo, g * 4 + 4)
                free = [False, gate_b is not None and (lambda m: pe.wait_ge(blk_free, gate_b + m + 1)),
                        lambda m: pe.wait_ge(dn_free, g * 16 + m + 1), lambda m: pe.wait_ge(dn_free, g * 16 + 4 + m + 1)]
                for n in range(4):
                    seg(c0, lc0 + 4 * n, 4, 0, 4, ud[n % 2], None, free[n])

            seg(C0["ffn0"], 0, 16, B0["ffn0"], 4, f1, ready=DC + 8)
            seg(C0["ffn0"], 16, 16, B0["ffn0"] + 4, 4, f1_up, None, False)
            with pe.Fori(0, 10) as it:
                c, b = C0["ffn"] + it * 48, B0["ffn"] + it * 8
                seg(c, 0, 16, b, 4, f1, None, False, between=lambda k: k == 3 and pe.wait_ge(blk_free, b))
                down(c, 16, it, b)
                seg(c, 32, 16, b + 4, 4, f1_up, None, lambda m: pe.wait_ge(dn_free, it * 16 + 8 + m + 1),
                    between=lambda k: k == 3 and pe.wait_ge(dn_free, it * 16 + 16))
            down(C0["ffn1"], 0, 10)
            pe.wait_ge(dn_free, 160 + 12)

            pe.wait_ge(crow_in, 32)
            for d in range(DC):
                if d >= 2:
                    pe.wait_ge(tr_out, DC + d - 1)
                for t in range(2):
                    tr = pe.transpose(PS[6 + d % 2][:, t * P:t * P + P], crow[:, t, d * P:d * P + P], ident)
                tr.then_inc(tr_done, 1)
            norm(DC, TOK)
            pe.wait_ge(lam_pr, 1)
            pe.matmul(PS[7][:, 256:260], ones, lam[:, 0:4], start=True, stop=True).then_inc(lam_mm, 1)
            for l in range(2):
                norm(DC, T2)
                hl = h2 if l == 0 else h1
                T = T2 if l == 0 else TOK
                t0 = T2 - T
                if l == 0:
                    pe.wait_ge(dn_free, 176)

                def v_rows(m, k, slot):
                    xh, xl = hhi[:, m // 2, k, (m % 2) * P:(m % 2) * P + P], hlo[:, m // 2, k, (m % 2) * P:(m % 2) * P + P]
                    return [(xh, whi[:, slot, :]), (xh, wlo[:, slot, :]), (xl, whi[:, slot, :])], PS[m][:, :], True

                for it in range(2):
                    seg(C0[f"poolv{l}"] + it * 16, 0, 16, B0[f"poolv{l}"] + it * 4, 4, hl, ready=(2 + l) * DC + 8 if it == 0 else None)
                    pe.wait_ge(pw_in, 16 * l + 16)
                    for g in range(2):
                        pe.wait_ge(pl_done, 8 * l + it * 4 + g * 2 + 2)
                        if 4 * l + it * 2 + g > 0:
                            pe.wait_ge(pm_done, 8 * l + it * 4 + g * 2)
                        for j in range(2):
                            for k in range(2):
                                mm = pe.matmul(PS[5 + j][:, 0:T], pw[:, it * 2 + g, k, j * P:j * P + P], pl[:, 2 * g + k, 0:T], start=(k == 0), stop=(k == 1))
                        mm.then_inc(pw_mm, 1)
                with pe.Fori(0, 2) as it:
                    c, b = C0[f"qkv{l}"] + it * 48, B0[f"qkv{l}"] + it * 12
                    done = lambda ins: ins.then_inc(at_pe[l], 1)
                    dve_at = lambda n: pe.wait_ge(at_dve[l], at(AT_DVE[l], n, it))
                    act_at = lambda n: pe.wait_ge(at_act[l], at(AT_ACT[l], n, it))
                    seg(c, 0, 16, b, 4, hl)
                    seg(c, 16, 16, b + 4, 4, h2)
                    def norms(k):
                        for b in {4: (0, 1, 2), 8: (3, 4, 5), 12: (6, 7)}.get(k, ()):
                            pe.wait_ge(blk_free, B0[f"qkv{l}"] + it * 12 + b + 1)
                            if b >= 3:
                                dve_at(f"t{b - 3}")
                            done(pe.matmul(PS[(4, 6, 7)[b % 3]][:, 0:TOK], rotw[:, b // 4, :], qk[:, b, TOK:T2], start=True, stop=True))
                            act_at(f"sq{b}")
                            j = 32 * (b % 4)
                            done(pe.matmul(PS[5][j:j + 32, :], H("sum_k" if b >= 4 else "sum_q"), sq2[:, b % 4, :], start=b < 4, stop=b >= 4,
                                           tile_position=(0, j), skip_group_check=True))
                    pe.wait_ge(hcon_in, 16)
                    pe.wait_ge(rotw_ok, l + 1)
                    seg(c, 32, 16, b + 8, 4, v_rows, between=norms)
                    pe.wait_ge(blk_free, b + 12)
                    dve_at("rc")
                    for i, b in enumerate(QK_HEADS):
                        ts = slice(t0 if b < 4 else 0, T2)
                        rows_ = slice(32 * (b % 4), 32 * (b % 4) + 32)
                        if i >= 4:
                            dve_at(f"f{QK_HEADS[i - 4]}")
                        done(pe.matmul(PS[4 + i % 4][:, ts], H("spread_k" if b >= 4 else "spread_q", rows_), rs2[rows_, ts], start=True, stop=True,
                                       tile_position=(32 * (b % 4), 0)))
                    units = UNITS[l]

                    def scores(u):
                        h, t = units[u]
                        if t == TILES[l][0]:
                            dve_at(f"f{4 + h}")
                        if u == 2:
                            dve_at("f7")
                        if u >= 3:
                            act_at(f"e{u - 3}")
                        pe.sem_inc(pe_gate, 1)
                        nk = TOK if t < 2 else T2
                        for n in range(2):
                            r = slice(64 * n, 64 * n + 64)
                            mm = pe.matmul(PS[2 * (u % 3) + n][:, 0:nk], qk[r, h, t * P:t * P + P], qk[r, 4 + h, 0:nk], start=True, stop=True)
                        done(mm)

                    def turn(u):
                        dve_at(f"a{u}")
                        for kt in range(2 if units[u][1] < 2 else 4):
                            tr = pe.transpose(PS[6][:, kt * P:kt * P + P], pr[:, u % 3, 0, kt * P:kt * P + P], ident)
                        done(tr)

                    def values(u):
                        h, t = units[u]
                        nk = 2 if t < 2 else 4
                        act_at(f"aT{u}")
                        if t == TILES[l][0] and h >= 1:
                            act_at(f"o{h - 1}")
                        for kt in range(nk):
                            mm = pe.matmul(PS[7][:, t * P:t * P + P], v2[:, kt, h * P:h * P + P], aTs[:, u % 2, kt, :], start=(kt == 0), stop=(kt == nk - 1))
                        done(mm)

                    for u in range(-2, len(units) + 1):
                        if u + 2 < len(units):
                            scores(u + 2)
                        if u >= 1:
                            values(u - 1)
                        if 0 <= u < len(units):
                            turn(u)
                    act_at("o3")
                    for h in range(4):
                        mm = pe.matmul(PS[4][32 * h:32 * h + 32, t0:T2], H("sum_o"), qk[:, h, t0:T2], start=True, stop=True, tile_position=(0, 32 * h))
                    done(mm)
                    dve_at("rco")
                    for h in range(4):
                        rows_ = slice(32 * h, 32 * h + 32)
                        done(pe.matmul(PS[h][:, t0:T2], H("spread_o", rows_), rs2[rows_, t0:T2], start=True, stop=True, tile_position=(32 * h, 0)))
                    pe.wait_ge(at_dve[l], it * len(AT_DVE[l]) + len(AT_DVE[l]))
                for name in ("poolg", "attng"):
                    with pe.Fori(0, 2) as it:
                        seg(C0[f"{name}{l}"] + it * 16, 0, 16, B0[f"{name}{l}"] + it * 4, 4, hl)
                xm = rows(lambda k: mixhi[:, k, t0:T2], lambda k: mixlo[:, k, t0:T2], T)
                with pe.Fori(0, 4) as it:
                    seg(C0[f"out{l}"] + it * 16, 0, 16, B0[f"out{l}"] + it * 4, 4, xm, parts=(10 + 8 * l, 2))
            pe.wait_ge(blk_free, B0["out1"] + 16)
            for d in range(DC):
                for t in range(2):
                    i = 2 * d + t
                    if i >= 2:
                        pe.wait_ge(fin_cp, i - 1)
                    pe.transpose(PS[6 + t][:, 0:P], xall[:, d, TOK + t * P:TOK + t * P + P], ident).then_inc(fin_tr, 1)

        @block.scalar
        def _(act):
            own = Own(act, act_own)

            def hi(c0, lcs, width=N):
                for lc in lcs:
                    c = c0 + lc
                    if lc % 2 == 0:
                        act.wait_ge(raw_in[(lc // 2) % RAW], 2 * c0 + 16 * (lc // 8 + 1))
                    if not isinstance(c, int) or c >= HL:
                        act.wait_ge(w_used, c - HL + 1)
                    act.activation(whi[:, lc % HL, 0:width], raw[:, (lc // 2) % RAW, lc % 2, 0:width], ACT.Copy).then_inc(w_hi, 1)

            def ada_take(g):
                act.wait_ge(ada_used, g * 8 + 8)
                act.activation(ada_sb[:, :], PS[4][:, 0:256], ACT.Copy).then_inc(ada_out, 1)

            def block_done(c_end, d0, m, nblk):
                if m < nblk - 1:
                    act.wait_ge(blk_done, d0 + m + 1)
                else:
                    act.wait_ge(w_used, c_end)

            nq, nn, na = [0], [0], [0]

            def norm(src, n, T, width, ready=None):
                sq, rs = nsq_of[nn[0]], nrs_of[nn[0]]
                for k in range(n):
                    if ready:
                        ready(k)
                    if nq[0] >= 2:
                        act.wait_ge(n_mm, nq[0] - 1)
                    act.activation(sq[:, nq[0] % 2, 0:T], src(k), ACT.Square).then_inc(n_sq, 1)
                    nq[0] += 1
                act.wait_ge(n_mm, nq[0])
                act.activation(rs[:, 0:T], PS[5][:, 0:T], ACT.Sqrt, bias=C("eps", 0, 1), scale=1.0 / width).then_inc(n_std, 1)
                nn[0] += 1

            def split(n, T, buf, dst, after=None):
                for k in range(n):
                    act.wait_ge(n_f32, na[0] + 1)
                    act.activation(dst(k), like(buf[:, 1 + na[0] % 2, 0:T], dst(k)), ACT.Copy).then_inc(n_hi, 1)
                    na[0] += 1
                    if after is not None and k >= 2:
                        hi(after, [LA + k - 2])

            act.wait_ge(const_in, 48)
            act.wait_ge(sc_zero, 2)
            act.activation(sc1[:, :, 0:2], cT[:, 0, :, :], ACT.Silu).then_inc(sc_ready, 1)
            act.activation(sc2[:, :, 0:2], cT[:, 1, :, :], ACT.Silu).then_inc(sc_ready, 1)
            for d in range(DC):
                act.wait_ge(tr_done, d + 1)
                act.activation(xT[:, d, :], PS[6 + d % 2][:, :], ACT.Copy).then_inc(tr_out, 1)
            norm(lambda k: xT[:, k, :], DC, T2, D, lambda k: act.wait_ge(tr_out, k + 1))
            with act.Fori(0, ADA_HEAD) as it:
                ada_take(it)
            hi(0, range(LA))
            c = C0["ckv"]
            split(DC, T2, nap0, lambda k: hhi[:, :, k, :], c)

            hi(c, range(LA + 14, 16 + LA))
            ada_take(A0["ckv"])
            act.wait_ge(x_saved, 16)
            for m in range(4):
                block_done(c + 16, D1["ckv"], m, 4)
                act.activation(ckv[:, m, :], PS[m][:, :], ACT.Copy).then_inc(blk_free, 1)
            c = C0["cq"]
            hi(c, range(LA, 16))
            hi(c, range(16, 16 + LA), P)
            for m in range(4):
                block_done(c + 16, D1["cq"], m, 4)
                act.activation(cq[:, m, :], PS[m][:, 0:TOK], ACT.Copy).then_inc(blk_free, 1)
            c = C0["kpe"]
            hi(c, range(LA, 16), P)
            hi(c, range(16, 16 + LA))
            ada_take(A0["kpe"])
            norm(lambda k: ckv[:, k, :], 4, T2, 512, lambda k: act.wait_ge(blk_free, B0["ckv"] + k + 1))
            act.wait_ge(w_used, c + 16)
            act.activation(kpe[:, :], PS[0][:, :], ACT.Copy).then_inc(blk_free, 1)
            norm(lambda k: cq[:, k, :], 4, TOK, 512, lambda k: act.wait_ge(blk_free, B0["cq"] + k + 1))
            split(4, T2, nap1, lambda k: ckvhi[:, k, :])
            split(4, TOK, nap1, lambda k: cqhi[:, k, :])

            with act.Fori(0, 8) as it:
                c = C0["mla"] + it * 8
                d0 = D1["mla"] + it * 7
                hi(c, range(LA, 4))
                hi(c, range(4, 4 + LA), 384)
                act.wait_ge(n_lo, DC + 8)
                for m, dst in enumerate((k_sb[:, 0, :], k_sb[:, 1, :], v_sb[:, 0:2, :], v_sb[:, 2:4, :])):
                    if m == 3:
                        act.wait_ge(w_used, c + 4)
                    else:
                        act.wait_ge(blk_done, d0 + (1, 2, 4)[m])
                    act.activation(dst, PS[m][:, :], ACT.Copy).then_inc(blk_free, 1)
                hi(c, range(4 + LA, 8), 384)
                hi(c, range(8, 8 + LA))
                for m, dst in enumerate((qn[:, 0, :], qn[:, 1, :], qraw[:, :])):
                    if m == 2:
                        act.wait_ge(w_used, c + 8)
                    else:
                        act.wait_ge(blk_done, d0 + 5 + m + 1)
                    act.activation(dst, PS[m][:, 0:TOK], ACT.Copy).then_inc(blk_free, 1)

                def exp(u):
                    act.wait_ge(mla_dve, at(MLA_DVE, f"nmx{u}", it))
                    act.activation(prob[:, u, :], PS[u % 2][:, :], ACT.Exp, bias=smx[:, 4 + u:5 + u], scale=ATTN_SCALE,
                                   accum_out=smx[:, 8 + u:9 + u]).then_inc(mla_act, 1)

                def turned(u):
                    act.wait_ge(mla_pe, at(MLA_PE, f"T{u}", it))
                    act.activation((probT, probT2)[u // 2][:, :, (u % 2) * P:(u % 2) * P + P],
                                   PS[6][:, :].rearrange("p (k q) -> p k q", q=P), ACT.Copy).then_inc(mla_act, 1)

                exp(0)
                exp(1)
                exp(2)
                turned(0)
                exp(3)
                turned(1)
                turned(2)
                turned(3)
                ada_take(A0["mla"] + it)

            def shifted(c, d0, m, nblk, latents=False, end=16, n=None):
                block_done(c + end, d0, m, nblk)
                act.wait_ge(sh_done, n + 1 - (m if nblk == 4 else 2 + m))
                if latents:
                    act.activation(pad[:, m, 1, 1:TOK + 1], PS[m][:, 0:TOK], ACT.Copy).then_inc(blk_free, 1)
                else:
                    act.activation(pad[:, m, :, 1:TOK + 1], PS[m][:, :].rearrange("p (s t) -> p s t", t=TOK), ACT.Copy).then_inc(blk_free, 1)

            with act.Fori(0, 4) as it:
                c = C0["kv"] + it * 16
                hi(c, range(LA, 16 + LA))
                ada_take(A0["kv"] + it)
                for m in range(4):
                    shifted(c, D1["kv"] + it * 3, m, 4, n=it * 4 + m)
            with act.Fori(0, 2) as it:
                c = C0["r"] + it * 16
                hi(c, range(LA, 16 + LA))
                for m in range(4):
                    shifted(c, D1["r"] + it * 3, m, 4, True, n=it * 4 + 16 + m)
            c = C0["lora"]
            hi(c, range(LA, 16))
            hi(c, range(16, 16 + LA), 256)
            ada_take(A0["lora"])
            for m in range(4):
                shifted(c, D1["lora"], m, 4, n=24 + m)
            c = C0["gl"]
            hi(c, range(LA, 16), 256)
            hi(c, range(16, 16 + LA))
            ada_take(A0["gl"])
            for m in range(2):
                shifted(c, D1["gl"], m, 2, True, n=28 + m)
            act.wait_ge(sh_done, 31)
            for d in range(2):
                act.activation(wl[0:LORA, d, :], wl[0:LORA, d, :], ACT.Tanh).then_inc(lora_act, 1)
            for m in range(2):
                act.activation(gl[:, m, :], gl[:, m, :], ACT.Sigmoid).then_inc(lora_act, 1)

            done = lambda ins: ins.then_inc(rw_act, 1)

            def decays(d, dve_at):
                dve_at("kk" if d == 0 else "L1")
                act.activation(e_ex[d][:, :], l_ex[d][:, :], ACT.Exp, scale=-DECAY_SCALE)
                act.activation(e_in[d][:, :], l_in[d][:, :], ACT.Exp, scale=DECAY_SCALE)
                act.activation(r_s[d][:, :], l_in[d][:, TOK:T2], ACT.Exp, scale=-DECAY_SCALE)
                done(act.activation(dec[d][:, :], tot[d][:, :], ACT.Exp, scale=-DECAY_SCALE))

            def first(p, pe_at, dve_at):
                act.wait_ge(rw_in, p * 80 + 80)
                for step in FIRST_ACT[:-1]:
                    if step == "kkrt":
                        pe_at("kksum")
                        done(act.activation(e_in[0][:, :], PS[5][:, :], ACT.Sqrt))
                    else:
                        i = ("w0", "w1", "a0", "a1").index(step)
                        pe_at(step)
                        done(act.activation((sig if i < 2 else icl)[:, i % 2, :], PS[5][:, :], ACT.Sigmoid, bias=pv[:, i:i + 1]))

            first(0, lambda n: act.wait_ge(rw_pe, at(FIRST_PE, n)), lambda n: act.wait_ge(rw_dve, at(FIRST_DVE, n)))
            decays(0, lambda n: act.wait_ge(rw_dve, at(FIRST_DVE, n)))
            with act.Fori(0, 8) as it:
                pe_at = lambda n: act.wait_ge(rw_pe, at(RW_PE, n, it, len(FIRST_PE)))
                dve_at = lambda n: act.wait_ge(rw_dve, at(RW_DVE, n, it, len(FIRST_DVE)))
                b4 = lambda bank: PS[bank][:, :].rearrange("p (b c) -> p b c", c=P)

                def turned(d, a, b, k):
                    pe_at(f"tr{d}")
                    act.activation(atok_r[:, :, :, 0:64].rearrange("p h b c -> p b h c"), PS[a][:, :].rearrange("p (b h c) -> p b h c", h=2, c=64), ACT.Copy)
                    act.activation(b_tok[:, :, :], b4(b), ACT.Copy)
                    done(act.activation(k_tok[:, :, :], b4(k), ACT.Copy))
                    if d == 0:
                        pe_at("trv")
                        done(act.activation(v_tok[:, :, :], b4(7), ACT.Copy))
                    pe_at(f"P1{d}")
                    act.activation(atok_r[:, 0, :, 64:P], b4(5)[:, :, 0:64], ACT.Copy)
                    done(act.activation(atok_r[:, 1, :, 64:P], b4(6)[:, :, 64:P], ACT.Copy))

                def solved(d):
                    pe_at(f"WU{d}")
                    done(act.activation(wu[:, 0, :, :], b4(0), ACT.Copy))

                turned(0, 5, 6, 7)
                decays(1, dve_at)
                ada_take(it * 3 + A0["rwkv"])
                solved(0)
                turned(1, 5, 7, 0)
                ada_take(it * 3 + A0["rwkv"] + 1)
                first(it + 1, pe_at, dve_at)
                solved(1)
                decays(0, dve_at)
                ada_take(it * 3 + A0["rwkv"] + 2)
                pe_at("var")
                done(act.activation(yacc[:, :], PS[1][:, 0:TOK], ACT.Sqrt, bias=C("eps", 1, 2)))

            def split_hi(src, dst, ready=None, n=4):
                for g in range(src.shape[1] // n):
                    if ready:
                        ready(g)
                    act.activation(dst[:, n * g:n * g + n, :], src[:, n * g:n * g + n, :], ACT.Copy).then_inc(s_hi, 1)

            act.wait_ge(rw_dve, RW_END)
            split_hi(y_all, yhi)
            for half, dst in enumerate((g_rwkv, g_mla)):
                with act.Fori(0, 4) as it:
                    c, d0 = C0["gate"] + half * 64 + it * 16, D1["gate"] + half * 12 + it * 3
                    hi(c, range(LA, 16 + LA))
                    for m in range(4):
                        block_done(c + 16, d0, m, 4)
                        act.activation(dst[:, bass.ds(it * 4 + m, 1), :], PS[m][:, 0:TOK].unsqueeze(1), ACT.Sigmoid,
                                       bias=Vd("gate_b", it * 4 + 16 * half + m)).then_inc(blk_free, 1)
            act.wait_ge(w_used, C0["rproj"])
            act.wait_ge(o_in, 16)
            split_hi(oT, ohi)
            for name, n in (("rproj", 8), ("mproj", 16)):
                with act.Fori(0, 4) as it:
                    hi(C0[name] + it * n, range(LA, n + LA))
            split_hi(mrg, mhi, lambda g: act.wait_ge(mg_done, g + 1 if g < 3 else 4))
            with act.Fori(0, 4) as it:
                c = C0["wout"] + it * 16
                hi(c, range(LA, 16 + LA))
                for m in range(4):
                    block_done(c + 16, D1["wout"] + it * 3, m, 4)
                    act.activation(wo[:, bass.ds(it * 4 + m, 1), :], PS[m][:, 0:TOK].unsqueeze(1), ACT.Copy).then_inc(blk_free, 1)
            norm(lambda k: wo[:, k, :], DC, TOK, D, lambda k: act.wait_ge(blk_free, B0["wout"] + k + 1))
            norm(lambda k: x1[:, k, :], DC, TOK, D, lambda k: act.wait_ge(x1_done, k + 1))
            split(DC, TOK, nap3, lambda k: fhi[:, k, :], C0["ffn0"])

            def gate_out(c_end, d0):
                for m in range(4):
                    block_done(c_end, d0, m, 4)
                    act.activation(gpad[:, m, 1:TOK + 1], PS[m][:, 0:TOK], ACT.Copy).then_inc(blk_free, 1)

            def gelu(g, c):
                hi(c, range(16 + LA, 20 + LA))
                for m in range(4):
                    act.wait_ge(cv_done, g * 4 + m + 1)
                    act.activation(ge[:, m, :], ge[:, m, :], ACT.Gelu_apprx_tanh, bias=Vd("conv_b", g * 4 + m)).then_inc(ge_done, 1)
                    hi(c, range(20 + 2 * m + LA, 22 + 2 * m + LA))

            def u_split(b):
                for m in range(4):
                    act.wait_ge(blk_free, b + m + 1)
                    act.activation(uhi[:, m, :], ge[:, m, :], ACT.Copy).then_inc(u_hi, 1)

            c, d0 = C0["ffn0"], D1["ffn0"]
            hi(c, range(LA + 14, 16 + LA))
            act.wait_ge(ff_zero, 1)
            gate_out(c + 16, d0)
            gelu(0, c)
            hi(c, range(28 + LA, 32 + LA))
            u_split(B0["ffn0"] + 4)
            with act.Fori(0, 10) as it:
                c, d0 = C0["ffn"] + it * 48, D1["ffn"] + it * 18
                hi(c, range(LA, 16 + LA))
                gate_out(c + 16, d0)
                gelu(it + 1, c)
                hi(c, range(28 + LA, 48 + LA))
                u_split(B0["ffn"] + it * 8 + 4)
            hi(C0["ffn1"], range(LA, 16 + LA))

            for d in range(DC):
                act.wait_ge(tr_done, DC + d + 1)
                act.activation(xall[:, d, 0:TOK], PS[6 + d % 2][:, 0:TOK], ACT.Copy).then_inc(tr_out, 1)
            norm(lambda k: yffn[:, k, :], DC, TOK, D, lambda k: act.wait_ge(dn_free, 160 + k + 1))
            act.wait_ge(lam_mm, 1)
            act.activation(lam[:, 0:4], PS[7][:, 256:260], ACT.Exp).then_inc(lam_e, 1)
            act.wait_ge(tr_out, 2 * DC)
            for l in range(2):
                if l == 0:
                    norm(lambda k: xall[:, k, :], DC, T2, D, lambda k: act.wait_ge(x1_done, DC + k + 1))
                else:
                    norm(lambda k: xall[:, k, :], DC, T2, D, lambda k: act.wait_ge(blk_free, B0["out0"] + k + 1))
                split(DC, T2, nap6, lambda k: hhi[:, :, k, :], C0[f"poolv{l}"])
                T = T2 if l == 0 else TOK
                t0 = T2 - T
                units = UNITS[l]
                act.wait_ge(x2_saved, 16 * l + 16)
                act.wait_ge(xp_zero, l + 1)
                for it in range(2):
                    c = C0[f"poolv{l}"] + it * 16
                    hi(c, range(LA if it else LA + 14, 16 + LA))
                    for m in range(4):
                        n = 8 * l + it * 4 + m
                        block_done(c + 16, D1[f"poolv{l}"] + 3 * it, m, 4)
                        if it * 4 + m >= 2:
                            act.wait_ge(pl_done, n - 1)
                        if l == 0:
                            act.activation(xp[:, m % 2, :, 16:16 + TOK], PS[m][:, :].rearrange("p (s t) -> p s t", t=TOK), ACT.Copy).then_inc(blk_free, 1)
                        else:
                            act.activation(xp[:, m % 2, 1, 16:16 + TOK], PS[m][:, 0:TOK], ACT.Copy).then_inc(blk_free, 1)
                act.wait_ge(pm_done, 8 * l + 8)
                with act.Fori(0, 2) as it:
                    c, d0, b = C0[f"qkv{l}"] + it * 48, D1[f"qkv{l}"] + it * 9, B0[f"qkv{l}"] + it * 12
                    done = lambda ins: ins.then_inc(at_act[l], 1)
                    pe_at = lambda n: act.wait_ge(at_pe[l], at(AT_PE[l], n, it))
                    dve_at = lambda n: act.wait_ge(at_dve[l], at(AT_DVE[l], n, it))
                    def squares(ns):
                        for n in ns:
                            ts = slice(t0 if n < 4 else 0, T2)
                            act.wait_ge(blk_free, b + n + 1)
                            if n >= 4:
                                pe_at(f"n{n - 4}")
                            done(act.activation(sq2[:, n % 4, ts], qk[:, n, ts], ACT.Square))

                    for i in range(3):
                        if i < 2:
                            hi(c, range(16 * i + LA, 16 * i + 16 + LA))
                        else:
                            if l:
                                dve_at("z")
                            squares(range(4))
                            hi(c, range(32 + LA, 41))
                            squares((4, 5))
                            hi(c, range(41, 45))
                            squares((6, 7))
                            hi(c, range(45, 48))
                            pe_at("n7")
                            done(act.activation(rs2[:, :], PS[5][:, :], ACT.Sqrt, bias=C("eps", 0, 1), scale=1.0 / 64))
                            hi(c, range(48, 48 + LA))
                        for m in range(4):
                            block_done(c + 16 * i + 16, d0 + 3 * i, m, 4)
                            ts = slice(t0 if i == 0 else 0, T2)
                            dst = qk[:, 4 * i + m, ts] if i < 2 else v2[:, m, :]
                            act.activation(dst, PS[m][:, 0:dst.shape[1]], ACT.Copy).then_inc(blk_free, 1)
                    act.wait_ge(blk_free, b + 12)

                    def exp(u):
                        nk = TOK if units[u][1] < 2 else T2
                        dve_at(f"mx{u}")
                        if u >= 3:
                            pe_at(f"T{u - 3}")
                        s, k = 8 * (u % 3), u % 3
                        act.activation(pr[:, k, 0, 0:nk], PS[2 * k][:, 0:nk], ACT.Exp, bias=smx2[:, s + 2:s + 3], scale=DIFF_SCALE,
                                       accum_out=smx2[:, s + 4:s + 5])
                        done(act.activation(pr[:, k, 1, 0:nk], PS[2 * k + 1][:, 0:nk], ACT.Exp, bias=smx2[:, s + 3:s + 4], scale=DIFF_SCALE,
                                            accum_out=smx2[:, s + 5:s + 6]))

                    for u in range(-2, len(units) + 1):
                        if u >= 1 and last_of(l, u - 1):
                            h = units[u - 1][0]
                            pe_at(f"PV{u - 1}")
                            act.activation(mix[:, bass.ds(it * 4 + 8 + h, 1), t0:T2], PS[7][:, t0:T2].unsqueeze(1), ACT.Copy)
                            done(act.activation(qk[:, h, t0:T2], PS[7][:, t0:T2], ACT.Square))
                        if 0 <= u < len(units):
                            nk = 2 if units[u][1] < 2 else 4
                            pe_at(f"T{u}")
                            done(act.activation(aTs[:, u % 2, 0:nk, :], PS[6][:, 0:nk * P].rearrange("p (k q) -> p k q", q=P), ACT.Copy))
                        if u + 2 < len(units):
                            exp(u + 2)
                    pe_at("no")
                    done(act.activation(rs2[:, t0:T2], PS[4][:, t0:T2], ACT.Sqrt, bias=C("eps", 0, 1), scale=1.0 / P))
                act.wait_ge(at_dve[l], 2 * len(AT_DVE[l]))
                for i, name in enumerate(("poolg", "attng")):
                    with act.Fori(0, 2) as it:
                        c = C0[f"{name}{l}"] + it * 16
                        hi(c, range(LA, 16 + LA))
                        for m in range(4):
                            block_done(c + 16, D1[f"{name}{l}"] + 3 * it, m, 4)
                            if m >= 2:
                                act.wait_ge(sg_done, it * 4 + 16 * l + 8 * i + m - 1)
                            act.activation(stmp[:, m % 2, 0:T], PS[m][:, 0:T], ACT.Silu).then_inc(blk_free, 1)
                        act.wait_ge(sg_done, it * 4 + 16 * l + 8 * i + 4)
                act.wait_ge(w_used, C0[f"out{l}"])
                split_hi(mix[:, :, t0:T2], mixhi[:, :, t0:T2], lambda g: act.wait_ge(sg_done, 16 * l + 16), 2)
                with act.Fori(0, 4 if l == 0 else 3) as it:
                    hi(C0[f"out{l}"] + it * 16, range(LA, 16 + LA))
            hi(C0["out1"] + 48, range(LA, 16))
            for d in range(DC):
                for t in range(2):
                    act.wait_ge(fin_tr, 2 * d + t + 1)
                    act.activation(orow[:, t, d * P:d * P + P], PS[6 + t][:, 0:P], ACT.Copy).then_inc(fin_cp, 1)

        @block.vector
        def _(dve):
            own = Own(dve, dve_own)

            def lo(c0, lcs, width=N):
                for lc in lcs:
                    dve.wait_ge(w_hi, c0 + lc + 1)
                    dve.tensor_tensor(wlo[:, lc % HL, 0:width], raw[:, (lc // 2) % RAW, lc % 2, 0:width],
                                      whi[:, lc % HL, 0:width].bitcast(F32), ALU.subtract).then_inc(w_lo, 1)

            def ada_bias(g, mod, bias, n):
                dve.wait_ge(ada_fin, g + 1)
                dve.tensor_tensor(mod[:, bass.ds(n, 4), :], PS[4][:, 256:264].rearrange("p (m j) -> p m j", j=2),
                                  Vd(bias, n, 4).unsqueeze(2).to_broadcast([P, 4, 2]), ALU.add).then_inc(mod_ready, 1)

            nn, na = [0], [0]

            def norm_scale():
                rs = nrs_of[nn[0]]
                dve.wait_ge(n_std, nn[0] + 1)
                own.then(dve.reciprocal(rs[:, 0:nt_of[nn[0]]], rs[:, 0:nt_of[nn[0]]]))
                nn[0] += 1
                return rs

            def rest(T, buf, dst, upto_):
                while rest.n < upto_:
                    k = rest.n
                    dve.wait_ge(n_hi, k + 1)
                    d = rest.dst[k]
                    dve.tensor_tensor(d[0], like(buf[:, 1 + k % 2, 0:T], d[0]), d[1].bitcast(F32), ALU.subtract).then_inc(n_lo, 1)
                    rest.n += 1
            rest.n, rest.dst = 0, {}

            def modulated(n, T, src, buf, rs, shift, hi_of, lo_of, after=None):
                for k in range(n):
                    i = na[0]
                    if i - rest.n >= 2:
                        rest(T, buf, None, i - 1)
                    if i >= 2:
                        dve.wait_ge(n_lo, i - 1)
                    if i >= 1:
                        dve.wait_ge(n_f32, i)
                    own.then(dve.tensor_tensor(buf[:, 0, 0:T], src(k), rs[:, 0:T], ALU.mult))
                    if T == T2:
                        own.then(dve.tensor_scalar(buf[:, 1 + i % 2, 0:TOK], buf[:, 0, 0:TOK], gain[:, k, 1:2], shift(k, 1), ALU.mult, ALU.add))
                        dve.tensor_scalar(buf[:, 1 + i % 2, TOK:T2], buf[:, 0, TOK:T2], gain[:, k, 0:1], shift(k, 0), ALU.mult, ALU.add).then_inc(n_f32, 1)
                    else:
                        dve.tensor_scalar(buf[:, 1 + i % 2, 0:T], buf[:, 0, 0:T], gain[:, k, 0:1], shift(k, 0), ALU.mult, ALU.add).then_inc(n_f32, 1)
                    rest.dst[i] = (lo_of(k), hi_of(k))
                    na[0] += 1
                    if after is not None and k >= 3:
                        lo(after, [LA + k - 3])
                rest(T, buf, None, na[0])
                if after is not None:
                    lo(after, [LA + n - 3])

            def gained(n, T, src, buf, rs, g, hi_of, lo_of):
                for k in range(n):
                    i = na[0]
                    if i - rest.n >= 2:
                        rest(T, buf, None, i - 1)
                    if i >= 2:
                        dve.wait_ge(n_lo, i - 1)
                    dve.scalar_tensor_tensor(buf[:, 1 + i % 2, 0:T], src(k), g(k), rs[:, 0:T], ALU.mult, ALU.mult).then_inc(n_f32, 1)
                    rest.dst[i] = (lo_of(k), hi_of(k))
                    na[0] += 1
                rest(T, buf, None, na[0])

            dve.memset(sc1[:, :, :], 0.0).then_inc(sc_zero, 1)
            dve.memset(sc2[:, :, :], 0.0).then_inc(sc_zero, 1)
            dve.wait_ge(const_in, 48)
            dve.tensor_scalar(mu_keep[:, :], V("mu", 0, 30), -1.0, 1.0, ALU.mult, ALU.add)
            dve.tensor_scalar(mu_half[:, :], V("mu", 0, 30), 0.5, None, ALU.mult)
            rs = norm_scale()
            with dve.Fori(0, ADA_HEAD) as it:
                ada_bias(it, mod1, "b_ada", it * 4)
            dve.wait_ge(mod_ready, ADA_HEAD)
            own.then(dve.scalar_tensor_tensor(gain[:, :, :], mod1[:, 16:32, :], 1.0, V("mix_pre", 0, 16).unsqueeze(2).to_broadcast([P, 16, 2]),
                                              ALU.add, ALU.mult))
            c = C0["ckv"]
            lo(0, range(LA))
            modulated(DC, T2, lambda k: xT[:, k, :], nap0, rs, lambda k, j: mod1[:, k, j:j + 1],
                      lambda k: hhi[:, :, k, :], lambda k: hlo[:, :, k, :], c)
            lo(c, range(LA + 14, 16 + LA))
            ada_bias(A0["ckv"], mod1, "b_ada", A0["ckv"] * 4)
            c = C0["cq"]
            lo(c, range(LA, 16))
            lo(c, range(16, 16 + LA), P)
            c = C0["kpe"]
            lo(c, range(LA, 16), P)
            lo(c, range(16, 16 + LA))
            ada_bias(A0["kpe"], mod1, "b_ada", A0["kpe"] * 4)
            rs = norm_scale()
            gained(4, T2, lambda k: ckv[:, k, :], nap1, rs, lambda k: V("kv_norm", k), lambda k: ckvhi[:, k, :], lambda k: ckvlo[:, k, :])
            rs = norm_scale()
            gained(4, TOK, lambda k: cq[:, k, :], nap1, rs, lambda k: V("q_norm", k), lambda k: cqhi[:, k, :], lambda k: cqlo[:, k, :])
            dve.wait_ge(rope_mm, 1)
            dve.tensor_tensor(ropet[:, 0, :], kpe[:, TOK:T2], cos, ALU.mult)
            own.then(dve.tensor_tensor(ropet[:, 1, :], PS[6][:, 0:TOK], sin, ALU.mult))
            own.then(dve.tensor_tensor(kpe[:, TOK:T2], ropet[:, 0, :], ropet[:, 1, :], ALU.add))
            own.then(dve.memset(qpad[:, :, :], 0.0))
            with dve.Fori(0, 8) as it:
                own.loop(it, 9)
                c = C0["mla"] + it * 8
                lo(c, range(LA, 4))
                lo(c, range(4, 4 + LA), 384)
                lo(c, range(4 + LA, 8), 384)
                lo(c, range(8, 8 + LA))
                dve.wait_ge(mla_pe, at(MLA_PE, "rot", it))
                dve.tensor_tensor(ropet[:, 0, :], qraw[:, :], cos, ALU.mult)
                own.then(dve.tensor_tensor(ropet[:, 1, :], PS[3][:, 0:TOK], sin, ALU.mult))
                dve.tensor_tensor(qpad[0:64, 0, :], ropet[0:64, 0, :], ropet[0:64, 1, :], ALU.add)
                dve.tensor_tensor(qpad[64:P, 1, :], ropet[64:P, 0, :], ropet[64:P, 1, :], ALU.add).then_inc(mla_dve, 1)

                def maximum(u):
                    dve.wait_ge(mla_pe, at(MLA_PE, f"S{u}", it))
                    own.then(dve.reduce_max(smx[:, u:u + 1], PS[u % 2][:, :], axis=AX.X))
                    dve.tensor_scalar(smx[:, 4 + u:5 + u], smx[:, u:u + 1], -ATTN_SCALE, None, ALU.mult).then_inc(mla_dve, 1)

                def normalise(u):
                    dve.wait_ge(mla_act, at(MLA_ACT, f"exp{u}", it))
                    own.then(dve.reciprocal(smx[:, 12 + u:13 + u], smx[:, 8 + u:9 + u]))
                    dve.tensor_scalar(prob[:, u, :], prob[:, u, :], smx[:, 12 + u:13 + u], None, ALU.mult).then_inc(mla_dve, 1)

                def head(h):
                    dve.wait_ge(mla_pe, at(MLA_PE, f"PV{h}", it))
                    dve.tensor_scalar(oT[:, bass.ds(it * 2 + h, 1), :], PS[7][:, 0:TOK].unsqueeze(1), 1.0, None, ALU.mult).then_inc(mla_dve, 1)

                maximum(0)
                maximum(1)
                normalise(0)
                maximum(2)
                normalise(1)
                maximum(3)
                normalise(2)
                normalise(3)
                head(0)
                head(1)
                ada_bias(A0["mla"] + it, mod1, "b_ada", it * 4 + A0["mla"] * 4)
            own.end(8)

            def shift(m, mu, n, dst, latents=False):
                s = slice(1, 2) if latents else slice(0, 2)
                dve.wait_ge(blk_free, n[0])
                src = pad[:, m, s, :]
                own.then(dve.tensor_tensor(sh_a[:, s, :], src[:, :, 0:TOK], src[:, :, 2:TOK + 2], ALU.add))
                own.then(dve.tensor_scalar(sh_a[:, s, :], sh_a[:, s, :], mu_half[:, bass.ds(mu, 1)], None, ALU.mult))
                dve.scalar_tensor_tensor(dst, src[:, :, 1:TOK + 1], mu_keep[:, bass.ds(mu, 1)], sh_a[:, s, :], ALU.mult, ALU.add).then_inc(sh_done, 1)
                dve.wait_ge(sh_done, n[1] + 1)

            both = lambda b: b.rearrange("p (s t) -> p s t", t=TOK)
            own.then(dve.memset(sh_a[:, 0, 0:1], 0.0))
            dve.memset(pad[:, :, :, :], 0.0).then_inc(sh_done, 1)
            with dve.Fori(0, 4) as it:
                own.loop(it, 8)
                c = C0["kv"] + it * 16
                lo(c, range(LA, 16 + LA))
                ada_bias(A0["kv"] + it, mod1, "b_ada", it * 4 + A0["kv"] * 4)
                for m in range(4):
                    if m == 0:
                        dve.wait_ge(sh_free, it + 1)
                    shift(m, it * 4 + 8 + m, (B0["kv"] + it * 4 + m + 1, it * 4 + m + 1), both(sh_out[:, m, :]))
            own.end(4)
            with dve.Fori(0, 2) as it:
                own.loop(it, 8)
                c = C0["r"] + it * 16
                lo(c, range(LA, 16 + LA))
                for m in range(4):
                    if m == 0:
                        dve.wait_ge(sh_free, it + 5)
                    shift(m, it * 4 + m, (B0["r"] + it * 4 + m + 1, it * 4 + 16 + m + 1), sh_out[:, m, 0:TOK].unsqueeze(1), True)
            own.end(2)
            c = C0["lora"]
            lo(c, range(LA, 16))
            lo(c, range(16, 16 + LA), 256)
            ada_bias(A0["lora"], mod1, "b_ada", A0["lora"] * 4)
            for m in range(4):
                shift(m, 24 + m, (B0["lora"] + m + 1, 24 + m + 1), both((wl if m < 2 else al)[:, m % 2, :]))
            c = C0["gl"]
            lo(c, range(LA, 16), 256)
            lo(c, range(16, 16 + LA))
            ada_bias(A0["gl"], mod1, "b_ada", A0["gl"] * 4)
            for m in range(2):
                shift(m, 28 + m, (B0["gl"] + m + 1, 28 + m + 1), gl[:, m, :].unsqueeze(1), True)

            pb = lambda n, h: PS[n + h][:, :].rearrange("p (b c) -> p b c", c=P)
            mask = lambda i: C("masks", i * P, i * P + P).unsqueeze(1).to_broadcast([P, 4, P])
            eye = ident.unsqueeze(1).to_broadcast([P, 4, P])
            TT, TS, STT = dve.tensor_tensor, dve.tensor_scalar, dve.scalar_tensor_tensor

            def sums(d, done, part):
                in3, ex3 = [x[d][:, :].rearrange("p (c t) -> p c t", t=CH) for x in (l_in, l_ex)]
                if part == 0:
                    own.then(dve.tensor_tensor_scan(l_in[d][:, :], C("restart"), sig[:, d, :], 0.0, ALU.mult, ALU.add))
                    return
                own.then(TS(tot[d][:, :], in3[:, :, CH - 1], 1.0, None, ALU.mult))
                if d == 0:
                    done(TT(l_ex[d][:, :], l_in[d][:, :], sig[:, d, :], ALU.subtract), f"L{d}")
                else:
                    own.then(TT(ex3, tot[d][:, :].unsqueeze(2).to_broadcast([P, 8, CH]), in3, ALU.subtract))
                    done(TT(l_in[d][:, :], l_ex[d][:, :], sig[:, d, :], ALU.add), f"L{d}")

            def scaled(d, done, act_at, part):
                if part == 0:
                    act_at(f"E{d}")
                    own.then(STT(a_s[d][:, :], kk[:, :], -1.0, e_ex[d][:, :], ALU.mult, ALU.mult))
                    own.then(TT(b_s[d][:, :], kk[:, :], icl[:, d, :], ALU.mult))
                elif part == 1:
                    own.then(TT(b_s[d][:, :], b_s[d][:, :], e_in[d][:, :], ALU.mult))
                    own.then(TT(k_s[d][:, :], kdir[:, d, :], e_in[d][:, :], ALU.mult))
                else:
                    done(TT(r_s[d][:, :], r_t[:, :], r_s[d][:, :], ALU.mult), f"abk{d}")

            def kk_squares(p, done):
                dve.wait_ge(rw_in, p * 80 + 80)
                own.then(TS(kk[:, :], k_t[:, :], pv[:, 4:5], None, ALU.mult))
                done(TT(e_ex[0][:, :], kk[:, :], kk[:, :], ALU.mult), "kksq")

            def kk_inverse(act_at, q):
                c = slice(q * P, q * P + P)
                if q == 0:
                    act_at("kkrt")
                    own.then(TS(e_in[0][:, :], e_in[0][:, :], 1e-12, None, ALU.max))
                own.then(dve.reciprocal(e_in[0][:, c], e_in[0][:, c]))

            def kk_unit(done):
                done(TT(kk[:, :], kk[:, :], e_in[0][:, :], ALU.mult), "kk")

            def k_direction(act_at, d):
                act_at(f"a{d}")
                own.then(TS(kdir[:, d, :], icl[:, d, :], 1.0, pv[:, 5:6], ALU.subtract, ALU.mult))
                own.then(STT(kdir[:, d, :], kdir[:, d, :], 1.0, k_t[:, :], ALU.add, ALU.mult))

            def mask_a(d, i, pe_at, done):
                h = i // 2
                if i == 0:
                    pe_at(f"A{d}")
                if i % 2 == 0:
                    own.then(TT(inv[:, h, :, :], pb(0, h), mask(M_LEVEL_T if d else M_LEVEL), ALU.mult))
                    return
                t = TT(inv[:, h, :, :], inv[:, h, :, :], eye, ALU.add)
                if i == 1:
                    own.then(t)
                else:
                    done(t, f"I{d}")

            def mask_at(d, h, pe_at, done):
                if h == 0:
                    pe_at(f"AT{d}")
                own.then(TT(aT[:, h, :, :], pb(2, h), mask(M_STRICT + 1 - d), ALU.mult))
                own.then(TT(invT[:, h, :, :], aT[:, h, :, :], mask(M_LEVEL if d else M_LEVEL_T), ALU.mult))
                t = TT(invT[:, h, :, :], invT[:, h, :, :], eye, ALU.add)
                if h == 0:
                    own.then(t)
                else:
                    done(t, f"A{d}")

            def first_done(ins, label):
                ins.then_inc(rw_dve, 1)
                dve.wait_ge(rw_dve, at(FIRST_DVE, label))

            first_act = lambda n: dve.wait_ge(rw_act, at(FIRST_ACT, n))
            kk_squares(0, first_done)
            first_act("w0")
            for part in range(2):
                sums(0, first_done, part)
            for q in range(4):
                kk_inverse(first_act, q)
            kk_unit(first_done)
            for d in range(2):
                k_direction(first_act, d)
            for part in range(3):
                scaled(0, first_done, first_act, part)
            first_pe = lambda n: dve.wait_ge(rw_pe, at(FIRST_PE, n))
            for i in range(4):
                mask_a(0, i, first_pe, first_done)
            for h in range(2):
                mask_at(0, h, first_pe, first_done)
            with dve.Fori(0, 8) as it:
                own.loop(it, RW_OWN)
                step = [0]
                pe_at = lambda n: dve.wait_ge(rw_pe, at(RW_PE, n, it, len(FIRST_PE)))
                act_at = lambda n: dve.wait_ge(rw_act, at(RW_ACT, n, it, len(FIRST_ACT)))

                def done(ins, label):
                    assert RW_DVE[step[0]] == label, (RW_DVE[step[0]], label)
                    step[0] += 1
                    ins.then_inc(rw_dve, 1)
                    dve.wait_ge(rw_dve, at(RW_DVE, label, it, len(FIRST_DVE)))

                def mask_keys(d):
                    pe_at(f"Ak{d}")
                    own.then(TT(akT[:, 0, :, :], pb(5, 0), mask(M_STRICT + 1 - d), ALU.mult))
                    done(TT(akT[:, 1, :, :], pb(5, 1), mask(M_STRICT + 1 - d), ALU.mult), f"Ak{d}")
                    pe_at(f"Ar{d}")
                    ar4 = lambda h: arx[d][:, h, :, :, :].rearrange("p i b c -> p (i b) c")
                    own.then(TT(ar4(0), pb(0, 0), mask(M_INCL + 1 - d), ALU.mult))
                    done(TT(ar4(1), pb(0, 1), mask(M_INCL + 1 - d), ALU.mult), f"Ar{d}")

                def level(d, l, between=None):
                    for h in range(2):
                        pe_at(f"B{d}{l}{h}")
                        done(TT(bm[:, h, :, :], pb(0, h), mask((M_LEVEL_T if d else M_LEVEL) + l), ALU.mult), f"B{d}{l}{h}")
                    if between:
                        between()
                    for h in range(2):
                        pe_at(f"G{d}{l}{h}")
                        t = TT(invT[:, h, :, :], invT[:, h, :, :], pb(2, h), ALU.add)
                        if l < len(LEVELS) - 1:
                            own.then(t)
                            t = TT(inv[:, h, :, :], inv[:, h, :, :], pb(6, h), ALU.add)
                        done(t, f"X{d}{l}{h}")

                def chunks(d, between):
                    pe_at(f"WU{d}")
                    done(TS(wu[:, 1, :, :], pb(0, 1), 1.0, None, ALU.mult), f"W{d}")
                    between()
                    pe_at(f"GH{d}")
                    for e in range(2):
                        g = lambda i: PS[2 + e][:, i * 256:i * 256 + 256].rearrange("p (b c) -> p b c", c=CH)
                        own.then(TT(g1t[d][:, e::2, :], g(0), C("eye64").unsqueeze(1).to_broadcast([P, 4, CH]), ALU.add))
                        t = TT(hd[d][:, e::2, :], g(1), dec[d][:, e::2].unsqueeze(2).to_broadcast([P, 4, CH]), ALU.mult)
                        if e == 0:
                            own.then(t)
                    done(t, f"GH{d}")
                    pe_at(f"Q{d}")
                    done(TT(qt[d][:, :], PS[6][:, 0:TOK], r_s[d][:, :], ALU.add), f"Q{d}")

                def within(d):
                    pe_at(f"YL{d}")
                    if d == 0:
                        own.then(TS(yacc[:, :], PS[7][:, 0:TOK], 1.0, None, ALU.mult))
                    else:
                        own.then(TT(yacc[:, :], yacc[:, :], PS[7][:, 0:TOK], ALU.add))

                def state(d, i):
                    c = SCAN[d][i]
                    pe_at(f"Z{d}{i}")
                    done(STT(zs[:, i + 1, :], PS[5][:, (i % 2) * CH:(i % 2) * CH + CH], dec[d][:, c:c + 1], hd[d][:, c, :], ALU.mult, ALU.add), f"Z{d}{i}")

                def outputs(d):
                    pe_at(f"YZ{d}")
                    done(TT(yacc[:, :], yacc[:, :], PS[6][:, TOK:T2], ALU.add), f"Y{d}")

                def ada(j):
                    ada_bias(it * 3 + A0["rwkv"] + j, mod2, "b_ada_2", it * 12 + 4 * j)

                def scan(d):
                    for i in range(1, 7):
                        state(d, i)
                        if i == 1:
                            within(d)
                        elif i < 6:
                            mask_a(1 - d, i - 2, pe_at, done)

                def second():
                    for part in range(3):
                        scaled(1, done, act_at, part)
                    dve.wait_ge(rw_in2, it * 32 + 32)
                    own.then(TT(bonus[:, :], kdir[:, 0, TOK:T2], kdir[:, 1, TOK:T2], ALU.add))
                    own.then(TT(bonus[:, :], bonus[:, :], r_t[:, :], ALU.mult))
                    done(TS(bonus[:, :], bonus[:, :], pv2[:, 0:1], 0.5, ALU.mult, ALU.mult), "bt")

                def next_pair():
                    for d in range(2):
                        k_direction(act_at, d)
                    for part in range(3):
                        scaled(0, done, act_at, part)

                def first_sum():
                    act_at("w0")
                    sums(0, done, 0)

                mask_keys(0)
                level(0, 1, lambda: sums(1, done, 0))
                sums(1, done, 1)
                level(0, 2)
                level(0, 3)
                level(0, 4)
                ada(0)
                level(0, 5)
                chunks(0, second)
                scan(0)
                outputs(0)
                for h in range(2):
                    mask_at(1, h, pe_at, done)
                mask_keys(1)
                level(1, 1, lambda: kk_squares(it + 1, done))
                ada(1)
                level(1, 2, first_sum)
                sums(0, done, 1)
                level(1, 3, lambda: kk_inverse(act_at, 0))
                kk_inverse(act_at, 1)
                level(1, 4, lambda: kk_inverse(act_at, 2))
                kk_inverse(act_at, 3)
                level(1, 5, lambda: kk_unit(done))
                chunks(1, next_pair)
                scan(1)
                outputs(1)
                pe_at("mean")
                own.then(TT(fin[:, 0, :], yacc[:, :], PS[0][:, 0:TOK], ALU.subtract))
                done(TT(fin[:, 1, :], fin[:, 0, :], fin[:, 0, :], ALU.mult), "sq")
                mask_at(0, 0, pe_at, done)
                ada(2)
                act_at("sd")
                own.then(dve.reciprocal(yacc[:, :], yacc[:, :]))
                own.then(TT(fin[:, 0, :], fin[:, 0, :], yacc[:, :], ALU.mult))
                own.then(TS(fin[:, 0, :], fin[:, 0, :], pv2[:, 1:2], pv2[:, 2:3], ALU.mult, ALU.add))
                pe_at("g")
                own.then(TT(fin[:, 1, :], PS[0][:, 0:TOK], v_t[:, TOK:T2], ALU.mult))
                own.then(TT(fin[:, 0, :], fin[:, 0, :], fin[:, 1, :], ALU.add))
                done(TT(y_all[:, bass.ds(it, 1), :], fin[:, 0, :].unsqueeze(1), PS[0][:, TOK:T2].unsqueeze(1), ALU.mult), "out")
                mask_at(0, 1, pe_at, done)
            own.end(8)
            TT, TS, STT = dve.tensor_tensor, dve.tensor_scalar, dve.scalar_tensor_tensor
            ns = [0]

            def split_lo(src, hi_, lo_, n=4):
                for g in range(src.shape[1] // n):
                    s = slice(n * g, n * g + n)
                    ns[0] += 1
                    dve.wait_ge(s_hi, ns[0])
                    TT(lo_[:, s, :], src[:, s, :], hi_[:, s, :].bitcast(F32), ALU.subtract).then_inc(s_lo, 1)

            def block_done(c_end, d0, m, nblk):
                if m < nblk - 1:
                    dve.wait_ge(blk_done, d0 + m + 1)
                else:
                    dve.wait_ge(w_used, c_end)

            split_lo(y_all, yhi, ylo)
            with dve.Fori(0, 8) as it:
                lo(C0["gate"] + it * 16, range(LA, 16 + LA))
            split_lo(oT, ohi, olo)
            dve.wait_ge(blk_free, B0["rproj"])
            with dve.Fori(0, 4) as it:
                c = C0["rproj"] + it * 8
                lo(c, range(LA, 8 + LA))
                for m in range(4):
                    block_done(c + 8, D1["rproj"] + it * 3, m, 4)
                    n = bass.ds(it * 4 + m, 1)
                    TT(mrg[:, n, :], PS[m][:, 0:TOK].unsqueeze(1), g_rwkv[:, n, :], ALU.mult).then_inc(blk_free, 1)
            dve.wait_ge(blk_free, B0["mproj"])
            with dve.Fori(0, 4) as it:
                own.loop(it, 3)
                c = C0["mproj"] + it * 16
                lo(c, range(LA, 16 + LA))
                for m in range(4):
                    block_done(c + 16, D1["mproj"] + it * 3, m, 4)
                    n = bass.ds(it * 4 + m, 1)
                    TT(g_mla[:, n, :], PS[m][:, 0:TOK].unsqueeze(1), g_mla[:, n, :], ALU.mult).then_inc(blk_free, 1)
                    dve.wait_ge(blk_free, B0["mproj"] + it * 4 + m + 1)
                    t = TT(mrg[:, n, :], mrg[:, n, :], g_mla[:, n, :], ALU.add)
                    if m < 3:
                        own.then(t)
                t.then_inc(mg_done, 1)
            own.end(4)
            split_lo(mrg, mhi, mlo)
            with dve.Fori(0, 4) as it:
                lo(C0["wout"] + it * 16, range(LA, 16 + LA))

            def residual(dst, src, g0, post, ready):
                own.then(TT(cf[:, :], mod1[:, g0:g0 + 16, 0], V(post, 0, 16), ALU.mult))
                rs = norm_scale()
                if ready:
                    ready()
                for k in range(DC):
                    if k % 4 == 0:
                        own.then(TT(src[:, k:k + 4, :], src[:, k:k + 4, :], rs[:, 0:TOK].unsqueeze(1).to_broadcast([P, 4, TOK]), ALU.mult))
                    STT(dst(k), src[:, k, :], cf[:, k:k + 1], x1[:, k, :], ALU.mult, ALU.add).then_inc(x1_done, 1)

            def gains(mod, s, g, n=DC):
                own.then(STT(gain[:, :, :], mod[:, s:s + DC, :], 1.0, g.unsqueeze(2).to_broadcast([P, DC, 2]), ALU.add, ALU.mult))

            dve.wait_ge(mod_ready, A0["ffn0"])
            residual(lambda k: x1[:, k, :], wo, 32, "mix_post", lambda: dve.wait_ge(x1_in, 16))
            gains(mod1, 64, V("ffn_pre", 0, 16))
            rs = norm_scale()
            modulated(DC, TOK, lambda k: x1[:, k, :], nap3, rs, lambda k, j: mod1[:, 48 + k, j:j + 1],
                      lambda k: fhi[:, k, :], lambda k: flo[:, k, :], C0["ffn0"])

            def conv(b, g, c, before_last=None):
                for m in range(4):
                    if m == 3 and before_last:
                        before_last()
                    lo(c, range(16 + 2 * m + LA, 18 + 2 * m + LA))
                    w = lambda j: Vd(f"conv_w{j}", g * 4 + m)
                    dve.wait_ge(blk_free, b + m + 1)
                    own.then(TS(ge[:, m, :], gpad[:, m, 0:TOK], w(0), None, ALU.mult))
                    own.then(STT(ge[:, m, :], gpad[:, m, 1:TOK + 1], w(1), ge[:, m, :], ALU.mult, ALU.add))
                    STT(ge[:, m, :], gpad[:, m, 2:TOK + 2], w(2), ge[:, m, :], ALU.mult, ALU.add).then_inc(cv_done, 1)

            def gated(c_end, d0, g):
                for m in range(4):
                    block_done(c_end, d0, m, 4)
                    dve.wait_ge(ge_done, g * 4 + m + 1)
                    TT(ge[:, m, :], ge[:, m, :], PS[4 + m][:, 0:TOK], ALU.mult).then_inc(blk_free, 1)
                for m in range(4):
                    dve.wait_ge(u_hi, g * 4 + m + 1)
                    TT(ulo[:, m, :], ge[:, m, :], uhi[:, m, :].bitcast(F32), ALU.subtract).then_inc(u_lo, 1)

            def add_up(c0, lc0, d0, n):
                for m in range(4):
                    block_done(c0 + lc0 + 4 * n + 4, d0 + 3 * n, m, 4)
                    k = 4 * n + m
                    TT(yffn[:, k, :], yffn[:, k, :], PS[(n + 1) % 2 * 4 + m][:, 0:TOK], ALU.add).then_inc(dn_free, 1)

            def down(c0, lc0, d0, first):
                for n in range(first, 4):
                    if n != 1 or first == 0:
                        lo(c0, range(lc0 + 4 * n + LA, lc0 + 4 * n + 4 + LA))
                    add_up(c0, lc0, d0, n)

            own.then(dve.memset(yffn[:, :, :], 0.0))
            dve.memset(gpad[:, :, :], 0.0).then_inc(ff_zero, 1)
            c, d0 = C0["ffn0"], D1["ffn0"]
            lo(c, range(LA + 14, 16 + LA))
            conv(B0["ffn0"], 0, c)
            lo(c, range(24 + LA, 32 + LA))
            gated(c + 32, d0 + 3, 0)
            with dve.Fori(0, 10) as it:
                own.loop(it, 8)
                c, d0 = C0["ffn"] + it * 48, D1["ffn"] + it * 18
                lo(c, range(LA, 16 + LA))
                conv(B0["ffn"] + it * 8, it + 1, c, lambda: add_up(c, 16, d0 + 3, 0))
                down(c, 16, d0 + 3, 1)
                dve.wait_ge(dn_free, it * 16 + 16)
                lo(c, range(32 + LA, 48 + LA))
                gated(c + 48, d0 + 15, it + 1)
            own.end(10)
            down(C0["ffn1"], 0, D1["ffn1"], 0)

            dve.wait_ge(dn_free, 176)
            own.then(TT(lam[:, 0:4].rearrange("p (a b) -> p a b", b=1), V("lambda", 0, 8).rearrange("p (a b) -> p a b", b=2)[:, :, 0:1],
                        V("lambda", 0, 8).rearrange("p (a b) -> p a b", b=2)[:, :, 1:2], ALU.mult))
            for l in range(2):
                t = TS(sub2[:, l:l + 1], V("subln", l), 1.0 - LAM_INIT[l], None, ALU.mult)
                if l == 0:
                    own.then(t)
            t.then_inc(lam_pr, 1)
            residual(lambda k: xall[:, k, TOK:T2], yffn, 80, "ffn_post", None)
            dve.wait_ge(lam_e, 1)
            for l in range(2):
                own.then(TT(lam[:, 4 + l:5 + l], lam[:, 2 * l:2 * l + 1], lam[:, 2 * l + 1:2 * l + 2], ALU.subtract))
                own.then(TS(lam[:, 4 + l:5 + l], lam[:, 4 + l:5 + l], LAM_INIT[l], None, ALU.add))
            dve.wait_ge(mod_ready, A0["ffn1"])
            for l in range(2):
                gains(mod2, 48 * l + 16, V("norm_2", 16 * l, 16))
                rs = norm_scale()
                modulated(DC, T2, lambda k: xall[:, k, :], nap6, rs, lambda k, j: mod2[:, 48 * l + k, j:j + 1],
                          lambda k: hhi[:, :, k, :], lambda k: hlo[:, :, k, :], C0[f"poolv{l}"])
                T = T2 if l == 0 else TOK
                t0 = T2 - T
                units = UNITS[l]
                dve.wait_ge(n_lo, (3 + l) * DC + 8)
                dve.wait_ge(x2_saved, 16 * l + 16)
                dve.memset(xp[:, :, :, :], 0.0).then_inc(xp_zero, 1)
                sq_ = slice(0, 2) if l == 0 else slice(1, 2)
                L = TOK + 32
                for it in range(2):
                    lo(C0[f"poolv{l}"] + it * 16, range(LA if it else LA + 14, 16 + LA))
                    for m in range(4):
                        n = 8 * l + it * 4 + m
                        g = it * 2 + m // 2
                        dve.wait_ge(blk_free, B0[f"poolv{l}"] + it * 4 + m + 1)
                        x_ = xp[:, m % 2, sq_, :]
                        own.then(TT(sw[:, 0, sq_, 1:L], x_[:, :, 0:L - 1], x_[:, :, 1:L], ALU.add))
                        a, cur = 1, 0
                        for j in range(g):
                            s = 1 << j
                            own.then(TT(sw[:, 1 - cur, sq_, a + s:L - a - s], sw[:, cur, sq_, a:L - a - 2 * s], sw[:, cur, sq_, a + 2 * s:L - a], ALU.add))
                            a, cur = a + s, 1 - cur
                        inv_ = C("invcnt", g * TOK, g * TOK + TOK).unsqueeze(1).to_broadcast([P, T // TOK, TOK])
                        own.then(TT(sw[:, 1 - cur, sq_, 16:16 + TOK], sw[:, cur, sq_, 16:16 + TOK], inv_, ALU.mult))
                        if it == 1 and m < 2:
                            dve.wait_ge(pw_mm, 4 * l + 2)
                        TT(pl[:, m, 0:T].rearrange("p (s t) -> p s t", t=TOK), sw[:, 1 - cur, sq_, 16:16 + TOK], x_[:, :, 16:16 + TOK], ALU.subtract).then_inc(pl_done, 1)
                        dve.wait_ge(pl_done, n + 1)
                    for g in range(2):
                        dve.wait_ge(pw_mm, 4 * l + it * 2 + g + 1)
                        for j in range(2):
                            k = it * 4 + g * 2 + j
                            TS(mix[:, k, t0:T2], PS[5 + j][:, 0:T], V("pool_scale", 8 * l + k), None, ALU.mult).then_inc(pm_done, 1)
                for i in range(2):
                    t = TS(rotw[:, i, :], rot, V(("qn_2", "kn_2")[i], l), None, ALU.mult)
                t.then_inc(rotw_ok, 1)
                with dve.Fori(0, 2) as it:
                    own.loop(it, AT_OWN[l])
                    c = C0[f"qkv{l}"] + it * 48
                    step = [0]
                    pe_at = lambda n: dve.wait_ge(at_pe[l], at(AT_PE[l], n, it))
                    act_at = lambda n: dve.wait_ge(at_act[l], at(AT_ACT[l], n, it))

                    def done(ins, label):
                        assert AT_DVE[l][step[0]] == label, (AT_DVE[l][step[0]], label)
                        step[0] += 1
                        ins.then_inc(at_dve[l], 1)
                        dve.wait_ge(at_dve[l], at(AT_DVE[l], label, it))

                    def ropes(bs):
                        for b in bs:
                            g = V("qn_2" if b < 4 else "kn_2", l)
                            act_at(f"sq{b}")
                            pe_at(f"r{b}")
                            own.then(STT(rope2[:, 0, :], qk[:, b, TOK:T2], g, cos, ALU.mult, ALU.mult))
                            own.then(TT(rope2[:, 1, :], PS[(4, 6, 7)[b % 3]][:, 0:TOK], sin, ALU.mult))
                            done(TT(qk[:, b, TOK:T2], rope2[:, 0, :], rope2[:, 1, :], ALU.add), f"t{b}")

                    if l:
                        done(dve.memset(sq2[:, :, 0:TOK], 0.0), "z")
                    lo(c, range(LA, 41))
                    ropes((0, 1, 2))
                    lo(c, range(41, 45))
                    ropes((3, 4, 5))
                    lo(c, range(45, 48))
                    ropes((6, 7))
                    lo(c, range(48, 48 + LA))
                    act_at("rt")
                    done(dve.reciprocal(rs2[:, :], rs2[:, :]), "rc")
                    for i, b in enumerate(QK_HEADS):
                        g = V("qn_2" if b < 4 else "kn_2", l)
                        pe_at(f"c{b}")
                        if b >= 4 or l == 0:
                            own.then(STT(qk[:, b, 0:TOK], qk[:, b, 0:TOK], g, PS[4 + i % 4][:, 0:TOK], ALU.mult, ALU.mult))
                        done(TT(qk[:, b, TOK:T2], qk[:, b, TOK:T2], PS[4 + i % 4][:, TOK:T2], ALU.mult), f"f{b}")

                    def maxima(u):
                        nk = TOK if units[u][1] < 2 else T2
                        pe_at(f"S{u}")
                        s, k = 8 * (u % 3), 2 * (u % 3)
                        own.then(dve.reduce_max(smx2[:, s:s + 2], psum[:, k:k + 2, 0:nk], axis=AX.X))
                        done(TS(smx2[:, s + 2:s + 4], smx2[:, s:s + 2], -DIFF_SCALE, None, ALU.mult), f"mx{u}")

                    for u in range(-2, len(units) + 1):
                        if 0 <= u < len(units):
                            nk = TOK if units[u][1] < 2 else T2
                            s, k = 8 * (u % 3), u % 3
                            act_at(f"e{u}")
                            own.then(dve.reciprocal(smx2[:, s + 6:s + 8], smx2[:, s + 4:s + 6]))
                            own.then(TT(smx2[:, s + 7:s + 8], smx2[:, s + 7:s + 8], lam[:, 4 + l:5 + l], ALU.mult))
                            own.then(TS(pr[:, k, 1, 0:nk], pr[:, k, 1, 0:nk], smx2[:, s + 7:s + 8], None, ALU.mult))
                            done(STT(pr[:, k, 0, 0:nk], pr[:, k, 0, 0:nk], smx2[:, s + 6:s + 7], pr[:, k, 1, 0:nk], ALU.mult, ALU.subtract), f"a{u}")
                        if u + 2 < len(units):
                            maxima(u + 2)
                    act_at("rto")
                    done(dve.reciprocal(rs2[:, t0:T2], rs2[:, t0:T2]), "rco")
                    for h in range(4):
                        n = bass.ds(it * 4 + 8 + h, 1)
                        pe_at(f"co{h}")
                        done(STT(mix[:, n, t0:T2], mix[:, n, t0:T2], sub2[:, l:l + 1], PS[h][:, t0:T2].unsqueeze(1), ALU.mult, ALU.mult), f"fo{h}")
                own.end(2)
                dve.wait_ge(pm_done, 8 * l + 8)
                for i, name in enumerate(("poolg", "attng")):
                    with dve.Fori(0, 2) as it:
                        lo(C0[f"{name}{l}"] + it * 16, range(LA, 16 + LA))
                        for m in range(4):
                            dve.wait_ge(blk_free, B0[f"{name}{l}"] + it * 4 + m + 1)
                            n = bass.ds(it * 4 + 8 * i + m, 1)
                            TT(mix[:, n, t0:T2], mix[:, n, t0:T2], stmp[:, m % 2, 0:T].unsqueeze(1), ALU.mult).then_inc(sg_done, 1)
                dve.wait_ge(sg_done, 16 * l + 16)
                split_lo(mix[:, :, t0:T2], mixhi[:, :, t0:T2], mixlo[:, :, t0:T2], 2)
                dve.wait_ge(x2_in, 16 * l + 16)

                def out_add(it, ahead):
                    own.loop(it, 4 if l == 0 else 0)
                    c = C0[f"out{l}"] + it * 16
                    lo(c, range(LA, 16 + ahead))
                    for m in range(4):
                        block_done(c + 16, D1[f"out{l}"] + it * 3, m, 4)
                        n = bass.ds(it * 4 + m, 1)
                        gate = lambda j: mod2[:, bass.ds(it * 4 + 48 * l + 32 + m, 1), j:j + 1].rearrange("p a b -> p (a b)")
                        if l == 0:
                            own.then(STT(xall[:, n, 0:TOK], PS[m][:, 0:TOK].unsqueeze(1), gate(1), xall[:, n, 0:TOK], ALU.mult, ALU.add))
                        STT(xall[:, n, TOK:T2], PS[m][:, T - TOK:T].unsqueeze(1), gate(0), xall[:, n, TOK:T2], ALU.mult, ALU.add).then_inc(blk_free, 1)

                with dve.Fori(0, 4 if l == 0 else 3) as it:
                    out_add(it, LA)
                own.end(4)
                if l == 1:
                    out_add(3, 0)
                dve.wait_ge(blk_free, B0[f"out{l}"] + 16)



def layout(x):
    def fm(v, n=P):
        v = v.reshape(-1, n).T
        return v if n == P else np.concatenate([v, np.zeros((P - n, v.shape[1]), np.float32)], 0)

    mu = x["rwkv_mu"][0]
    lams = [x[f"lambda_{n}_2"][l] for l in range(2) for n in ("q1", "k1", "q2", "k2")]
    vec = [fm(x["b_ada"][0]), fm(x["norm_mix_pre"][0]), fm(x["norm_mix_post"][0]), fm(x["norm_ffn_pre"][0]),
           fm(x["norm_ffn_post"][0]), fm(x["gate_b"][0]), fm(x["ffn_conv_w"][0, 0]), fm(x["ffn_conv_w"][0, 1]),
           fm(x["ffn_conv_w"][0, 2]), fm(x["ffn_conv_b"][0]), fm(x["mla_q_norm"][0]), fm(x["mla_kv_norm"][0]),
           fm(mu[:3 * RW]), fm(mu[3 * RW:3 * RW + 4 * LORA], LORA), fm(mu[3 * RW + 4 * LORA:]),
           fm(x["b_ada_2"]), fm(x["norm_w_2"]), fm(x["pool_scale_2"]),
           np.concatenate([fm(x["q_norm_w_2"], 64)[:64]] * 2, 0), np.concatenate([fm(x["k_norm_w_2"], 64)[:64]] * 2, 0),
           fm(x["subln_w_2"]), fm(np.stack(lams), 64)]
    vec = np.ascontiguousarray(np.concatenate(vec, 1))
    assert vec.shape == (P, VCOLS)
    pair = [x["rwkv_w0"][0, 0], x["rwkv_w0"][0, 1], x["rwkv_a0"][0, 0], x["rwkv_a0"][0, 1], x["rwkv_k_k"][0],
            x["rwkv_k_a"][0], x["rwkv_r_k"][0].reshape(-1), x["rwkv_lnx_w"][0], x["rwkv_lnx_b"][0]]
    pvec = np.stack([fm(v).T for v in pair], 2)
    pvec = np.concatenate([pvec, np.zeros_like(pvec[:1])], 0)

    def two(a, b):
        return np.stack([a.reshape(DC, P).T, b.reshape(DC, P).T], 2)

    cT = np.ascontiguousarray(np.stack([two(x["c"], x["c_ctx"]), two(x["c_2"], x["c_ctx_2"])], 1))
    uq = x["mla_w_uq"][0].reshape(512, 8, 2, 192)
    uq = np.concatenate([uq[..., :128].reshape(512, 8, 256), uq[..., 128:].reshape(512, 8, 128)], 2).reshape(512, 8 * 384)
    ukv = x["mla_w_ukv"][0].reshape(512, 8, 2, 2, 128).transpose(0, 1, 3, 2, 4).reshape(512, 8 * 512)
    w_in = x["w_in"][0]
    kpe = w_in[:, MLA0 + 1024:MLA0 + 1088]
    lora = lambda w: np.concatenate([w[0].transpose(1, 0, 2), np.zeros((LORA, 2, P), np.float32)], 2)
    return {"consts": constants(), "hconsts": head_constants(), "vec": vec, "pvec": pvec, "cT": cT, "x": x["x"][0], "ctx": x["ctx"][0], "ctx_2": x["ctx_2"][0],
            "w_ada": x["w_ada"][0], "w_in": w_in, "w_kpe": np.ascontiguousarray(np.concatenate([kpe, kpe], 1)),
            "w_uq": np.ascontiguousarray(uq), "w_ukv": np.ascontiguousarray(ukv), "w2": lora(x["rwkv_w2"]), "a2": lora(x["rwkv_a2"]),
            "g2": x["rwkv_g2"][0], "w_rwkv_proj": x["w_rwkv_proj"][0], "w_mla_proj": x["w_mla_proj"][0], "w_out": x["w_out"][0],
            "w_gate": x["ffn_w_gate"][0], "w_val": x["ffn_w_val"][0], "w_down": x["ffn_w_down"][0],
            "w_ada_2": np.ascontiguousarray(np.concatenate(list(x["w_ada_2"]), 1)), "w_in_2": x["w_in_2"], "pool_w": x["pool_w_2"], "w_out_2": x["w_out_2"]}


def kernel(**inputs):
    import concourse.bacc as bacc
    from concourse.bass_utils import run_bass_kernel_spmd

    arrays = layout({k: np.asarray(v) for k, v in inputs.items()})
    nc = bacc.Bacc("TRN2", target_bir_lowering=False, num_devices=1)
    A = {k: nc.dram_tensor(f"in_{k}", a.shape, F32, kind="ExternalInput").ap() for k, a in arrays.items()}
    out = nc.dram_tensor("out", (TOK, D), F32, kind="ExternalOutput").ap()
    build(nc, A, out)
    r = run_bass_kernel_spmd(nc, [{f"in_{k}": a for k, a in arrays.items()}], core_ids=[0])
    return r.results[0]["out"].reshape(1, TOK, D)
```
